# Optimizing a Trainium2 kernel written in Bass

```python
import jax, jax.numpy as jnp
from jax import lax
import numpy as np

D_MODEL = 1024
BATCH = 1
SEQ = 256
DEPTH = 1

SSD_INNER = 2 * D_MODEL
SSD_HEAD_DIM = 64
SSD_HEADS = SSD_INNER // SSD_HEAD_DIM
SSD_GROUPS = 8
SSD_HEADS_PER_GROUP = SSD_HEADS // SSD_GROUPS
SSD_STATE = 128
SSD_CONV = 4
SSD_CHUNK = 128
SSD_CONV_DIM = SSD_INNER + 2 * SSD_GROUPS * SSD_STATE
SC_WIDTH = D_MODEL
SC_KERNEL = 3
N_EXPERTS = 64
TOP_K = 8
N_EXPERT_GROUPS = 8
TOPK_EXPERT_GROUPS = 4
D_EXPERT = 256
ROUTED_SCALE = 2.5
MOE_BLOCK = 128
LN_EPS = 1e-5
RMS_EPS = 1e-5
ALPHA = (2.0 * DEPTH) ** 0.25
BETA = (8.0 * DEPTH) ** -0.25
_IN_SIZES = (SSD_INNER, SSD_CONV_DIM, SSD_HEADS, SC_WIDTH, SC_WIDTH, SC_WIDTH, D_MODEL, D_MODEL)
IN_COLS = int(sum(_IN_SIZES))
IN_SPLITS = [int(v) for v in np.cumsum(_IN_SIZES)[:-1]]


def layer_norm(x):
    xf = x.astype(jnp.float32)
    mu = jnp.mean(xf, axis=-1, keepdims=True)
    xc = xf - mu
    var = jnp.mean(xc * xc, axis=-1, keepdims=True)
    return xc * lax.rsqrt(var + LN_EPS)

def causal_depthwise_conv(u, w):
    k = w.shape[0]
    return lax.conv_general_dilated(
        u, w[:, None, :].astype(u.dtype), window_strides=(1,), padding=[(k - 1, 0)],
        dimension_numbers=("NWC", "WIO", "NWC"), feature_group_count=u.shape[-1])

def gated_rmsnorm(y, z, w):
    g = y.astype(jnp.float32) * jax.nn.silu(z.astype(jnp.float32))
    g = g.reshape(*y.shape[:-1], SSD_GROUPS, -1)
    g = g * lax.rsqrt(jnp.mean(g * g, axis=-1, keepdims=True) + RMS_EPS)
    return g.reshape(y.shape) * w.astype(jnp.float32)

def ssd_chunked(xg, dt, A, Bg, Cg):
    b, s, g, r, p = xg.shape
    n = Bg.shape[-1]
    nc = s // SSD_CHUNK
    l = SSD_CHUNK
    X = (xg * dt[..., None]).reshape(b, nc, l, g, r, p)
    dA = (dt * A).reshape(b, nc, l, g, r).transpose(0, 1, 3, 4, 2)
    Bc = Bg.reshape(b, nc, l, g, n)
    Cc = Cg.reshape(b, nc, l, g, n)
    A_cs = jnp.cumsum(dA, axis=-1)
    seg = A_cs[..., :, None] - A_cs[..., None, :]
    causal = jnp.tril(jnp.ones((l, l), dtype=bool))
    Lmat = jnp.exp(jnp.where(causal, seg, -jnp.inf))
    CB = jnp.einsum("bclgn,bcsgn->bcgls", Cc, Bc)
    scores = CB[:, :, :, None] * Lmat
    y_diag = jnp.einsum("bcgrls,bcsgrp->bclgrp", scores, X)
    decay_states = jnp.exp(A_cs[..., -1:] - A_cs).transpose(0, 1, 4, 2, 3)
    states = jnp.einsum("bclgn,bclgrp->bcgrpn", Bc, X * decay_states[..., None])
    chunk_decay = jnp.exp(A_cs[..., -1])

    def step(h, inp):
        st, dec = inp
        return dec[..., None, None] * h + st, h

    h0 = jnp.zeros((b, g, r, p, n), jnp.float32)
    _, prev = lax.scan(step, h0, (states.transpose(1, 0, 2, 3, 4, 5).astype(jnp.float32),
                                  chunk_decay.transpose(1, 0, 2, 3)))
    prev = prev.transpose(1, 0, 2, 3, 4, 5)
    out_decay = jnp.exp(A_cs).transpose(0, 1, 4, 2, 3)
    y_off = jnp.einsum("bclgn,bcgrpn->bclgrp", Cc, prev) * out_decay[..., None]
    return (y_diag + y_off).reshape(b, s, g, r, p)

def hybrid_mixer(h, w_in, ssd_conv_w, ssd_conv_b, ssd_dt_bias, ssd_A_log, ssd_D, ssd_norm_w,
                 w_ssd_out, sc_conv_w, w_sc_out, w_o):
    b, s, _ = h.shape
    z, xbc, dt_raw, sc_b, sc_c, sc_h, gate_a, gate_b = jnp.split(h @ w_in, IN_SPLITS, axis=-1)
    xbc = jax.nn.silu(causal_depthwise_conv(xbc, ssd_conv_w) + ssd_conv_b)
    xs, Bm, Cm = jnp.split(xbc, [SSD_INNER, SSD_INNER + SSD_GROUPS * SSD_STATE], axis=-1)
    dt = jax.nn.softplus(dt_raw.astype(jnp.float32) + ssd_dt_bias.astype(jnp.float32))
    A = -jnp.exp(ssd_A_log.astype(jnp.float32))
    G, R = SSD_GROUPS, SSD_HEADS_PER_GROUP
    xg = xs.reshape(b, s, G, R, SSD_HEAD_DIM)
    y = ssd_chunked(xg, dt.reshape(b, s, G, R), A.reshape(G, R),
                    Bm.reshape(b, s, G, SSD_STATE), Cm.reshape(b, s, G, SSD_STATE))
    y = y + ssd_D.reshape(G, R)[:, :, None] * xg
    y = gated_rmsnorm(y.reshape(b, s, SSD_INNER), z, ssd_norm_w).astype(h.dtype)
    y_a = y @ w_ssd_out
    u = causal_depthwise_conv(sc_c * sc_h, sc_conv_w)
    y_b = (sc_b * u) @ w_sc_out
    merged = jax.nn.sigmoid(gate_a) * y_a + jax.nn.sigmoid(gate_b) * y_b
    return merged @ w_o

def moe_ffn(h, router_w, router_bias, w_gate, w_up, w_down, sh_gate, sh_up, sh_down):
    b, s, d = h.shape
    T = b * s
    hf = h.reshape(T, d)
    scores = jax.nn.sigmoid((hf @ router_w).astype(jnp.float32))
    biased = scores + router_bias.astype(jnp.float32)
    grp = biased.reshape(T, N_EXPERT_GROUPS, N_EXPERTS // N_EXPERT_GROUPS)
    grp_score = lax.top_k(grp, 2)[0].sum(-1)
    _, grp_idx = lax.top_k(grp_score, TOPK_EXPERT_GROUPS)
    grp_mask = jax.nn.one_hot(grp_idx, N_EXPERT_GROUPS, dtype=jnp.float32).sum(1) > 0
    expert_mask = jnp.repeat(grp_mask, N_EXPERTS // N_EXPERT_GROUPS, axis=1)
    _, e_idx = lax.top_k(jnp.where(expert_mask, biased, -jnp.inf), TOP_K)
    gate = jnp.take_along_axis(scores, e_idx, axis=1)
    gate = gate / jnp.sum(gate, axis=-1, keepdims=True) * ROUTED_SCALE
    n_assign = T * TOP_K
    nb = (n_assign + MOE_BLOCK - 1) // MOE_BLOCK + N_EXPERTS
    n_rows = nb * MOE_BLOCK
    e_flat = e_idx.reshape(-1)
    tok_flat = jnp.arange(n_assign, dtype=jnp.int32) // TOP_K
    order = jnp.argsort(e_flat)
    e_sorted = e_flat[order]
    tok_sorted = tok_flat[order]
    gate_sorted = gate.reshape(-1)[order]
    counts = jnp.bincount(e_flat, length=N_EXPERTS)
    padded = (counts + MOE_BLOCK - 1) // MOE_BLOCK * MOE_BLOCK
    start = jnp.cumsum(counts) - counts
    pend = jnp.cumsum(padded)
    pstart = pend - padded
    dest = pstart[e_sorted] + (jnp.arange(n_assign) - start[e_sorted])
    row_tok = jnp.full((n_rows,), T, jnp.int32).at[dest].set(tok_sorted)
    row_gate = jnp.zeros((n_rows,), jnp.float32).at[dest].set(gate_sorted)
    block_expert = jnp.minimum(
        jnp.searchsorted(pend, jnp.arange(nb) * MOE_BLOCK, side="right"), N_EXPERTS - 1)
    h_pad = jnp.concatenate([hf, jnp.zeros((1, d), hf.dtype)], axis=0)
    xin = h_pad[row_tok].reshape(nb, MOE_BLOCK, d)

    def expert_block(args):
        xb, e = args
        return (jax.nn.silu(xb @ w_gate[e]) * (xb @ w_up[e])) @ w_down[e]

    yb = lax.map(expert_block, (xin, block_expert)).reshape(n_rows, d)
    routed = jax.ops.segment_sum(yb * row_gate[:, None], row_tok, num_segments=T + 1)[:T]
    shared = (jax.nn.silu(hf @ sh_gate) * (hf @ sh_up)) @ sh_down
    return (routed + shared).reshape(b, s, d)

def first_inputs(seed: int = 0) -> dict:
    key = jax.random.key(seed)
    ks = jax.random.split(key, 32)
    L, D, E = DEPTH, D_MODEL, N_EXPERTS
    f32 = jnp.float32

    def nrm(k, shape, fan_in, scale=1.0):
        return jax.random.normal(k, shape, f32) * (scale * fan_in ** -0.5)

    u = jax.random.uniform(ks[5], (L, SSD_HEADS), f32)
    dt0 = jnp.exp(u * (np.log(0.1) - np.log(1e-3)) + np.log(1e-3))
    return {
        "x": jax.random.normal(ks[0], (BATCH, SEQ, D), f32),
        "c": jax.random.normal(ks[1], (BATCH, D), f32),
        "w_ada": nrm(ks[2], (L, D, 6 * D), D),
        "b_ada": 0.02 * jax.random.normal(ks[3], (L, 6 * D), f32),
        "w_in": nrm(ks[4], (L, D, IN_COLS), D),
        "ssd_conv_w": nrm(ks[6], (L, SSD_CONV, SSD_CONV_DIM), SSD_CONV),
        "ssd_conv_b": 0.02 * jax.random.normal(ks[7], (L, SSD_CONV_DIM), f32),
        "ssd_dt_bias": dt0 + jnp.log(-jnp.expm1(-dt0)),
        "ssd_A_log": jnp.log(jax.random.uniform(ks[8], (L, SSD_HEADS), f32, 1.0, 16.0)),
        "ssd_D": 1.0 + 0.1 * jax.random.normal(ks[9], (L, SSD_HEADS), f32),
        "ssd_norm_w": 1.0 + 0.1 * jax.random.normal(ks[10], (L, SSD_INNER), f32),
        "w_ssd_out": nrm(ks[11], (L, SSD_INNER, D), SSD_INNER, BETA),
        "sc_conv_w": nrm(ks[12], (L, SC_KERNEL, SC_WIDTH), SC_KERNEL),
        "w_sc_out": nrm(ks[13], (L, SC_WIDTH, D), SC_WIDTH, BETA),
        "w_o": nrm(ks[14], (L, D, D), D, BETA),
        "ln1_g": 1.0 + 0.1 * jax.random.normal(ks[15], (L, D), f32),
        "ln1_b": 0.02 * jax.random.normal(ks[16], (L, D), f32),
        "router_w": nrm(ks[17], (L, D, E), D),
        "router_bias": 0.01 * jax.random.normal(ks[18], (L, E), f32),
        "w_gate": nrm(ks[19], (L, E, D, D_EXPERT), D, BETA),
        "w_up": nrm(ks[20], (L, E, D, D_EXPERT), D, BETA),
        "w_down": nrm(ks[21], (L, E, D_EXPERT, D), D_EXPERT, BETA),
        "sh_gate": nrm(ks[22], (L, D, D_EXPERT), D, BETA),
        "sh_up": nrm(ks[23], (L, D, D_EXPERT), D, BETA),
        "sh_down": nrm(ks[24], (L, D_EXPERT, D), D_EXPERT, BETA),
        "ln2_g": 1.0 + 0.1 * jax.random.normal(ks[25], (L, D), f32),
        "ln2_b": 0.02 * jax.random.normal(ks[26], (L, D), f32),
    }

def first_block(x, c, w_ada, b_ada, w_in, ssd_conv_w, ssd_conv_b, ssd_dt_bias, ssd_A_log, ssd_D,
              ssd_norm_w, w_ssd_out, sc_conv_w, w_sc_out, w_o, ln1_g, ln1_b, router_w,
              router_bias, w_gate, w_up, w_down, sh_gate, sh_up, sh_down, ln2_g, ln2_b):
    dtype = x.dtype
    for l in range(DEPTH):
        mod = jax.nn.silu(c) @ w_ada[l] + b_ada[l]
        sh1, sc1, g1, sh2, sc2, g2 = jnp.split(mod[:, None, :], 6, axis=-1)
        h = (layer_norm(x) * (1.0 + sc1) + sh1).astype(dtype)
        mix = hybrid_mixer(h, w_in[l], ssd_conv_w[l], ssd_conv_b[l], ssd_dt_bias[l], ssd_A_log[l],
                           ssd_D[l], ssd_norm_w[l], w_ssd_out[l], sc_conv_w[l], w_sc_out[l], w_o[l])
        x = (layer_norm(ALPHA * x + g1 * mix) * ln1_g[l] + ln1_b[l]).astype(dtype)
        h = (layer_norm(x) * (1.0 + sc2) + sh2).astype(dtype)
        ffn = moe_ffn(h, router_w[l], router_bias[l], w_gate[l], w_up[l], w_down[l],
                      sh_gate[l], sh_up[l], sh_down[l])
        x = (layer_norm(ALPHA * x + g2 * ffn) * ln2_g[l] + ln2_b[l]).astype(dtype)
    return x


DEPTH_2 = 2

HEAD_DIM = 64
FOX_HEADS = 8
FOX_WIDTH = FOX_HEADS * HEAD_DIM
POOL_GROUPS = 4
POOL_WINDOWS = (2, 4, 8, 16)
POOL_WIDTH = D_MODEL - FOX_WIDTH
POOL_GROUP_DIM = POOL_WIDTH // POOL_GROUPS
Q_BLOCK = 128
IN_COLS_2 = 4 * FOX_WIDTH + FOX_HEADS + POOL_WIDTH
SPLITS = (FOX_WIDTH, 2 * FOX_WIDTH, 3 * FOX_WIDTH, 4 * FOX_WIDTH, 4 * FOX_WIDTH + FOX_HEADS)
RWKV_HEADS = D_MODEL // HEAD_DIM
DECAY_LORA = 64
AAA_LORA = 64
MV_LORA = 32
GATE_LORA = 160
D_FF = -(-(8 * D_MODEL) // (3 * 256)) * 256
RMS_EPS_2 = 1e-6
GN_EPS = 64e-5
N_EVEN = (DEPTH_2 + 1) // 2
N_ODD = DEPTH_2 // 2


def _rmsnorm(x, gain):
    xf = x.astype(jnp.float32)
    y = xf * lax.rsqrt(jnp.mean(xf * xf, axis=-1, keepdims=True) + RMS_EPS_2)
    return (y * gain.astype(jnp.float32)).astype(x.dtype)

def _swiglu(h, w_gate, w_up, w_down):
    return (jax.nn.silu(h @ w_gate) * (h @ w_up)) @ w_down

def _token_shift(x):
    return jnp.pad(x, ((0, 0), (1, 0), (0, 0)))[:, :-1]

def _forgetting_attention(q, k, v, cum):
    b, h, s, dh = q.shape
    nb = s // Q_BLOCK
    scale = dh ** -0.5
    qb = q.reshape(b, h, nb, Q_BLOCK, dh).transpose(2, 0, 1, 3, 4)
    cb = cum.reshape(b, h, nb, Q_BLOCK).transpose(2, 0, 1, 3)
    key_pos = jnp.arange(s)

    def one_block(args):
        i, q_i, c_i = args
        q_pos = i * Q_BLOCK + jnp.arange(Q_BLOCK)
        logits = (jnp.einsum('bhqd,bhkd->bhqk', q_i, k).astype(jnp.float32) * scale
                  + c_i[..., :, None] - cum[..., None, :])
        causal = key_pos[None, :] <= q_pos[:, None]
        p = jax.nn.softmax(jnp.where(causal, logits, -1e30), axis=-1)
        return jnp.einsum('bhqk,bhkd->bhqd', p.astype(v.dtype), v)

    out = lax.map(one_block, (jnp.arange(nb), qb, cb))
    return out.transpose(1, 2, 0, 3, 4).reshape(b, h, s, dh)

def _multiscale_causal_pool(u, pool_w, pool_scale):
    b, s, _ = u.shape
    uf = u.astype(jnp.float32).reshape(b, s, POOL_GROUPS, POOL_GROUP_DIM)
    csum = jnp.cumsum(uf, axis=1)
    pos = jnp.arange(s)
    groups = []
    for g, w in enumerate(POOL_WINDOWS):
        cg = csum[:, :, g]
        prev = jnp.pad(cg, ((0, 0), (w, 0), (0, 0)))[:, :s]
        count = jnp.minimum(pos + 1, w).astype(jnp.float32)[None, :, None]
        groups.append((cg - prev) / count - uf[:, :, g])
    pooled = jnp.stack(groups, axis=2).astype(u.dtype)
    mixed = jnp.einsum('bsgc,gcd->bsgd', pooled, pool_w)
    return mixed.reshape(b, s, POOL_WIDTH) * pool_scale

def _fox_pool_mixer(h, w_in, f_bias, q_gain, k_gain, pool_w, pool_scale, w_out):
    b, s, _ = h.shape
    proj = h @ w_in
    q, k, v, og, f_logit, u = jnp.split(proj, SPLITS, axis=-1)

    def heads(t):
        return t.reshape(b, s, FOX_HEADS, HEAD_DIM)

    q = _rmsnorm(heads(q), q_gain).transpose(0, 2, 1, 3)
    k = _rmsnorm(heads(k), k_gain).transpose(0, 2, 1, 3)
    v = heads(v).transpose(0, 2, 1, 3)
    log_f = jax.nn.log_sigmoid(f_logit.astype(jnp.float32) + f_bias.astype(jnp.float32))
    cum = jnp.cumsum(log_f, axis=1).transpose(0, 2, 1)
    attn = _forgetting_attention(q, k, v, cum).transpose(0, 2, 1, 3).reshape(b, s, FOX_WIDTH)
    attn = attn * jax.nn.sigmoid(og)
    pool = _multiscale_causal_pool(u, pool_w, pool_scale)
    return jnp.concatenate([attn, pool], axis=-1) @ w_out

def _rwkv7_step(state, inp):
    r_t, w_t, k_t, v_t, a_t, b_t = inp
    sa = jnp.einsum('bhvk,bhk->bhv', state, a_t)
    state = (state * w_t[:, :, None, :] + sa[..., None] * b_t[:, :, None, :]
             + v_t[..., None] * k_t[:, :, None, :])
    return state, jnp.einsum('bhvk,bhk->bhv', state, r_t)

def _rwkv7_time_mix(h, mu, w_r, w_k, w_v, w0, w1, w2, a0, a1, a2, g1, g2,
                    k_k, k_a, r_k, ln_w, ln_b, w_o, v_first, v_mix):
    b, s, d = h.shape
    f32 = jnp.float32
    xx = _token_shift(h) - h
    xr, xw, xk, xv, xa, xg = [h + xx * mu[i] for i in range(6)]
    r = (xr @ w_r).astype(f32)
    k = (xk @ w_k).astype(f32)
    v = (xv @ w_v).astype(f32)
    w = -jax.nn.softplus(-(w0 + jnp.tanh(xw @ w1) @ w2).astype(f32)) - 0.5
    a = jax.nn.sigmoid((a0 + (xa @ a1) @ a2).astype(f32))
    g = jax.nn.sigmoid(xg @ g1) @ g2
    if v_mix is None:
        v_first = v
    else:
        v0, v1, v2 = v_mix
        v = v + (v_first - v) * jax.nn.sigmoid((v0 + (xv @ v1) @ v2).astype(f32))

    def heads(t):
        return t.reshape(b, s, RWKV_HEADS, HEAD_DIM)

    kk = heads(k * k_k.astype(f32))
    kk = kk / jnp.maximum(jnp.sqrt(jnp.sum(kk * kk, axis=-1, keepdims=True)), 1e-12)
    k = k * (1.0 + (a - 1.0) * k_a.astype(f32))
    decay = jnp.exp(-jnp.exp(w))
    rh, kh, vh, ah = heads(r), heads(k), heads(v), heads(a)
    seq_first = lambda t: t.transpose(1, 0, 2, 3)
    xs = (seq_first(rh), seq_first(heads(decay)), seq_first(kh), seq_first(vh),
          seq_first(-kk), seq_first(kk * ah))
    state0 = jnp.zeros((b, RWKV_HEADS, HEAD_DIM, HEAD_DIM), f32)
    _, ys = lax.scan(_rwkv7_step, state0, xs)
    y = ys.transpose(1, 0, 2, 3)
    mean = jnp.mean(y, axis=-1, keepdims=True)
    var = jnp.mean(jnp.square(y - mean), axis=-1, keepdims=True)
    y = ((y - mean) * lax.rsqrt(var + GN_EPS)).reshape(b, s, d) * ln_w.astype(f32) + ln_b.astype(f32)
    bonus = jnp.sum(rh * kh * r_k.astype(f32), axis=-1, keepdims=True) * vh
    y = (y + bonus.reshape(b, s, d)).astype(h.dtype)
    return (y * g) @ w_o, v_first

def second_inputs(seed: int = 0) -> dict:
    key = jax.random.key(seed)
    keys = jax.random.split(key, 40)
    counter = [0]
    f32 = jnp.float32

    def nk():
        counter[0] += 1
        return keys[counter[0] - 1]

    def nrm(shape, scale):
        return jax.random.normal(nk(), shape, f32) * scale

    def gain(shape):
        return 1.0 + 0.1 * jax.random.normal(nk(), shape, f32)

    D, F, ne, no = D_MODEL, D_FF, N_EVEN, N_ODD
    return {
        'x': nrm((BATCH, SEQ, D), 1.0),
        'mix_norm': gain((DEPTH_2, D)),
        'ffn_norm': gain((DEPTH_2, D)),
        'ffn_w_gate': nrm((DEPTH_2, D, F), D ** -0.5),
        'ffn_w_up': nrm((DEPTH_2, D, F), D ** -0.5),
        'ffn_w_down': nrm((DEPTH_2, F, D), F ** -0.5),
        'hy_w_in': nrm((ne, D, IN_COLS_2), D ** -0.5),
        'hy_f_bias': 2.0 + 0.5 * jax.random.normal(nk(), (ne, FOX_HEADS), f32),
        'hy_q_gain': gain((ne, HEAD_DIM)),
        'hy_k_gain': gain((ne, HEAD_DIM)),
        'hy_pool_w': nrm((ne, POOL_GROUPS, POOL_GROUP_DIM, POOL_GROUP_DIM), POOL_GROUP_DIM ** -0.5),
        'hy_pool_scale': gain((ne, POOL_WIDTH)),
        'hy_w_out': nrm((ne, D, D), D ** -0.5),
        'rw_mu': jax.random.uniform(nk(), (no, 6, D), f32),
        'rw_w_r': nrm((no, D, D), D ** -0.5),
        'rw_w_k': nrm((no, D, D), D ** -0.5),
        'rw_w_v': nrm((no, D, D), D ** -0.5),
        'rw_w0': nrm((no, D), 0.5),
        'rw_w1': nrm((no, D, DECAY_LORA), D ** -0.5),
        'rw_w2': nrm((no, DECAY_LORA, D), 0.5 * DECAY_LORA ** -0.5),
        'rw_a0': nrm((no, D), 0.5),
        'rw_a1': nrm((no, D, AAA_LORA), D ** -0.5),
        'rw_a2': nrm((no, AAA_LORA, D), 0.5 * AAA_LORA ** -0.5),
        'rw_g1': nrm((no, D, GATE_LORA), D ** -0.5),
        'rw_g2': nrm((no, GATE_LORA, D), GATE_LORA ** -0.5),
        'rw_k_k': gain((no, D)),
        'rw_k_a': gain((no, D)),
        'rw_r_k': nrm((no, RWKV_HEADS, HEAD_DIM), 0.1),
        'rw_ln_w': gain((no, D)),
        'rw_ln_b': nrm((no, D), 0.02),
        'rw_w_o': nrm((no, D, D), D ** -0.5),
        'rw_v0': nrm((max(no - 1, 0), D), 0.5),
        'rw_v1': nrm((max(no - 1, 0), D, MV_LORA), D ** -0.5),
        'rw_v2': nrm((max(no - 1, 0), MV_LORA, D), 0.5 * MV_LORA ** -0.5),
    }

def second_block(x, mix_norm, ffn_norm, ffn_w_gate, ffn_w_up, ffn_w_down,
              hy_w_in, hy_f_bias, hy_q_gain, hy_k_gain, hy_pool_w, hy_pool_scale, hy_w_out,
              rw_mu, rw_w_r, rw_w_k, rw_w_v, rw_w0, rw_w1, rw_w2, rw_a0, rw_a1, rw_a2,
              rw_g1, rw_g2, rw_k_k, rw_k_a, rw_r_k, rw_ln_w, rw_ln_b, rw_w_o,
              rw_v0, rw_v1, rw_v2):
    v_first = None
    for layer in range(DEPTH_2):
        h = _rmsnorm(x, mix_norm[layer])
        if layer % 2 == 0:
            e = layer // 2
            y = _fox_pool_mixer(h, hy_w_in[e], hy_f_bias[e], hy_q_gain[e], hy_k_gain[e],
                                hy_pool_w[e], hy_pool_scale[e], hy_w_out[e])
        else:
            o = layer // 2
            v_mix = None if o == 0 else (rw_v0[o - 1], rw_v1[o - 1], rw_v2[o - 1])
            y, v_first = _rwkv7_time_mix(h, rw_mu[o], rw_w_r[o], rw_w_k[o], rw_w_v[o],
                                         rw_w0[o], rw_w1[o], rw_w2[o], rw_a0[o], rw_a1[o], rw_a2[o],
                                         rw_g1[o], rw_g2[o], rw_k_k[o], rw_k_a[o], rw_r_k[o],
                                         rw_ln_w[o], rw_ln_b[o], rw_w_o[o], v_first, v_mix)
        x = x + y
        x = x + _swiglu(_rmsnorm(x, ffn_norm[layer]), ffn_w_gate[layer], ffn_w_up[layer], ffn_w_down[layer])
    return x


def setup_inputs(seed=0):
    out = dict(first_inputs(seed))
    for name, value in second_inputs(seed + 1).items():
        if name != "x":
            out[name + "_2"] = value
    return out


def reference(
    x, c, w_ada, b_ada, w_in, ssd_conv_w, ssd_conv_b, ssd_dt_bias, ssd_A_log, ssd_D, ssd_norm_w,
    w_ssd_out, sc_conv_w, w_sc_out, w_o, ln1_g, ln1_b, router_w, router_bias, w_gate, w_up,
    w_down, sh_gate, sh_up, sh_down, ln2_g, ln2_b, mix_norm_2, ffn_norm_2, ffn_w_gate_2,
    ffn_w_up_2, ffn_w_down_2, hy_w_in_2, hy_f_bias_2, hy_q_gain_2, hy_k_gain_2, hy_pool_w_2,
    hy_pool_scale_2, hy_w_out_2, rw_mu_2, rw_w_r_2, rw_w_k_2, rw_w_v_2, rw_w0_2, rw_w1_2,
    rw_w2_2, rw_a0_2, rw_a1_2, rw_a2_2, rw_g1_2, rw_g2_2, rw_k_k_2, rw_k_a_2, rw_r_k_2,
    rw_ln_w_2, rw_ln_b_2, rw_w_o_2, rw_v0_2, rw_v1_2, rw_v2_2,
):
    x = first_block(
        x, c, w_ada, b_ada, w_in, ssd_conv_w, ssd_conv_b, ssd_dt_bias, ssd_A_log, ssd_D,
        ssd_norm_w, w_ssd_out, sc_conv_w, w_sc_out, w_o, ln1_g, ln1_b, router_w, router_bias,
        w_gate, w_up, w_down, sh_gate, sh_up, sh_down, ln2_g, ln2_b,
    )
    return second_block(
        x, mix_norm_2, ffn_norm_2, ffn_w_gate_2, ffn_w_up_2, ffn_w_down_2, hy_w_in_2,
        hy_f_bias_2, hy_q_gain_2, hy_k_gain_2, hy_pool_w_2, hy_pool_scale_2, hy_w_out_2,
        rw_mu_2, rw_w_r_2, rw_w_k_2, rw_w_v_2, rw_w0_2, rw_w1_2, rw_w2_2, rw_a0_2, rw_a1_2,
        rw_a2_2, rw_g1_2, rw_g2_2, rw_k_k_2, rw_k_a_2, rw_r_k_2, rw_ln_w_2, rw_ln_b_2, rw_w_o_2,
        rw_v0_2, rw_v1_2, rw_v2_2,
    )


_drawn_inputs = setup_inputs


def setup_inputs(seed=0):
    import zlib

    import numpy as np

    out = dict(_drawn_inputs(seed))
    spreads = {}
    factors = {'ssd_conv_b': 8.0,
     'ssd_D': 7.569,
     'ssd_norm_w': 2.861,
     'hy_q_gain_2': 4.024,
     'hy_k_gain_2': 4.089,
     'rw_k_k_2': 6.462,
     'rw_ln_b_2': 6.932}
    for name, (base, spread) in spreads.items():
        noise = np.random.default_rng([zlib.crc32(name.encode()), seed]).standard_normal(out[name].shape)
        drawn = base * np.exp(spread * noise) if base else spread * noise
        out[name] = __import__('jax').numpy.asarray(drawn.astype(out[name].dtype))
    for name, factor in factors.items():
        out[name] = (out[name] * factor).astype(out[name].dtype)
    return out
```

```python
from contextlib import ExitStack

import numpy as np

import concourse.bass as bass
from concourse import mybir
from concourse.alu_op_type import AluOpType as ALU

ACT = mybir.ActivationFunctionType
F32 = mybir.dt.float32
F32R = mybir.dt.float32r
BF16 = mybir.dt.bfloat16
I32 = mybir.dt.int32
AX = mybir.AxisListType.X

P = 128
T = 256
D = 1024
ALPHA = 2.0 ** 0.25
TILE = 128
SLOT = 16 * TILE
RING = 7
NARROW = 4
RING_KB = 10
HI_KB = RING_KB + 8 * RING
HIS = 3
AREA = HI_KB + 8 * HIS
N_EXPERTS = 64
FIXED = 5
MORE = (68, 76, 84, 92, 8, 48)


class Count:

    def __init__(self, name, sem):
        self.name, self.sem, self.count = name, sem, 0


class Branch:
    def __init__(self, flag, limit, after):
        self.flag, self.limit, self.after, self.items, self.adds = flag, limit, after, [], 0


class Queue:

    def __init__(self, name, core):
        self.main = Count(name, core.sem("s_" + name))
        self.side = Count(name + "_if", core.sem("s_" + name + "_if"))
        self.items, self.open = [], []
        self.flags = None

    def into(self):
        return self.open[-1].items if self.open else self.items

    def do(self, after, emit):
        count = self.side if self.open else self.main
        for b in self.open:
            b.adds += 1
        count.count += 1
        self.into().append((tuple(flat(after)), emit, count, 1))
        return (count, count.count)

    def dma(self, after, load, out, in_):
        load.count += 16
        self.into().append((tuple(flat(after)), lambda e: e.dma_start(out, in_), load, 16))
        return (load, load.count)

    def load_flags(self, after, row):
        self.flags = (tuple(flat(after)), row)
        self.items.append(("flags",))

    def branch(self, flag, limit, after=()):
        b = Branch(flag, limit, tuple(flat(after)))
        self.into().append(b)
        self.open.append(b)

    def close(self):
        self.open.pop()

    def run(self, eng):
        self.emit(eng, self.items, {})

    def emit(self, eng, items, seen):
        def wait(after):
            for count, value in after:
                if seen.get(count.name, 0) < value:
                    eng.wait_ge(count.sem, value)
                    seen[count.name] = value

        for item in items:
            if isinstance(item, Branch):
                with eng.If_cmp(self.regs[item.flag], item.limit, "IS_GT"):
                    self.emit(eng, item.items, dict(seen))
                with eng.Else():
                    for count, value in item.after:
                        eng.wait_ge(count.sem, value)
                    eng.sem_inc(self.side.sem, item.adds)
            elif item[0] == "flags":
                after, row = self.flags
                n = row.shape[1]
                self.regs = [eng.alloc_register(f"{self.main.name}_flag{i}") for i in range(n)]
                wait(after)
                eng.reg_load(self.regs, row)
            else:
                after, emit, count, add = item
                wait(after)
                emit(eng).then_inc(count.sem, add)

    def act(self, after, out, in_, func=ACT.Copy, **kw):
        return self.do(after, lambda e: e.activation(out, in_, func, **kw))

    def tt(self, after, out, a, b, op):
        return self.do(after, lambda e: e.tensor_tensor(out, a, b, op=op))

    def ts(self, after, out, a, s1, op0, s2=None, op1=ALU.bypass, **kw):
        return self.do(after, lambda e: e.tensor_scalar(out, a, s1, s2, op0=op0, op1=op1, **kw))

    def stt(self, after, out, a, s, b, op0, op1):
        return self.do(after, lambda e: e.scalar_tensor_tensor(out, a, s, b, op0=op0, op1=op1))

    def copy(self, after, out, a):
        return self.do(after, lambda e: e.tensor_copy(out, a))

    def recip(self, after, out, a):
        return self.do(after, lambda e: e.reciprocal(out, a))

    def fill(self, after, out, value):
        return self.do(after, lambda e: e.memset(out, value))

    def mm(self, after, *calls):

        def emit(e):
            for out, lhsT, rhs, start, stop in calls:
                ins = e.matmul(out, lhsT, rhs, start=start, stop=stop, skip_group_check=True)
            return ins

        return self.do(after, emit)

    def tr(self, after, ident, *calls):

        def emit(e):
            for out, in_ in calls:
                n = in_.shape[0]
                ins = e.transpose(out, in_, ident[0:n, 0:n])
            return ins

        return self.do(after, emit)


def flat(x):
    if isinstance(x, tuple) and len(x) == 2 and isinstance(x[1], int):
        yield x
        return
    for y in x or ():
        yield from flat(y)


class Bank:

    def __init__(self, t):
        self.t, self.free = t, []

    def __getitem__(self, k):
        return self.t[k]


class Slot:
    def __init__(self, index, key, tiles, split):
        self.index, self.key, self.tiles, self.split = index, key, tiles, split
        self.done = []


class Core:
    def __init__(self, nc, ctx, ins):
        self.nc, self.ctx, self.ins = nc, ctx, ins
        self.arena = ctx.enter_context(nc.sbuf_tensor("arena", [P, 53200], F32))
        self.base = 16512
        self.pe = Queue("pe", self)
        self.act = Queue("act", self)
        self.dve = Queue("dve", self)
        self.pool = Queue("pool", self)
        self.sp = []
        self.actdma = []
        self.banks = [Bank(ctx.enter_context(nc.psum_tensor(f"ps{i}", [P, 512], F32))) for i in range(8)]
        self.nload = 0
        self.final = []
        self.turn = 0

    def sem(self, name):
        return self.ctx.enter_context(self.nc.semaphore(name))

    def buf(self, name, kb, shape, dt=F32):
        n = 1
        for s in shape[1:]:
            n *= s
        assert kb * 1024 + n * (2 if dt == BF16 else 4) <= 212800, (name, kb)
        return self.nc.alloc_sbuf_tensor_at(name, list(shape), dt, offset=self.base + int(kb * 1024))

    def load(self, out, in_, after=(), queue=None):
        self.nload += 1
        load = Count(f"ld{self.nload}", self.sem(f"ld{self.nload}"))
        if queue:
            return queue.dma(after, load, out, in_)
        load.count = 16
        self.sp.append((list(flat(after)), lambda e: e.dma_start(out, in_).then_inc(load.sem, 16)))
        return (load, 16)

    def run(self):
        with self.nc.Block() as block:

            @block.sync
            def _(eng):
                seen = {}
                for after, emit in self.sp:
                    for queue, count in flat(after() if callable(after) else after):
                        if seen.get(queue.name, 0) < count:
                            eng.wait_ge(queue.sem, count)
                            seen[queue.name] = count
                    emit(eng)
                for queue, count in self.final:
                    eng.wait_ge(queue.sem, count)

            @block.tensor
            def _(eng):
                self.pe.run(eng)

            @block.scalar
            def _(eng):
                self.act.run(eng)

            @block.vector
            def _(eng):
                self.dve.run(eng)

            @block.gpsimd
            def _(eng):
                self.pool.run(eng)


class Stream:

    def __init__(self, core, plan, wts, experts):
        self.core, self.experts = core, experts
        self.order, self.order_ready, self.regs = None, [], None
        self.slots = [Slot(i, *p) for i, p in enumerate(plan)]
        self.next = self.nready = self.issued = 0
        at = [RING_KB + 8 * i for i in range(RING)] + [AREA + k for k in MORE] + [HI_KB + 8 * i for i in range(HIS)]
        self.raw = [core.buf(f"wraw{i}", kb, [P, SLOT]) for i, kb in enumerate(at)]
        self.lo = [core.buf(f"wlo{i}", kb, [P, SLOT], F32R) for i, kb in enumerate(at[:RING])]
        self.hi = [core.buf(f"whi{i}", HI_KB + 8 * i, [P, SLOT], F32R) for i in range(HIS)]
        self.before = [()] * len(at)
        sems = [Count(f"ring{i}", core.sem(f"ring{i}")) for i in range(len(at))]
        user = [None] * len(at)
        hi_user = [None] * HIS
        at = turn = wide = nsplit = 0
        narrow = False
        for s in self.slots:
            s.n = len(s.tiles) * TILE
            if s.key[0] == "expert":
                order = [*range(RING, RING + 4), *[(turn + i) % RING for i in range(RING)], *range(RING + 6, RING + 9),
                         RING + 4, RING + 5]
                s.place = order[wide % len(order)]
                wide += 1
            else:
                n = NARROW if narrow or s.key == "w1" else RING
                narrow = n == NARROW
                s.place = turn % n
                turn += 1
            h = s.place - RING - len(MORE)
            if s.split:
                h = nsplit % HIS
                nsplit += 1
                s.hi, s.hi_prev, hi_user[h] = self.hi[h], hi_user[h], s
            load = sems[s.place]
            load.count += 16
            s.landed = (load, load.count)
            s.prev, user[s.place] = user[s.place], s
            if s.place >= RING + len(MORE):
                s.prev, hi_user[h] = hi_user[h], s
            s.raw = self.raw[s.place]
            if s.key[0] != "expert":
                s.src = wts[at:at + P * s.n].rearrange("(p n) -> p n", p=P)
                at += P * s.n
        self.total = at
        self.user = user

    def find(self, key):
        return next(s for s in self.slots if s.key == key)

    def issue(self, upto):
        while self.issued < min(upto, len(self.slots)):
            s = self.slots[self.issued]
            free = lambda s=s: s.prev.done if s.prev else self.before[s.place]
            if s.key[0] == "expert":
                self.issue_expert(s, free)
            else:
                self.core.sp.append((free, lambda e, s=s: e.dma_start(s.raw[:, 0:s.n], s.src).then_inc(s.landed[0].sem, 16)))
            self.issued += 1

    def issue_expert(self, s, free):
        _, place, part, group = s.key

        def fixed(e):
            e.dma_start(s.raw[:, :], self.experts[place, part]).then_inc(s.landed[0].sem, 16)

        def sorted_(e):
            if not self.regs:
                self.regs = [e.alloc_register(f"expert{i}") for i in range(4)]
            if part == 0 and place == group[0]:
                regs = self.regs[0:len(group)]
                e.reg_load(regs, self.order[:, place:place + len(group)])
                self.which = [e.snap(r, min_val=0, max_val=N_EXPERTS - 1) for r in regs]
            src = self.experts[bass.ds(self.which[place - group[0]], 1), part, :, :].rearrange("o p n -> (o p) n")
            e.dma_start(s.raw[:, :], src).then_inc(s.landed[0].sem, 16)

        if place < FIXED:
            self.core.sp.append((free, fixed))
        else:
            waits = lambda: [free(), self.order_ready]
            self.core.sp.append((waits, sorted_))

    def split(self, s):
        core, last = self.core, s.hi_prev
        s.lo = self.lo[s.place]
        a = core.act.act([s.landed, last.done if last else []], s.hi[:, 0:s.n], s.raw[:, 0:s.n])
        b = core.dve.tt([a], s.lo[:, 0:s.n], s.raw[:, 0:s.n], s.hi[:, 0:s.n].bitcast(F32), ALU.subtract)
        s.ready = [a, b]

    def take(self, key):
        s = self.slots[self.next]
        assert s.key == key, (s.key, key)
        self.next += 1
        self.issue(s.index + len(self.raw))
        while self.nready < min(s.index + HIS, len(self.slots)):
            f = self.slots[self.nready]
            if f.split and not s.split and s.key[0] == "expert":
                break
            self.nready += 1
            if f.split:
                self.split(f)
            else:
                f.ready = [f.landed]
        return s



FIXED_PAIRS = [(0, 1), (2, 3)]
SOLOS = [(p,) for p in range(4, 12)]
PAIRS = [(p, p + 1) for p in range(12, 32, 2)]
QUADS = [tuple(range(p, p + 4)) for p in range(32, 64, 4)]
FLAGS = FIXED_PAIRS + SOLOS + PAIRS + QUADS
KINDS = dict(f=iter(FIXED_PAIRS), s=iter(SOLOS), p=iter(PAIRS), q=iter(QUADS))
GROUPS = [next(KINDS[k]) for k in "ffsqqsqqsspqspqspqspqpppppps"]
ROUNDS = {1: 2, 2: 4, 4: 3}

PARAMS = []


def param(name, n):
    at = sum(k for _, k in PARAMS)
    PARAMS.append((name, n))
    return at


C_BADA = param("b_ada", 48)
C_CONVW = param("ssd_conv_w", 128)
C_CONVB = param("ssd_conv_b", 32)
C_D = param("ssd_D", 16)
C_NORM = param("ssd_norm_w", 16)
C_SCW = param("sc_conv_w", 24)
C_LN1G = param("ln1_g", 8)
C_LN1B = param("ln1_b", 8)
C_LN2G = param("ln2_g", 8)
C_LN2B = param("ln2_b", 8)
C_MIX = param("mix_norm", 16)
C_FFN = param("ffn_norm", 16)
C_DTB = param("dt_bias", 1)
C_ALOG = param("A_log", 1)
C_EPS = param("eps", 4)
C_QG = param("q_gain", 1)
C_KG = param("k_gain", 1)
C_QKE = param("qk_eps", 1)
C_FB = param("f_bias", 1)
C_PSC = param("pool_scale", 4)
C_MU = param("rw_mu", 48)
C_W0 = param("rw_w0", 8)
C_A0 = param("rw_a0", 8)
C_KK = param("rw_k_k", 8)
C_KA = param("rw_k_a", 8)
C_RK = param("rw_r_k", 8)
NPAR = sum(k for _, k in PARAMS)


def plan():
    out = []

    def add(key, tiles, split=True):
        out.append((key, tiles, split))

    def pair(key, mat, m0, nk=8, split=True):
        add(key, [(mat, P * k, m0 + P * m) for k in range(nk) for m in range(2)], split)

    def rows(key, *r0):
        add(key, [("ada", r, P * q) for r in r0 for q in range(8)], False)

    for j in range(8):
        rows(("ada", j), 1024 + P * j, P * j)
    add("dt", [("w_dt", P * k, 0) for k in range(8)])
    for i in range(4):
        pair(("B", i), "w_in", 4096 + 256 * i)
    for i in range(4):
        pair(("C", i), "w_in", 5120 + 256 * i)
    for i in range(8):
        pair(("xs", i), "w_in", 2048 + 256 * i)
    for i in range(4):
        for what, m0 in (("sc_c", 7200), ("sc_h", 8224), ("sc_b", 6176)):
            pair((what, i), "w_in", m0 + 256 * i)
    for i in range(4):
        pair(("sc_out", i), "w_sc_out", 256 * i)
    for i in range(4):
        pair(("gb", i), "w_in", 10272 + 256 * i)
    spare = [[2048 + 256 * j, 2048 + 256 * j + P] for j in range(4)]
    spare += [[4096 + P * j, 3072 + P * j] for j in range(8)]
    for i in range(8):
        pair(("z", i), "w_in", 256 * i)
        rows(("ada", 8 + i), *spare[i])
    for i in range(4):
        pair(("ga", i), "w_in", 9248 + 256 * i)
        rows(("ada", 16 + i), *spare[8 + i])
    for i in range(8):
        add(("ssd_out", i), [("w_ssd_out", P * k, P * i) for k in range(16)])
    for i in range(4):
        pair(("w_o", i), "w_o", 256 * i)
        rows(("ada", 20 + i), 5120 + 256 * i, 5120 + 256 * i + P)
    add("router", [("w_router", P * k, 0) for k in range(4)], False)
    pair("sh_gate", "sh_gate", 0)
    pair("sh_up", "sh_up", 0)
    add("sh_down", [("sh_down", P * k, P * m) for m in range(8) for k in range(2)])
    for group in GROUPS:
        for half in range(2):
            for p in group:
                add(("expert", p, half, group), range(16), False)
        for p in group:
            add(("expert", p, 2, group), range(16), False)

    def across(key, mat, m0):
        for half in range(2):
            add((key, half), [(mat, P * k, m0 + P * m) for k in range(4 * half, 4 * half + 4) for m in range(4)])

    def ffn(n):
        for m in range(22):
            add(("gate_up", n, m), [(f"{w}{n}", P * k, P * m) for k in range(8) for w in ("ffn_gate", "ffn_up")])
        tiles = [(f"ffn_down{n}", P * k, P * m) for m in range(8) for k in range(22)]
        for i in range(11):
            add(("down", n, i), tiles[16 * i:16 * i + 16])

    add("hy_f", [("w_f", P * k, 0) for k in range(8)])
    for i in range(2):
        pair(("q", i), "hy_in", 256 * i)
    for i in range(2):
        pair(("k", i), "hy_in", 512 + 256 * i)
    across("v", "hy_in", 1024)
    across("u", "hy_in", 2056)
    add("pool", [("pool_w", P * g, 0) for g in range(4)])
    for i in range(2):
        pair(("og", i), "hy_in", 1536 + 256 * i)
    for i in range(4):
        pair(("hy_out", i), "hy_out", 256 * i)
    ffn(0)
    for x in ("w", "a"):
        add(x + "1", [(f"rw_{x}1", P * k, 0) for k in range(8)])
        add(x + "2", [(f"rw_{x}2", 0, P * m) for m in range(8)])
    for x in ("rw_k", "rw_r"):
        for i in range(4):
            pair((x, i), x, 256 * i)
    across("rw_v0", "rw_v", 0)
    across("rw_v1", "rw_v", 512)
    pair("g1", "rw_g1", 0)
    add("g2", [("rw_g2", P * k, P * m) for k in range(2) for m in range(8)])
    for i in range(4):
        pair(("rw_o", i), "rw_o", 256 * i)
    ffn(1)
    return out


def constants():
    c = {}
    c["ident"] = np.eye(P)
    c["mean"] = np.full((P, P), 1.0 / D)
    c["sel8"] = np.broadcast_to(np.eye(8).reshape(1, 64) / 256, (P, 64))
    k = np.arange(P)
    tri = (k[:, None] <= k[None, :]) * 1.0
    c["iota"] = np.broadcast_to(np.arange(1.0, 257), (P, 256))
    for n in ROUNDS:
        w = P // n
        c[f"slot{n}"] = k[:, None] % w + w * np.arange(ROUNDS[n])[None, :] + 1.0
        c[f"of{n}"] = np.tile(k[:, None] // w == np.arange(n)[None, :], 2) * 1.0
    e = np.arange(N_EXPERTS)
    bump = np.maximum(FIXED - e, 0) * 1000.0
    c["bump"] = np.broadcast_to(bump, (P, N_EXPERTS))
    c["own"] = np.stack([np.tile(bump, 2), np.tile(e, 2)], axis=1)
    c["upto"] = (e[None, :] <= (k % N_EXPERTS)[:, None]) * 1.0
    g = np.arange(8)
    c["before"] = np.broadcast_to((g[None, :] < g[:, None]).reshape(1, 64), (P, 64)) * 1.0
    c["tri"] = tri
    n = np.arange(8)
    c["heads"] = np.concatenate([((2 * i + k[:, None] // 64) == np.arange(16)[None, :]) * (1.0 if i < 4 else 1.0 / 64) for i in n], axis=1)
    c["neg"] = np.concatenate([np.zeros((P, P)), (k[None, :] > k[:, None]) * -1e30], axis=1)
    s, t = np.arange(T)[:, None], np.arange(T)[None, :]
    bands = []
    for w in (2, 4, 8, 16):
        b = ((s <= t) & (s > t - w)) / np.minimum(t + 1, w) - (s == t)
        bands += [b[0:P], b[P:, P:]]
    c["band"] = np.concatenate(bands, axis=1)
    c["sum16"] = np.concatenate([(2 * i + k[:, None] // 64) == np.arange(16)[None, :] for i in n], axis=1) * 1.0
    s, t = k[:, None] % 64, np.arange(64)[None, :]
    c["chunk"] = np.concatenate([s <= t, s < t, s < t, s <= t], axis=1) * 1.0
    c["mask"] = np.concatenate([tri, np.ones((P, P)), tri], axis=1)
    return c


STAY = ["mean", "ident", "sel8"]
LATE_COLS = dict(iota=256, slot1=2, of1=2, slot2=4, of2=4, slot4=3, of4=8, before=64, tri=P, router_bias=64, bump=64, own=2, upto=64)
LATE = list(LATE_COLS)
CONST = ["mask", "heads", "neg", "band", "sum16", "chunk"]


def layer(S, keys, x, evac, banks, nk=8, steps=2):
    K = S.core
    hi, lo, ready = x
    mts = {}
    for key in keys:
        for mat, _, m0 in S.find(key).tiles:
            mts.setdefault((mat, m0), len(mts))
    for key in keys:
        s = S.take(key)
        nt = len(s.tiles)
        for t, (mat, k0, m0) in enumerate(s.tiles):
            mt, k = mts[mat, m0], k0 // P
            pairno, half = divmod(mt, 2)
            first, last = k == 0 and half == 0, k == nk - 1
            if first:
                bank = banks[K.turn % len(banks)]
                K.turn += 1
            after = [s.ready if t == 0 else [], bank.free if first else [], ready[k]]
            o = bank[:, T * half:T * (half + 1)]
            wh, wl = s.hi[:, TILE * t:TILE * (t + 1)], s.lo[:, TILE * t:TILE * (t + 1)]
            tok = K.pe.mm(after, (o, wh, hi[:, k, :], first, False), (o, wh, lo[:, k, :], False, False),
                          (o, wl, hi[:, k, :], False, last))
            if t == nt - 1:
                s.done.append(tok)
            if last and (half == 1 or mt == len(mts) - 1):
                bank.free = list(flat(evac(pairno, bank, tok)))
            if (t + 1) % max(1, nt // steps) == 0:
                yield


def weave(main, side, per):
    for _ in main:
        for _ in range(per):
            next(side, None)
    return side


def drain(*gens):
    for gen in gens:
        for _ in gen:
            pass


def halves(ap):
    return ap.rearrange("p (i t) -> p i t", i=2)


def split_x(K, xh, xl, k, x32, after, eng=None):
    a = K.act.act(after, xh[:, k, :], x32)
    b = (eng or K.dve).tt([a], xl[:, k, :], x32, xh[:, k, :].bitcast(F32), ALU.subtract)
    return [a, b]


def layer_norm(K, src, ready, sq, r, bm, bv, sq_free, out, between=None, dst=None, mean=None, gain=None):
    dst = dst or src
    made = []
    if mean:
        for j in range(8):
            made.append(K.dve.stt([ready[j], mean[2]], dst[:, j, :], src[:, j, :], mean[0], mean[1], ALU.subtract, ALU.subtract))
    else:
        for j in range(8):
            if gain:
                tg = K.pe.mm([ready[j], K.t_cst, gain[2].free if j == 0 else []], (gain[2][:, 0:T], K.par[:, gain[0] + j:gain[0] + j + 1].to_broadcast([P, P]),
                                                              src[:, j, :], j == 0, j == 7))
            t = K.pe.mm([ready[j], bm.free if j == 0 else [], K.t_cst],
                        (bm[:, 0:T], K.c["mean"][:, :], src[:, j, :], j == 0, j == 7))
        for j in range(8):
            made.append(K.dve.tt([t], dst[:, j, :], src[:, j, :], bm[:, 0:T], ALU.subtract))
        bm.free = [made]
    if gain:
        _, gmean, bg, tile, spare = gain
        a = K.dve.ts([t, gmean[1]], spare, bm[:, 0:T], gmean[0], ALU.mult)
        a = K.dve.stt([a, tg], tile, bg[:, 0:T], 1.0 / D, spare, ALU.mult, ALU.subtract)
        bm.free, bg.free = [made, a], [a]
    for j in range(8):
        b = K.act.act([made[j], sq_free], sq[:, j, :], dst[:, j, :], ACT.Square)
        tv = K.pe.mm([b, bv.free if j == 0 else []], (bv[:, 0:T], K.c["mean"][:, :], sq[:, j, :], j == 0, j == 7))
    t = K.act.act([tv, K.t_par], r, bv[:, 0:T], ACT.Sqrt, bias=K.par[:, C_EPS:C_EPS + 1])
    bv.free = [t]
    if between:
        between()
    t = K.dve.recip([t], r, r)
    late = []
    for j in range(8):
        late.append((j, K.dve.tt([t], dst[:, j, :], dst[:, j, :], r, ALU.mult)))
        if j == 3 and gain:
            tg = K.dve.tt([a, t], tile, tile, r, ALU.mult)
        if j > 1:
            out(*late[j - 2])
    out(*late[6])
    out(*late[7])
    return tg if gain else tv


def modulation(K, S, i, share=False):
    s = S.take(("ada", i))
    for h in range(2):
        j = s.tiles[8 * h][1] // P
        w, a = s.raw[:, D * h:D * (h + 1)], K.acc[:, j:j + 1]
        if share and h:
            t = K.pool.tt([s.ready, K.t_csil, K.prod_free], K.prod[:, :], w, K.csil[:, :], ALU.mult)
            s.done.append(t)
            t = K.act.act([t], K.prod[:, :], K.prod[:, :], accum_out=a)
            K.prod_free = [t]
        else:
            t = K.dve.do([s.ready, K.t_csil, K.ada_last],
                         lambda e, w=w, a=a: e.tensor_tensor_reduce(K.scr[:, :], w, K.csil[:, :], 1.0, 0.0, ALU.mult, ALU.add, a))
            K.ada_last = [t]
            s.done.append(t)
        plus = 1.0 if j // 8 in (1, 4) else 0.0
        K.mod_ready[j] = K.dve.stt([t, K.t_par], K.mod[:, j:j + 1], a, plus, K.par[:, C_BADA + j:C_BADA + j + 1], ALU.add, ALU.add)


def first_block(K, S):
    pe, act, dve, pool = K.pe, K.act, K.dve, K.pool
    B = K.banks
    A = AREA

    h_hi = K.buf("h_hi", A, [P, 8, T], F32R)
    h_lo = K.buf("h_lo", A + 8, [P, 8, T], F32R)
    xs = K.buf("xs", A + 16, [P, 16, T])
    Bm = K.buf("Bm", A + 32, [P, 8, T])
    Cm = K.buf("Cm", A + 40, [P, 8, T])
    s_hi = K.buf("s_hi", A + 48, [P, 8, T], F32R)
    s_lo = K.buf("s_lo", A + 56, [P, 8, T], F32R)
    K.csil = csil = K.buf("csil", A + 64, [P, D])
    xT = K.buf("xT", A + 68, [P, 2, 2, T])
    CBm = K.buf("CBm", A + 72, [P, 2, 384])
    E = K.buf("E", A + 75, [P, 2, 2, 384])
    sc = K.buf("sc", A + 81, [P, 2, 2, 384])
    mask = K.buf("mask", A + 87, [P, 384])
    dtT = K.buf("dtT", A + 88.5, [P, 2, 32])
    AcsT = K.buf("AcsT", A + 88.75, [P, 2, 32])
    dt = K.buf("dt", A + 89, [32, T])
    dA = K.buf("dA", A + 90, [32, T])
    Acs = K.buf("Acs", A + 91, [32, T])
    tmp = K.buf("tmp", A + 92, [P, 4, T])
    scb = K.buf("scb", A + 96, [P, 2, T])
    K.scr = K.buf("scr", A + 115, [P, D], BF16)
    yb = K.buf("yb", A + 100, [P, 8, T])
    gate = K.buf("gate", A + 108, [P, 2, 2, T])

    xf = K.buf("xf", A + 16, [P, 8, T])
    sq = K.buf("sq", A + 24, [P, 8, T])
    rs = K.buf("rs", A + 92, [P, T])
    K.prod = K.buf("prod", A + 100, [P, D])
    K.prod_free = []

    t_x = K.load(xf[:, :, :], K.ins["xT"].rearrange("p (j t) -> p j t", t=T))
    setup(K)
    par, t_par, ident = K.par, K.t_par, K.c["ident"]
    K.t_csil = K.load(csil[:, :], K.ins["c"].to_broadcast([P, D]))
    S.issue(1)
    t_mask = K.load(mask[:, :], K.cst("mask"), queue=act)
    K.t_csil = act.act([K.t_csil], csil[:, :], csil[:, :], ACT.Silu)

    h_ready = []
    todo = iter(range(8))

    def mod_some(n):
        for _, i in zip(range(n), todo):
            modulation(K, S, i, True)

    def out_h(j, t):
        while K.mod_ready[8 + j] is None:
            mod_some(1)
        t = act.act([t, K.mod_ready[8 + j], K.mod_ready[j]], xf[:, j, :], xf[:, j, :], ACT.Identity,
                    scale=K.mod[:, 8 + j:9 + j], bias=K.mod[:, j:j + 1])
        h_ready.append(split_x(K, h_hi, h_lo, j, xf[:, j, :], [t]))

    layer_norm(K, xf, [t_x] * 8, sq, rs[:, :], B[0], B[1], [], out_h, between=lambda: mod_some(2))
    h = (h_hi, h_lo, h_ready)

    t_dt = []
    dt_raw = []

    def evac_dt(_, bank, done):
        t = act.act([done, t_par], dt[:, :], bank[0:32, 0:T], ACT.Identity, bias=par[0:32, C_DTB:C_DTB + 1])
        dt_raw.append(t)
        return [t]

    def steps_dt():
        d = dt[:, :]
        u, p, z, z2 = (tmp[0:32, i, :] for i in range(4))
        t = dve.stt([dt_raw], u, d, -1.0, d, ALU.mult, ALU.min)
        t = act.act([t], u, u, ACT.Exp)
        ta = act.act([t_par], K.small[0:32, 0:1], par[0:32, C_ALOG:C_ALOG + 1], ACT.Exp)
        yield
        t = dve.ts([t], z, u, 2.0, ALU.add)
        t = dve.recip([t], z, z)
        t = dve.tt([t], z, z, u, ALU.mult)
        t = dve.tt([t], z2, z, z, ALU.mult)
        yield
        t = dve.ts([t], p, z2, 2.0 / 17, ALU.mult)
        for c in (15, 13, 11, 9, 7, 5, 3):
            t = dve.stt([t], p, p, 2.0 / c, z2, ALU.add, ALU.mult)
        yield
        t = dve.stt([t], p, p, 2.0, z, ALU.add, ALU.mult)
        t = dve.stt([t], d, d, 0.0, p, ALU.max, ALU.add)
        t1 = dve.ts([t, ta], dA[:, :], d, K.small[0:32, 0:1], ALU.mult, -1.0, ALU.mult)
        t2 = dve.fill([t], z2, 0.0)
        t3 = dve.do([t1, t2], lambda e: e.tensor_tensor_scan(Acs[:, :], dA[:, :], z2, 0.0, ALU.add, ALU.add))
        yield
        for _ in range(6):
            yield
        b = B[7]
        tt = pe.tr([t3, K.t_cst, b.free], ident,
                   *[(b[:, 32 * i:32 * (i + 1)], d[:, P * i:P * (i + 1)]) for i in range(2)],
                   *[(b[:, 64 + 32 * i:96 + 32 * i], Acs[:, P * i:P * (i + 1)]) for i in range(2)])
        t4 = dve.copy([tt], dtT[:, :, :], b[:, 0:64].rearrange("p (i h) -> p i h", i=2))
        t5 = dve.copy([tt], AcsT[:, :, :], b[:, 64:128].rearrange("p (i h) -> p i h", i=2))
        b.free = [t4, t5]
        t_dt.append([t3, t4, t5])
        yield

    dense = [B[0], B[1], B[2]]
    drain(layer(S, ["dt"], h, evac_dt, dense, steps=1))

    late = []

    def silu_late():
        for made, o, t in late:
            made.append(act.act([t], o, o, ACT.Silu))
        late.clear()

    def conv(dst, tile0, made):
        def evac(pairno, bank, done):
            t, js = [], (2 * pairno, 2 * pairno + 1)
            src = [bank[:, T * i:T * (i + 1)] for i in range(2)]
            for i, j in enumerate(js):
                f = tile0 + j
                t.append(act.act([done, t_par], dst[:, j, :], src[i], ACT.Identity, bias=par[:, C_CONVB + f:C_CONVB + f + 1],
                                 scale=par[:, C_CONVW + 96 + f:C_CONVW + 97 + f]))
            silu_late()
            for n in range(1, 4):
                for i, j in enumerate(js):
                    k = C_CONVW + 32 * (3 - n) + tile0 + j
                    o = dst[:, j, n:T]
                    t[i] = dve.stt([t] if n == 1 else [t[i]], o, src[i][:, 0:T - n], par[:, k:k + 1], o, ALU.mult, ALU.add)
            late.extend((made, dst[:, j, :], t[i]) for i, j in enumerate(js))
            return t
        return evac

    B_made, C_made, xs_made = [], [], []
    side = weave(layer(S, [("B", i) for i in range(4)], h, conv(Bm, 16, B_made), dense), steps_dt(), 1)
    weave(layer(S, [("C", i) for i in range(4)], h, conv(Cm, 24, C_made), dense), side, 1)
    drain(side)
    drain(layer(S, [("xs", i) for i in range(8)], h, conv(xs, 0, xs_made), dense))
    silu_late()

    y_made = [None] * 16

    def ssd():
        bT, bC, bR, bY = B[3], B[4], [B[5], B[6]], B[7]
        xT_made, xT_free, CB_made, CB_free = {}, {}, {}, {}
        E_free, sc_free = {}, {}

        def group(g):
            q = g % 2
            tt = pe.tr([bT.free, xs_made[2 * g], xs_made[2 * g + 1], K.t_cst], ident,
                       *[(bT[:, T * i + P * f:T * i + P * (f + 1)], xs[:, 2 * g + f, P * i:P * (i + 1)])
                         for i in range(2) for f in range(2)])
            tc = pe.mm([bC.free, B_made[g], C_made[g]],
                       (bC[:, 0:T], Bm[:, g, 0:P], Cm[:, g, :], True, True),
                       (bC[:, T:384], Bm[:, g, P:T], Cm[:, g, P:T], False, True))
            t = dve.tt([tt, t_dt, xT_free.get(g - 2)], xT[:, q, :, :].rearrange("p i (h d) -> p i h d", h=4),
                       bT[:, :].rearrange("p (i h d) -> p i h d", i=2, h=4),
                       dtT[:, :, 4 * g:4 * g + 4].unsqueeze(3).to_broadcast([P, 2, 4, 64]), ALU.mult)
            bT.free = [t]
            xT_made[g] = [t, tt]
            t = dve.tt([tc, t_mask, CB_free.get(g - 2)], CBm[:, q, :], bC[:, 0:384], mask[:, :], ALU.mult)
            bC.free = [t]
            CB_made[g] = [t]

        def decay(n):
            r, h0, bank = n % 2, 2 * n, bR[n % 2]
            tr = pe.mm([bank.free, t_dt], *[(bank[:, T * j:T * (j + 1)], ident[0:32, h0 + j:h0 + j + 1].to_broadcast([32, P]),
                                             Acs[:, :], j == 0, True) for j in range(2)])
            te = []
            for j in range(2):
                te.append(act.act([tr, E_free.get(n - 2)], E[:, r, j, 0:T], bank[:, T * j:T * (j + 1)], ACT.Relu, scale=-1.0,
                                  bias=AcsT[:, 0, h0 + j:h0 + j + 1]))
                te.append(act.act([tr, E_free.get(n - 2)], E[:, r, j, T:384], bank[:, T * j + P:T * (j + 1)], ACT.Relu,
                                  scale=-1.0, bias=AcsT[:, 1, h0 + j:h0 + j + 1]))
            bank.free = te
            E_made[n] = act.act([te], E[:, r, :, :], E[:, r, :, :], ACT.Exp, scale=-1.0)

        def score(n):
            r, g = n % 2, n // 2
            t = dve.tt([E_made[n], CB_made[g], sc_free.get(n - 2)], sc[:, r, :, :], E[:, r, :, :],
                       CBm[:, g % 2, :].unsqueeze(1).to_broadcast([P, 2, 384]), ALU.mult)
            E_free[n] = [t]
            CB_free.setdefault(g, []).append(t)
            sc_made[n] = [t]

        def output(n):
            r, g, i = n % 2, n // 2, n % 2
            calls = []
            for st in range(2):
                for j in range(2):
                    o = bY[64 * j:64 * (j + 1), 0:T] if st == 0 else bY[64 * j:64 * (j + 1), P:T]
                    w_ = xT[:, g % 2, st, P * i + 64 * j:P * i + 64 * (j + 1)]
                    calls.append((o, w_, sc[:, r, j, 0:T] if st == 0 else sc[:, r, j, T:384], st == 0, st == 1))
            ty = pe.mm([bY.free, sc_made[n], xT_made[g]], *calls)
            sc_free[n] = [ty]
            xT_free.setdefault(g, []).append(ty)
            t = dve.stt([ty, xT_made[g]], xs[:, n, :], xs[:, n, :], par[:, C_D + n:C_D + n + 1], bY[:, 0:T], ALU.mult, ALU.add)
            bY.free = [t]
            y_made[n] = t

        E_made, sc_made = {}, {}
        group(0)
        yield
        decay(0)
        yield
        for n in range(16):
            if n + 1 < 16:
                decay(n + 1)
            score(n)
            yield
            if n:
                output(n - 1)
                yield
            if n % 2 == 0 and n + 2 < 16:
                group(n // 2 + 1)
                yield
        output(15)
        yield

    side = ssd()

    u_ready = []
    st = dict(scb_free=[], tmp_free=[t_dt])

    def sc_c(pairno, bank, done):
        st["c"] = act.act([done, st["scb_free"]], scb[:, :, :], halves(bank[:, :]))
        return [st["c"]]

    def sc_h(pairno, bank, done):
        t = dve.tt([done, st["c"]], scb[:, :, :], halves(bank[:, :]), scb[:, :, :], ALU.mult)
        st["u"] = []
        for i in range(2):
            f = 2 * pairno + i
            o = tmp[:, i, :]
            a = dve.ts([t, st["tmp_free"]], o, scb[:, i, :], par[:, C_SCW + 16 + f:C_SCW + 17 + f], ALU.mult)
            for n in (1, 2):
                k = C_SCW + 8 * (2 - n) + f
                a = dve.stt([a], o[:, n:T], scb[:, i, 0:T - n], par[:, k:k + 1], o[:, n:T], ALU.mult, ALU.add)
            st["u"].append(a)
        st["scb_free"] = st["u"]
        return [t]

    def sc_b(pairno, bank, done):
        a = dve.tt([done, st["u"], st["tmp_free"]], tmp[:, 2:4, :], halves(bank[:, :]), tmp[:, 0:2, :], ALU.mult)
        for i in range(2):
            u_ready.append(split_x(K, s_hi, s_lo, 2 * pairno + i, tmp[:, 2 + i, :], [a], pool))
        st["tmp_free"] = u_ready[-2:]
        return [a]

    for i in range(4):
        for key, evac in (("sc_c", sc_c), ("sc_h", sc_h), ("sc_b", sc_b)):
            weave(layer(S, [(key, i)], h, lambda _, b, d, f=evac, i=i: f(i, b, d), dense), side, 1)

    yb_made = [None] * 8

    def evac_sc(pairno, bank, done):
        t = act.act([done], yb[:, 2 * pairno:2 * pairno + 2, :], halves(bank[:, :]))
        yb_made[2 * pairno] = yb_made[2 * pairno + 1] = t
        return [t]

    weave(layer(S, [("sc_out", i) for i in range(4)], (s_hi, s_lo, u_ready), evac_sc, dense), side, 1)

    ga = K.buf("ga", A + 48, [P, 8, T])
    ga_made = [None] * 8
    gate_free = [[], []]

    def evac_gb(i):
        def evac(_, bank, done):
            q = i % 2
            t = act.act([done, gate_free[q]], gate[:, q, :, :], halves(bank[:, :]), ACT.Tanh, scale=0.5)
            t2 = pool.ts([t], gate[:, q, :, :], gate[:, q, :, :], 0.5, ALU.mult, 0.5, ALU.add)
            o = yb[:, 2 * i:2 * i + 2, :]
            t2 = pool.tt([t2, yb_made[2 * i]], o, o, gate[:, q, :, :], ALU.mult)
            yb_made[2 * i] = yb_made[2 * i + 1] = t2
            gate_free[q] = [t2]
            return [t]
        return evac

    def evac_ga(i):
        def evac(_, bank, done):
            o = ga[:, 2 * i:2 * i + 2, :]
            t = act.act([done, yb_made], o, halves(bank[:, :]), ACT.Tanh, scale=0.5)
            t2 = pool.ts([t], o, o, 0.5, ALU.mult, 0.5, ALU.add)
            ga_made[2 * i] = ga_made[2 * i + 1] = t2
            return [t]
        return evac

    for i in range(4):
        weave(layer(S, [("gb", i)], h, evac_gb(i), dense), side, 1)
    drain(side)

    tz = K.buf("tz", A + 68, [P, 2, 2, T])
    sqz = K.buf("sqz", A + 72, [P, 2, 2, T])
    y_hi = K.buf("y_hi", A + 68, [P, 16, T], F32R)
    y_lo = K.buf("y_lo", A + 84, [P, 16, T], F32R)
    yn = K.buf("yn", A + 112, [P, 2, T])
    r8 = K.buf("r8", A + 114, [8, T])
    tz_free, sq_free, sq_made, g_made = [[], []], [[], []], {}, []
    ms, rb = B[3], [B[4], B[5]]

    def evac_z(g):
        def evac(_, bank, done):
            q, y = g % 2, xs[:, 2 * g:2 * g + 2, :]
            t = act.act([done, tz_free[q]], tz[:, q, :, :], halves(bank[:, :]), ACT.Silu)
            t2 = dve.tt([t, y_made], y, y, tz[:, q, :, :], ALU.mult)
            tz_free[q] = [t2]
            g_made.append(t2)
            sq_made[g] = act.act([t2, sq_free[q]], sqz[:, q, :, :], y, ACT.Square)
            return [t]
        return evac

    def mean_square(g):
        q = g % 2
        t = pe.mm([sq_made[g], ms.free if g == 0 else []],
                  *[(ms[0:8, 0:T], K.c["sel8"][:, 8 * g:8 * g + 8], sqz[:, q, i, :], g == 0 and i == 0, g == 7 and i == 1)
                    for i in range(2)])
        sq_free[q] = [t]
        return t

    for g in range(8):
        drain(layer(S, [("z", g)], h, evac_z(g), dense))
        modulation(K, S, 8 + g)
        if g:
            mean_square(g - 1)

    y_ready = []

    def norm_y():
        t_ms = mean_square(7)
        t = act.act([t_ms], r8[:, :], ms[0:8, 0:T], ACT.Sqrt, bias=par[0:8, C_EPS:C_EPS + 1])
        ms.free = [t]
        t_r = dve.recip([t], r8[:, :], r8[:, :])
        yield
        yn_free = [[], []]
        made = []
        for g in range(8):
            if g % 2 == 0:
                b = rb[g // 2 % 2]
                t_b = pe.mm([t_r, b.free], *[(b[:, T * j:T * (j + 1)], ident[0:8, g + j:g + j + 1].to_broadcast([8, P]), r8[:, :],
                                              j == 0, True) for j in range(2)])
                made = []
            for i in range(2):
                f = 2 * g + i
                t = dve.stt([t_b, g_made[g], yn_free[i]], yn[:, i, :], xs[:, f, :], par[:, C_NORM + f:C_NORM + f + 1],
                            b[:, T * (g % 2):T * (g % 2 + 1)], ALU.mult, ALU.mult)
                made.append(t)
                yn_free[i] = split_x(K, y_hi, y_lo, f, yn[:, i, :], [t, t_ms], pool if i else dve)
                y_ready.append(yn_free[i])
            b.free = made
            yield

    m_hi = K.buf("m_hi", A, [P, 8, T], F32R)
    m_lo = K.buf("m_lo", A + 8, [P, 8, T], F32R)
    m_ready = []

    def evac_ssd(pairno, bank, done):
        out = []
        for i in range(2):
            j = 2 * pairno + i
            t = dve.tt([done, ga_made[j]], ga[:, j, :], bank[:, T * i:T * (i + 1)], ga[:, j, :], ALU.mult)
            out.append(t)
            t = dve.tt([t, yb_made[j]], ga[:, j, :], ga[:, j, :], yb[:, j, :], ALU.add)
            m_ready.append(split_x(K, m_hi, m_lo, j, ga[:, j, :], [t], pool))
        return out

    xa = K.buf("xa", A + 16, [P, 8, T])
    v = K.buf("v", A + 24, [P, 8, T])
    sq1 = K.buf("sq1", A + 32, [P, 8, T])
    x1 = K.buf("x1", A + 40, [P, 8, T])
    rs1 = K.buf("rs1", A + 60, [P, T])
    setup_late(K)
    side = norm_y()
    for i in range(4):
        weave(layer(S, [("ga", i)], h, evac_ga(i), dense), side, 2)
        modulation(K, S, 16 + i)
    drain(side)
    t_xa = K.load(xa[:, :, :], K.ins["xT"].rearrange("p (j t) -> p j t", t=T), after=[y_ready], queue=act)
    drain(layer(S, [("ssd_out", i) for i in range(8)], (y_hi, y_lo, y_ready), evac_ssd, dense, nk=16))
    t_xa = act.act([t_xa], xa[:, :, :], xa[:, :, :], ACT.Copy, scale=ALPHA)

    v_ready = []

    def evac_o(pairno, bank, done):
        for i in range(2):
            j = 2 * pairno + i
            v_ready.append(dve.stt([done, t_xa, K.mod_ready[16 + j]], v[:, j, :], bank[:, T * i:T * (i + 1)],
                                   K.mod[:, 16 + j:17 + j], xa[:, j, :], ALU.mult, ALU.add))
        return v_ready[-2:]

    K.prod_free = m_ready
    gmean = K.buf("gmean", A + 61, [P, 2, T])
    t = pe.mm([B[6].free], (B[6][:, 0:16], K.c["mean"][:, :], par[:, C_LN1G:C_LN1G + 16], True, True))
    t_gb = dve.do([t], lambda e: e.tensor_reduce(K.small[:, 16:18], B[6][:, 0:16].rearrange("p (n j) -> p n j", n=2), AX, ALU.add))
    B[6].free = [t_gb]
    for i in range(4):
        drain(layer(S, [("w_o", i)], (m_hi, m_lo, m_ready), lambda _, b, d, i=i: evac_o(i, b, d), dense))
        modulation(K, S, 20 + i, True)
    for i in range(RING, RING + 4):
        S.before[i] = m_ready
    x1_ready = []

    def out_x1(j, t):
        x1_ready.append(act.act([t], x1[:, j, :], v[:, j, :], ACT.Identity, bias=par[:, C_LN1B + j:C_LN1B + j + 1],
                                scale=par[:, C_LN1G + j:C_LN1G + j + 1]))

    t = layer_norm(K, v, v_ready, sq1, rs1[:, :], B[3], B[4], [], out_x1, gain=(C_LN1G, (K.small[:, 16:17], t_gb), B[5], gmean[:, 0, :], gmean[:, 1, :]))
    return x1, x1_ready, (K.small[:, 17:18], gmean[:, 0, :], [t, t_gb])


def moe(K, S, x1, x1_ready, x1_mean):
    pe, act, dve = K.pe, K.act, K.dve
    B, A, R = K.banks, AREA, AREA + 56
    par, ident = K.par, K.c["ident"]
    iota = K.c["iota"]

    h2 = K.buf("h2", A, [P, 8, T])
    h2_hi = K.buf("h2_hi", A + 8, [P, 8, T], F32R)
    h2_lo = K.buf("h2_lo", A + 48, [P, 8, T], F32R)
    v2 = K.buf("v2", A + 24, [P, 8, T])
    sq2 = K.buf("sq2", A + 32, [P, 8, T])
    rs2 = K.buf("rs2", A + 60, [P, T])
    n_hi = K.buf("n_hi", A + 16, [P, 2, D], F32R)
    n_lo = K.buf("n_lo", A + 32, [P, 2, D], F32R)
    hs = K.buf("hs", A + 100, [P, 2, T])
    hs_hi = K.buf("hs_hi", A + 102, [P, 2, T], F32R)
    hs_lo = K.buf("hs_lo", A + 104, [P, 2, T], F32R)

    h2_ready, h2_split = [], []

    def out_h2(j, t):
        t = act.act([t, K.mod_ready[32 + j], K.mod_ready[24 + j]], h2[:, j, :], v2[:, j, :], ACT.Identity,
                    scale=K.mod[:, 32 + j:33 + j], bias=K.mod[:, 24 + j:25 + j])
        h2_ready.append(t)
        h2_split.append(split_x(K, h2_hi, h2_lo, j, h2[:, j, :], [t]))

    layer_norm(K, x1, x1_ready, sq2, rs2[:, :], B[3], B[4], [], out_h2, dst=v2, mean=x1_mean)

    s = S.take("router")
    b = B[7]
    for k in range(8):
        w = s.raw[:, P * (k // 2) + 64 * (k % 2):P * (k // 2) + 64 * (k % 2) + 64]
        t = pe.mm([s.ready, h2_ready[k], b.free if k == 0 else []],
                  *[(b[:, 64 * i:64 * (i + 1)], h2[:, k, P * i:P * (i + 1)], w, k == 0 and i == 0, k == 7) for i in range(2)])
    s.done.append(t)
    sig = K.buf("sig", R, [P, 2, 64])
    bi = K.buf("bi", R + 0.5, [P, 2, 64])
    bm = K.buf("bm", R + 1, [P, 2, 64])
    mr = K.buf("mr", R + 1.5, [P, 2, 64])
    g8 = K.buf("g8", R + 2, [P, 16, 8])
    gt = K.buf("gt", R + 2.5, [P, 16, 8])
    eq = K.buf("eq", R + 3, [P, 16, 8])
    gs = K.buf("gs", R + 3.5, [P, 16])
    cnt = K.buf("cnt", R + 3.5625, [P, 16])
    mx = K.buf("mx", R + 3.625, [P, 2, 8])
    gsum = K.buf("gsum", R + 3.6875, [P, 2])
    M = K.buf("M", R + 4, [P, 2, 64], BF16)
    tri = K.buf("tri", R + 4.25, [P, P], BF16)
    ones = K.buf("ones", R + 4.5, [P, P], BF16)
    one_of = K.buf("one_of", R + 4.75, [64, 64], BF16)
    G = K.buf("G", R + 5, [P, 2, 64])
    Gs = K.buf("Gs", R + 5.5, [P, 2, 2, 64], F32R)
    rm = K.buf("rm", R + 6.5, [P, 2, 64])
    rmT = K.buf("rmT", R + 7, [64, T], BF16)
    flags = K.buf("flags", R + 7.5, [1, len(GROUPS)], I32)
    gc = K.buf("gc", R + 7.625, [P, 2])
    junk = K.buf("junk", R + 7.6875, [P, 8])
    order = K.buf("order", R + 7.75, [1, N_EXPERTS], I32)
    rmU = K.buf("rmU", R + 1.5, [P, 2, 64])
    kb = K.buf("kb", R + 2, [64, 64])
    tie = K.buf("tie", R + 2.25, [64, 64])
    Pi = K.buf("Pi", R + 2.5, [64, 64])
    Pib = K.buf("Pib", R + 2.75, [64, 64], BF16)
    rmTu = K.buf("rmTu", R + 3, [64, T], BF16)
    kc = K.buf("kc", R + 3.75, [64, 2])
    cb = K.buf("cb", R + 3.875, [64, 2], BF16)
    GT = K.buf("GT", R, [64, T])

    t_sig = act.act([t], sig[:, :, :], halves(b[:, 0:P]), ACT.Sigmoid)
    b.free = [t_sig]
    t = dve.copy([K.t_late], tri[:, :], K.c["tri"])
    t_bf = [t, dve.fill([], ones[:, :], 1.0), dve.copy([K.t_cst], one_of[:, :], ident[0:64, 0:64])]

    bias = K.c["router_bias"]
    t = dve.tt([t_sig, K.t_late], bi[:, :, :], sig[:, :, :], bias.unsqueeze(1).to_broadcast([P, 2, 64]), ALU.add)
    t = [dve.do([t], lambda e, i=i, g=g: e.max(out=g8[:, 8 * i + g, :], in_=bi[:, i, 8 * g:8 * g + 8]))
         for i in range(2) for g in range(8)]
    t = dve.tt([t], gs[:, :], g8[:, :, 0], g8[:, :, 1], ALU.add)
    one = gs[:, :].unsqueeze(2).to_broadcast([P, 16, 8])
    for i in range(2):
        a = slice(8 * i, 8 * i + 8)
        other = gs[:, a].unsqueeze(1).to_broadcast([P, 8, 8])
        one = gs[:, a].unsqueeze(2).to_broadcast([P, 8, 8])
        t1 = dve.tt([t], eq[:, a, :], other, one, ALU.is_equal)
        t2 = dve.tt([t], gt[:, a, :], other, one, ALU.is_gt)
        t1 = dve.tt([t1], eq[:, a, :], eq[:, a, :], K.c["before"].rearrange("p (g h) -> p g h", g=8), ALU.mult)
        t3 = dve.tt([t1, t2], gt[:, a, :], gt[:, a, :], eq[:, a, :], ALU.add)
        t3 = dve.do([t3], lambda e, a=a: e.tensor_reduce(cnt[:, a], gt[:, a, :], AX, ALU.add))
        t3 = dve.ts([t3], cnt[:, a], cnt[:, a], 4.0, ALU.is_ge, -1e30, ALU.mult)
        c = cnt[:, a].unsqueeze(2).to_broadcast([P, 8, 8])
        t3 = dve.tt([t3], bm[:, i, :].rearrange("p (g h) -> p g h", g=8), bi[:, i, :].rearrange("p (g h) -> p g h", g=8), c, ALU.add)
        t3 = dve.do([t3], lambda e, i=i: e.max(out=mx[:, i, :], in_=bm[:, i, :]))
        t3 = dve.do([t3], lambda e, i=i: e.match_replace(out=mr[:, i, :], in_to_replace=mx[:, i, :], in_values=bm[:, i, :], imm_value=-2e30))
        t_M = dve.tt([t3], M[:, i, :], mr[:, i, :], bm[:, i, :], ALU.is_lt)

    two = [B[5], B[6]]
    hs_ready = []
    st = {}

    def evac_gate(_, bank, done):
        st["g"] = act.act([done], hs[:, :, :], halves(bank[:, :]), ACT.Silu)
        return [st["g"]]

    def evac_up(_, bank, done):
        t = dve.tt([done, st["g"]], hs[:, :, :], halves(bank[:, :]), hs[:, :, :], ALU.mult)
        for i in range(2):
            hs_ready.append(split_x(K, hs_hi, hs_lo, i, hs[:, i, :], [t]))
        return [t]

    drain(layer(S, ["sh_gate"], (h2_hi, h2_lo, h2_split), evac_gate, two))
    drain(layer(S, ["sh_up"], (h2_hi, h2_lo, h2_split), evac_up, two))
    S.before[RING + 4] = S.before[RING + 5] = [hs_ready]

    b = B[7]
    t = pe.mm([b.free, t_bf, t_M], (b[:, 0:64], tri[:, :], M[:, 0, :], True, True),
              (b[:, 64:P], ones[:, :], M[:, 0, :], False, False), (b[:, 64:P], tri[:, :], M[:, 1, :], False, True),
              *[(b[0:64, P:P + 64], ones[:, 0:64], M[:, i, :], False, i == 1) for i in range(2)],
              *[(b[0:64, P + 64:P + 65], M[:, i, :], ones[:, 0:1], False, i == 1) for i in range(2)])
    own = K.c["own"]
    t1 = dve.tt([t], kb[:, :], b[0:64, P:P + 64], K.c["bump"][0:64, :], ALU.add)
    t2 = dve.tt([t], kc[:, 0:1], b[0:64, P + 64:P + 65], own[0:64, 0:1], ALU.add)
    t3 = dve.copy([t], cb[:, 0:1], b[0:64, P + 64:P + 65])
    t4 = dve.copy([K.t_late], cb[:, 1:2], own[0:64, 1:2])
    t_rm = dve.tt([t], rmU[:, :, :], halves(b[:, 0:P]), M[:, :, :], ALU.mult)
    b.free = [t1, t2, t3, t_rm]
    t1 = dve.stt([t1, t2], tie[:, :], kb[:, :], kc[:, 0:1], K.c["upto"][0:64, :], ALU.is_equal, ALU.mult)
    t1 = dve.stt([t1], kb[:, :], kb[:, :], kc[:, 0:1], tie[:, :], ALU.is_gt, ALU.add)
    t1 = dve.do([t1], lambda e: e.tensor_reduce(kc[:, 1:2], kb[:, :], AX, ALU.add))
    t_Pi = dve.ts([t1, K.t_late], Pi[:, :], iota[0:64, 0:64], kc[:, 1:2], ALU.is_equal)
    t_Pib = dve.copy([t_Pi], Pib[:, :], Pi[:, :])
    n_made = []
    for i in range(2):
        for q in range(2):
            b = two[q]
            t = pe.tr([b.free, h2_ready], ident, *[(b[:, P * f:P * (f + 1)], h2[:, 4 * q + f, P * i:P * (i + 1)]) for f in range(4)])
            o = slice(512 * q, 512 * (q + 1))
            t1 = act.act([t], n_hi[:, i, o], b[:, :])
            t2 = dve.tt([t1], n_lo[:, i, o], b[:, :], n_hi[:, i, o].bitcast(F32), ALU.subtract)
            b.free = [t2]
            n_made.append(t2)

    b = B[4]
    t = pe.mm([b.free, t_Pib, t3, t4], (b[0:1, 0:64], cb[:, 1:2], Pib[:, :], True, True), (b[0:1, 64:P], cb[:, 0:1], Pib[:, :], False, True))
    t1 = dve.copy([t], order[:, :], b[0:1, 0:64])
    S.order, S.order_ready = order, [t1]
    t2 = dve.copy([t], K.small[0:1, 0:64], b[0:1, 64:P])
    b.free = [t1, t2]
    t1 = [dve.do([t2], lambda e, f=f, n=n, o=o: e.tensor_reduce(flags[:, o], K.small[0:1, f].rearrange("p (g e) -> p g e", e=n), AX, ALU.max))
          for f, n, o in ((slice(0, 4), 2, slice(0, 2)), (slice(4, 12), 1, slice(2, 10)), (slice(12, 32), 2, slice(10, 20)),
                          (slice(32, 64), 4, slice(20, 28)))]
    for q in (pe, act, dve):
        q.load_flags(t1, flags[:, :])
    b = B[7]
    t = pe.tr([b.free, t_rm], ident, *[(b[0:64, P * i:P * (i + 1)], rmU[:, i, :]) for i in range(2)])
    t_rm = dve.copy([t], rmTu[:, :], b[0:64, 0:T])
    b.free = [t_rm]
    t = pe.mm([b.free, t_Pib], *[(b[:, 64 * i:64 * (i + 1)], rmTu[:, P * i:P * (i + 1)], Pib[:, :], i == 0, True) for i in range(2)],
              (b[0:64, P:P + T], Pib[:, :], rmTu[:, :], False, True))
    t1 = dve.copy([t], rm[:, :, :], halves(b[:, 0:P]))
    t2 = dve.copy([t], rmT[:, :], b[0:64, P:P + T])
    b.free = t_rm = [t1, t2]

    t = dve.tt([t_M], G[:, :, :], sig[:, :, :], M[:, :, :], ALU.mult)
    t = dve.do([t], lambda e: e.tensor_reduce(gsum[:, :], G[:, :, :], AX, ALU.add))
    t = dve.recip([t], gsum[:, :], gsum[:, :])
    t = [dve.ts([t], G[:, i, :], G[:, i, :], gsum[:, i:i + 1], ALU.mult, 2.5, ALU.mult) for i in range(2)]
    b = B[4]
    t = pe.tr([b.free, t], ident, *[(b[0:64, P * i:P * (i + 1)], G[:, i, :]) for i in range(2)])
    t = dve.copy([t], GT[:, :], b[0:64, 0:T])
    b.free = [t]
    t = pe.mm([t, t_Pi], *[(b[:, 64 * i:64 * (i + 1)], GT[:, P * i:P * (i + 1)], Pi[:, :], i == 0, True) for i in range(2)])
    t = dve.copy([t], Gs[:, :, 0, :], halves(b[:, 0:P]))
    t_G = dve.tt([t], Gs[:, :, 1, :], halves(b[:, 0:P]), Gs[:, :, 0, :].bitcast(F32), ALU.subtract)
    b.free = [t_G]

    s = S.take("sh_down")
    for n, (_, k0, m0) in enumerate(s.tiles):
        m, k = m0 // P, k0 // P
        o = B[m // 2][:, T * (m % 2):T * (m % 2 + 1)]
        wh, wl = s.hi[:, P * n:P * (n + 1)], s.lo[:, P * n:P * (n + 1)]
        first = k == 0 and m % 2 == 0
        t_acc = pe.mm([s.ready, hs_ready[k], B[m // 2].free if first else []],
                      (o, wh, hs_hi[:, k, :], first, False), (o, wh, hs_lo[:, k, :], False, False),
                      (o, wl, hs_hi[:, k, :], False, False))
    s.done.append(t_acc)

    t_x1 = act.act([h2_ready], x1[:, :, :], x1[:, :, :], ACT.Copy, scale=ALPHA)

    Pm = K.buf("Pm", A + 108, [P, 2, 2, P], F32R)
    PT = [K.buf("PT", A + 110, [P, 2, T], F32R)[:, q, :] for q in range(2)] + [K.buf("PT2", A + 64, [P, T], F32R)[:, :]]
    xg = K.buf("xg", A + 100, [P, 2, 8, P])
    sg = K.buf("sg", A + 112, [P, T])
    hm = K.buf("hm", A + 113, [P, T])
    hmT = K.buf("hmT", A + 114, [P, 2, P])
    y_hi = K.buf("ye_hi", A + 24, [P, 2, D], F32R)
    y_lo = K.buf("ye_lo", A, [P, 2, D], F32R)
    acc = B[0:4]
    free = {"xg0": [t_acc], "xg1": [t_acc], "y0": [n_made], "y1": [n_made]}
    made = {}

    def onehot(g, j, q):
        n = len(g)
        w = P // n
        made["P"] = dve.tt([t_rm, K.t_late, free.get(f"P{q}")], Pm[:, q, :, :].rearrange("p i (e s) -> p i e s", e=n),
                           rm[:, :, g[0]:g[0] + n].unsqueeze(3).to_broadcast([P, 2, n, w]),
                           iota[:, w * j:w * (j + 1)].unsqueeze(1).unsqueeze(1).to_broadcast([P, 2, n, w]), ALU.is_equal)

    def gather(q):
        out = []
        for half in range(2):
            b = B[5 + half]
            t = pe.mm([made["P"], n_made, b.free, free[f"xg{q}"]],
                      *[(b[:, P * f:P * (f + 1)], n[:, i, 512 * half + P * f:512 * half + P * (f + 1)], Pm[:, q, i, :],
                         f == 0 and i == 0 and n is n_hi, False) for f in range(4) for i in range(2) for n in (n_hi, n_lo)])
            o, src = xg[:, q, 4 * half:4 * half + 4, :], b[:, :].rearrange("p (f s) -> p f s", f=4)
            out.append(act.act([t], o, src) if half == 0 else dve.copy([t], o, src))
            b.free = [out[-1]]
        made[f"xg{q}"] = out

    def places(g, j, q, z):
        n = len(g)
        w = P // n
        b = B[7]
        t = pe.mm([b.free, t_rm, made["P"], t_G, t_bf],
                  *[(b[w * e:w * (e + 1), 0:T], one_of[:, g[e]:g[e] + 1].to_broadcast([64, w]), rmT[:, :], True, True) for e in range(n)],
                  *[(b[:, T:T + 2 * n], Pm[:, q, i, :], Gs[:, i, :, g[0]:g[0] + n], False, i == 1) for i in range(2)])
        free[f"P{q}"] = [t]
        a = dve.ts([t, K.t_late, free.get(f"PT{z}")], PT[z], b[:, 0:T], K.c[f"slot{n}"][:, j:j + 1], ALU.is_equal)
        c = dve.do([t, free.get(f"gc{q}"), free.get("junk")],
                   lambda e: e.tensor_tensor_reduce(junk[:, 0:2 * n], b[:, T:T + 2 * n], K.c[f"of{n}"], 1.0, 0.0, ALU.mult, ALU.add,
                                                    gc[:, q:q + 1]))
        free["junk"] = [c]
        b.free = [a, c]
        made[f"PT{z}"], made[f"gc{q}"] = a, c

    def up(b, q, ws):
        n = len(ws) // 2
        w = P // n
        for half in range(2):
            calls = []
            for k in range(4 * half, 4 * half + 4):
                for e in range(n):
                    calls.append((b[w * e:w * (e + 1), :], xg[:, q, k, w * e:w * (e + 1)],
                                  ws[n * half + e].raw[:, 512 * (k % 4):512 * (k % 4 + 1)], k == 0, k == 7))
            mine = ws[n * half:n * (half + 1)]
            t = pe.mm([b.free if half == 0 else [], made[f"xg{q}"], [s.ready for s in mine]], *calls)
            for s in mine:
                s.done.append(t)
        free[f"xg{q}"] = [t]
        made["up"] = t

    def middle(b, q):
        t = act.act([made["up"], free.get("sg")], sg[:, :], b[:, 0:T], ACT.Silu)
        t = dve.stt([t, made[f"gc{q}"], free.get("hm")], hm[:, :], sg[:, :], gc[:, q:q + 1], b[:, T:2 * T], ALU.mult, ALU.mult)
        b.free = free["sg"] = free[f"gc{q}"] = [t]
        made["hm"] = t

    def turn(b):
        t = pe.tr([b.free, made["hm"]], ident, *[(b[:, P * k:P * (k + 1)], hm[:, P * k:P * (k + 1)]) for k in range(2)])
        free["hm"] = [t]
        t = act.act([t, free.get("hmT")], hmT[:, :, :], b[:, 0:T].rearrange("p (k s) -> p k s", k=2))
        b.free = [t]
        made["hmT"] = t

    def down(q, ws):
        out, w = [], P // len(ws)
        for n in range(2):
            b, o = B[5 + n], slice(512 * n, 512 * (n + 1))
            t = pe.mm([b.free, made["hmT"], [s.ready for s in ws]],
                      *[(b[w * e:w * (e + 1), :], hmT[:, k, w * e:w * (e + 1)], s.raw[:, D * k + 512 * n:D * k + 512 * (n + 1)],
                         k == 0, k == 1) for k in range(2) for e, s in enumerate(ws)])
            a = act.act([t, free[f"y{q}"]], y_hi[:, q, o], b[:, :])
            a = dve.tt([a], y_lo[:, q, o], b[:, :], y_hi[:, q, o].bitcast(F32), ALU.subtract)
            b.free = [a]
            out.append(a)
        for s in ws:
            s.done.append(t)
        free["hmT"] = [t]
        made[f"y{q}"] = out

    def combine(q, z):
        calls = []
        for m in range(8):
            o = acc[m // 2][:, T * (m % 2):T * (m % 2 + 1)]
            for y in (y_hi, y_lo):
                calls.append((o, y[:, q, P * m:P * (m + 1)], PT[z], False, False))
        t = pe.mm([made[f"y{q}"], made[f"PT{z}"]], *calls)
        free[f"y{q}"] = free[f"PT{z}"] = [t]
        made["acc"] = t

    onehot(GROUPS[0], 0, 0)
    gather(0)
    places(GROUPS[0], 0, 0, 0)
    for i, g in enumerate(GROUPS):
        q, r = i % 2, 1 - i % 2
        then = GROUPS[i + 1] if i + 1 < len(GROUPS) else None
        wu = [S.take(("expert", p, half, g)) for half in range(2) for p in g]
        up(B[4], q, wu)
        if then:
            onehot(then, 0, r)
        middle(B[4], q)
        if i:
            combine(r, r)
        turn(B[7])
        if then:
            gather(r)
            places(then, 0, r, r)
        wd = [S.take(("expert", p, 2, g)) for p in g]
        down(q, wd)
        flag = FLAGS.index(g)
        before = dict(free), [list(flat(b.free)) for b in B]
        for j in range(1, ROUNDS[len(g)]):
            for queue in (pe, act, dve):
                queue.branch(flag, P // len(g) * j, made["acc"] if j > 1 else [])
            onehot(g, j, q)
            gather(q)
            places(g, j, q, 2)
            up(B[7], q, wu)
            middle(B[7], q)
            turn(B[5])
            down(r, wd)
            combine(r, 2)
        for j in range(1, ROUNDS[len(g)]):
            for queue in (pe, act, dve):
                queue.close()
        for k, tokens in before[0].items():
            free[k] = list(dict.fromkeys(flat([free[k], tokens])))
        for b, tokens in zip(B, before[1]):
            b.free = list(dict.fromkeys(flat([b.free, tokens])))
    combine(1, 1)

    v3 = K.buf("v3", A + 16, [P, 8, T])
    sq3 = K.buf("sq3", A + 32, [P, 8, T])
    rs3 = K.buf("rs3", A + 62, [P, T])
    x2 = K.buf("x2", A + 40, [P, 8, T])
    v_ready, x2_ready = [], []
    for j in range(8):
        v_ready.append(dve.stt([made["acc"], t_x1, K.mod_ready[40 + j]], v3[:, j, :], acc[j // 2][:, T * (j % 2):T * (j % 2 + 1)],
                               K.mod[:, 40 + j:41 + j], x1[:, j, :], ALU.mult, ALU.add))
        acc[j // 2].free = [v_ready[-1]]

    def out_x2(j, t):
        x2_ready.append(act.act([t], x2[:, j, :], v3[:, j, :], ACT.Identity, bias=par[:, C_LN2B + j:C_LN2B + j + 1],
                                scale=par[:, C_LN2G + j:C_LN2G + j + 1]))

    layer_norm(K, v3, v_ready, sq3, rs3[:, :], B[4], B[5], [made["acc"]], out_x2)
    return x2, x2_ready, [made["acc"]] + [s.done for s in S.user[RING:]]


def layer_across(S, keys, x, evac, banks):
    K = S.core
    hi, lo, ready = x
    mine = [banks[(K.turn + i) % len(banks)] for i in range(2)]
    K.turn += 2
    for n, key in enumerate(keys):
        s = S.take(key)
        for q in range(4):
            k = 4 * n + q
            w = slice(512 * q, 512 * (q + 1))
            first, last = k == 0, k == 4 * len(keys) - 1
            for i in range(2):
                b, t = mine[i], slice(P * i, P * (i + 1))
                tok = K.pe.mm([s.ready, ready[k], b.free if first else []],
                              (b[:, :], hi[:, k, t], s.hi[:, w], first, False), (b[:, :], lo[:, k, t], s.hi[:, w], False, False),
                              (b[:, :], hi[:, k, t], s.lo[:, w], False, last))
                if q == 3 and i == 1:
                    s.done.append(tok)
                if last:
                    b.free = list(flat(evac(i, b, tok)))
            yield


def rms_norm(K, x, ready, gain, hi, lo, spare, r, bank, after):
    for j in range(8):
        t = K.dve.tt([ready[j], after], spare[:, j, :], x[:, j, :], x[:, j, :], ALU.mult)
        t = K.pe.mm([t, bank.free if j == 0 else []], (bank[:, 0:T], K.c["mean"][:, :], spare[:, j, :], j == 0, j == 7))
    t = K.act.act([t], r, bank[:, 0:T], ACT.Sqrt, bias=K.par[:, C_EPS + 1:C_EPS + 2])
    bank.free = [t]
    t = K.dve.recip([t], r, r)
    late, out = [], []
    for j in range(9):
        if j < 8:
            late.append(K.dve.stt([t], spare[:, j, :], x[:, j, :], K.par[:, gain + j:gain + j + 1], r, ALU.mult, ALU.mult))
        if j:
            out.append(split_x(K, hi, lo, j - 1, spare[:, j - 1, :], [late[j - 1]]))
    return out


def log1p_exp(dve, act, u, p, z, z2, t):
    t = act.act([t], u, u, ACT.Exp)
    t = dve.ts([t], z, u, 2.0, ALU.add)
    t = dve.recip([t], z, z)
    yield
    t = dve.tt([t], z, z, u, ALU.mult)
    t = dve.tt([t], z2, z, z, ALU.mult)
    t = dve.ts([t], p, z2, 2.0 / 17, ALU.mult)
    for c in (15, 13, 11, 9, 7, 5, 3):
        t = dve.stt([t], p, p, 2.0 / c, z2, ALU.add, ALU.mult)
    t = dve.stt([t], p, p, 2.0, z, ALU.add, ALU.mult)
    yield t


def fox(K, S, x2, x2_ready, after):
    pe, act, dve, pool = K.pe, K.act, K.dve, K.pool
    B, A = K.banks, AREA
    par, ident = K.par, K.c["ident"]
    dense = B[0:3]

    h_hi = K.buf("f_hi", A, [P, 8, T], F32R)
    h_lo = K.buf("f_lo", A + 8, [P, 8, T], F32R)
    spare = K.buf("f_spare", A + 48, [P, 8, T])
    r = K.buf("f_r", A + 56, [P, T])
    q = K.buf("q", A + 16, [P, 8, T])
    sq = K.buf("f_sq", A + 24, [P, 8, T])
    v = K.buf("f_v", A + 32, [P, 2, 512])
    u = K.buf("f_u", A + 36, [P, 2, 512])
    og = K.buf("og", A + 57, [P, 4, T])
    r16 = K.buf("r16", A + 61, [16, T])
    c = K.buf("f_c", A + 62, [8, T])
    nc = K.buf("f_nc", A + 63, [8, T])
    f = K.buf("f_f", A + 64, [8, 5, T])
    cT = K.buf("f_cT", A + 69, [P, 2, 8])
    small = K.buf("f_small", A + 69.25, [P, 8, 6])
    lg = K.buf("lg", A + 70, [P, 2, 384])
    pT = K.buf("pT", A + 73, [P, 2, 384])
    at = K.buf("at", A + 76, [P, 2, T])
    heads = K.buf("heads", A + 78, [P, P])
    neg = K.buf("neg", A + 78.5, [P, 256])
    band = K.buf("band", A + 79.5, [P, 4, 384])
    pl = K.buf("pl", A + 86, [P, 4, T])
    pl_hi = K.buf("pl_hi", A + 90, [P, 4, T], F32R)
    pl_lo = K.buf("pl_lo", A + 94, [P, 4, T], F32R)
    cat_hi = K.buf("cat_hi", A + 98, [P, 8, T], F32R)
    cat_lo = K.buf("cat_lo", A + 106, [P, 8, T], F32R)

    t_heads = K.load(heads[:, :], K.cst("heads"), after=after, queue=act)
    t_neg = K.load(neg[:, :], K.cst("neg"), after=after, queue=act)
    t_band = K.load(band[:, :, :], K.cst("band").rearrange("p (g t) -> p g t", g=4), after=after, queue=act)
    ready = rms_norm(K, x2, x2_ready, C_MIX, h_hi, h_lo, spare, r[:, :], B[7], after)
    h = (h_hi, h_lo, ready)

    st = {}

    def evac_f(_, bank, done):
        st["f"] = act.act([done], f[:, 0, :], bank[0:8, 0:T], ACT.Identity, bias=par[0:8, C_FB:C_FB + 1])
        return [st["f"]]

    def steps_c():
        x, w, p, z, z2 = (f[:, i, :] for i in range(5))
        t = dve.stt([st["f"]], w, x, -1.0, x, ALU.mult, ALU.min)
        for t in log1p_exp(dve, act, w, p, z, z2, t):
            yield
        t = dve.stt([t], w, x, 0.0, p, ALU.min, ALU.subtract)
        t = dve.do([t, dve.fill([], z2, 0.0)], lambda e: e.tensor_tensor_scan(c[:, :], w, z2, 0.0, ALU.add, ALU.add))
        t2 = dve.ts([t], nc[:, :], c[:, :], -1.0, ALU.mult)
        yield
        b = B[7]
        tt = pe.tr([t, b.free], ident, *[(b[:, 8 * i:8 * (i + 1)], c[:, P * i:P * (i + 1)]) for i in range(2)])
        t3 = dve.copy([tt], cT[:, :, :], b[:, 0:16].rearrange("p (i h) -> p i h", i=2))
        b.free = [t3]
        st["c"] = [t2, t3]
        yield

    drain(layer(S, ["hy_f"], h, evac_f, dense, steps=1))
    side = steps_c()

    q_made = [None] * 8
    sq_made = [None] * 8

    def evac_qk(half):
        def evac(pairno, bank, done):
            j = 4 * half + 2 * pairno
            t = act.act([done], q[:, j:j + 2, :], halves(bank[:, :]))
            for i in range(2):
                q_made[j + i] = t
                sq_made[j + i] = dve.tt([t], sq[:, j + i, :], q[:, j + i, :], q[:, j + i, :], ALU.mult)
            return [t]
        return evac

    side = weave(layer(S, [("q", 0), ("q", 1)], h, evac_qk(0), dense), side, 1)
    side = weave(layer(S, [("k", 0), ("k", 1)], h, evac_qk(1), dense), side, 1)

    def qk_norm():
        b = B[7]
        for n in range(8):
            t = pe.mm([sq_made[n], t_heads, b.free if n == 0 else []], (b[0:16, 0:T], heads[:, 16 * n:16 * n + 16], sq[:, n, :], n == 0, n == 7))
        yield
        t = act.act([t], r16[:, :], b[0:16, 0:T], ACT.Sqrt, bias=par[0:16, C_QKE:C_QKE + 1])
        b.free = [t]
        t_r = dve.recip([t], r16[:, :], r16[:, :])
        yield
        for j in range(4):
            b = B[6 + j % 2]
            t = pe.mm([t_r, b.free], *[(b[64 * e:64 * (e + 1), T * m:T * (m + 1)],
                                        ident[0:16, 2 * (j + 4 * m) + e:2 * (j + 4 * m) + e + 1].to_broadcast([16, 64]), r16[:, :], m == 0, True)
                                       for m in range(2) for e in range(2)])
            out = []
            for m in range(2):
                n = j + 4 * m
                col = (C_QG, C_KG)[m]
                out.append(dve.stt([t, q_made[n]], q[:, n, :], q[:, n, :], par[:, col:col + 1], b[:, T * m:T * (m + 1)], ALU.mult, ALU.mult))
                q_made[n] = out[-1]
            b.free = out
            yield

    v_made, og_made, cat_ready = [None] * 2, [None] * 4, [None] * 8
    lg_free, pT_free, at_free = [[], []], [[], []], [[], []]

    def attention():
        spans = ((0, P, 0), (P, 384, 1))
        p_made = {}

        def scores(j):
            calls = [[], []]
            for a, z, i in spans:
                for e in range(2):
                    n = 64 * e
                    calls[e].append((B[3 + e][:, a:z], q[n:n + 64, j, P * i:P * (i + 1)], q[n:n + 64, 4 + j, 0:z - a], a == 0, False))
            more = [[(B[3 + e][:, a:z], ident[0:8, 2 * j + e:2 * j + e + 1].to_broadcast([8, P]), nc[:, 0:z - a], False, True)
                     for a, z, i in spans] for e in range(2)]
            inter = [x for ab in zip(*calls) for x in ab]
            t = pe.mm([q_made[j], q_made[4 + j], st["c"], B[3].free, B[4].free], *inter, *more[0], *more[1])
            for e in range(2):
                h_ = 2 * j + e
                m = small[:, h_, :]
                made = []
                for a, z, i in spans:
                    made.append(dve.stt([t, st["c"], t_neg, lg_free[e]], lg[:, e, a:z], B[3 + e][:, a:z], cT[:, i, h_:h_ + 1],
                                        neg[:, 256 - (z - a):256], ALU.add, ALU.add))
                B[3 + e].free = made
                sums = []
                for a, z, i in spans:
                    t2 = dve.do([made[i]], lambda e_, a=a, z=z, i=i, m=m, e=e: e_.tensor_reduce(m[:, i:i + 1], lg[:, e, a:z], AX, ALU.max, negate=True))
                    sums.append(act.act([t2], lg[:, e, a:z], lg[:, e, a:z], ACT.Exp, bias=m[:, i:i + 1], accum_out=m[:, 2 + i:3 + i]))
                t2 = dve.recip([sums], m[:, 4:6], m[:, 2:4])
                p_made[e] = [dve.ts([t2], lg[:, e, a:z], lg[:, e, a:z], m[:, 4 + i:5 + i], ALU.mult) for a, z, i in spans]

        def values(j):
            for e in range(2):
                b = B[5]
                t = pe.tr([p_made[e], b.free], ident, *[(b[:, P * n:P * (n + 1)], lg[:, e, P * n:P * (n + 1)]) for n in range(3)])
                lg_free[e] = [t]
                t = act.act([t, pT_free[e]], pT[:, e, :], b[:, 0:384])
                b.free = [t]
                p_made[e] = [t]
            b = B[6]
            t = pe.mm([p_made[0], p_made[1], v_made, b.free],
                      *[(b[64 * e:64 * (e + 1), P * i:T], v[:, i, P * j + 64 * e:P * j + 64 * (e + 1)], pT[:, e, T * i:(T, 384)[i]], i == 0, i == 1)
                        for i in range(2) for e in range(2)])
            pT_free[0] = pT_free[1] = [t]
            m = j % 2
            t = dve.tt([t, og_made[j], at_free[m]], at[:, m, :], b[:, 0:T], og[:, j, :], ALU.mult)
            b.free = [t]
            cat_ready[j] = at_free[m] = split_x(K, cat_hi, cat_lo, j, at[:, m, :], [t])

        scores(0)
        yield
        for j in range(4):
            values(j)
            yield
            if j < 3:
                scores(j + 1)
                yield

    def evac_v(i, bank, done):
        v_made[i] = act.act([done], v[:, i, :], bank[:, :])
        return [v_made[i]]

    u_made = [None] * 2

    def evac_u(i, bank, done):
        u_made[i] = act.act([done], u[:, i, :], bank[:, :])
        return [u_made[i]]

    def evac_og(pairno, bank, done):
        o = og[:, 2 * pairno:2 * pairno + 2, :]
        t = act.act([done], o, halves(bank[:, :]), ACT.Tanh, scale=0.5)
        og_made[2 * pairno] = og_made[2 * pairno + 1] = pool.ts([t], o, o, 0.5, ALU.mult, 0.5, ALU.add)
        return [t]

    drain(side)
    norm = qk_norm()
    weave(layer_across(S, [("v", 0), ("v", 1)], h, evac_v, dense), norm, 1)
    drain(norm)
    weave(layer_across(S, [("u", 0), ("u", 1)], h, evac_u, dense), iter(()), 1)

    pl_ready = []
    for g in range(4):
        b = dense[K.turn % 3]
        K.turn += 1
        t = pe.mm([u_made, t_band, b.free], (b[:, 0:T], u[:, 0, P * g:P * (g + 1)], band[:, g, 0:T], True, False),
                  (b[:, P:T], u[:, 1, P * g:P * (g + 1)], band[:, g, T:384], False, True))
        t = act.act([t], pl[:, g, :], b[:, 0:T])
        b.free = [t]
        pl_ready.append(split_x(K, pl_hi, pl_lo, g, pl[:, g, :], [t]))

    side = attention()
    next(side)
    s = S.take("pool")
    for g in range(4):
        b = dense[K.turn % 3]
        K.turn += 1
        wh, wl = s.hi[:, P * g:P * (g + 1)], s.lo[:, P * g:P * (g + 1)]
        t = pe.mm([s.ready, pl_ready[g], b.free], (b[:, 0:T], wh, pl_hi[:, g, :], True, False), (b[:, 0:T], wh, pl_lo[:, g, :], False, False),
                  (b[:, 0:T], wl, pl_hi[:, g, :], False, True))
        if g == 3:
            s.done.append(t)
        t = act.act([t], pl[:, g, :], b[:, 0:T], ACT.Copy, scale=par[:, C_PSC + g:C_PSC + g + 1])
        b.free = [t]
        cat_ready[4 + g] = split_x(K, cat_hi, cat_lo, 4 + g, pl[:, g, :], [t])
    drain(layer(S, [("og", 0), ("og", 1)], h, evac_og, dense))
    drain(side)

    x_ready = [None] * 8

    def evac_out(pairno, bank, done):
        o = x2[:, 2 * pairno:2 * pairno + 2, :]
        t = dve.tt([done], o, halves(bank[:, :]), o, ALU.add)
        x_ready[2 * pairno] = x_ready[2 * pairno + 1] = t
        return [t]

    drain(layer(S, [("hy_out", i) for i in range(4)], (cat_hi, cat_lo, cat_ready), evac_out, dense))
    return x2, x_ready


def ffn(K, S, n, x, x_ready, after=()):
    pe, act, dve, pool = K.pe, K.act, K.dve, K.pool
    B, A = K.banks, AREA
    dense = B[0:4]
    h_hi = K.buf(f"g{n}_hi", A, [P, 8, T], F32R)
    h_lo = K.buf(f"g{n}_lo", A + 8, [P, 8, T], F32R)
    spare = K.buf(f"g{n}_spare", A + 16, [P, 8, T])
    r = K.buf(f"g{n}_r", A + 24, [P, T])
    sg = K.buf(f"g{n}_sg", A + 25, [P, 2, T])
    mid = K.buf(f"g{n}_mid", A + 27, [P, 2, T])
    m_hi = K.buf(f"g{n}_mhi", A + 48, [P, 22, T], F32R)
    m_lo = K.buf(f"g{n}_mlo", A + 70, [P, 22, T], F32R)
    h = (h_hi, h_lo, rms_norm(K, x, x_ready, C_FFN + 8 * n, h_hi, h_lo, spare, r[:, :], B[7], after))
    m_ready = []
    free = [[], []]

    def evac(m):
        def f(_, bank, done):
            q = m % 2
            t = act.act([done, free[q]], sg[:, q, :], bank[:, 0:T], ACT.Silu)
            t = dve.tt([t, free[q]], mid[:, q, :], bank[:, T:2 * T], sg[:, q, :], ALU.mult)
            free[q] = split_x(K, m_hi, m_lo, m, mid[:, q, :], [t, after])
            m_ready.append(free[q])
            return [t]
        return f

    for m in range(22):
        drain(layer(S, [("gate_up", n, m)], h, evac(m), dense))

    def evac_down(pairno, bank, done):
        o = x[:, 2 * pairno:2 * pairno + 2, :]
        t = dve.tt([done], o, halves(bank[:, :]), o, ALU.add)
        out[2 * pairno] = out[2 * pairno + 1] = t
        return [t]

    out = [None] * 8
    drain(layer(S, [("down", n, i) for i in range(11)], (m_hi, m_lo, m_ready), evac_down, dense, nk=22))
    return x, out


def rwkv(K, S, x, x_ready):
    pe, act, dve, pool = K.pe, K.act, K.dve, K.pool
    B, A, Q = K.banks, AREA, RING_KB + 8 * NARROW
    par, ident = K.par, K.c["ident"]
    dense = B[0:3]
    X = "(i q) t -> i q t"

    h = K.buf("r_h", A, [P, 8, T])
    xx = K.buf("r_xx", A + 8, [P, 8, T])
    mix = [(K.buf(f"mix{m}_hi", kb, [P, 8, T], F32R), K.buf(f"mix{m}_lo", kb + 8, [P, 8, T], F32R)) for m, kb in enumerate((A + 16, A + 48))]
    spare = K.buf("r_spare", A + 64, [P, 8, T])
    rr = K.buf("r_r", A + 72, [P, T])
    ar = K.buf("ar", A + 64, [P, 8, 512])
    bk = K.buf("bk", A + 80, [P, 8, 512])
    lora = K.buf("lora", A + 112, [P, 2, T])
    lora_hi = K.buf("lora_hi", A + 114, [P, 2, T], F32R)
    lora_lo = K.buf("lora_lo", A + 32, [P, 2, T], F32R)
    sum16 = K.buf("sum16", A + 116, [P, P])
    cmask = K.buf("cmask", A + 116.5, [P, 256])
    cols = K.buf("r_cols", A + 117.5, [P, 8])
    Pt = K.buf("Pt", A + 96, [P, 8, 260])
    Z = K.buf("Z", A + 104.25, [P, 2, T])
    iP = K.buf("iP", A + 106.25, [P, 2, T])
    kkn = K.buf("kkn", A + 108.25, [P, 2, T])
    sq = K.buf("r_sq", A + 110.25, [P, T])
    tmp = [K.buf(f"r_tmp{i}", Q + 20 + i, [P, T]) for i in range(2)]
    inv = K.buf("r_inv", A + 111.25, [16, T])
    zero = K.buf("r_zero", A + 35, [P, 64])
    k_raw = K.buf("k_raw", Q, [P, 8, T])
    r_raw = K.buf("r_raw", Q + 8, [P, 8, T])
    PL = K.buf("PL", A + 117.53125, [P, 8, 4])

    def split(ap, which):
        v = ap.rearrange("p (i q s t) -> p i q s t", i=2, q=2, s=2)
        return v[:, :, 0, which, :], v[:, :, 1, 1 - which, :]

    def both(ap, which):
        o = 64 * which
        step = 192 if which == 0 else 64
        return bass.AP(tensor=ap.tensor, offset=ap.offset + o, ap=[list(ap.ap[0]), [256, 2], [step, 2], [1, 64]])

    quads = lambda ap: ap.rearrange("p (i q t) -> p i q t", i=2, q=2)

    t_sum = K.load(sum16[:, :], K.cst("sum16"), after=x_ready, queue=act)
    t_mask = K.load(cmask[:, :], K.cst("chunk"), after=x_ready, queue=act)
    t_zero = dve.fill([x_ready], zero[:, :], 0.0)
    bank = B[7]
    for j in range(8):
        t = dve.tt([x_ready[j]], spare[:, j, :], x[:, j, :], x[:, j, :], ALU.mult)
        t = pe.mm([t, bank.free if j == 0 else []], (bank[:, 0:T], K.c["mean"][:, :], spare[:, j, :], j == 0, j == 7))
    t = act.act([t], rr[:, :], bank[:, 0:T], ACT.Sqrt, bias=par[:, C_EPS + 1:C_EPS + 2])
    bank.free = [t]
    t = dve.recip([t], rr[:, :], rr[:, :])
    h_made, xx_made = [], []
    for j in range(8):
        m = C_MIX + 8 + j
        a = dve.stt([t], h[:, j, :], x[:, j, :], par[:, m:m + 1], rr[:, :], ALU.mult, ALU.mult)
        b = dve.ts([a], xx[:, j, 0:1], h[:, j, 0:1], -1.0, ALU.mult)
        c = dve.tt([a], xx[:, j, 1:T], h[:, j, 0:T - 1], h[:, j, 1:T], ALU.subtract)
        h_made.append(a)
        xx_made.append([b, c])
    mix_free = [[], []]
    raw = K.buf("mix_raw", Q + 16, [P, 4, T])
    raw_free = [[] for _ in range(4)]

    def mixed(i, m, eng):
        ready = []
        for j in range(8):
            f, c = raw[:, j % 4, :], C_MU + 8 * i + j
            t = dve.stt([h_made[j], xx_made[j], raw_free[j % 4]], f, xx[:, j, :], par[:, c:c + 1], h[:, j, :], ALU.mult, ALU.add)
            a = act.act([t, mix_free[m]], mix[m][0][:, j, :], f)
            b = eng.tt([a], mix[m][1][:, j, :], f, mix[m][0][:, j, :].bitcast(F32), ALU.subtract)
            raw_free[j % 4] = [a, b]
            ready.append([a, b])
        return (*mix[m], ready)

    mw = mixed(1, 0, dve)
    ma = mixed(4, 1, dve)
    st = {}

    def evac_lora(func):
        def evac(_, bank, done):
            t = act.act([done, st.get("lora", [])], lora[:, 0, :], bank[:, 0:T], func)
            st["l"] = split_x(K, lora_hi, lora_lo, 0, lora[:, 0, :], [t])
            return [t]
        return evac

    sig_made = [None] * 8
    a_made = [None] * 8

    def evac_sig(dst, which, col, made):
        def evac(pairno, bank, done):
            for i in range(2):
                j = 2 * pairno + i
                made[j] = act.act([done, t], both(dst[:, j, :], which), quads(bank[:, T * i:T * (i + 1)]), ACT.Sigmoid, bias=par[:, col + j:col + j + 1])
            return [made[2 * pairno], made[2 * pairno + 1]]
        return evac

    def low(x, key1, key2, func, evac):
        drain(layer(S, [key1], x, evac_lora(func), dense, steps=1))
        lx = (lora_hi, lora_lo, [st["l"]])
        drain(layer(S, [key2], lx, evac, dense, nk=1, steps=1))
        st["lora"] = [S.slots[S.next - 1].done]

    low(mw, "w1", "w2", ACT.Tanh, evac_sig(ar, 1, C_W0, sig_made))
    mix_free[0] = [st["lora"]]
    mk = mixed(2, 0, pool)
    low(ma, "a1", "a2", ACT.Copy, evac_sig(bk, 1, C_A0, a_made))
    mix_free[1] = [st["lora"]]
    mr = mixed(0, 1, pool)

    k_made, sq_free = [None] * 8, []
    ss = B[7]

    def evac_k(pairno, bank, done):
        nonlocal sq_free
        out = []
        for i in range(2):
            j = 2 * pairno + i
            src = bank[:, T * i:T * (i + 1)]
            k_made[j] = act.act([done], k_raw[:, j, :], src)
            a = act.act([done, sq_free], sq[:, :], src, ACT.Square, scale=par[:, C_KK + j:C_KK + j + 1])
            late.append((j, a))
            out += [k_made[j], a]
            sq_free = [sum_sq()]
        return out

    late = []

    def sum_sq():
        j, a = late.pop()
        st["ss"] = pe.mm([a, t_sum, ss.free if j == 0 else []], (ss[0:16, 0:T], sum16[:, 16 * j:16 * j + 16], sq[:, :], j == 0, j == 7))
        return st["ss"]

    drain(layer(S, [("rw_k", i) for i in range(4)], mk, evac_k, dense))
    mix_free[0] = [S.slots[S.next - 1].done]
    mv = mixed(3, 0, pool)
    t = act.act([st["ss"]], inv[:, :], ss[0:16, 0:T], ACT.Sqrt)
    ss.free = [t]
    t = dve.ts([t], inv[:, :], inv[:, :], 1e-12, ALU.max)
    t_inv = dve.recip([t], inv[:, :], inv[:, :])
    t_omka = dve.ts([K.t_par], cols[:, :], par[:, C_KA:C_KA + 8], -1.0, ALU.mult, 1.0, ALU.add)
    t_one = dve.fill([x_ready], Pt[:, :, :].rearrange("p j (c t) -> p j c t", c=4)[:, :, :, 0], 1.0)

    cdec = float(np.exp(-0.5))
    alpha, beta, kappa, P_made = [None] * 8, [None] * 8, [None] * 8, [None] * 8
    Z_free, iP_free, kkn_free, tmp_free = [[], []], [[], []], [[], []], [[], []]
    PL_made = []

    def prepare():
        for j in range(8):
            q = j % 2
            arj, bkj = ar[:, j, :], bk[:, j, :]
            p4 = Pt[:, j, :].rearrange("p (i q t) -> p i q t", i=2, q=2)
            t = []
            for c in range(4):
                src = split(arj, 1)[c % 2][:, c // 2, :]
                t.append(dve.do([sig_made[j], t_zero, Z_free[q]], lambda e, src=src, c=c, q=q: e.tensor_tensor_scan(
                    Z[:, q, 64 * c:64 * (c + 1)], src, zero[:, :], 0.0, ALU.add, ALU.add)))
            tp = act.act([t, t_one], p4[:, :, :, 1:65], quads(Z[:, q, :]), ACT.Exp, scale=-cdec)
            ti = act.act([t, iP_free[q]], iP[:, q, :], Z[:, q, :], ACT.Exp, scale=cdec)
            Z_free[q] = [tp, ti]
            P_made[j] = tp
            PL_made.append(pool.copy([tp], PL[:, j, :], Pt[:, j, :].rearrange("p (c t) -> p c t", c=4)[:, :, 64]))
            if q == 0:
                b = B[6 + j // 2 % 2]
                tb = pe.mm([t_inv, b.free], *[(b[64 * e:64 * (e + 1), T * m:T * (m + 1)],
                                               ident[0:16, 2 * (j + m) + e:2 * (j + m) + e + 1].to_broadcast([16, 64]), inv[:, :], m == 0, True)
                                              for m in range(2) for e in range(2)])
            kk = dve.stt([tb, k_made[j], kkn_free[q]], kkn[:, q, :], k_raw[:, j, :], par[:, C_KK + j:C_KK + j + 1],
                         b[:, T * q:T * (q + 1)], ALU.mult, ALU.mult)
            if q:
                b.free = [kk]
            tka = act.act([a_made[j], t_omka, tmp_free[0]], quads(tmp[0][:, :]), both(bkj, 1), ACT.Identity, scale=par[:, C_KA + j:C_KA + j + 1],
                          bias=cols[:, j:j + 1])
            tk = pool.tt([tka, k_made[j]], tmp[0][:, :], tmp[0][:, :], k_raw[:, j, :], ALU.mult)
            tb2 = pool.tt([kk, a_made[j], tmp_free[1]], quads(tmp[1][:, :]), quads(kkn[:, q, :]), both(bkj, 1), ALU.mult)
            alpha[j] = dve.stt([kk, tp, t], both(arj, 1), quads(kkn[:, q, :]), -1.0, p4[:, :, :, 0:64], ALU.mult, ALU.mult)
            kkn_free[q] = [alpha[j], tb2]
            beta[j] = dve.tt([tb2, ti, tka], both(bkj, 1), quads(tmp[1][:, :]), quads(iP[:, q, :]), ALU.mult)
            kappa[j] = dve.tt([tk, ti], both(bkj, 0), quads(tmp[0][:, :]), quads(iP[:, q, :]), ALU.mult)
            tmp_free[0], tmp_free[1] = [kappa[j]], [beta[j]]
            iP_free[q] = [beta[j], kappa[j]]
            yield

    rho = [None] * 8

    def evac_r(pairno, bank, done):
        out = []
        for i in range(2):
            j = 2 * pairno + i
            out.append(act.act([done], r_raw[:, j, :], bank[:, T * i:T * (i + 1)]))
            late.append((j, out[-1]))
        return out

    side = prepare()
    weave(layer(S, [("rw_r", i) for i in range(4)], mr, evac_r, dense), side, 1)
    drain(side)
    mix_free[1] = [S.slots[S.next - 1].done]
    mg = mixed(5, 1, pool)
    for j, t in late:
        p4 = Pt[:, j, :].rearrange("p (i q t) -> p i q t", i=2, q=2)
        rho[j] = dve.tt([t, P_made[j]], both(ar[:, j, :], 0), quads(r_raw[:, j, :]), p4[:, :, :, 1:65], ALU.mult)
    late.clear()

    LT = K.buf("LT", A + 32, [P, 2, 16, 64])
    ur = lambda c: slice(64 * (1 - c % 2), 64 * (2 - c % 2))
    vr = lambda c: slice(64 * (c % 2), 64 * (c % 2) + 64)
    strict = cmask[:, 64:128]
    lt_made = []
    for i in range(2):
        for e in range(2):
            b, r_, calls = B[3 + e], slice(64 * e, 64 * e + 64), []
            for j in range(8):
                for q in range(2):
                    o = 128 * (2 * i + q) + 64 * (1 - q)
                    calls.append((b[ur(q), 64 * j:64 * (j + 1)], bk[r_, j, o:o + 64], ar[r_, j, o:o + 64], j == 0, True))
            t = pe.mm([alpha, beta, b.free], *calls)
            t = dve.tt([t, t_mask], LT[:, i, e::2, :], b[:, :].rearrange("p (h t) -> p h t", h=8),
                       strict.unsqueeze(1).to_broadcast([P, 8, 64]), ALU.mult)
            b.free = [t]
            lt_made.append(t)
    zd, td, ttd = K.scratch
    out = []
    for b in range(2):
        for q in range(2):
            n = 2 * b + q
            base = 64 * (1 - q) + 32 * b
            dst = zd[32 * n:32 * (n + 1), :].rearrange("h (s t) -> s h t", s=32)
            src = LT[base:base + 32, :, :, 32 * b:32 * b + 32].rearrange("s i h t -> s (i h) t")
            out.append(K.load(dst, src, after=[lt_made], queue=act))
    K.final += out
    Zb = K.buf("Zb", Q, [P, 32, 32])
    Tm = K.buf("Tm", Q + 4, [P, 32, 32])
    prod = K.buf("r_prod", Q + 8, [P, 1024])
    Tt = K.buf("Tt", Q + 12, [P, 32, 32])
    t_Z = K.load(Zb[:, :, :], zd.rearrange("b (s t) -> b s t", s=32), after=out, queue=act)

    def invert():
        t = dve.fill([x_ready, mw[2], ma[2]], Tm[:, :, :], 0.0)
        t = dve.fill([t], Tm[:, :, :].rearrange("p i c -> p (i c)")[:, 0:1024:33], 1.0)
        for i in range(1, 32):
            o = prod[:, 0:i * i].rearrange("p (c j) -> p c j", c=i)
            t = dve.tt([t, t_Z], o, Tm[:, 0:i, 0:i].rearrange("p j c -> p c j"), Zb[:, 0:i, i].unsqueeze(1).to_broadcast([P, i, i]), ALU.mult)
            t = dve.do([t], lambda e, o=o, i=i: e.tensor_reduce(Tm[:, i, 0:i], o, AX, ALU.add))
            yield
        st["T"] = t
        st["Tt"] = act.act([t], Tt[:, :, :], Tm[:, :, :].rearrange("p i c -> p c i"))

    bonus = K.buf("bonus", A + 117.65625, [P, 2, 16])
    rk = [K.buf(f"rk{i}", Q + 20 + i, [P, T]) for i in range(2)]
    b = B[7]
    rk_free = [[], []]
    v = sum16[:, :].rearrange("p (j h) -> p j h", j=8)
    t_sumrk = dve.tt([st["ss"]], v, v, par[:, C_RK:C_RK + 8].unsqueeze(2).to_broadcast([P, 8, 16]), ALU.mult)
    for j in range(8):
        q = j % 2
        t = dve.tt([rho[j], kappa[j], rk_free[q], tmp_free], quads(rk[q][:, :]), both(ar[:, j, :], 0), both(bk[:, j, :], 0), ALU.mult)
        t = pe.mm([t, t_sumrk, b.free if j == 0 else []], *[(b[:, 16 * i:16 * (i + 1)], rk[q][:, P * i:P * (i + 1)], sum16[:, 16 * j:16 * j + 16],
                                                    j == 0 and i == 0, j == 7) for i in range(2)])
        rk_free[q] = [t]
    t_bonus = dve.copy([t], bonus[:, :, :], b[:, 0:32].rearrange("p (i h) -> p i h", i=2))
    b.free = [t_bonus]

    UV = K.buf("UV", A + 96, [P, 4, D])
    bv = K.buf("bv", A, [P, 2, D])
    g = K.buf("r_g", A + 8, [P, 2, D])
    V_made = [[[], []] for _ in range(4)]
    bv_made, g_made = [[[], []], [[], []]], [[], []]
    raw_done = [mg[2], rho]

    def evac_v(n):
        def evac(i, bank, done):
            o = slice(512 * n, 512 * (n + 1))
            t = []
            for q in range(2):
                c = 2 * i + q
                V_made[c][n] = act.act([done, raw_done, t_bonus], UV[vr(c), c, o], bank[vr(c), :])
                t.append(V_made[c][n])
            bv_made[i][n] = dve.tt([done, t, raw_done, t_bonus], bv[:, i, o].rearrange("p (h v) -> p h v", h=8), bank[:, :].rearrange("p (h v) -> p h v", h=8),
                                   bonus[:, i, 8 * n:8 * n + 8].unsqueeze(2).to_broadcast([P, 8, 64]), ALU.mult)
            return [t, bv_made[i][n]]
        return evac

    Gm = [K.buf(f"Gm{c}", (A + 16, A + 24, A + 48, A + 56)[c], [P, 16, P]) for c in range(4)]
    G_made = [[], [], [], []]
    ring = B[4:7]
    nring = 0

    def products(c, after):
        nonlocal nring
        m = cmask[:, P * (c % 2):P * (c % 2 + 1)]
        for n in range(4):
            b = ring[nring % 3]
            nring += 1
            calls = []
            e, h0 = n % 2, n // 2 * 8 + n % 2
            r_ = slice(64 * e, 64 * e + 64)
            for f in range(4):
                j = n // 2 * 4 + f
                calls.append((b[:, P * f:P * (f + 1)], bk[r_, j, P * c:P * (c + 1)], ar[r_, j, P * c:P * (c + 1)], f == 0, True))
            t = pe.mm([rho, kappa, b.free], *calls)
            t = dve.tt([t, after], Gm[c][:, h0:h0 + 7:2, :], b[:, :].rearrange("p (h t) -> p h t", h=4), m.unsqueeze(1).to_broadcast([P, 4, P]), ALU.mult)
            b.free = [t]
            G_made[c].append(t)
            yield

    bkT = [K.buf(f"bkT{c}", kb, [P, 8, P]) for c, kb in enumerate((A + 112, Q + 12, Q + 16))]
    bkT_made = [[], [], []]
    diag = [K.c["iota"][:, 0:P], K.c["iota"][:, P:2 * P], K.c["tri"]]
    diag_free = [[], [], []]

    def turned(c, after):
        for n in range(2):
            b = B[7]
            for f in range(4):
                j, d = 4 * n + f, (8 * c + 4 * n + f) % 3
                t = act.act([PL_made[j], diag_free[d]], diag[d], ident, ACT.Copy, scale=PL[:, j, c:c + 1])
                t = pe.mm([t, b.free if f == 0 else []], (b[:, P * f:P * (f + 1)], bk[:, j, P * c:P * (c + 1)], diag[d], f == 0, True))
                diag_free[d] = [t]
            t = act.act([t, after], bkT[c][:, 4 * n:4 * n + 4, :], b[:, :].rearrange("p (j k) -> p j k", j=4))
            b.free = [t]
            bkT_made[c].append(t)

    side = invert()
    four = B[0:4]
    K.turn += -K.turn % 4
    side = weave(layer_across(S, [("rw_v0", 0), ("rw_v0", 1)], mv, evac_v(0), four), side, 3)
    side = weave(layer_across(S, [("rw_v1", 0), ("rw_v1", 1)], mv, evac_v(1), four), side, 3)
    mix_free[0] = [S.slots[S.next - 1].done]

    gl = K.buf("r_gl", Q + 18, [P, 2, T])
    gl_hi = K.buf("r_glhi", Q + 22, [P, 2, T], F32R)
    gl_lo = K.buf("r_gllo", Q + 16, [P, 2, T], F32R)
    gl_made = []

    def evac_gl(_, bank, done):
        t = act.act([done, raw_free], gl[:, :, :], halves(bank[:, :]), ACT.Sigmoid)
        for k in range(2):
            gl_made.append(split_x(K, gl_hi, gl_lo, k, gl[:, k, :], [t]))
        return [t]

    drain(layer(S, ["g1"], mg, evac_gl, dense))
    mix_free[1] = [S.slots[S.next - 1].done]
    s = S.take("g2")
    for n in range(2):
        for i in range(2):
            bank = dense[K.turn % 3]
            K.turn += 1
            t, calls = slice(P * i, P * (i + 1)), []
            for k in range(2):
                w = slice(D * k + 512 * n, D * k + 512 * (n + 1))
                calls += [(bank[:, :], gl_hi[:, k, t], s.hi[:, w], k == 0, False), (bank[:, :], gl_lo[:, k, t], s.hi[:, w], False, False),
                          (bank[:, :], gl_hi[:, k, t], s.lo[:, w], False, k == 1)]
            t = pe.mm([s.ready, gl_made, bank.free], *calls)
            bank.free = [act.act([t, raw_done], g[:, i, 512 * n:512 * (n + 1)], bank[:, :])]
            g_made[i].append(bank.free)
    s.done.append(t)
    t_g2 = [t]
    for c in range(2):
        weave(products(c, mix_free[0]), side, 2)
    turned(0, st["lora"])
    for c in range(2, 4):
        weave(products(c, mix_free[1]), side, 2)
    turned(2, t_g2)
    drain(side)

    TT = K.buf("TT", Q, [P, 32, 64])
    T11 = K.buf("T11", Q + 8, [P, 32, 32])
    w_tt = K.load(ttd, Tt[:, :, :].rearrange("p c i -> p (c i)"), after=[st["Tt"]], queue=act)
    w_t = K.load(td, Tm[0:64, :, :].rearrange("p i c -> p (i c)"), after=[st["T"]], queue=act)
    K.final += [w_tt, w_t]
    t_TT = []
    for q in range(2):
        for b in range(2):
            base = 64 * (1 - q) + 32 * b
            n = 2 * b + q
            t_TT.append(K.load(TT[base:base + 32, :, 32 * b:32 * b + 32], ttd[32 * n:32 * (n + 1), :].rearrange("h (s t) -> s h t", s=32),
                               after=[w_tt, w_t], queue=act))
        base = 64 * (1 - q)
        t_TT.append(K.load(T11[base:base + 32, :, :], td[32 * q:32 * (q + 1), :].rearrange("h (i c) -> i h c", i=32), after=[w_t], queue=act))
        t_TT.append(pool.fill([w_tt, w_t, t_TT], TT[base + 32:base + 64, :, 0:32], 0.0))
    turned(1, [w_tt])
    t_bk = [bkT_made]
    R0 = K.buf("R0", Q + 8, [P, D])
    SB = K.buf("SB", Q + 20, [P, 8, P])
    y = K.buf("r_y", A + 32, [P, 2, D])
    first = lambda q: slice(64 * (1 - q), 64 * (1 - q) + 32)
    second = lambda q: slice(64 * (1 - q) + 32, 64 * (2 - q))
    t_SB = pool.fill([rk_free, tmp_free, t_g2, t_TT], SB[:, :, :], 0.0)
    TT_made = [[], []]
    for i in range(2):
        b = B[i]
        t = pe.mm([t_TT, b.free], *[(b[second(q), 32 * n:32 * n + 32], LT[first(q), i, n, 32:64], T11[first(q), 16 * i + n, :], n == 0, True)
                                    for n in range(16) for q in range(2)])
        made = []
        for q in range(2):
            o, f = T11[second(q), 16 * i:16 * i + 16, :], b[second(q), :].rearrange("p (h c) -> p h c", h=16)
            made.append(dve.copy([t, made], o, f) if q else act.act([t], o, f))
        b.free = made
        b = B[2 + i]
        t = pe.mm([made, b.free], *[(b[first(q), 32 * n:32 * n + 32], T11[second(q), 16 * i + n, :], TT[second(q), 16 * i + n, 32:64], n == 0, True)
                                    for n in range(16) for q in range(2)])
        made = []
        for q in range(2):
            o, f = TT[first(q), 16 * i:16 * i + 16, 32:64], b[first(q), :].rearrange("p (h c) -> p h c", h=16)
            made.append(dve.copy([t, made], o, f) if q else act.act([t], o, f))
        b.free = made
        TT_made[i] = [t_TT, made]
    t_W = [t]

    R0_free, SB_made, y_made = [t_W], [t_SB, t_SB], [[], []]
    hs = lambda half: range(8 * half, 8 * half + 8)
    U_made = [[[], []] for _ in range(4)]
    ry = lambda c, half: B[2 * (c % 2) + half]

    def values(c):
        for half in range(2):
            b = ry(c, half)
            st["av", c, half] = pe.mm([G_made[c], V_made[c], b.free], *[
                (b[r_, 64 * (n % 8):64 * (n % 8) + 64], Gm[c][vr(c), n, r_], UV[vr(c), c, 64 * n:64 * n + 64], n % 8 == 0, c == 0)
                for n in hs(half) for r_ in [slice(0, P) if n % 8 == 0 else ur(c)]])

    lnw = K.buf("lnw", A + 16, [P, D])
    lnb = K.buf("lnb", A + 20, [P, D])
    ysq = K.buf("ysq", A + 24, [P, D])
    ysc = K.buf("ysc", A + 28, [P, D])
    stat = K.buf("stat", 10 - 0.25, [P, 2, 32])
    o_hi = K.buf("o_hi", A + 80, [P, 8, T], F32R)
    o_lo = K.buf("o_lo", A + 88, [P, 8, T], F32R)
    gw_made, gb_made, out_made, o_ready = [None] * 2, [None] * 2, [None] * 2, [[] for _ in range(8)]

    def gains(after):
        tw = K.load(lnw[:, :], K.ins["rw_ln"][0:1, :].to_broadcast([P, D]), after=after, queue=act)
        tb = K.load(lnb[:, :], K.ins["rw_ln"][1:2, :].to_broadcast([P, D]), after=after, queue=act)
        for i in range(2):
            t = pool.tt([tb, bv_made[i]], bv[:, i, :], bv[:, i, :], lnb[:, :], ALU.add)
            t = gb_made[i] = pool.tt([t, g_made[i]], bv[:, i, :], bv[:, i, :], g[:, i, :], ALU.mult)
            gw_made[i] = pool.tt([t, tw], g[:, i, :], g[:, i, :], lnw[:, :], ALU.mult)

    def normed(i, after):
        per = lambda ap: ap.rearrange("p (h v) -> p h v", h=16)
        col = lambda k: stat[:, i, 16 * k:16 * k + 16]
        each = lambda k: col(k).unsqueeze(2).to_broadcast([P, 16, 64])
        yi = y[:, i, :]
        t = dve.do([y_made[i]], lambda e: e.tensor_reduce(col(0), per(yi), AX, ALU.add))
        t = dve.ts([t], col(0), col(0), 1.0 / 64, ALU.mult)
        t = dve.tt([t], per(yi), per(yi), each(0), ALU.subtract)
        t1 = act.act([t, after], ysq[:, :], yi, ACT.Square)
        t2 = pool.tt([t, gw_made[i], after], ysc[:, :], yi, g[:, i, :], ALU.mult)
        t = dve.do([t1], lambda e: e.tensor_reduce(col(1), per(ysq[:, :]), AX, ALU.add))
        t = act.act([t], col(1), col(1), ACT.Sqrt, scale=1.0 / 64, bias=par[:, C_EPS + 2:C_EPS + 3])
        t = dve.recip([t], col(1), col(1))
        t = dve.tt([t, t2], per(ysc[:, :]), per(ysc[:, :]), each(1), ALU.mult)
        out_made[i] = t = dve.tt([t, gb_made[i]], yi, ysc[:, :], bv[:, i, :], ALU.add)
        for n in range(2):
            b = B[6 + n]
            t = pe.tr([out_made[i], b.free], ident, *[(b[:, P * f:P * (f + 1)], y[:, i, P * (4 * n + f):P * (4 * n + f + 1)]) for f in range(4)])
            src = b[:, :].rearrange("p (j t) -> p j t", j=4)
            hi, lo = (o[:, 4 * n:4 * n + 4, P * i:P * (i + 1)] for o in (o_hi, o_lo))
            ta = act.act([t, t_bk], hi, src)
            tb = dve.tt([ta], lo, src, hi.bitcast(F32), ALU.subtract)
            b.free = [ta, tb]
            for f in range(4):
                o_ready[4 * n + f] += [ta, tb]

    values(0)
    for c in range(4):
        i = c // 2
        R0_made = []
        S_read = []
        for half in range(2):
            b = ry(c, half)
            t = st["av", c, half]
            if c:
                t = pe.mm([SB_made[half], t], *[(b[:, P * f:P * (f + 1)], ar[:, 4 * half + f, P * c:P * (c + 1)], SB[:, 4 * half + f, :], False, False) for f in range(4)])
                S_read.append(t)
            o = R0[ur(c), 512 * half:512 * (half + 1)]
            R0_made.append(act.act([t, R0_free], o, b[ur(c), :]) if half else dve.copy([t, R0_free], o, b[ur(c), :]))
        if c and c < 3:
            for half in range(2):
                v = SB[:, 4 * half:4 * half + 4, :]
                SB_made[half] = [pool.tt([S_read[half]], v, v, PL[:, 4 * half:4 * half + 4, c:c + 1].to_broadcast([P, 4, P]), ALU.mult)]
        if c < 3:
            values(c + 1)
        for half in range(2):
            b = B[4 + half]
            t = pe.mm([R0_made[half], TT_made[i], b.free], *[
                (b[ur(c), 64 * (n % 8):64 * (n % 8) + 64], TT[ur(c), 16 * i + n, :], R0[ur(c), 64 * n:64 * n + 64], n % 8 == 0, True) for n in hs(half)])
            o = UV[ur(c), c, 512 * half:512 * (half + 1)]
            t = act.act([t, raw_done], o, b[ur(c), :]) if half else dve.copy([t, raw_done], o, b[ur(c), :])
            b.free = [t]
            U_made[c][half] = t
        R0_free = U_made[c]
        if c < 3:
            for half in range(2):
                b = B[6 + half]
                t = pe.mm([U_made[c][half], bkT_made[c][half], b.free], *[
                    (b[:, P * f:P * (f + 1)], bkT[c][:, 4 * half + f, :], UV[:, c, P * (4 * half + f):P * (4 * half + f + 1)], f == 0, True) for f in range(4)])
                made = []
                for e in range(2):
                    r_ = slice(64 * e, 64 * e + 64)
                    o = SB[r_, 4 * half:4 * half + 4, r_]
                    f = b[r_, :].rearrange("p (j k) -> p j k", j=4)[:, :, r_]
                    made.append(dve.tt([t, SB_made[half]], o, f, o, ALU.add) if c else dve.copy([t, SB_made[half]], o, f))
                b.free = SB_made[half] = made
        for half in range(2):
            b = ry(c, half)
            t = pe.mm([U_made[c][half], R0_made[half]], *[
                (b[vr(c), 64 * (n % 8):64 * (n % 8) + 64], Gm[c][r_, n, vr(c)], UV[r_, c, 64 * n:64 * n + 64], False, True)
                for n in hs(half) for r_ in [ur(c) if n % 8 == 0 else slice(0, P)]])
            st["y"] = [t]
            t = act.act([t, t_W], y[vr(c), i, 512 * half:512 * (half + 1)], b[vr(c), :])
            b.free = [t]
            y_made[i].append(t)
        if c == 0:
            gains(st["y"])
        if c % 2:
            normed(i, st["y"])

    x_ready = [None] * 8

    def evac_out(pairno, bank, done):
        o = x[:, 2 * pairno:2 * pairno + 2, :]
        t = dve.tt([done], o, halves(bank[:, :]), o, ALU.add)
        x_ready[2 * pairno] = x_ready[2 * pairno + 1] = t
        return [t]

    drain(layer(S, [("rw_o", i) for i in range(4)], (o_hi, o_lo, o_ready), evac_out, dense))
    return x, x_ready, out_made


def tile_cols(v):
    v = np.asarray(v).reshape(-1)
    return v.reshape(-1, P).T


def pack(i):
    f = np.float32
    z = lambda r, c: np.zeros((r, c), f)
    mats = {
        "ada": i["w_ada"][0].T,
        "w_in": i["w_in"][0],
        "w_dt": np.concatenate([i["w_in"][0][:, 6144:6176], z(D, 96)], axis=1),
        "w_sc_out": i["w_sc_out"][0],
        "w_ssd_out": i["w_ssd_out"][0],
        "w_o": i["w_o"][0],
        "w_router": i["router_w"][0].reshape(4, 2, P, 64).transpose(0, 2, 1, 3).reshape(512, P),
        "hy_in": i["hy_w_in_2"][0],
        "w_f": np.concatenate([i["hy_w_in_2"][0][:, 2048:2056], z(D, 120)], axis=1),
        "pool_w": i["hy_pool_w_2"][0].reshape(512, P),
        "hy_out": i["hy_w_out_2"][0],
        "rw_w1": np.concatenate([i["rw_w1_2"][0], z(D, 64)], axis=1),
        "rw_w2": np.concatenate([i["rw_w2_2"][0], z(64, D)], axis=0),
        "rw_a1": np.concatenate([i["rw_a1_2"][0], z(D, 64)], axis=1),
        "rw_a2": np.concatenate([i["rw_a2_2"][0], z(64, D)], axis=0),
        "rw_g1": np.concatenate([i["rw_g1_2"][0], z(D, 96)], axis=1),
        "rw_g2": np.concatenate([i["rw_g2_2"][0], z(96, D)], axis=0),
        "rw_k": i["rw_w_k_2"][0],
        "rw_r": i["rw_w_r_2"][0],
        "rw_v": i["rw_w_v_2"][0],
        "rw_o": i["rw_w_o_2"][0],
        "sh_gate": i["sh_gate"][0],
        "sh_up": i["sh_up"][0],
        "sh_down": i["sh_down"][0],
    }
    for n in range(2):
        mats[f"ffn_gate{n}"], mats[f"ffn_up{n}"], mats[f"ffn_down{n}"] = i["ffn_w_gate_2"][n], i["ffn_w_up_2"][n], i["ffn_w_down_2"][n]
    slots = plan()
    slots = [x for x in slots if x[0][0] != "expert"]
    wts = np.empty(sum(len(t) for _, t, _ in slots) * P * P, f)
    at = 0
    for _, tiles, _ in slots:
        n = len(tiles)
        out = wts[at:at + n * P * P].reshape(P, n, P)
        for t, (m, r, c) in enumerate(tiles):
            out[:, t, :] = mats[m][r:r + P, c:c + P]
        at += n * P * P
    experts = np.empty((N_EXPERTS, 3, P, SLOT), f)
    for e in range(N_EXPERTS):
        up = np.concatenate([i["w_gate"][0][e], i["w_up"][0][e]], axis=1)
        experts[e, 0:2] = up.reshape(2, 4, P, 512).transpose(0, 2, 1, 3).reshape(2, P, SLOT)
        experts[e, 2] = i["w_down"][0][e].reshape(2, P, D).transpose(1, 0, 2).reshape(P, SLOT)
    cols = {
        "b_ada": i["b_ada"],
        "ssd_conv_w": i["ssd_conv_w"][0],
        "ssd_conv_b": i["ssd_conv_b"],
        "ssd_D": np.repeat(i["ssd_D"][0], 64),
        "ssd_norm_w": i["ssd_norm_w"],
        "sc_conv_w": i["sc_conv_w"][0],
        "ln1_g": i["ln1_g"],
        "ln1_b": i["ln1_b"],
        "ln2_g": i["ln2_g"],
        "ln2_b": i["ln2_b"],
        "mix_norm": i["mix_norm_2"],
        "ffn_norm": i["ffn_norm_2"],
        "dt_bias": np.concatenate([i["ssd_dt_bias"][0], np.zeros(96, f)]),
        "A_log": np.concatenate([i["ssd_A_log"][0], np.zeros(96, f)]),
        "eps": np.repeat(np.array([1e-5, 1e-6, 64e-5, 1e-12], f), P),
    }
    cols["q_gain"] = np.tile(i["hy_q_gain_2"][0], 2)
    cols["k_gain"] = np.tile(i["hy_k_gain_2"][0], 2)
    cols["qk_eps"] = np.concatenate([np.full(8, 64e-6, f), np.full(120, 1e-6, f)])
    cols["f_bias"] = np.concatenate([i["hy_f_bias_2"][0], np.zeros(120, f)])
    cols["pool_scale"] = i["hy_pool_scale_2"]
    for n in ("mu", "w0", "a0", "k_k", "k_a", "r_k"):
        cols[f"rw_{n}"] = i[f"rw_{n}_2"]
    con = constants()
    con["router_bias"] = np.broadcast_to(i["router_bias"], (P, 64))
    par = np.concatenate([tile_cols(cols[n]) for n, _ in PARAMS] + [con[n] for n in STAY + LATE], axis=1).astype(f)
    xT = np.ascontiguousarray(i["x"][0].T).reshape(8, P, T).transpose(1, 0, 2).reshape(P, 8 * T)
    return {
        "xT": np.ascontiguousarray(xT),
        "c": np.ascontiguousarray(i["c"]),
        "wts": wts,
        "experts": experts,
        "rw_ln": np.stack([i["rw_ln_w_2"][0], i["rw_ln_b_2"][0]]),
        "par": np.ascontiguousarray(par),
        "cst": np.ascontiguousarray(np.concatenate([con[n] for n in CONST], axis=1).astype(f)),
    }


def setup(K):
    con = constants()
    K.c = {}
    K.ccol = {}
    at = 0
    for n in CONST:
        K.ccol[n] = (at, con[n].shape[1])
        at += con[n].shape[1]
    K.cst = lambda n: K.ins["cst"][:, K.ccol[n][0]:K.ccol[n][0] + K.ccol[n][1]]
    n = NPAR + sum(con[n].shape[1] for n in STAY)
    K.par = K.buf("par", 0, [P, n + sum(LATE_COLS.values())])
    K.t_par = K.load(K.par[:, 0:n], K.ins["par"][:, 0:n])
    K.t_cst = [K.t_par]
    at = NPAR
    for n in STAY:
        K.c[n] = K.par[:, at:at + con[n].shape[1]]
        at += con[n].shape[1]
    for n in LATE:
        K.c[n] = K.par[:, at:at + LATE_COLS[n]]
        at += LATE_COLS[n]
    assert at * 4 <= 8 * 1024
    K.acc = K.buf("acc", 9, [P, 48])
    K.mod = K.buf("mod", 9.25, [P, 48])
    K.small = K.buf("small", 9.5, [P, 64])
    K.mod_ready = [None] * 48
    K.ada_last = []


def setup_late(K):
    n = NPAR + sum(K.c[m].shape[1] for m in STAY)
    K.t_late = K.load(K.par[:, n:], K.ins["par"][:, n:], queue=K.act)


SCRATCH = dict(zd=(P, 1024), td=(64, 1024), ttd=(P, 1024))


def program(nc, ins, out, scratch):
    with ExitStack() as ctx:
        K = Core(nc, ctx, ins)
        K.scratch = scratch
        S = Stream(K, plan(), ins["wts"], ins["experts"])
        x, ready, after = rwkv(K, S, *ffn(K, S, 0, *fox(K, S, *moe(K, S, *first_block(K, S)))))
        x, ready = ffn(K, S, 1, x, ready, after)
        for i in range(4):
            o = out.rearrange("p (j t) -> p j t", j=8)[:, 2 * i:2 * i + 2, :]
            K.final.append(K.load(o, x[:, 2 * i:2 * i + 2, :], after=ready[2 * i:2 * i + 2]))
        K.run()


def kernel(**inputs):
    import concourse.bacc as _bacc
    from concourse.bass_utils import run_bass_kernel_spmd as _run

    nc = _bacc.Bacc("TRN2", target_bir_lowering=False, num_devices=1)
    arrays, args = {}, {}
    for name, a in pack({n: np.asarray(v) for n, v in inputs.items()}).items():
        arrays["in_" + name] = a
        args[name] = nc.dram_tensor("in_" + name, a.shape, mybir.dt.from_np(a.dtype), kind="ExternalInput").ap()
    out = nc.dram_tensor("out", (P, 8 * T), F32, kind="ExternalOutput").ap()
    scratch = [nc.dram_tensor(n, s, F32, kind="ExternalOutput").ap() for n, s in SCRATCH.items()]
    program(nc, args, out, scratch)
    r = _run(nc, [arrays], core_ids=[0])
    got = r.results[0]["out"].reshape(P, 8, T)
    return np.ascontiguousarray(got.transpose(2, 1, 0)).reshape(1, T, D)
```

```python
from contextlib import ExitStack

import numpy as np

import concourse.bass as bass
from concourse import mybir
from concourse.alu_op_type import AluOpType as ALU

ACT = mybir.ActivationFunctionType
F32 = mybir.dt.float32
F32R = mybir.dt.float32r
BF16 = mybir.dt.bfloat16
I32 = mybir.dt.int32
AX = mybir.AxisListType.X

P = 128
T = 256
D = 1024
ALPHA = 2.0 ** 0.25
TILE = 128
SLOT = 16 * TILE
RING = 7
NARROW = 4
RING_KB = 10
HI_KB = RING_KB + 8 * RING
HIS = 3
AREA = HI_KB + 8 * HIS
N_EXPERTS = 64
FIXED = 5
MORE = (68, 76, 84, 92, 8, 48)


class Count:

    def __init__(self, name, sem):
        self.name, self.sem, self.count = name, sem, 0


class Branch:
    def __init__(self, flag, limit, after):
        self.flag, self.limit, self.after, self.items, self.adds = flag, limit, after, [], 0


class Queue:

    def __init__(self, name, core):
        self.main = Count(name, core.sem("s_" + name))
        self.side = Count(name + "_if", core.sem("s_" + name + "_if"))
        self.items, self.open = [], []
        self.flags = None

    def into(self):
        return self.open[-1].items if self.open else self.items

    def do(self, after, emit):
        count = self.side if self.open else self.main
        for b in self.open:
            b.adds += 1
        count.count += 1
        self.into().append((tuple(flat(after)), emit, count, 1))
        return (count, count.count)

    def dma(self, after, load, out, in_):
        load.count += 16
        self.into().append((tuple(flat(after)), lambda e: e.dma_start(out, in_), load, 16))
        return (load, load.count)

    def load_flags(self, after, row):
        self.flags = (tuple(flat(after)), row)
        self.items.append(("flags",))

    def branch(self, flag, limit, after=()):
        b = Branch(flag, limit, tuple(flat(after)))
        self.into().append(b)
        self.open.append(b)

    def close(self):
        self.open.pop()

    def run(self, eng):
        self.emit(eng, self.items, {})

    def emit(self, eng, items, seen):
        def wait(after):
            for count, value in after:
                if seen.get(count.name, 0) < value:
                    eng.wait_ge(count.sem, value)
                    seen[count.name] = value

        for item in items:
            if isinstance(item, Branch):
                with eng.If_cmp(self.regs[item.flag], item.limit, "IS_GT"):
                    self.emit(eng, item.items, dict(seen))
                with eng.Else():
                    for count, value in item.after:
                        eng.wait_ge(count.sem, value)
                    eng.sem_inc(self.side.sem, item.adds)
            elif item[0] == "flags":
                after, row = self.flags
                n = row.shape[1]
                self.regs = [eng.alloc_register(f"{self.main.name}_flag{i}") for i in range(n)]
                wait(after)
                eng.reg_load(self.regs, row)
            else:
                after, emit, count, add = item
                wait(after)
                emit(eng).then_inc(count.sem, add)

    def act(self, after, out, in_, func=ACT.Copy, **kw):
        return self.do(after, lambda e: e.activation(out, in_, func, **kw))

    def tt(self, after, out, a, b, op):
        return self.do(after, lambda e: e.tensor_tensor(out, a, b, op=op))

    def ts(self, after, out, a, s1, op0, s2=None, op1=ALU.bypass, **kw):
        return self.do(after, lambda e: e.tensor_scalar(out, a, s1, s2, op0=op0, op1=op1, **kw))

    def stt(self, after, out, a, s, b, op0, op1):
        return self.do(after, lambda e: e.scalar_tensor_tensor(out, a, s, b, op0=op0, op1=op1))

    def copy(self, after, out, a):
        return self.do(after, lambda e: e.tensor_copy(out, a))

    def recip(self, after, out, a):
        return self.do(after, lambda e: e.reciprocal(out, a))

    def fill(self, after, out, value):
        return self.do(after, lambda e: e.memset(out, value))

    def mm(self, after, *calls):

        def emit(e):
            for out, lhsT, rhs, start, stop in calls:
                ins = e.matmul(out, lhsT, rhs, start=start, stop=stop, skip_group_check=True)
            return ins

        return self.do(after, emit)

    def tr(self, after, ident, *calls):

        def emit(e):
            for out, in_ in calls:
                n = in_.shape[0]
                ins = e.transpose(out, in_, ident[0:n, 0:n])
            return ins

        return self.do(after, emit)


def flat(x):
    if isinstance(x, tuple) and len(x) == 2 and isinstance(x[1], int):
        yield x
        return
    for y in x or ():
        yield from flat(y)


class Bank:

    def __init__(self, t):
        self.t, self.free = t, []

    def __getitem__(self, k):
        return self.t[k]


class Slot:
    def __init__(self, index, key, tiles, split):
        self.index, self.key, self.tiles, self.split = index, key, tiles, split
        self.done = []


class Core:
    def __init__(self, nc, ctx, ins):
        self.nc, self.ctx, self.ins = nc, ctx, ins
        self.arena = ctx.enter_context(nc.sbuf_tensor("arena", [P, 53200], F32))
        self.base = 16512
        self.pe = Queue("pe", self)
        self.act = Queue("act", self)
        self.dve = Queue("dve", self)
        self.pool = Queue("pool", self)
        self.sp = []
        self.actdma = []
        self.banks = [Bank(ctx.enter_context(nc.psum_tensor(f"ps{i}", [P, 512], F32))) for i in range(8)]
        self.nload = 0
        self.final = []
        self.turn = 0

    def sem(self, name):
        return self.ctx.enter_context(self.nc.semaphore(name))

    def buf(self, name, kb, shape, dt=F32):
        n = 1
        for s in shape[1:]:
            n *= s
        assert kb * 1024 + n * (2 if dt == BF16 else 4) <= 212800, (name, kb)
        return self.nc.alloc_sbuf_tensor_at(name, list(shape), dt, offset=self.base + int(kb * 1024))

    def load(self, out, in_, after=(), queue=None):
        self.nload += 1
        load = Count(f"ld{self.nload}", self.sem(f"ld{self.nload}"))
        if queue:
            return queue.dma(after, load, out, in_)
        load.count = 16
        self.sp.append((list(flat(after)), lambda e: e.dma_start(out, in_).then_inc(load.sem, 16)))
        return (load, 16)

    def run(self):
        with self.nc.Block() as block:

            @block.sync
            def _(eng):
                seen = {}
                for after, emit in self.sp:
                    for queue, count in flat(after() if callable(after) else after):
                        if seen.get(queue.name, 0) < count:
                            eng.wait_ge(queue.sem, count)
                            seen[queue.name] = count
                    emit(eng)
                for queue, count in self.final:
                    eng.wait_ge(queue.sem, count)

            @block.tensor
            def _(eng):
                self.pe.run(eng)

            @block.scalar
            def _(eng):
                self.act.run(eng)

            @block.vector
            def _(eng):
                self.dve.run(eng)

            @block.gpsimd
            def _(eng):
                self.pool.run(eng)


class Stream:

    def __init__(self, core, plan, wts, experts):
        self.core, self.experts = core, experts
        self.order, self.order_ready, self.regs = None, [], None
        self.lo_engines = (core.dve,)
        self.lead = HIS
        self.slots = [Slot(i, *p) for i, p in enumerate(plan)]
        self.next = self.nready = self.issued = 0
        at = [RING_KB + 8 * i for i in range(RING)] + [AREA + k for k in MORE] + [HI_KB + 8 * i for i in range(HIS)]
        self.raw = [core.buf(f"wraw{i}", kb, [P, SLOT]) for i, kb in enumerate(at)]
        self.lo = [core.buf(f"wlo{i}", kb, [P, SLOT], F32R) for i, kb in enumerate(at[:RING])]
        self.hi = [core.buf(f"whi{i}", HI_KB + 8 * i, [P, SLOT], F32R) for i in range(HIS)]
        self.before = [()] * len(at)
        sems = [Count(f"ring{i}", core.sem(f"ring{i}")) for i in range(len(at))]
        user = [None] * len(at)
        hi_user = [None] * HIS
        at = turn = wide = nsplit = 0
        narrow = False
        for s in self.slots:
            s.n = len(s.tiles) * TILE
            if s.key[0] == "expert":
                order = [*range(RING, RING + 4), *[(turn + i) % RING for i in range(RING)], *range(RING + 6, RING + 9),
                         RING + 4, RING + 5]
                s.place = order[wide % len(order)]
                wide += 1
            else:
                n = NARROW if narrow or s.key == "wa1" else RING
                narrow = n == NARROW
                s.place = turn % n
                turn += 1
            h = s.place - RING - len(MORE)
            if s.split:
                h = nsplit % HIS
                nsplit += 1
                s.hi, s.hi_prev, hi_user[h] = self.hi[h], hi_user[h], s
            load = sems[s.place]
            load.count += 16
            s.landed = (load, load.count)
            s.prev, user[s.place] = user[s.place], s
            if s.place >= RING + len(MORE):
                s.prev, hi_user[h] = hi_user[h], s
            s.raw = self.raw[s.place]
            if s.key[0] != "expert":
                s.src = wts[at:at + P * s.n].rearrange("(p n) -> p n", p=P)
                at += P * s.n
        self.total = at
        self.user = user

    def find(self, key):
        return next(s for s in self.slots if s.key == key)

    def issue(self, upto):
        while self.issued < min(upto, len(self.slots)):
            s = self.slots[self.issued]
            free = lambda s=s: s.prev.done if s.prev else self.before[s.place]
            if s.key[0] == "expert":
                self.issue_expert(s, free)
            else:
                self.core.sp.append((free, lambda e, s=s: e.dma_start(s.raw[:, 0:s.n], s.src).then_inc(s.landed[0].sem, 16)))
            self.issued += 1

    def issue_expert(self, s, free):
        _, place, part, group = s.key

        def fixed(e):
            e.dma_start(s.raw[:, :], self.experts[place, part]).then_inc(s.landed[0].sem, 16)

        def sorted_(e):
            if not self.regs:
                self.regs = [e.alloc_register(f"expert{i}") for i in range(4)]
            if part == 0 and place == group[0]:
                regs = self.regs[0:len(group)]
                e.reg_load(regs, self.order[:, place:place + len(group)])
                self.which = [e.snap(r, min_val=0, max_val=N_EXPERTS - 1) for r in regs]
            src = self.experts[bass.ds(self.which[place - group[0]], 1), part, :, :].rearrange("o p n -> (o p) n")
            e.dma_start(s.raw[:, :], src).then_inc(s.landed[0].sem, 16)

        if place < FIXED:
            self.core.sp.append((free, fixed))
        else:
            waits = lambda: [free(), self.order_ready]
            self.core.sp.append((waits, sorted_))

    def split(self, s, engine=None):
        core, last = self.core, s.hi_prev
        engine = engine or self.lo_engines[s.index % len(self.lo_engines)]
        s.lo = self.lo[s.place]
        a = core.act.act([s.landed, last.done if last else []], s.hi[:, 0:s.n], s.raw[:, 0:s.n])
        b = engine.tt([a], s.lo[:, 0:s.n], s.raw[:, 0:s.n], s.hi[:, 0:s.n].bitcast(F32), ALU.subtract)
        s.ready = [a, b]

    def take(self, key):
        s = self.slots[self.next]
        assert s.key == key, (s.key, key)
        self.next += 1
        self.issue(s.index + len(self.raw))
        self.ahead(s.index + self.lead, None, s)
        return s

    def ahead(self, upto, engine=None, now=None):
        while self.nready < min(upto, len(self.slots)):
            f = self.slots[self.nready]
            if f.split and now and not now.split and now.key[0] == "expert":
                break
            self.nready += 1
            if f.split:
                self.split(f, engine)
            else:
                f.ready = [f.landed]



FIXED_PAIRS = [(0, 1), (2, 3)]
SOLOS = [(p,) for p in range(4, 12)]
PAIRS = [(p, p + 1) for p in range(12, 32, 2)]
QUADS = [tuple(range(p, p + 4)) for p in range(32, 64, 4)]
FLAGS = FIXED_PAIRS + SOLOS + PAIRS + QUADS
KINDS = dict(f=iter(FIXED_PAIRS), s=iter(SOLOS), p=iter(PAIRS), q=iter(QUADS))
GROUPS = [next(KINDS[k]) for k in "ffqsqsqsqpqsqssqsqsppppppppp"]
ROUNDS = {1: 2, 2: 4, 4: 3}

PARAMS = []


def param(name, n):
    at = sum(k for _, k in PARAMS)
    PARAMS.append((name, n))
    return at


C_BADA = param("b_ada", 48)
C_CONVW = param("ssd_conv_w", 128)
C_CONVB = param("ssd_conv_b", 32)
C_D = param("ssd_D", 16)
C_NORM = param("ssd_norm_w", 16)
C_SCW = param("sc_conv_w", 24)
C_LN1G = param("ln1_g", 8)
C_LN1B = param("ln1_b", 8)
C_LN2G = param("ln2_g", 8)
C_LN2B = param("ln2_b", 8)
C_MIX = param("mix_norm", 16)
C_FFN = param("ffn_norm", 16)
C_DTB = param("dt_bias", 1)
C_ALOG = param("A_log", 1)
C_EPS = param("eps", 4)
C_QG = param("q_gain", 1)
C_KG = param("k_gain", 1)
C_QKE = param("qk_eps", 1)
C_FB = param("f_bias", 1)
C_PSC = param("pool_scale", 4)
C_MU = param("rw_mu", 48)
C_W0 = param("rw_w0", 8)
C_A0 = param("rw_a0", 8)
C_KK = param("rw_k_k", 8)
C_KA = param("rw_k_a", 8)
C_RK = param("rw_r_k", 8)
NPAR = sum(k for _, k in PARAMS)


def plan():
    out = []

    def add(key, tiles, split=True):
        out.append((key, tiles, split))

    def pair(key, mat, m0, nk=8, split=True):
        add(key, [(mat, P * k, m0 + P * m) for k in range(nk) for m in range(2)], split)

    def rows(key, *r0):
        add(key, [("ada", r, P * q) for r in r0 for q in range(8)], False)

    for j in range(8):
        rows(("ada", j), 1024 + P * j, P * j)
    add("dt", [("w_dt", P * k, 0) for k in range(8)])
    for i in range(4):
        pair(("B", i), "w_in", 4096 + 256 * i)
    for i in range(4):
        pair(("C", i), "w_in", 5120 + 256 * i)
    for i in range(8):
        pair(("xs", i), "w_in", 2048 + 256 * i)
    for i in range(4):
        for what, m0 in (("sc_c", 7200), ("sc_h", 8224), ("sc_b", 6176)):
            pair((what, i), "w_in", m0 + 256 * i)
    for i in range(4):
        pair(("sc_out", i), "w_sc_out", 256 * i)
    for i in range(4):
        pair(("gb", i), "w_in", 10272 + 256 * i)
    spare = [[2048 + 256 * j, 2048 + 256 * j + P] for j in range(4)]
    spare += [[4096 + P * j, 3072 + P * j] for j in range(8)]
    for i in range(8):
        pair(("z", i), "w_in", 256 * i)
        rows(("ada", 8 + i), *spare[i])
    for i in range(4):
        pair(("ga", i), "w_in", 9248 + 256 * i)
        rows(("ada", 16 + i), *spare[8 + i])
    for i in range(8):
        add(("ssd_out", i), [("w_ssd_out", P * k, P * i) for k in range(16)])
    for i in range(4):
        pair(("w_o", i), "w_o", 256 * i)
        rows(("ada", 20 + i), 5120 + 256 * i, 5120 + 256 * i + P)
    add("router", [("w_router", P * k, 0) for k in range(4)], False)
    pair("sh_gate", "sh_gate", 0)
    pair("sh_up", "sh_up", 0)
    add("sh_down", [("sh_down", P * k, P * m) for m in range(8) for k in range(2)])
    for group in GROUPS:
        for half in range(2):
            for p in group:
                add(("expert", p, half, group), range(16), False)
        for p in group:
            add(("expert", p, 2, group), range(16), False)

    def across(key, mat, m0, split=True):
        for half in range(2):
            add((key, half), [(mat, P * k, m0 + P * m) for k in range(4 * half, 4 * half + 4) for m in range(4)], split)

    def ffn(n):
        for m in range(22):
            add(("gate_up", n, m), [(f"{w}{n}", P * k, P * m) for k in range(8) for w in ("ffn_gate", "ffn_up")])
        tiles = [(f"ffn_down{n}", P * k, P * m) for m in range(8) for k in range(22)]
        for i in range(11):
            add(("down", n, i), tiles[16 * i:16 * i + 16])

    pair(("q", 0), "hy_in", 0)
    add("hy_f", [("w_f", P * k, 0) for k in range(8)])
    pair(("q", 1), "hy_in", 256)
    for i in range(2):
        pair(("k", i), "hy_in", 512 + 256 * i)
    across("v", "hy_in", 1024)
    pair(("og", 0), "hy_in", 1536)
    across("u", "hy_in", 2056)
    pair(("og", 1), "hy_in", 1792)
    add("pool", [("pool_w", P * g, 0) for g in range(4)])
    for i, k0 in enumerate((4, 6, 0, 2)):
        add(("hy_out", i), [("hy_out", P * k, P * m) for m in range(8) for k in (k0, k0 + 1)])
    ffn(0)
    add("wa1", [(f"rw_{x}1", P * k, 0) for x in "wa" for k in range(8)], False)
    add("wa2", [(f"rw_{x}2", 0, P * m) for x in "wa" for m in range(8)], False)
    for i in range(4):
        pair(("rw_k", i), "rw_k", 256 * i, split=False)
    for i in range(4):
        pair(("rw_r", i), "rw_r", 256 * i)
    across("rw_v0", "rw_v", 0, False)
    across("rw_v1", "rw_v", 512, False)
    pair("g1", "rw_g1", 0, split=False)
    add("g2", [("rw_g2", P * k, P * m) for k in range(2) for m in range(8)], False)
    for i in range(4):
        pair(("rw_o", i), "rw_o", 256 * i)
    ffn(1)
    return out


def constants():
    c = {}
    c["ident"] = np.eye(P)
    c["mean"] = np.full((P, P), 1.0 / D)
    c["sel8"] = np.broadcast_to(np.eye(8).reshape(1, 64) / 256, (P, 64))
    k = np.arange(P)
    tri = (k[:, None] <= k[None, :]) * 1.0
    c["iota"] = np.broadcast_to(np.arange(1.0, 257), (P, 256))
    for n in ROUNDS:
        w = P // n
        c[f"slot{n}"] = k[:, None] % w + w * np.arange(ROUNDS[n])[None, :] + 1.0
        c[f"of{n}"] = np.tile(k[:, None] // w == np.arange(n)[None, :], 2) * 1.0
    e = np.arange(N_EXPERTS)
    bump = np.maximum(FIXED - e, 0) * 1000.0
    c["bump"] = np.broadcast_to(bump, (P, N_EXPERTS))
    c["own"] = np.stack([np.tile(bump, 2), np.tile(e, 2)], axis=1)
    c["upto"] = (e[None, :] <= (k % N_EXPERTS)[:, None]) * 1.0
    g = np.arange(8)
    c["before"] = np.broadcast_to((g[None, :] < g[:, None]).reshape(1, 64), (P, 64)) * 1.0
    c["tri"] = tri
    n = np.arange(8)
    c["heads"] = np.concatenate([((2 * i + k[:, None] // 64) == np.arange(16)[None, :]) * (1.0 if i < 4 else 1.0 / 64) for i in n], axis=1)
    c["neg"] = np.concatenate([np.zeros((P, P)), (k[None, :] > k[:, None]) * -1e30], axis=1)
    s, t = np.arange(T)[:, None], np.arange(T)[None, :]
    bands = []
    for w in (2, 4, 8, 16):
        b = ((s <= t) & (s > t - w)) / np.minimum(t + 1, w) - (s == t)
        bands += [b[0:P], b[P:, P:]]
    c["band"] = np.concatenate(bands, axis=1)
    c["sum16"] = np.concatenate([(2 * i + k[:, None] // 64) == np.arange(16)[None, :] for i in n], axis=1) * 1.0
    s, t = k[:, None] % 64, np.arange(64)[None, :]
    c["chunk"] = np.concatenate([s <= t, s < t, s < t, s <= t], axis=1) * 1.0
    c["mask"] = np.concatenate([tri, np.ones((P, P)), tri], axis=1)
    return c


STAY = ["mean", "ident", "sel8"]
LATE_COLS = dict(iota=256, slot1=2, of1=2, slot2=4, of2=4, slot4=3, of4=8, before=64, tri=P, router_bias=64, bump=64, own=2, upto=64)
LATE = list(LATE_COLS)
CONST = ["mask", "heads", "neg", "band", "sum16", "chunk"]


def layer(S, keys, x, evac, banks, nk=8, steps=2, half=None):
    K = S.core
    hi, lo, ready = x
    mts = {}
    mine = {}
    for key in keys:
        tiles = list(enumerate(S.find(key).tiles))
        n = len(tiles) // 2
        mine[key] = tiles if half is None else tiles[n * half:n * (half + 1)]
        for _, (mat, _, m0) in mine[key]:
            mts.setdefault((mat, m0), len(mts))
    for key in keys:
        s = S.find(key) if half else S.take(key)
        nt = len(mine[key])
        for n, (t, (mat, k0, m0)) in enumerate(mine[key]):
            mt, k = mts[mat, m0], k0 // P
            pairno, odd = divmod(mt, 2)
            first, last = k == 0 and odd == 0, k == nk - 1
            if first:
                bank = banks[K.turn % len(banks)]
                K.turn += 1
            after = [s.ready if n == 0 else [], bank.free if first else [], ready[k]]
            o = bank[:, T * odd:T * (odd + 1)]
            w = slice(TILE * t, TILE * (t + 1))
            if s.split:
                tok = K.pe.mm(after, (o, s.hi[:, w], hi[:, k, :], first, False), (o, s.hi[:, w], lo[:, k, :], False, False),
                              (o, s.lo[:, w], hi[:, k, :], False, last))
            else:
                tok = K.pe.mm(after, (o, s.raw[:, w], hi[:, k, :], first, last))
            if n == nt - 1:
                s.done.append(tok)
            if last and (odd == 1 or mt == len(mts) - 1):
                bank.free = evac(pairno, bank, tok)
            if (n + 1) % max(1, nt // steps) == 0:
                yield


def weave(main, side, per):
    for _ in main:
        for _ in range(per):
            next(side, None)
    return side


def chained(*gens):
    for gen in gens:
        yield from gen


def drain(*gens):
    for gen in gens:
        for _ in gen:
            pass


def halves(ap):
    return ap.rearrange("p (i t) -> p i t", i=2)


def split_x(K, xh, xl, k, x32, after, eng=None):
    a = K.act.act(after, xh[:, k, :], x32)
    b = (eng or K.dve).tt([a], xl[:, k, :], x32, xh[:, k, :].bitcast(F32), ALU.subtract)
    return [a, b]


class InverseRoot:

    def __init__(self, K, bank, eps):
        self.K, self.bank, self.eps = K, bank, eps
        self.cols = K.buf(f"root{K.nroot}", 8 + K.nroot / 32, [P, 2])[:, :]
        K.nroot += 1
        self.early = K.act.act([K.t_par], self.cols[:, 0:1], K.par[:, C_EPS:C_EPS + 1], ACT.Sqrt)

    def add(self, ready, tile, first, last):
        b = self.bank
        self.done = self.K.pe.mm([ready, b.free if first else []], *[
            (b[:, i:i + 1], tile[:, P * i:P * (i + 1)], self.K.c["mean"][:, 0:1], first and i == 0, last) for i in range(2)])

    def columns(self):
        K, b = self.K, self.bank
        t = K.act.act([self.done, self.early], self.cols, b[:, 0:2], ACT.Sqrt, bias=K.par[:, C_EPS + self.eps:C_EPS + self.eps + 1])
        b.free = [t]
        return K.dve.recip([t], self.cols, self.cols)

    def row(self, t):
        K, b = self.K, self.bank
        t = K.pe.mm([t, b.free], *[(b[:, P * i:P * (i + 1)], self.cols[:, i:i + 1].to_broadcast([P, P]), K.c["ident"][:, :], i == 0, True) for i in range(2)])
        return b[:, 0:T], t


def layer_norm(K, src, ready, sq, bm, bv, sq_free, out, between=None, dst=None, mean=None, gain=None):
    dst = dst or src
    made = []
    if mean:
        for j in range(8):
            made.append(K.dve.stt([ready[j], mean[2]], dst[:, j, :], src[:, j, :], mean[0], mean[1], ALU.subtract, ALU.subtract))
    else:
        for j in range(8):
            if gain:
                tg = K.pe.mm([ready[j], K.t_cst, gain[2].free if j == 0 else []], (gain[2][:, 0:T], K.par[:, gain[0] + j:gain[0] + j + 1].to_broadcast([P, P]),
                                                              src[:, j, :], j == 0, j == 7))
            t = K.pe.mm([ready[j], bm.free if j == 0 else [], K.t_cst],
                        (bm[:, 0:T], K.c["mean"][:, :], src[:, j, :], j == 0, j == 7))
        for j in range(8):
            made.append(K.dve.tt([t], dst[:, j, :], src[:, j, :], bm[:, 0:T], ALU.subtract))
        bm.free = [made]
    if gain:
        _, gmean, bg, tile, spare = gain
        a = K.dve.ts([t, gmean[1]], spare, bm[:, 0:T], gmean[0], ALU.mult)
        a = K.dve.stt([a, tg], tile, bg[:, 0:T], 1.0 / D, spare, ALU.mult, ALU.subtract)
        bm.free, bg.free = [made, a], [a]
    root = InverseRoot(K, bv, 0)
    for j in range(8):
        b = K.act.act([made[j], sq_free], sq[:, j, :], dst[:, j, :], ACT.Square)
        root.add(b, sq[:, j, :], j == 0, j == 7)
    t = root.columns()
    if between:
        between()
    r, t = root.row(t)
    late = []
    for j in range(8):
        late.append((j, K.dve.tt([t], dst[:, j, :], dst[:, j, :], r, ALU.mult)))
        if j == 3 and gain:
            tg = K.dve.tt([a, t], tile, tile, r, ALU.mult)
        if j > 1:
            out(*late[j - 2])
    bv.free = [late[7][1]]
    out(*late[6])
    out(*late[7])
    return tg if gain else t


def modulation(K, S, i, share=False):
    s = S.take(("ada", i))
    for h in range(2):
        j = s.tiles[8 * h][1] // P
        w, a = s.raw[:, D * h:D * (h + 1)], K.acc[:, j:j + 1]
        if share and h:
            t = K.pool.tt([s.ready, K.t_csil, K.prod_free], K.prod[:, :], w, K.csil[:, :], ALU.mult)
            s.done.append(t)
            t = K.act.act([t], K.prod[:, :], K.prod[:, :], accum_out=a)
            K.prod_free = [t]
        else:
            t = K.dve.do([s.ready, K.t_csil, K.ada_last],
                         lambda e, w=w, a=a: e.tensor_tensor_reduce(K.scr[:, :], w, K.csil[:, :], 1.0, 0.0, ALU.mult, ALU.add, a))
            K.ada_last = [t]
            s.done.append(t)
        plus = 1.0 if j // 8 in (1, 4) else 0.0
        K.mod_ready[j] = K.dve.stt([t, K.t_par], K.mod[:, j:j + 1], a, plus, K.par[:, C_BADA + j:C_BADA + j + 1], ALU.add, ALU.add)


def first_block(K, S):
    pe, act, dve, pool = K.pe, K.act, K.dve, K.pool
    B = K.banks
    A = AREA

    h_hi = K.buf("h_hi", A, [P, 8, T], F32R)
    h_lo = K.buf("h_lo", A + 8, [P, 8, T], F32R)
    xs = K.buf("xs", A + 16, [P, 16, T])
    Bm = K.buf("Bm", A + 32, [P, 8, T])
    Cm = K.buf("Cm", A + 40, [P, 8, T])
    s_hi = K.buf("s_hi", A + 48, [P, 8, T], F32R)
    s_lo = K.buf("s_lo", A + 56, [P, 8, T], F32R)
    K.csil = csil = K.buf("csil", A + 64, [P, D])
    xT = K.buf("xT", A + 68, [P, 2, 2, T])
    CBm = K.buf("CBm", A + 72, [P, 2, 384])
    E = K.buf("E", A + 75, [P, 2, 2, 384])
    sc = K.buf("sc", A + 81, [P, 2, 2, 384])
    mask = K.buf("mask", A + 87, [P, 384])
    dtT = K.buf("dtT", A + 88.5, [P, 2, 32])
    AcsT = K.buf("AcsT", A + 88.75, [P, 2, 32])
    dt = K.buf("dt", A + 89, [32, T])
    dA = K.buf("dA", A + 90, [32, T])
    Acs = K.buf("Acs", A + 91, [32, T])
    tmp = K.buf("tmp", A + 92, [P, 4, T])
    scb = K.buf("scb", A + 96, [P, 2, T])
    K.scr = K.buf("scr", A + 115, [P, D], BF16)
    yb = K.buf("yb", A + 100, [P, 8, T])
    gate = K.buf("gate", A + 108, [P, 2, 2, T])

    xf = K.buf("xf", A + 16, [P, 8, T])
    sq = K.buf("sq", A + 24, [P, 8, T])
    K.prod = K.buf("prod", A + 100, [P, D])
    K.prod_free = []

    t_x = K.load(xf[:, :, :], K.ins["xT"].rearrange("p (j t) -> p j t", t=T))
    setup(K)
    par, t_par, ident = K.par, K.t_par, K.c["ident"]
    K.t_csil = K.load(csil[:, :], K.ins["c"].to_broadcast([P, D]))
    S.issue(1)
    t_mask = K.load(mask[:, :], K.cst("mask"), queue=act)
    K.t_csil = act.act([K.t_csil], csil[:, :], csil[:, :], ACT.Silu)

    h_ready = []
    todo = iter(range(8))

    def mod_some(n):
        for _, i in zip(range(n), todo):
            modulation(K, S, i, True)

    def out_h(j, t):
        while K.mod_ready[8 + j] is None:
            mod_some(1)
        t = act.act([t, K.mod_ready[8 + j], K.mod_ready[j]], xf[:, j, :], xf[:, j, :], ACT.Identity,
                    scale=K.mod[:, 8 + j:9 + j], bias=K.mod[:, j:j + 1])
        h_ready.append(split_x(K, h_hi, h_lo, j, xf[:, j, :], [t]))

    layer_norm(K, xf, [t_x] * 8, sq, B[0], B[1], [], out_h, between=lambda: mod_some(2))
    h = (h_hi, h_lo, h_ready)

    t_dt = []
    dt_raw = []

    def evac_dt(_, bank, done):
        t = act.act([done, t_par], dt[:, :], bank[0:32, 0:T], ACT.Identity, bias=par[0:32, C_DTB:C_DTB + 1])
        dt_raw.append(t)
        return [t]

    def steps_dt():
        d = dt[:, :]
        u, p, z, z2 = (tmp[0:32, i, :] for i in range(4))
        t = dve.stt([dt_raw], u, d, -1.0, d, ALU.mult, ALU.min)
        t = act.act([t], u, u, ACT.Exp)
        ta = act.act([t_par], K.small[0:32, 0:1], par[0:32, C_ALOG:C_ALOG + 1], ACT.Exp)
        yield
        t = dve.ts([t], z, u, 2.0, ALU.add)
        t = dve.recip([t], z, z)
        t = dve.tt([t], z, z, u, ALU.mult)
        t = dve.tt([t], z2, z, z, ALU.mult)
        yield
        t = dve.ts([t], p, z2, 2.0 / 17, ALU.mult)
        for c in (15, 13, 11, 9, 7, 5, 3):
            t = dve.stt([t], p, p, 2.0 / c, z2, ALU.add, ALU.mult)
        yield
        t = dve.stt([t], p, p, 2.0, z, ALU.add, ALU.mult)
        t = dve.stt([t], d, d, 0.0, p, ALU.max, ALU.add)
        t1 = dve.ts([t, ta], dA[:, :], d, K.small[0:32, 0:1], ALU.mult, -1.0, ALU.mult)
        t2 = dve.fill([t], z2, 0.0)
        t3 = dve.do([t1, t2], lambda e: e.tensor_tensor_scan(Acs[:, :], dA[:, :], z2, 0.0, ALU.add, ALU.add))
        yield
        for _ in range(6):
            yield
        b = B[7]
        tt = pe.tr([t3, K.t_cst, b.free], ident,
                   *[(b[:, 32 * i:32 * (i + 1)], d[:, P * i:P * (i + 1)]) for i in range(2)],
                   *[(b[:, 64 + 32 * i:96 + 32 * i], Acs[:, P * i:P * (i + 1)]) for i in range(2)])
        t4 = dve.copy([tt], dtT[:, :, :], b[:, 0:64].rearrange("p (i h) -> p i h", i=2))
        t5 = dve.copy([tt], AcsT[:, :, :], b[:, 64:128].rearrange("p (i h) -> p i h", i=2))
        b.free = [t4, t5]
        t_dt.append([t3, t4, t5])
        yield

    dense = [B[0], B[1], B[2]]
    drain(layer(S, ["dt"], h, evac_dt, dense, steps=1))

    late = []

    def silu_late():
        for made, o, t in late:
            made.append(act.act([t], o, o, ACT.Silu))
        late.clear()

    def conv(dst, tile0, made):
        def evac(pairno, bank, done):
            t, js = [], (2 * pairno, 2 * pairno + 1)
            src = [bank[:, T * i:T * (i + 1)] for i in range(2)]
            for i, j in enumerate(js):
                f = tile0 + j
                t.append(act.act([done, t_par], dst[:, j, :], src[i], ACT.Identity, bias=par[:, C_CONVB + f:C_CONVB + f + 1],
                                 scale=par[:, C_CONVW + 96 + f:C_CONVW + 97 + f]))
            silu_late()
            for n in range(1, 4):
                for i, j in enumerate(js):
                    k = C_CONVW + 32 * (3 - n) + tile0 + j
                    o = dst[:, j, n:T]
                    t[i] = dve.stt([t] if n == 1 else [t[i]], o, src[i][:, 0:T - n], par[:, k:k + 1], o, ALU.mult, ALU.add)
            late.extend((made, dst[:, j, :], t[i]) for i, j in enumerate(js))
            return t
        return evac

    B_made, C_made, xs_made = [], [], []
    side = weave(layer(S, [("B", i) for i in range(4)], h, conv(Bm, 16, B_made), dense), steps_dt(), 1)
    weave(layer(S, [("C", i) for i in range(4)], h, conv(Cm, 24, C_made), dense), side, 1)
    drain(side)
    drain(layer(S, [("xs", i) for i in range(8)], h, conv(xs, 0, xs_made), dense))
    silu_late()

    y_made = [None] * 16

    def ssd():
        bT, bC, bR, bY = B[3], B[4], [B[5], B[6]], B[7]
        xT_made, xT_free, CB_made, CB_free = {}, {}, {}, {}
        E_free, sc_free = {}, {}

        def group(g):
            q = g % 2
            tt = pe.tr([bT.free, xs_made[2 * g], xs_made[2 * g + 1], K.t_cst], ident,
                       *[(bT[:, T * i + P * f:T * i + P * (f + 1)], xs[:, 2 * g + f, P * i:P * (i + 1)])
                         for i in range(2) for f in range(2)])
            tc = pe.mm([bC.free, B_made[g], C_made[g]],
                       (bC[:, 0:T], Bm[:, g, 0:P], Cm[:, g, :], True, True),
                       (bC[:, T:384], Bm[:, g, P:T], Cm[:, g, P:T], False, True))
            t = dve.tt([tt, t_dt, xT_free.get(g - 2)], xT[:, q, :, :].rearrange("p i (h d) -> p i h d", h=4),
                       bT[:, :].rearrange("p (i h d) -> p i h d", i=2, h=4),
                       dtT[:, :, 4 * g:4 * g + 4].unsqueeze(3).to_broadcast([P, 2, 4, 64]), ALU.mult)
            bT.free = [t]
            xT_made[g] = [t, tt]
            t = dve.tt([tc, t_mask, CB_free.get(g - 2)], CBm[:, q, :], bC[:, 0:384], mask[:, :], ALU.mult)
            bC.free = [t]
            CB_made[g] = [t]

        def decay(n):
            r, h0, bank = n % 2, 2 * n, bR[n % 2]
            tr = pe.mm([bank.free, t_dt], *[(bank[:, T * j:T * (j + 1)], ident[0:32, h0 + j:h0 + j + 1].to_broadcast([32, P]),
                                             Acs[:, :], j == 0, True) for j in range(2)])
            te = []
            for j in range(2):
                te.append(act.act([tr, E_free.get(n - 2)], E[:, r, j, 0:T], bank[:, T * j:T * (j + 1)], ACT.Relu, scale=-1.0,
                                  bias=AcsT[:, 0, h0 + j:h0 + j + 1]))
                te.append(act.act([tr, E_free.get(n - 2)], E[:, r, j, T:384], bank[:, T * j + P:T * (j + 1)], ACT.Relu,
                                  scale=-1.0, bias=AcsT[:, 1, h0 + j:h0 + j + 1]))
            bank.free = te
            E_made[n] = act.act([te], E[:, r, :, :], E[:, r, :, :], ACT.Exp, scale=-1.0)

        def score(n):
            r, g = n % 2, n // 2
            t = dve.tt([E_made[n], CB_made[g], sc_free.get(n - 2)], sc[:, r, :, :], E[:, r, :, :],
                       CBm[:, g % 2, :].unsqueeze(1).to_broadcast([P, 2, 384]), ALU.mult)
            E_free[n] = [t]
            CB_free.setdefault(g, []).append(t)
            sc_made[n] = [t]

        def output(n):
            r, g, i = n % 2, n // 2, n % 2
            calls = []
            for st in range(2):
                for j in range(2):
                    o = bY[64 * j:64 * (j + 1), 0:T] if st == 0 else bY[64 * j:64 * (j + 1), P:T]
                    w_ = xT[:, g % 2, st, P * i + 64 * j:P * i + 64 * (j + 1)]
                    calls.append((o, w_, sc[:, r, j, 0:T] if st == 0 else sc[:, r, j, T:384], st == 0, st == 1))
            ty = pe.mm([bY.free, sc_made[n], xT_made[g]], *calls)
            sc_free[n] = [ty]
            xT_free.setdefault(g, []).append(ty)
            t = dve.stt([ty, xT_made[g]], xs[:, n, :], xs[:, n, :], par[:, C_D + n:C_D + n + 1], bY[:, 0:T], ALU.mult, ALU.add)
            bY.free = [t]
            y_made[n] = t

        E_made, sc_made = {}, {}
        group(0)
        yield
        decay(0)
        yield
        for n in range(16):
            if n + 1 < 16:
                decay(n + 1)
            score(n)
            yield
            if n:
                output(n - 1)
                yield
            if n % 2 == 0 and n + 2 < 16:
                group(n // 2 + 1)
                yield
        output(15)
        yield

    side = ssd()

    u_ready = []
    st = dict(scb_free=[], tmp_free=[t_dt])

    def sc_c(pairno, bank, done):
        st["c"] = act.act([done, st["scb_free"]], scb[:, :, :], halves(bank[:, :]))
        return [st["c"]]

    def sc_h(pairno, bank, done):
        t = dve.tt([done, st["c"]], scb[:, :, :], halves(bank[:, :]), scb[:, :, :], ALU.mult)
        st["u"] = []
        for i in range(2):
            f = 2 * pairno + i
            o = tmp[:, i, :]
            a = dve.ts([t, st["tmp_free"]], o, scb[:, i, :], par[:, C_SCW + 16 + f:C_SCW + 17 + f], ALU.mult)
            for n in (1, 2):
                k = C_SCW + 8 * (2 - n) + f
                a = dve.stt([a], o[:, n:T], scb[:, i, 0:T - n], par[:, k:k + 1], o[:, n:T], ALU.mult, ALU.add)
            st["u"].append(a)
        st["scb_free"] = st["u"]
        return [t]

    def sc_b(pairno, bank, done):
        a = dve.tt([done, st["u"], st["tmp_free"]], tmp[:, 2:4, :], halves(bank[:, :]), tmp[:, 0:2, :], ALU.mult)
        for i in range(2):
            u_ready.append(split_x(K, s_hi, s_lo, 2 * pairno + i, tmp[:, 2 + i, :], [a], pool))
        st["tmp_free"] = u_ready[-2:]
        return [a]

    for i in range(4):
        for key, evac in (("sc_c", sc_c), ("sc_h", sc_h), ("sc_b", sc_b)):
            weave(layer(S, [(key, i)], h, lambda _, b, d, f=evac, i=i: f(i, b, d), dense), side, 1)

    yb_made = [None] * 8

    def evac_sc(pairno, bank, done):
        t = act.act([done], yb[:, 2 * pairno:2 * pairno + 2, :], halves(bank[:, :]))
        yb_made[2 * pairno] = yb_made[2 * pairno + 1] = t
        return [t]

    weave(layer(S, [("sc_out", i) for i in range(4)], (s_hi, s_lo, u_ready), evac_sc, dense), side, 1)

    ga = K.buf("ga", A + 48, [P, 8, T])
    ga_made = [None] * 8
    gate_free = [[], []]

    def evac_gb(i):
        def evac(_, bank, done):
            q = i % 2
            t = act.act([done, gate_free[q]], gate[:, q, :, :], halves(bank[:, :]), ACT.Tanh, scale=0.5)
            t2 = pool.ts([t], gate[:, q, :, :], gate[:, q, :, :], 0.5, ALU.mult, 0.5, ALU.add)
            o = yb[:, 2 * i:2 * i + 2, :]
            t2 = pool.tt([t2, yb_made[2 * i]], o, o, gate[:, q, :, :], ALU.mult)
            yb_made[2 * i] = yb_made[2 * i + 1] = t2
            gate_free[q] = [t2]
            return [t]
        return evac

    def evac_ga(i):
        def evac(_, bank, done):
            o = ga[:, 2 * i:2 * i + 2, :]
            t = act.act([done, yb_made], o, halves(bank[:, :]), ACT.Tanh, scale=0.5)
            t2 = pool.ts([t], o, o, 0.5, ALU.mult, 0.5, ALU.add)
            ga_made[2 * i] = ga_made[2 * i + 1] = t2
            return [t]
        return evac

    for i in range(4):
        weave(layer(S, [("gb", i)], h, evac_gb(i), dense), side, 1)
    drain(side)

    tz = K.buf("tz", A + 68, [P, 2, 2, T])
    sqz = K.buf("sqz", A + 72, [P, 2, 2, T])
    y_hi = K.buf("y_hi", A + 68, [P, 16, T], F32R)
    y_lo = K.buf("y_lo", A + 84, [P, 16, T], F32R)
    yn = K.buf("yn", A + 112, [P, 2, T])
    r8 = K.buf("r8", A + 114, [8, T])
    tz_free, sq_free, sq_made, g_made = [[], []], [[], []], {}, []
    ms, rb = B[3], [B[4], B[5]]

    def evac_z(g):
        def evac(_, bank, done):
            q, y = g % 2, xs[:, 2 * g:2 * g + 2, :]
            t = act.act([done, tz_free[q]], tz[:, q, :, :], halves(bank[:, :]), ACT.Silu)
            t2 = dve.tt([t, y_made], y, y, tz[:, q, :, :], ALU.mult)
            tz_free[q] = [t2]
            g_made.append(t2)
            sq_made[g] = act.act([t2, sq_free[q]], sqz[:, q, :, :], y, ACT.Square)
            return [t]
        return evac

    def mean_square(g):
        q = g % 2
        t = pe.mm([sq_made[g], ms.free if g == 0 else []],
                  *[(ms[0:8, 0:T], K.c["sel8"][:, 8 * g:8 * g + 8], sqz[:, q, i, :], g == 0 and i == 0, g == 7 and i == 1)
                    for i in range(2)])
        sq_free[q] = [t]
        return t

    for g in range(8):
        drain(layer(S, [("z", g)], h, evac_z(g), dense))
        modulation(K, S, 8 + g)
        if g:
            mean_square(g - 1)

    y_ready = []

    def norm_y():
        t_ms = mean_square(7)
        t = act.act([t_ms], r8[:, :], ms[0:8, 0:T], ACT.Sqrt, bias=par[0:8, C_EPS:C_EPS + 1])
        ms.free = [t]
        t_r = dve.recip([t], r8[:, :], r8[:, :])
        yield
        yn_free = [[], []]
        made = []
        for g in range(8):
            if g % 2 == 0:
                b = rb[g // 2 % 2]
                t_b = pe.mm([t_r, b.free], *[(b[:, T * j:T * (j + 1)], ident[0:8, g + j:g + j + 1].to_broadcast([8, P]), r8[:, :],
                                              j == 0, True) for j in range(2)])
                made = []
            for i in range(2):
                f = 2 * g + i
                t = dve.stt([t_b, g_made[g], yn_free[i]], yn[:, i, :], xs[:, f, :], par[:, C_NORM + f:C_NORM + f + 1],
                            b[:, T * (g % 2):T * (g % 2 + 1)], ALU.mult, ALU.mult)
                made.append(t)
                yn_free[i] = split_x(K, y_hi, y_lo, f, yn[:, i, :], [t, t_ms], pool if i else dve)
                y_ready.append(yn_free[i])
            b.free = made
            yield

    m_hi = K.buf("m_hi", A, [P, 8, T], F32R)
    m_lo = K.buf("m_lo", A + 8, [P, 8, T], F32R)
    m_ready = []

    def evac_ssd(pairno, bank, done):
        out = []
        for i in range(2):
            j = 2 * pairno + i
            t = dve.tt([done, ga_made[j]], ga[:, j, :], bank[:, T * i:T * (i + 1)], ga[:, j, :], ALU.mult)
            out.append(t)
            t = dve.tt([t, yb_made[j]], ga[:, j, :], ga[:, j, :], yb[:, j, :], ALU.add)
            m_ready.append(split_x(K, m_hi, m_lo, j, ga[:, j, :], [t], pool))
        return out

    xa = K.buf("xa", A + 16, [P, 8, T])
    v = K.buf("v", A + 24, [P, 8, T])
    sq1 = K.buf("sq1", A + 32, [P, 8, T])
    x1 = K.buf("x1", A + 40, [P, 8, T])
    setup_late(K)
    side = norm_y()
    for i in range(4):
        weave(layer(S, [("ga", i)], h, evac_ga(i), dense), side, 2)
        modulation(K, S, 16 + i)
    drain(side)
    t_xa = K.load(xa[:, :, :], K.ins["xT"].rearrange("p (j t) -> p j t", t=T), after=[y_ready], queue=act)
    drain(layer(S, [("ssd_out", i) for i in range(8)], (y_hi, y_lo, y_ready), evac_ssd, dense, nk=16))
    t_xa = act.act([t_xa], xa[:, :, :], xa[:, :, :], ACT.Copy, scale=ALPHA)

    v_ready = []

    def evac_o(pairno, bank, done):
        for i in range(2):
            j = 2 * pairno + i
            v_ready.append(dve.stt([done, t_xa, K.mod_ready[16 + j]], v[:, j, :], bank[:, T * i:T * (i + 1)],
                                   K.mod[:, 16 + j:17 + j], xa[:, j, :], ALU.mult, ALU.add))
        return v_ready[-2:]

    K.prod_free = m_ready
    gmean = K.buf("gmean", A + 61, [P, 2, T])
    t = pe.mm([B[6].free], (B[6][:, 0:16], K.c["mean"][:, :], par[:, C_LN1G:C_LN1G + 16], True, True))
    t_gb = dve.do([t], lambda e: e.tensor_reduce(K.small[:, 16:18], B[6][:, 0:16].rearrange("p (n j) -> p n j", n=2), AX, ALU.add))
    B[6].free = [t_gb]
    for i in range(4):
        drain(layer(S, [("w_o", i)], (m_hi, m_lo, m_ready), lambda _, b, d, i=i: evac_o(i, b, d), dense))
        modulation(K, S, 20 + i, True)
    for i in range(RING, RING + 4):
        S.before[i] = m_ready
    x1_ready = []

    def out_x1(j, t):
        x1_ready.append(act.act([t], x1[:, j, :], v[:, j, :], ACT.Identity, bias=par[:, C_LN1B + j:C_LN1B + j + 1],
                                scale=par[:, C_LN1G + j:C_LN1G + j + 1]))

    t = layer_norm(K, v, v_ready, sq1, B[3], B[4], [], out_x1, gain=(C_LN1G, (K.small[:, 16:17], t_gb), B[5], gmean[:, 0, :], gmean[:, 1, :]))
    return x1, x1_ready, (K.small[:, 17:18], gmean[:, 0, :], [t, t_gb])


def moe(K, S, x1, x1_ready, x1_mean, norm):
    pe, act, dve = K.pe, K.act, K.dve
    B, A, R = K.banks, AREA, AREA + 56
    par, ident = K.par, K.c["ident"]
    iota = K.c["iota"]

    h2 = K.buf("h2", A, [P, 8, T])
    h2_hi = K.buf("h2_hi", A + 8, [P, 8, T], F32R)
    h2_lo = K.buf("h2_lo", A + 48, [P, 8, T], F32R)
    v2 = K.buf("v2", A + 24, [P, 8, T])
    sq2 = K.buf("sq2", A + 32, [P, 8, T])
    n_hi = K.buf("n_hi", A + 16, [P, 2, D], F32R)
    n_lo = K.buf("n_lo", A + 32, [P, 2, D], F32R)
    hs = K.buf("hs", A + 100, [P, 2, T])
    hs_hi = K.buf("hs_hi", A + 102, [P, 2, T], F32R)
    hs_lo = K.buf("hs_lo", A + 104, [P, 2, T], F32R)

    h2_ready, h2_split = [], []

    def out_h2(j, t):
        t = act.act([t, K.mod_ready[32 + j], K.mod_ready[24 + j]], h2[:, j, :], v2[:, j, :], ACT.Identity,
                    scale=K.mod[:, 32 + j:33 + j], bias=K.mod[:, 24 + j:25 + j])
        h2_ready.append(t)
        h2_split.append(split_x(K, h2_hi, h2_lo, j, h2[:, j, :], [t]))

    layer_norm(K, x1, x1_ready, sq2, B[3], B[4], [], out_h2, dst=v2, mean=x1_mean)

    s = S.take("router")
    b = B[7]
    for k in range(8):
        w = s.raw[:, P * (k // 2) + 64 * (k % 2):P * (k // 2) + 64 * (k % 2) + 64]
        t = pe.mm([s.ready, h2_ready[k], b.free if k == 0 else []],
                  *[(b[:, 64 * i:64 * (i + 1)], h2[:, k, P * i:P * (i + 1)], w, k == 0 and i == 0, k == 7) for i in range(2)])
    s.done.append(t)
    sig = K.buf("sig", R, [P, 2, 64])
    bi = K.buf("bi", R + 0.5, [P, 2, 64])
    bm = K.buf("bm", R + 1, [P, 2, 64])
    mr = K.buf("mr", R + 1.5, [P, 2, 64])
    g8 = K.buf("g8", R + 2, [P, 16, 8])
    gt = K.buf("gt", R + 2.5, [P, 16, 8])
    eq = K.buf("eq", R + 3, [P, 16, 8])
    gs = K.buf("gs", R + 3.5, [P, 16])
    cnt = K.buf("cnt", R + 3.5625, [P, 16])
    mx = K.buf("mx", R + 3.625, [P, 2, 8])
    gsum = K.buf("gsum", R + 3.6875, [P, 2])
    M = K.buf("M", R + 4, [P, 2, 64], BF16)
    tri = K.buf("tri", R + 4.25, [P, P], BF16)
    ones = K.buf("ones", R + 4.5, [P, P], BF16)
    one_of = K.buf("one_of", R + 4.75, [64, 64], BF16)
    G = K.buf("G", R + 5, [P, 2, 64])
    Gs = K.buf("Gs", R + 5.5, [P, 2, 2, 64], F32R)
    rm = K.buf("rm", R + 6.5, [P, 2, 64])
    rmT = K.buf("rmT", R + 7, [64, T], BF16)
    flags = K.buf("flags", R + 7.5, [1, len(GROUPS)], I32)
    gc = K.buf("gc", R + 7.625, [P, 2])
    junk = K.buf("junk", R + 7.6875, [P, 8])
    order = K.buf("order", R + 7.75, [1, N_EXPERTS], I32)
    rmU = K.buf("rmU", R + 1.5, [P, 2, 64])
    kb = K.buf("kb", R + 2, [64, 64])
    tie = K.buf("tie", R + 2.25, [64, 64])
    Pi = K.buf("Pi", R + 2.5, [64, 64])
    Pib = K.buf("Pib", R + 2.75, [64, 64], BF16)
    rmTu = K.buf("rmTu", R + 3, [64, T], BF16)
    kc = K.buf("kc", R + 3.75, [64, 2])
    cb = K.buf("cb", R + 3.875, [64, 2], BF16)
    GT = K.buf("GT", R, [64, T])

    t_sig = act.act([t], sig[:, :, :], halves(b[:, 0:P]), ACT.Sigmoid)
    b.free = [t_sig]
    t = dve.copy([K.t_late], tri[:, :], K.c["tri"])
    t_bf = [t, dve.fill([], ones[:, :], 1.0), dve.copy([K.t_cst], one_of[:, :], ident[0:64, 0:64])]

    bias = K.c["router_bias"]
    t = dve.tt([t_sig, K.t_late], bi[:, :, :], sig[:, :, :], bias.unsqueeze(1).to_broadcast([P, 2, 64]), ALU.add)
    t = [dve.do([t], lambda e, i=i, g=g: e.max(out=g8[:, 8 * i + g, :], in_=bi[:, i, 8 * g:8 * g + 8]))
         for i in range(2) for g in range(8)]
    t = dve.tt([t], gs[:, :], g8[:, :, 0], g8[:, :, 1], ALU.add)
    one = gs[:, :].unsqueeze(2).to_broadcast([P, 16, 8])
    for i in range(2):
        a = slice(8 * i, 8 * i + 8)
        other = gs[:, a].unsqueeze(1).to_broadcast([P, 8, 8])
        one = gs[:, a].unsqueeze(2).to_broadcast([P, 8, 8])
        t1 = dve.tt([t], eq[:, a, :], other, one, ALU.is_equal)
        t2 = dve.tt([t], gt[:, a, :], other, one, ALU.is_gt)
        t1 = dve.tt([t1], eq[:, a, :], eq[:, a, :], K.c["before"].rearrange("p (g h) -> p g h", g=8), ALU.mult)
        t3 = dve.tt([t1, t2], gt[:, a, :], gt[:, a, :], eq[:, a, :], ALU.add)
        t3 = dve.do([t3], lambda e, a=a: e.tensor_reduce(cnt[:, a], gt[:, a, :], AX, ALU.add))
        t3 = dve.ts([t3], cnt[:, a], cnt[:, a], 4.0, ALU.is_ge, -1e30, ALU.mult)
        c = cnt[:, a].unsqueeze(2).to_broadcast([P, 8, 8])
        t3 = dve.tt([t3], bm[:, i, :].rearrange("p (g h) -> p g h", g=8), bi[:, i, :].rearrange("p (g h) -> p g h", g=8), c, ALU.add)
        t3 = dve.do([t3], lambda e, i=i: e.max(out=mx[:, i, :], in_=bm[:, i, :]))
        t3 = dve.do([t3], lambda e, i=i: e.match_replace(out=mr[:, i, :], in_to_replace=mx[:, i, :], in_values=bm[:, i, :], imm_value=-2e30))
        t_M = dve.tt([t3], M[:, i, :], mr[:, i, :], bm[:, i, :], ALU.is_lt)

    two = [B[5], B[6]]
    hs_ready = []
    st = {}

    def evac_gate(_, bank, done):
        st["g"] = act.act([done], hs[:, :, :], halves(bank[:, :]), ACT.Silu)
        return [st["g"]]

    def evac_up(_, bank, done):
        t = dve.tt([done, st["g"]], hs[:, :, :], halves(bank[:, :]), hs[:, :, :], ALU.mult)
        for i in range(2):
            hs_ready.append(split_x(K, hs_hi, hs_lo, i, hs[:, i, :], [t]))
        return [t]

    drain(layer(S, ["sh_gate"], (h2_hi, h2_lo, h2_split), evac_gate, two))
    drain(layer(S, ["sh_up"], (h2_hi, h2_lo, h2_split), evac_up, two))
    S.before[RING + 4] = S.before[RING + 5] = [hs_ready]

    b = B[7]
    t = pe.mm([b.free, t_bf, t_M], (b[:, 0:64], tri[:, :], M[:, 0, :], True, True),
              (b[:, 64:P], ones[:, :], M[:, 0, :], False, False), (b[:, 64:P], tri[:, :], M[:, 1, :], False, True),
              *[(b[0:64, P:P + 64], ones[:, 0:64], M[:, i, :], False, i == 1) for i in range(2)],
              *[(b[0:64, P + 64:P + 65], M[:, i, :], ones[:, 0:1], False, i == 1) for i in range(2)])
    own = K.c["own"]
    t1 = dve.tt([t], kb[:, :], b[0:64, P:P + 64], K.c["bump"][0:64, :], ALU.add)
    t2 = dve.tt([t], kc[:, 0:1], b[0:64, P + 64:P + 65], own[0:64, 0:1], ALU.add)
    t3 = dve.copy([t], cb[:, 0:1], b[0:64, P + 64:P + 65])
    t4 = dve.copy([K.t_late], cb[:, 1:2], own[0:64, 1:2])
    t_rm = dve.tt([t], rmU[:, :, :], halves(b[:, 0:P]), M[:, :, :], ALU.mult)
    b.free = [t1, t2, t3, t_rm]
    t1 = dve.stt([t1, t2], tie[:, :], kb[:, :], kc[:, 0:1], K.c["upto"][0:64, :], ALU.is_equal, ALU.mult)
    t1 = dve.stt([t1], kb[:, :], kb[:, :], kc[:, 0:1], tie[:, :], ALU.is_gt, ALU.add)
    t1 = dve.do([t1], lambda e: e.tensor_reduce(kc[:, 1:2], kb[:, :], AX, ALU.add))
    t_Pi = dve.ts([t1, K.t_late], Pi[:, :], iota[0:64, 0:64], kc[:, 1:2], ALU.is_equal)
    t_Pib = dve.copy([t_Pi], Pib[:, :], Pi[:, :])
    n_made = []
    for i in range(2):
        for q in range(2):
            b = two[q]
            t = pe.tr([b.free, h2_ready], ident, *[(b[:, P * f:P * (f + 1)], h2[:, 4 * q + f, P * i:P * (i + 1)]) for f in range(4)])
            o = slice(512 * q, 512 * (q + 1))
            t1 = act.act([t], n_hi[:, i, o], b[:, :])
            t2 = dve.tt([t1], n_lo[:, i, o], b[:, :], n_hi[:, i, o].bitcast(F32), ALU.subtract)
            b.free = [t2]
            n_made.append(t2)

    b = B[4]
    t = pe.mm([b.free, t_Pib, t3, t4], (b[0:1, 0:64], cb[:, 1:2], Pib[:, :], True, True), (b[0:1, 64:P], cb[:, 0:1], Pib[:, :], False, True))
    t1 = dve.copy([t], order[:, :], b[0:1, 0:64])
    S.order, S.order_ready = order, [t1]
    t2 = dve.copy([t], K.small[0:1, 0:64], b[0:1, 64:P])
    b.free = [t1, t2]
    t1 = [dve.do([t2], lambda e, f=f, n=n, o=o: e.tensor_reduce(flags[:, o], K.small[0:1, f].rearrange("p (g e) -> p g e", e=n), AX, ALU.max))
          for f, n, o in ((slice(0, 4), 2, slice(0, 2)), (slice(4, 12), 1, slice(2, 10)), (slice(12, 32), 2, slice(10, 20)),
                          (slice(32, 64), 4, slice(20, 28)))]
    for q in (pe, act, dve):
        q.load_flags(t1, flags[:, :])
    b = B[7]
    t = pe.tr([b.free, t_rm], ident, *[(b[0:64, P * i:P * (i + 1)], rmU[:, i, :]) for i in range(2)])
    t_rm = dve.copy([t], rmTu[:, :], b[0:64, 0:T])
    b.free = [t_rm]
    t = pe.mm([b.free, t_Pib], *[(b[:, 64 * i:64 * (i + 1)], rmTu[:, P * i:P * (i + 1)], Pib[:, :], i == 0, True) for i in range(2)],
              (b[0:64, P:P + T], Pib[:, :], rmTu[:, :], False, True))
    t1 = dve.copy([t], rm[:, :, :], halves(b[:, 0:P]))
    t2 = dve.copy([t], rmT[:, :], b[0:64, P:P + T])
    b.free = t_rm = [t1, t2]

    t = dve.tt([t_M], G[:, :, :], sig[:, :, :], M[:, :, :], ALU.mult)
    t = dve.do([t], lambda e: e.tensor_reduce(gsum[:, :], G[:, :, :], AX, ALU.add))
    t = dve.recip([t], gsum[:, :], gsum[:, :])
    t = [dve.ts([t], G[:, i, :], G[:, i, :], gsum[:, i:i + 1], ALU.mult, 2.5, ALU.mult) for i in range(2)]
    b = B[4]
    t = pe.tr([b.free, t], ident, *[(b[0:64, P * i:P * (i + 1)], G[:, i, :]) for i in range(2)])
    t = dve.copy([t], GT[:, :], b[0:64, 0:T])
    b.free = [t]
    t = pe.mm([t, t_Pi], *[(b[:, 64 * i:64 * (i + 1)], GT[:, P * i:P * (i + 1)], Pi[:, :], i == 0, True) for i in range(2)])
    t = dve.copy([t], Gs[:, :, 0, :], halves(b[:, 0:P]))
    t_G = dve.tt([t], Gs[:, :, 1, :], halves(b[:, 0:P]), Gs[:, :, 0, :].bitcast(F32), ALU.subtract)
    b.free = [t_G]

    s = S.take("sh_down")
    for n, (_, k0, m0) in enumerate(s.tiles):
        m, k = m0 // P, k0 // P
        o = B[m // 2][:, T * (m % 2):T * (m % 2 + 1)]
        wh, wl = s.hi[:, P * n:P * (n + 1)], s.lo[:, P * n:P * (n + 1)]
        first = k == 0 and m % 2 == 0
        t_acc = pe.mm([s.ready, hs_ready[k], B[m // 2].free if first else []],
                      (o, wh, hs_hi[:, k, :], first, False), (o, wh, hs_lo[:, k, :], False, False),
                      (o, wl, hs_hi[:, k, :], False, False))
    s.done.append(t_acc)

    t_x1 = act.act([h2_ready], x1[:, :, :], x1[:, :, :], ACT.Copy, scale=ALPHA)

    Pm = K.buf("Pm", A + 108, [P, 2, 2, P], F32R)
    PT = [K.buf("PT", A + 110, [P, 2, T], F32R)[:, q, :] for q in range(2)] + [K.buf("PT2", A + 64, [P, T], F32R)[:, :]]
    xg = K.buf("xg", A + 100, [P, 2, 8, P])
    sg = K.buf("sg", A + 112, [P, T])
    hm = K.buf("hm", A + 113, [P, T])
    hmT = K.buf("hmT", A + 114, [P, 2, P])
    y_hi = K.buf("ye_hi", A + 24, [P, 2, D], F32R)
    y_lo = K.buf("ye_lo", A, [P, 2, D], F32R)
    acc = B[0:4]
    free = {"xg0": [t_acc], "xg1": [t_acc], "y0": [n_made], "y1": [n_made]}
    made = {}

    def onehot(g, j, q):
        n = len(g)
        w = P // n
        made["P"] = dve.tt([t_rm, K.t_late, free.get(f"P{q}")], Pm[:, q, :, :].rearrange("p i (e s) -> p i e s", e=n),
                           rm[:, :, g[0]:g[0] + n].unsqueeze(3).to_broadcast([P, 2, n, w]),
                           iota[:, w * j:w * (j + 1)].unsqueeze(1).unsqueeze(1).to_broadcast([P, 2, n, w]), ALU.is_equal)

    def gather(q):
        out = []
        for half in range(2):
            b = B[5 + half]
            t = pe.mm([made["P"], n_made, b.free, free[f"xg{q}"]],
                      *[(b[:, P * f:P * (f + 1)], n[:, i, 512 * half + P * f:512 * half + P * (f + 1)], Pm[:, q, i, :],
                         f == 0 and i == 0 and n is n_hi, False) for f in range(4) for i in range(2) for n in (n_hi, n_lo)])
            o, src = xg[:, q, 4 * half:4 * half + 4, :], b[:, :].rearrange("p (f s) -> p f s", f=4)
            out.append(act.act([t], o, src) if half == 0 else dve.copy([t], o, src))
            b.free = [out[-1]]
        made[f"xg{q}"] = out

    def places(g, j, q, z):
        n = len(g)
        w = P // n
        b = B[7]
        t = pe.mm([b.free, t_rm, made["P"], t_G, t_bf],
                  *[(b[w * e:w * (e + 1), 0:T], one_of[:, g[e]:g[e] + 1].to_broadcast([64, w]), rmT[:, :], True, True) for e in range(n)],
                  *[(b[:, T:T + 2 * n], Pm[:, q, i, :], Gs[:, i, :, g[0]:g[0] + n], False, i == 1) for i in range(2)])
        free[f"P{q}"] = [t]
        a = dve.ts([t, K.t_late, free.get(f"PT{z}")], PT[z], b[:, 0:T], K.c[f"slot{n}"][:, j:j + 1], ALU.is_equal)
        c = dve.do([t, free.get(f"gc{q}"), free.get("junk")],
                   lambda e: e.tensor_tensor_reduce(junk[:, 0:2 * n], b[:, T:T + 2 * n], K.c[f"of{n}"], 1.0, 0.0, ALU.mult, ALU.add,
                                                    gc[:, q:q + 1]))
        free["junk"] = [c]
        b.free = [a, c]
        made[f"PT{z}"], made[f"gc{q}"] = a, c

    def up(b, q, ws):
        n = len(ws) // 2
        w = P // n
        for half in range(2):
            calls = []
            for k in range(4 * half, 4 * half + 4):
                for e in range(n):
                    calls.append((b[w * e:w * (e + 1), :], xg[:, q, k, w * e:w * (e + 1)],
                                  ws[n * half + e].raw[:, 512 * (k % 4):512 * (k % 4 + 1)], k == 0, k == 7))
            mine = ws[n * half:n * (half + 1)]
            t = pe.mm([b.free if half == 0 else [], made[f"xg{q}"], [s.ready for s in mine]], *calls)
            for s in mine:
                s.done.append(t)
        free[f"xg{q}"] = [t]
        made["up"] = t

    def middle(b, q):
        t = act.act([made["up"], free.get("sg")], sg[:, :], b[:, 0:T], ACT.Silu)
        t = dve.stt([t, made[f"gc{q}"], free.get("hm")], hm[:, :], sg[:, :], gc[:, q:q + 1], b[:, T:2 * T], ALU.mult, ALU.mult)
        b.free = free["sg"] = free[f"gc{q}"] = [t]
        made["hm"] = t

    def turn(b):
        t = pe.tr([b.free, made["hm"]], ident, *[(b[:, P * k:P * (k + 1)], hm[:, P * k:P * (k + 1)]) for k in range(2)])
        free["hm"] = [t]
        t = act.act([t, free.get("hmT")], hmT[:, :, :], b[:, 0:T].rearrange("p (k s) -> p k s", k=2))
        b.free = [t]
        made["hmT"] = t

    def down(q, ws):
        out, w = [], P // len(ws)
        for n in range(2):
            b, o = B[5 + n], slice(512 * n, 512 * (n + 1))
            t = pe.mm([b.free, made["hmT"], [s.ready for s in ws]],
                      *[(b[w * e:w * (e + 1), :], hmT[:, k, w * e:w * (e + 1)], s.raw[:, D * k + 512 * n:D * k + 512 * (n + 1)],
                         k == 0, k == 1) for k in range(2) for e, s in enumerate(ws)])
            a = act.act([t, free[f"y{q}"]], y_hi[:, q, o], b[:, :])
            a = dve.tt([a], y_lo[:, q, o], b[:, :], y_hi[:, q, o].bitcast(F32), ALU.subtract)
            b.free = [a]
            out.append(a)
        for s in ws:
            s.done.append(t)
        free["hmT"] = [t]
        made[f"y{q}"] = out

    def combine(q, z):
        calls = []
        for m in range(8):
            o = acc[m // 2][:, T * (m % 2):T * (m % 2 + 1)]
            for y in (y_hi, y_lo):
                calls.append((o, y[:, q, P * m:P * (m + 1)], PT[z], False, False))
        t = pe.mm([made[f"y{q}"], made[f"PT{z}"]], *calls)
        free[f"y{q}"] = free[f"PT{z}"] = [t]
        made["acc"] = t

    onehot(GROUPS[0], 0, 0)
    gather(0)
    places(GROUPS[0], 0, 0, 0)
    for i, g in enumerate(GROUPS):
        q, r = i % 2, 1 - i % 2
        then = GROUPS[i + 1] if i + 1 < len(GROUPS) else None
        wu = [S.take(("expert", p, half, g)) for half in range(2) for p in g]
        up(B[4], q, wu)
        if then:
            onehot(then, 0, r)
        middle(B[4], q)
        if i:
            combine(r, r)
        turn(B[7])
        if then:
            gather(r)
            places(then, 0, r, r)
        wd = [S.take(("expert", p, 2, g)) for p in g]
        down(q, wd)
        flag = FLAGS.index(g)
        before = dict(free), [list(flat(b.free)) for b in B]
        for j in range(1, ROUNDS[len(g)]):
            for queue in (pe, act, dve):
                queue.branch(flag, P // len(g) * j, made["acc"] if j > 1 else [])
            onehot(g, j, q)
            gather(q)
            places(g, j, q, 2)
            up(B[7], q, wu)
            middle(B[7], q)
            turn(B[5])
            down(r, wd)
            combine(r, 2)
        for j in range(1, ROUNDS[len(g)]):
            for queue in (pe, act, dve):
                queue.close()
        for k, tokens in before[0].items():
            free[k] = list(dict.fromkeys(flat([free[k], tokens])))
        for b, tokens in zip(B, before[1]):
            b.free = list(dict.fromkeys(flat([b.free, tokens])))
    combine(1, 1)

    v3 = K.buf("v3", A + 16, [P, 8, T])
    sq3 = K.buf("sq3", A + 32, [P, 8, T])
    x2 = K.buf("x2", A + 40, [P, 8, T])
    v_ready, x2_ready = [], []
    for j in range(8):
        v_ready.append(dve.stt([made["acc"], t_x1, K.mod_ready[40 + j]], v3[:, j, :], acc[j // 2][:, T * (j % 2):T * (j % 2 + 1)],
                               K.mod[:, 40 + j:41 + j], x1[:, j, :], ALU.mult, ALU.add))
        acc[j // 2].free = [v_ready[-1]]

    def out_x2(j, t):
        x2_ready.append(act.act([t], x2[:, j, :], v3[:, j, :], ACT.Identity, bias=par[:, C_LN2B + j:C_LN2B + j + 1],
                                scale=par[:, C_LN2G + j:C_LN2G + j + 1]))
        if j % 2:
            norm.pair(j // 2, x2, x2_ready[j - 1:], after)

    after = [made["acc"]] + [s.done for s in S.user[RING:]]
    S.ahead(S.next + HIS, K.pool)
    layer_norm(K, v3, v_ready, sq3, B[4], B[5], [made["acc"]], out_x2)
    return x2, x2_ready, after, norm


def layer_across(S, keys, x, evac, banks):
    K = S.core
    hi, lo, ready = x
    mine = [banks[(K.turn + i) % len(banks)] for i in range(2)]
    K.turn += 2
    for n, key in enumerate(keys):
        s = S.take(key)
        for q in range(4):
            k = 4 * n + q
            w = slice(512 * q, 512 * (q + 1))
            first, last = k == 0, k == 4 * len(keys) - 1
            for i in range(2):
                b, t = mine[i], slice(P * i, P * (i + 1))
                after = [s.ready, ready[k], b.free if first else []]
                if s.split:
                    tok = K.pe.mm(after, (b[:, :], hi[:, k, t], s.hi[:, w], first, False), (b[:, :], lo[:, k, t], s.hi[:, w], False, False),
                                  (b[:, :], hi[:, k, t], s.lo[:, w], False, last))
                else:
                    tok = K.pe.mm(after, (b[:, :], hi[:, k, t], s.raw[:, w], first, last))
                if q == 3 and i == 1:
                    s.done.append(tok)
                if last:
                    b.free = evac(i, b, tok)
            yield


class Rms:

    def __init__(self, K, total, sq, r=None, gain=None, hi=None, lo=None):
        self.K, self.total, self.sq, self.r, self.gain, self.hi, self.lo = K, total, sq, r, gain, hi, lo
        self.ready = [None] * 8
        self.done = []

    def pair(self, n, x, ready, after=(), eng=None):
        K = self.K
        for j in (2 * n, 2 * n + 1):
            if self.hi is None:
                break
            c = K.par[:, self.gain + j:self.gain + j + 1]
            a = K.act.act([ready, after], self.hi[:, j, :], x[:, j, :], ACT.Copy, scale=c)
            b = K.dve.stt([a], self.lo[:, j, :], x[:, j, :], c, self.hi[:, j, :].bitcast(F32), ALU.mult, ALU.subtract)
            self.ready[j] = [a, b]
        eng = eng or K.pool
        o = x[:, 2 * n:2 * n + 2, :]
        t = eng.tt([ready, after, self.done], self.sq if n else self.total, o, o, ALU.mult)
        if n and eng is K.pool:
            t = eng.tt([t], self.total, self.total, self.sq, ALU.add)
        self.done = [t] if eng is K.pool else [self.done, t]

    def sums(self):
        o = self.total[:, 0, :]
        self.done = [self.K.pool.tt(self.done, o, o, self.total[:, 1, :], ALU.add)]

    def finish(self, bank, parts):
        root = InverseRoot(self.K, bank, 1)
        for n, p in enumerate(parts):
            root.add(self.done, p, n == 0, n == len(parts) - 1)
        t = root.columns()
        return root.row(t), (root.cols, t)

    def keep(self, bank):
        (row, t), cols = self.finish(bank, [self.total[:, 0, :]])
        t = self.K.act.act([t], self.r, row)
        bank.free = [t]
        return t, cols


def log1p_exp(dve, act, u, p, z, z2, t):
    t = act.act([t], u, u, ACT.Exp)
    t = dve.ts([t], z, u, 2.0, ALU.add)
    t = dve.recip([t], z, z)
    yield
    t = dve.tt([t], z, z, u, ALU.mult)
    t = dve.tt([t], z2, z, z, ALU.mult)
    t = dve.ts([t], p, z2, 2.0 / 17, ALU.mult)
    for c in (15, 13, 11, 9, 7, 5, 3):
        t = dve.stt([t], p, p, 2.0 / c, z2, ALU.add, ALU.mult)
    t = dve.stt([t], p, p, 2.0, z, ALU.add, ALU.mult)
    yield t


def fox_norm(K):
    A = AREA
    spare = K.buf("f_spare", A + 48, [P, 2, 2, T])
    return Rms(K, spare[:, 0, :, :], spare[:, 1, :, :], K.buf("f_r", A + 56, [P, T])[:, :], C_MIX,
               K.buf("f_hi", A, [P, 8, T], F32R), K.buf("f_lo", A + 8, [P, 8, T], F32R))


def fox(K, S, x2, x2_ready, after, norm, out):
    pe, act, dve, pool = K.pe, K.act, K.dve, K.pool
    B, A = K.banks, AREA
    par, ident = K.par, K.c["ident"]
    dense = B[0:5]

    q = K.buf("q", A + 16, [P, 8, T])
    sq = K.buf("f_sq", A + 24, [P, 8, T])
    v = K.buf("f_v", A + 32, [P, 2, 512])
    u = K.buf("f_u", A + 36, [P, 2, 512])
    og = K.buf("og", A + 57, [P, 4, T])
    r16 = K.buf("r16", A + 61, [16, T])
    c = K.buf("f_c", A + 62, [8, T])
    nc = K.buf("f_nc", A + 63, [8, T])
    f = K.buf("f_f", A + 64, [8, 5, T])
    cT = K.buf("f_cT", A + 69, [P, 2, 8])
    small = K.buf("f_small", A + 69.25, [P, 8, 6])
    lg = K.buf("lg", A + 70, [P, 2, 2, 384])
    at = K.buf("at", A + 76, [P, 2, T])
    heads = K.buf("heads", A + 78, [P, P])
    neg = K.buf("neg", A + 78.5, [P, 256])
    band = K.buf("band", A + 79.5, [P, 4, 384])
    pl = K.buf("pl", A + 86, [P, 4, T])
    pl_hi = K.buf("pl_hi", A + 90, [P, 4, T], F32R)
    pl_lo = K.buf("pl_lo", A + 94, [P, 4, T], F32R)
    cat_hi = K.buf("cat_hi", A + 98, [P, 8, T], F32R)
    cat_lo = K.buf("cat_lo", A + 106, [P, 8, T], F32R)
    pT = K.buf("pT", A + 114, [P, 2, 384])

    t_heads = K.load(heads[:, :], K.cst("heads"), after=after, queue=act)
    t_neg = K.load(neg[:, :], K.cst("neg"), after=after, queue=act)
    t_band = K.load(band[:, :, :], K.cst("band").rearrange("p (g t) -> p g t", g=4), after=after, queue=act)
    h = (norm.hi, norm.lo, norm.ready)
    st = {}
    r = norm.r
    twice = r.unsqueeze(1).to_broadcast([P, 2, T])
    waiting = []

    def later(evac):
        def f(n, bank, done):
            free = []
            todo = lambda: free.extend(evac(n, bank, done))
            if waiting is None:
                todo()
            else:
                waiting.append(todo)
            return free
        return f

    def evac_f(_, bank, done):
        t = dve.tt([done, st["r"]], f[:, 0, :], bank[0:8, 0:T], r[0:8, :], ALU.mult)
        st["f"] = act.act([t], f[:, 0, :], f[:, 0, :], ACT.Identity, bias=par[0:8, C_FB:C_FB + 1])
        return [t]

    def steps_c():
        x, w, p, z, z2 = (f[:, i, :] for i in range(5))
        t = dve.stt([st["f"]], w, x, -1.0, x, ALU.mult, ALU.min)
        for t in log1p_exp(dve, act, w, p, z, z2, t):
            yield
        t = dve.stt([t], w, x, 0.0, p, ALU.min, ALU.subtract)
        t = dve.do([t, dve.fill([], z2, 0.0)], lambda e: e.tensor_tensor_scan(c[:, :], w, z2, 0.0, ALU.add, ALU.add))
        t2 = dve.ts([t], nc[:, :], c[:, :], -1.0, ALU.mult)
        for _ in range(4):
            yield
        b = B[7]
        tt = pe.tr([t, b.free], ident, *[(b[:, 8 * i:8 * (i + 1)], c[:, P * i:P * (i + 1)]) for i in range(2)])
        t3 = dve.copy([tt], cT[:, :, :], b[:, 0:16].rearrange("p (i h) -> p i h", i=2))
        b.free = [t3]
        st["c"] = [t2, t3]
        yield

    q_made = [None] * 8
    sq_made = [None] * 8

    def evac_qk(half):
        def evac(pairno, bank, done):
            j = 4 * half + 2 * pairno
            t = dve.tt([done, st["r"]], q[:, j:j + 2, :], halves(bank[:, :]), twice, ALU.mult)
            q_made[j] = q_made[j + 1] = t
            sq_made[j] = sq_made[j + 1] = pool.tt([t], sq[:, j:j + 2, :], q[:, j:j + 2, :], q[:, j:j + 2, :], ALU.mult)
            return [t]
        return evac

    def rms():
        nonlocal waiting
        norm.sums()
        st["r"], (st["cols"], st["rT"]) = norm.keep(B[7])
        todo, waiting = waiting, None
        for t in todo:
            t()

    drain(layer(S, [("q", 0)], h, later(evac_qk(0)), dense), layer(S, ["hy_f"], h, later(evac_f), dense, steps=1))
    rms()
    evac = evac_qk(0)
    side = steps_c()
    side = weave(layer(S, [("q", 1)], h, lambda n, b, d: evac(1, b, d), dense), side, 1)
    side = weave(layer(S, [("k", 0), ("k", 1)], h, evac_qk(1), dense), side, 1)

    def qk_norm():
        b = B[6]
        for n in range(8):
            t = pe.mm([sq_made[n], t_heads, b.free if n == 0 else []], (b[0:16, 0:T], heads[:, 16 * n:16 * n + 16], sq[:, n, :], n == 0, n == 7))
        yield
        t = act.act([t], r16[:, :], b[0:16, 0:T], ACT.Sqrt, bias=par[0:16, C_QKE:C_QKE + 1])
        b.free = [t]
        t_r = dve.recip([t], r16[:, :], r16[:, :])
        yield
        for j in range(4):
            b = B[6 + j % 2]
            t = pe.mm([t_r, b.free], *[(b[64 * e:64 * (e + 1), T * m:T * (m + 1)],
                                        ident[0:16, 2 * (j + 4 * m) + e:2 * (j + 4 * m) + e + 1].to_broadcast([16, 64]), r16[:, :], m == 0, True)
                                       for m in range(2) for e in range(2)])
            out = []
            for m in range(2):
                n = j + 4 * m
                col = (C_QG, C_KG)[m]
                out.append(dve.stt([t, q_made[n]], q[:, n, :], q[:, n, :], par[:, col:col + 1], b[:, T * m:T * (m + 1)], ALU.mult, ALU.mult))
                q_made[n] = out[-1]
            b.free = out
            yield

    v_made, og_made, cat_ready = [None] * 2, [None] * 4, [None] * 8
    lg_free, pT_free, at_free = {}, [], [[], []]

    def attention():
        spans = ((0, P, 0), (P, 384, 1))
        p_made = {}

        def scores(j):
            calls = [[], []]
            for a, z, i in spans:
                for e in range(2):
                    n = 64 * e
                    calls[e].append((B[3 + e][:, a:z], q[n:n + 64, j, P * i:P * (i + 1)], q[n:n + 64, 4 + j, 0:z - a], a == 0, False))
            more = [[(B[3 + e][:, a:z], ident[0:8, 2 * j + e:2 * j + e + 1].to_broadcast([8, P]), nc[:, 0:z - a], False, True)
                     for a, z, i in spans] for e in range(2)]
            inter = [x for ab in zip(*calls) for x in ab]
            t = pe.mm([q_made[j], q_made[4 + j], st["c"], B[3].free, B[4].free], *inter, *more[0], *more[1])
            for e in range(2):
                h_, l = 2 * j + e, lg[:, j % 2, e, :]
                m = small[:, h_, :]
                made = []
                for a, z, i in spans:
                    made.append(dve.stt([t, st["c"], t_neg, lg_free.get((j - 2, e))], l[:, a:z], B[3 + e][:, a:z], cT[:, i, h_:h_ + 1],
                                        neg[:, 256 - (z - a):256], ALU.add, ALU.add))
                B[3 + e].free = made
                sums = []
                for a, z, i in spans:
                    t2 = dve.do([made[i]], lambda e_, l=l, a=a, z=z, i=i, m=m: e_.tensor_reduce(m[:, i:i + 1], l[:, a:z], AX, ALU.max, negate=True))
                    sums.append(act.act([t2], l[:, a:z], l[:, a:z], ACT.Exp, bias=m[:, i:i + 1], accum_out=m[:, 2 + i:3 + i]))
                t2 = dve.recip([sums], m[:, 4:6], m[:, 2:4])
                p_made[j, e] = [dve.ts([t2], l[:, a:z], l[:, a:z], m[:, 4 + i:5 + i], ALU.mult) for a, z, i in spans]

        def turn(j):
            for e in range(2):
                b = B[5 + e]
                t = pe.tr([p_made[j, e], b.free], ident, *[(b[:, P * n:P * (n + 1)], lg[:, j % 2, e, P * n:P * (n + 1)]) for n in range(3)])
                lg_free[j, e] = [t]
                t = act.act([t, pT_free], pT[:, e, :], b[:, 0:384])
                b.free = [t]
                p_made[j, e] = [t]

        def values(j):
            b = B[5]
            t = pe.mm([p_made[j, 0], p_made[j, 1], v_made, b.free],
                      *[(b[64 * e:64 * (e + 1), P * i:T], v[:, i, P * j + 64 * e:P * j + 64 * (e + 1)], pT[:, e, T * i:(T, 384)[i]], i == 0, i == 1)
                        for i in range(2) for e in range(2)])
            pT_free[:] = [t]
            m = j % 2
            t = dve.tt([t, og_made[j], at_free[m]], at[:, m, :], b[:, 0:T], og[:, j, :], ALU.mult)
            b.free = [t]
            cat_ready[j] = at_free[m] = split_x(K, cat_hi, cat_lo, j, at[:, m, :], [t])

        scores(0)
        yield
        scores(1)
        yield
        for j in range(4):
            turn(j)
            yield
            values(j)
            if j < 2:
                scores(j + 2)
            yield

    def evac_v(i, bank, done):
        v_made[i] = act.act([done, st["rT"]], v[:, i, :], bank[:, :], ACT.Copy, scale=st["cols"][:, i:i + 1])
        return [v_made[i]]

    u_made = [None] * 2

    def evac_u(i, bank, done):
        u_made[i] = act.act([done, st["rT"]], u[:, i, :], bank[:, :], ACT.Copy, scale=st["cols"][:, i:i + 1])
        return [u_made[i]]

    def evac_og(pairno, bank, done):
        o = og[:, 2 * pairno:2 * pairno + 2, :]
        t = dve.tt([done, st["r"]], o, halves(bank[:, :]), twice, ALU.mult)
        a = act.act([t], o, o, ACT.Tanh, scale=0.5)
        og_made[2 * pairno] = og_made[2 * pairno + 1] = pool.ts([a], o, o, 0.5, ALU.mult, 0.5, ALU.add)
        return [t]

    norm_qk = chained(side, qk_norm())
    weave(layer_across(S, [("v", 0), ("v", 1)], h, evac_v, dense), norm_qk, 1)
    drain(norm_qk)

    pl_ready = []

    def pooled():
        for g in range(4):
            b = dense[K.turn % 3]
            K.turn += 1
            t = pe.mm([u_made, t_band, b.free], (b[:, 0:T], u[:, 0, P * g:P * (g + 1)], band[:, g, 0:T], True, False),
                      (b[:, P:T], u[:, 1, P * g:P * (g + 1)], band[:, g, T:384], False, True))
            t = act.act([t], pl[:, g, :], b[:, 0:T])
            b.free = [t]
            pl_ready.append(split_x(K, pl_hi, pl_lo, g, pl[:, g, :], [t]))
            if g % 2:
                yield

    def mixed():
        s = S.take("pool")
        for g in range(4):
            b = dense[K.turn % 3]
            K.turn += 1
            wh, wl = s.hi[:, P * g:P * (g + 1)], s.lo[:, P * g:P * (g + 1)]
            t = pe.mm([s.ready, pl_ready[g], b.free], (b[:, 0:T], wh, pl_hi[:, g, :], True, False), (b[:, 0:T], wh, pl_lo[:, g, :], False, False),
                      (b[:, 0:T], wl, pl_hi[:, g, :], False, True))
            if g == 3:
                s.done.append(t)
            t = act.act([t], pl[:, g, :], b[:, 0:T], ACT.Copy, scale=par[:, C_PSC + g:C_PSC + g + 1])
            b.free = [t]
            cat_ready[4 + g] = split_x(K, cat_hi, cat_lo, 4 + g, pl[:, g, :], [t])
        yield

    x_ready = [None] * 8
    four = [B[0], B[1], B[2], B[7]]

    def project(n):
        s = S.take(("hy_out", n))
        for t, (_, k0, m0) in enumerate(s.tiles):
            k, m = k0 // P, m0 // P
            b = four[m // 2]
            o = b[:, T * (m % 2):T * (m % 2 + 1)]
            wh, wl = s.hi[:, P * t:P * (t + 1)], s.lo[:, P * t:P * (t + 1)]
            first, last = n == 0 and t % 2 == 0 and m % 2 == 0, n == 3 and t % 2 == 1
            tok = pe.mm([s.ready if t == 0 else [], b.free if first else [], cat_ready[k]],
                        (o, wh, cat_hi[:, k, :], first, False), (o, wh, cat_lo[:, k, :], False, False), (o, wl, cat_hi[:, k, :], False, last))
            if last and m % 2:
                i = slice(m - 1, m + 1)
                e = dve.tt([tok], x2[:, i, :], halves(b[:, :]), x2[:, i, :], ALU.add)
                b.free = [e]
                x_ready[m - 1] = x_ready[m] = e
                out(m // 2, x2, [e])
            if t % 4 == 3:
                if t == 15:
                    s.done.append(tok)
                yield

    S.lo_engines = (pool,)
    side = attention()
    next(side)
    dense = B[0:3]
    fill = chained(layer(S, [("og", 0)], h, evac_og, dense, steps=4), layer_across(S, [("u", 0), ("u", 1)], h, evac_u, dense), pooled(),
                   layer(S, [("og", 1)], h, lambda _, b, d: evac_og(1, b, d), dense, steps=4), mixed(), project(0), project(1))
    for n, _ in enumerate(fill):
        if n % 3 == 2:
            next(side, None)
    drain(side)
    drain(project(2), project(3))
    S.lo_engines = (dve,)
    return x2, x_ready


def ffn_norm(K, n):
    A = AREA
    spare = K.buf(f"g{n}_spare", A + 16, [P, 2, 2, T])
    return Rms(K, spare[:, 0, :, :], spare[:, 1, :, :], K.buf(f"g{n}_r", A + 24, [P, T])[:, :], C_FFN + 8 * n,
               K.buf(f"g{n}_hi", A, [P, 8, T], F32R), K.buf(f"g{n}_lo", A + 8, [P, 8, T], F32R))


def ffn(K, S, n, x, x_ready, norm, out, after=()):
    pe, act, dve, pool = K.pe, K.act, K.dve, K.pool
    B, A = K.banks, AREA
    dense = B[0:4]
    sg = K.buf(f"g{n}_sg", A + 25, [P, 2, 2, T])
    mid = K.buf(f"g{n}_mid", A + 29, [P, 2, T])
    m_hi = K.buf(f"g{n}_mhi", A + 48, [P, 22, T], F32R)
    m_lo = K.buf(f"g{n}_mlo", A + 70, [P, 22, T], F32R)
    h = (norm.hi, norm.lo, norm.ready)
    twice = norm.r.unsqueeze(1).to_broadcast([P, 2, T])
    m_ready = []
    free, sg_free = [[], []], [[], []]
    st = {}
    waiting = []
    K.turn += (3 - K.turn) % 4

    late, last = [], []

    def rest():
        for m, t in last:
            free[m % 2] = split_x(K, m_hi, m_lo, m, mid[:, m % 2, :], [t, after], pool)
            m_ready.append(free[m % 2])
        last.clear()
        for m, t in late:
            q = m % 2
            a = act.act([t], sg[:, q, 0, :], sg[:, q, 0, :], ACT.Silu)
            last.append((m, dve.tt([a, free[q]], mid[:, q, :], sg[:, q, 1, :], sg[:, q, 0, :], ALU.mult)))
            sg_free[q] = [last[-1][1]]
        late.clear()

    def evac(m, bank, done):
        rest()
        t = dve.tt([done, st["r"], sg_free[m % 2], after], sg[:, m % 2, :, :], halves(bank[:, :]), twice, ALU.mult)
        late.append((m, t))
        return [t]

    def later(m):
        def f(_, bank, done):
            if m > 1:
                return evac(m, bank, done)
            free = []
            waiting.append(lambda: free.extend(evac(m, bank, done)))
            return free
        return f

    for m in range(22):
        drain(layer(S, [("gate_up", n, m)], h, later(m), dense))
        if m == 1:
            norm.sums()
            st["r"], _ = norm.keep(B[7])
            for t in waiting:
                t()
    rest()
    rest()

    def evac_down(pairno, bank, done):
        o = x[:, 2 * pairno:2 * pairno + 2, :]
        t = dve.tt([done], o, halves(bank[:, :]), o, ALU.add)
        ready[2 * pairno] = ready[2 * pairno + 1] = t
        out(pairno, x, [t])
        return [t]

    ready = [None] * 8
    drain(layer(S, [("down", n, i) for i in range(11)], (m_hi, m_lo, m_ready), evac_down, dense, nk=22))
    return x, ready


def rwkv_norm(K):
    spare = K.buf("r_spare", AREA + 32, [P, 2, 2, T])
    return Rms(K, spare[:, 0, :, :], spare[:, 1, :, :])


def rwkv(K, S, x, x_ready, norm, out):
    pe, act, dve, pool = K.pe, K.act, K.dve, K.pool
    B, A, Q = K.banks, AREA, RING_KB + 8 * NARROW
    par, ident = K.par, K.c["ident"]
    dense = B[0:4]

    h = K.buf("r_h", A, [P, 8, T])
    xx = K.buf("r_xx", A + 8, [P, 8, T])
    mixes = {c: K.buf(f"mix_{c}", kb, [P, 8, T]) for c, kb in dict(w=A + 48, a=A + 56, k=Q + 16, r=A + 16, v=A + 24, g=A + 48).items()}
    mix_hi = {c: K.buf(f"hi_{c}", kb, [P, 8, T], F32R) for c, kb in dict(r=A + 56).items()}
    mix_lo = {c: K.buf(f"lo_{c}", kb, [P, 8, T], F32R) for c, kb in dict(r=A + 16).items()}
    ar = K.buf("ar", A + 64, [P, 8, 512])
    bk = K.buf("bk", A + 80, [P, 8, 512])
    sig = K.buf("r_sig", A + 72, [P, 8, T])
    lora = K.buf("lora", A + 104.25, [P, 2, T])
    sum16 = K.buf("sum16", A + 116, [P, P])
    cmask = K.buf("cmask", A + 116.5, [P, 256])
    cols = K.buf("r_cols", A + 117.5, [P, 8])
    Pt = K.buf("Pt", A + 96, [P, 8, 260])
    kkn = [K.buf(f"kkn{i}", kb, [P, 2 * T]) for i, kb in enumerate((A + 108.25, A + 38))]
    sq = K.buf("r_sq", A + 34, [P, 2, T])
    tmp = [[K.buf(f"r_tmp{i}{q}", kb + 2 * q, [P, 2 * T]) for q in range(2)] for i, kb in enumerate((A + 48, A + 112))]
    inv = K.buf("r_inv", A + 36, [P, 2, 16])
    going = K.buf("r_going", A + 110.25, [P, T])
    k_raw = K.buf("k_raw", Q, [P, 8, T])
    iP = K.buf("iP", Q + 8, [P, 8, T])
    PL = K.buf("PL", A + 117.53125, [P, 8, 4])

    def both(buf, j, n, which):
        ap = buf[:, j:j + n, :]
        return bass.AP(tensor=ap.tensor, offset=ap.offset + 64 * which, ap=[list(ap.ap[0]), [256, 2 * n], [64 if which else 192, 2], [1, 64]])

    quads = lambda ap: ap.rearrange("p (i q t) -> p i q t", q=2, t=64)
    flat2 = lambda buf, j: buf[:, j:j + 2, :].rearrange("p j t -> p (j t)")

    t_sum = K.load(sum16[:, :], K.cst("sum16"), after=x_ready, queue=act)
    t_mask = K.load(cmask[:, :], K.cst("chunk"), after=x_ready, queue=act)
    t_going = pool.fill([x_ready], going[:, :], 1.0)
    t_going = pool.fill([t_going], going[:, 0:T:64], 0.0)
    t_one = pool.fill([x_ready], Pt[:, :, :].rearrange("p j (c t) -> p j c t", c=4)[:, :, :, 0], 1.0)
    t_omka = pool.ts([K.t_par], cols[:, :], par[:, C_KA:C_KA + 8], -1.0, ALU.mult, 1.0, ALU.add)
    (rr, t_r), _ = norm.finish(B[7], [norm.total[:, 0, :], norm.total[:, 1, :], norm.sq[:, 0, :], norm.sq[:, 1, :]])
    h_made, xx_made = [None] * 8, [None] * 8
    mixed = {c: [None] * 8 for c in "rwkvag"}

    def shift(n):
        pair = slice(2 * n, 2 * n + 2)
        for j in (2 * n, 2 * n + 1):
            m = C_MIX + 8 + j
            h_made[j] = dve.stt([t_r], h[:, j, :], x[:, j, :], par[:, m:m + 1], rr, ALU.mult, ALU.mult)
        a = pool.ts([h_made[pair]], xx[:, pair, 0:1], h[:, pair, 0:1], -1.0, ALU.mult)
        b = (pool if n else dve).tt([h_made[pair]], xx[:, pair, 1:T], h[:, pair, 0:T - 1], h[:, pair, 1:T], ALU.subtract)
        xx_made[2 * n] = xx_made[2 * n + 1] = [a, b]

    def mix(c, after=()):
        for n in range(4):
            for j in (2 * n, 2 * n + 1):
                m = C_MU + 8 * "rwkvag".index(c) + j
                mixed[c][j] = dve.stt([h_made[j], xx_made[j], after], mixes[c][:, j, :], xx[:, j, :], par[:, m:m + 1], h[:, j, :], ALU.mult, ALU.add)
            yield

    def halve(c, after=()):
        pairs = [slice(2 * n, 2 * n + 2) for n in range(4)]
        made = [act.act([mixed[c][pair], after], mix_hi[c][:, pair, :], mixes[c][:, pair, :]) for pair in pairs]
        for pair, a in zip(pairs, made):
            b = dve.tt([a], mix_lo[c][:, pair, :], mixes[c][:, pair, :], mix_hi[c][:, pair, :].bitcast(F32), ALU.subtract)
            mixed[c][pair] = [[a, b]] * 2
            yield

    def product(c):
        return (mix_hi[c], mix_lo[c], mixed[c]) if c in mix_hi else (mixes[c], None, mixed[c])

    first = mix("w")
    shift(0)
    for n in range(4):
        if n < 3:
            shift(n + 1)
        next(first)
    B[7].free = [h_made]
    drain(mix("a"), mix("k"))
    st = {}
    S.lead = 1

    def last():
        return [S.slots[S.next - 1].done]

    low_made = {}
    sig_made, a_made = [None] * 8, [None] * 8

    def evac_lora(n, func):
        def evac(_, bank, done):
            low_made[n] = act.act([done], lora[:, n, :], bank[:, 0:T], func)
            return [low_made[n]]
        return evac

    def evac_sig(dst, col, made):
        def evac(pairno, bank, done):
            for i in range(2):
                j = 2 * pairno + i
                made[j] = act.act([done], dst(j), quads(bank[:, T * i:T * (i + 1)]), ACT.Sigmoid, bias=par[:, col + j:col + j + 1])
            return [made[2 * pairno], made[2 * pairno + 1]]
        return evac

    drain(layer(S, ["wa1"], product("w"), evac_lora(0, ACT.Tanh), dense, steps=1, half=0))
    drain(layer(S, ["wa1"], product("a"), evac_lora(1, ACT.Copy), dense, steps=1, half=1))
    t_low1 = last()
    drain(layer(S, ["wa2"], (lora, None, [low_made[0]]), evac_sig(lambda j: quads(sig[:, j, :]), C_W0, sig_made), dense, nk=1, steps=1, half=0))
    drain(layer(S, ["wa2"], (lora[:, 1:2, :], None, [low_made[1]]), evac_sig(lambda j: both(bk, j, 1, 1), C_A0, a_made), dense, nk=1, steps=1, half=1))
    t_low2 = last()

    cdec = float(np.exp(-0.5))
    alpha, beta, kappa, rho, P_made, iP_made, PL_made = ([None] * 4 for _ in range(7))
    steps_of = Pt[:, :, :].rearrange("p j (c t) -> p j c t", c=4)
    logs = [dve.do([sig_made[j], t_going], lambda e, j=j: e.tensor_tensor_scan(
        sig[:, j, :], going[:, :], sig[:, j, :], 0.0, ALU.mult, ALU.add)) for j in range(8)]
    drain(mix("r"))
    for n in range(4):
        pair = slice(2 * n, 2 * n + 2)
        decay = Pt[:, pair, :].rearrange("p j (i q t) -> p (j i) q t", i=2, q=2)
        P_made[n] = tp = act.act([logs[pair], t_one], decay[:, :, :, 1:65], quads(flat2(sig, 2 * n)), ACT.Exp, scale=-cdec)
        ti = act.act([logs[pair]], flat2(iP, 2 * n), flat2(sig, 2 * n), ACT.Exp, scale=cdec)
        iP_made[n] = [tp, ti]
        PL_made[n] = pool.copy([tp], PL[:, pair, :], steps_of[:, pair, :, 64])

    drain(halve("r", t_low1), mix("v"))

    k_made, sq_free = [None] * 8, [t_r]

    def evac_k(n):
        def evac(_, bank, done):
            nonlocal sq_free
            j = 2 * n
            t = act.act([done], k_raw[:, j:j + 2, :], halves(bank[:, :]))
            k_made[j] = k_made[j + 1] = t
            made = [act.act([done, sq_free], sq[:, i, :], bank[:, T * i:T * (i + 1)], ACT.Square, scale=par[:, C_KK + j + i:C_KK + j + i + 1]) for i in range(2)]
            st["sq", n] = made
            sq_free = []
            return [t, made]
        return evac

    def root(n):
        nonlocal sq_free
        ss, o = B[4 + n % 2], inv[:, :, 4 * n:4 * n + 4]
        t = pe.mm([st["sq", n], t_sum, ss.free], *[
            (ss[:, 4 * i + 2 * m:4 * i + 2 * m + 2], sq[:, m, P * i:P * (i + 1)], sum16[:, 18 * (2 * n + m):18 * (2 * n + m) + 2], i + m == 0, True)
            for m in range(2) for i in range(2)])
        sq_free = [t]
        ss.free = t = act.act([t], o, ss[:, 0:8].rearrange("p (i h) -> p i h", i=2), ACT.Sqrt)
        t = dve.ts([t], o, o, 1e-12, ALU.max)
        return dve.recip([t], o, o)

    kkn_free, tmp_free = [[], []], [[], []]

    def prepare(n):
        t_inv = st["inv"] = root(n)
        j, q = 2 * n, n % 2
        decay = Pt[:, j:j + 2, :].rearrange("p j (i q t) -> p (j i) q t", i=2, q=2)
        inverse = quads(flat2(iP, j))
        tk, tb = tmp[q][0][:, :], tmp[q][1][:, :]
        tka = []
        for i in range(2):
            o, c = slice(T * i, T * (i + 1)), j + i
            tka.append(act.act([a_made[c], t_omka, t_low1, tmp_free[q]], quads(tk[:, o]), both(bk, c, 1, 1), ACT.Identity,
                               scale=par[:, C_KA + c:C_KA + c + 1], bias=cols[:, c:c + 1]))
        t = dve.tt([tka, k_made[j]], tk, tk, flat2(k_raw, j), ALU.mult)
        kappa[n] = dve.tt([t, iP_made[n]], both(bk, j, 2, 0), quads(tk), inverse, ALU.mult)
        yield
        b = B[6 + q]
        t = pe.mm([t_inv, b.free], *[
            (b[64 * e:64 * (e + 1), T * m + P * i:T * m + P * (i + 1)],
             inv[:, i, 2 * (j + m) + e:2 * (j + m) + e + 1].to_broadcast([P, 64]), ident[:, :], m + i == 0, True)
            for m in range(2) for i in range(2) for e in range(2)])
        kk = []
        for i in range(2):
            o, c = slice(T * i, T * (i + 1)), j + i
            kk.append(dve.stt([t, k_made[c], kkn_free[q]], kkn[q][:, o], k_raw[:, c, :], par[:, C_KK + c:C_KK + c + 1], b[:, o], ALU.mult, ALU.mult))
        b.free = kk
        t = dve.tt([kk, a_made[j:j + 2], tmp_free[q]], quads(tb), quads(kkn[q][:, :]), both(bk, j, 2, 1), ALU.mult)
        alpha[n] = dve.stt([kk, iP_made], both(ar, j, 2, 1), quads(kkn[q][:, :]), -1.0, decay[:, :, :, 0:64], ALU.mult, ALU.mult)
        beta[n] = dve.tt([t, iP_made[n], tka], both(bk, j, 2, 1), quads(tb), inverse, ALU.mult)
        kkn_free[q] = [alpha[n], t]
        tmp_free[q] = [kappa[n], beta[n]]
        yield

    drain(layer(S, [("rw_k", 0)], product("k"), evac_k(0), dense))
    for n in range(3):
        part = layer(S, [("rw_k", n + 1)], product("k"), evac_k(n + 1), dense, steps=8)
        side = prepare(n)
        for i, _ in enumerate(part):
            if i in (1, 3):
                next(side)
            if i == 4:
                S.ahead(S.find(("rw_r", n)).index + 1)
    t_k = last()

    def evac_r(n):
        def evac(_, bank, done):
            decay = Pt[:, 2 * n:2 * n + 2, :].rearrange("p j (i q t) -> p (j i) q t", i=2, q=2)
            rho[n] = dve.tt([done, iP_made], both(ar, 2 * n, 2, 0), quads(bank[:, :]), decay[:, :, :, 1:65], ALU.mult)
            return [rho[n]]
        return evac

    ur = lambda c: slice(64 * (1 - c % 2), 64 * (2 - c % 2))
    vr = lambda c: slice(64 * (c % 2), 64 * (c % 2) + 64)
    UV = K.buf("UV", A + 96, [P, 4, D])
    bv = K.buf("bv", A, [P, 2, D])
    g = K.buf("r_g", A + 8, [P, 2, D])
    stat = K.buf("stat", 10 - 0.25, [P, 2, 32])
    bonus = K.buf("bonus", A + 117.65625, [P, 2, 16])
    V_made = [[[], []] for _ in range(4)]
    bv_made, g_made = [[[], []], [[], []]], [[], []]
    raw_done = [rho, alpha, P_made]
    held = []

    def evac_v(n):
        def evac(i, bank, done):
            held.append((i, n, bank, done))
            return []
        return evac

    def center():
        per = lambda ap: ap.rearrange("p (h v) -> p h v", h=8)
        for i, n, bank, done in held:
            o, mean = slice(512 * n, 512 * (n + 1)), stat[:, i, 8 * n:8 * n + 8]
            t = dve.do([done, bank.free], lambda e, mean=mean, bank=bank: e.tensor_reduce(mean, per(bank[:, :]), AX, ALU.add))
            made = []
            for c in (2 * i, 2 * i + 1):
                V_made[c][n] = dve.stt([t, raw_done], per(UV[vr(c), c, o]), mean[vr(c)].unsqueeze(2).to_broadcast([64, 8, 64]), -1.0 / 64,
                                       per(bank[vr(c), :]), ALU.mult, ALU.add)
                made.append(V_made[c][n])
            t = dve.tt([done, mixed["g"], t_bonus], per(bv[:, i, o]), per(bank[:, :]), bonus[:, i, 8 * n:8 * n + 8].unsqueeze(2).to_broadcast([P, 8, 64]), ALU.mult)
            bv_made[i][n] = t
            bank.free = [made, t]
            yield

    LT = K.buf("LT", A + 32, [P, 2, 16, 64])
    Zb = K.buf("Zb", A + 112, [P, 32, 32])
    Tm = K.buf("Tm", Q + 12, [P, 32, 32])
    prod = K.buf("r_prod", Q + 8, [P, 1024])
    TT = K.buf("TT", Q, [P, 32, 64])
    T11 = K.buf("T11", Q + 8, [P, 32, 32])
    strict = cmask[:, 64:128]
    lt_made = []
    every, upper, second = slice(0, P), [slice(0, 32), slice(64, 96)], [slice(32, 64), slice(96, P)]
    t_TT = []

    def turn(after, out, out_dims, in_, in_dims, rows):
        return dve.do(after, lambda e: e.transpose(out.rearrange(out_dims)[rows], in_.rearrange(in_dims)[rows]))

    def pairs_of_tokens():
        for i in range(2):
            for e in range(2):
                b, r_, calls = B[4 + 2 * i + e], slice(64 * e, 64 * e + 64), []
                for j in range(8):
                    for q in range(2):
                        o = 128 * (2 * i + q) + 64 * (1 - q)
                        calls.append((b[ur(q), 64 * j:64 * (j + 1)], bk[r_, j, o:o + 64], ar[r_, j, o:o + 64], j == 0, True))
                t = pe.mm([alpha, beta, b.free], *calls)
                yield
                t = dve.tt([t, t_mask], LT[:, i, e::2, :], b[:, :].rearrange("p (h t) -> p h t", h=8),
                           strict.unsqueeze(1).to_broadcast([P, 8, 64]), ALU.mult)
                b.free = [t]
                lt_made.append(t)
        t = [pool.fill([beta, kappa], Tm[:, :, :], 0.0)]
        st["unit"] = t = [pool.fill(t, Tm[:, :, :].rearrange("p i c -> p (i c)")[:, 0:1024:33], 1.0)]
        st["zero"] = [pool.fill(t, TT[:, :, 0:32], 0.0)]
        yield
        t = []
        for rows in (every, *second):
            half = 32 * (rows is not every)
            t = turn([lt_made, kappa, t], Zb[:, :, :], "p s t -> p t s", LT[:, :, :, half:half + 32], "p i h t -> p t (i h)", rows)
        st["Z"] = t
        yield

    def invert():
        t = [st["unit"], st["Z"]]
        for j in range(31):
            m, n = 31 - j, j + 1
            o = prod[:, 0:m * n].rearrange("p (i c) -> p i c", i=m)
            t = dve.tt(t, o, Zb[:, j, n:32].unsqueeze(2).to_broadcast([P, m, n]), Tm[:, j, 0:n].unsqueeze(1).to_broadcast([P, m, n]), ALU.mult)
            t = dve.tt([t], Tm[:, n:32, 0:n], Tm[:, n:32, 0:n], o, ALU.add)
            yield
        t11 = turn([t], T11[:, :, :], "p h s -> p s h", Tm[:, :, :], "p m s -> p s m", every)
        t = [t11, st["zero"]]
        for rows in (every, *upper):
            half = 32 * (rows is every)
            t = turn([t], TT[:, :, half:half + 32], "p h t -> p t h", Tm[:, :, :], "p t s -> p t s", rows)
        t_TT.extend([t11, t])

    rk_in = [K.buf(f"rk{n}", A + 16 + 2 * n, [P, 2 * T])[:, :] for n in range(2)]

    def bonuses():
        v = sum16[:, :].rearrange("p (j h) -> p j h", j=8)
        t_rk = pool.tt([st["inv"]], v, v, par[:, C_RK:C_RK + 8].unsqueeze(2).to_broadcast([P, 8, 16]), ALU.mult)
        b = B[7]
        t = []
        for half in range(2):
            made = [pool.tt([rho, kappa, beta, t], quads(rk_in[n % 2]), both(ar, 2 * n, 2, 0), both(bk, 2 * n, 2, 0), ALU.mult)
                    for n in (2 * half, 2 * half + 1)]
            yield
            t = pe.mm([made, t_rk, b.free if half == 0 else []], *[
                (b[:, 16 * i:16 * (i + 1)], rk_in[n][:, T * f + P * i:T * f + P * (i + 1)], sum16[:, 16 * (4 * half + 2 * n + f):16 * (4 * half + 2 * n + f) + 16],
                 half + n + f + i == 0, half + n + f == 3) for n in range(2) for f in range(2) for i in range(2)])
            yield
        st["rk"] = [t]
        st["bonus"] = act.act([t], bonus[:, :, :], b[:, 0:32].rearrange("p (i h) -> p i h", i=2))
        b.free = [st["bonus"]]

    def beside(main, *sides):
        for i, _ in enumerate(main):
            for side, start, per in sides:
                for _ in range(int(per * (i + 1 - start)) - int(per * (i - start)) if i >= start else 0):
                    next(side, None)

    Gm = [K.buf(f"Gm{c}", (A + 56, A + 16, A + 48, A + 56)[c], [P, 16, P]) for c in range(4)]
    G_made = [[], [], [], []]
    ring = B[6:8]

    def spot():
        K.turn += 1
        return ring[K.turn % len(ring)]

    def products(c, after, eng):
        m = cmask[:, P * (c % 2):P * (c % 2 + 1)]
        for n in range(4):
            b, calls = spot(), []
            e, h0 = n % 2, n // 2 * 8 + n % 2
            r_ = slice(64 * e, 64 * e + 64)
            for f in range(4):
                j = n // 2 * 4 + f
                calls.append((b[:, P * f:P * (f + 1)], bk[r_, j, P * c:P * (c + 1)], ar[r_, j, P * c:P * (c + 1)], f == 0, True))
            t = pe.mm([rho, kappa, b.free], *calls)
            o, f = Gm[c][:, h0:h0 + 7:2, :], b[:, :].rearrange("p (h t) -> p h t", h=4)
            if eng is pool:
                b.free = t = act.act([t, after], o, f)
                f = o
            t = eng.tt([t, after], o, f, m.unsqueeze(1).to_broadcast([P, 4, P]), ALU.mult)
            if eng is dve:
                b.free = [t]
            G_made[c].append(t)
            yield

    bkT = [K.buf(f"bkT{c}", kb, [P, 8, P]) for c, kb in enumerate((A + 112, Q + 12, Q + 16))]
    bkT_made = [[], [], []]

    def turned(c, after):
        for n in range(2):
            b = spot()
            t = pe.tr([beta, kappa, b.free], ident, *[(b[:, P * f:P * (f + 1)], bk[:, 4 * n + f, P * c:P * (c + 1)]) for f in range(4)])
            t = act.act([t, after], bkT[c][:, 4 * n:4 * n + 4, :], b[:, :].rearrange("p (j k) -> p j k", j=4))
            b.free = [t]
            bkT_made[c].append(t)
            yield

    scaled = [[], [], [], []]

    def scale(c):
        o = ar[:, :, P * c:P * (c + 1)]
        scaled[c] = [dve.tt([G_made[c], lt_made, st["rk"], PL_made], o, o, PL[:, :, c - 1:c].to_broadcast([P, 8, P]), ALU.mult)]
        yield

    R0 = K.buf("R0", Q + 8, [P, D])
    SB = K.buf("SB", Q + 20, [P, 8, P])
    up = lambda q: upper[1 - q]
    low = lambda q: second[1 - q]
    TT_made = [[], []]
    t_W = []

    def lower():
        t11 = [None] * 2
        for i in range(2):
            b = B[4 + i]
            t = pe.mm([t_TT[0], lt_made, b.free], *[(b[low(q), 32 * n:32 * n + 32], LT[up(q), i, n, 32:64], T11[up(q), 16 * i + n, :], n == 0, True)
                                                    for n in range(16) for q in range(2)])
            made = []
            for q in range(2):
                o, f = T11[low(q), 16 * i:16 * i + 16, :], b[low(q), :].rearrange("p (h c) -> p h c", h=16)
                made.append(dve.copy([t, made], o, f) if q else act.act([t], o, f))
            b.free = t11[i] = made
            yield
        for i in range(2):
            b = B[4 + i]
            t = pe.mm([t11[i], t_TT[0:2], b.free], *[(b[up(q), 32 * n:32 * n + 32], T11[low(q), 16 * i + n, :], TT[low(q), 16 * i + n, 32:64], n == 0, True)
                                                      for n in range(16) for q in range(2)])
            made = []
            for q in range(2):
                o, f = TT[up(q), 16 * i:16 * i + 16, 32:64], b[up(q), :].rearrange("p (h c) -> p h c", h=16)
                made.append(dve.copy([t, made], o, f) if q else act.act([t], o, f))
            b.free = made
            TT_made[i] = [t_TT, made]
            t_W[:] = [t]
            yield

    gl = K.buf("r_gl", Q + 16, [P, 2, T])
    lnw, lnb = (K.buf(n, A + 24 + kb, [P, D]) for n, kb in (("lnw", 0), ("lnb", 4)))
    gl_made = []

    def evac_gl(_, bank, done):
        gl_made.append(act.act([done, rho], gl[:, :, :], halves(bank[:, :]), ACT.Sigmoid))
        return gl_made[-1:]

    gw_made, gb_made = [None] * 2, [None] * 2

    def gate():
        s = S.take("g2")
        for i in range(2):
            for n in range(2):
                bank = spot()
                t, calls = slice(P * i, P * (i + 1)), []
                for k in range(2):
                    w = slice(D * k + 512 * n, D * k + 512 * (n + 1))
                    calls.append((bank[:, :], gl[:, k, t], s.raw[:, w], k == 0, k == 1))
                t = pe.mm([s.ready, gl_made, bank.free], *calls)
                bank.free = [act.act([t, mixed["g"]], g[:, i, 512 * n:512 * (n + 1)], bank[:, :])]
                g_made[i].append(bank.free)
                if n == 0:
                    yield
            t1 = pool.tt([t_ln, bv_made[i]], bv[:, i, :], bv[:, i, :], lnb[:, :], ALU.add)
            gb_made[i] = pool.tt([t1, g_made[i]], bv[:, i, :], bv[:, i, :], g[:, i, :], ALU.mult)
            gw_made[i] = pool.tt([gb_made[i], t_ln], g[:, i, :], g[:, i, :], lnw[:, :], ALU.mult)
            if i:
                s.done.append(t)
                st["g2"] = [t]
            yield

    y = K.buf("r_y", A + 32, [P, 2, D])
    ysq = K.buf("ysq", A + 112, [P, D])
    o_hi = K.buf("o_hi", A + 80, [P, 8, T], F32R)
    o_lo = K.buf("o_lo", A + 88, [P, 8, T], F32R)
    out_made, o_ready = [[None, None], [None, None]], [[] for _ in range(8)]
    y_made, y_sq = [[None, None], [None, None]], [[], []]

    def weighed(i, half, after):
        o = slice(512 * half, 512 * (half + 1))
        rows = slice(0, P) if i == 0 else vr(2)
        y_sq[i].append(act.act([y_made[i][half], after], ysq[rows, o], y[rows, i, o], ACT.Square))
        y_made[i][half] = [pool.tt([y_made[i][half], gw_made[i], y_sq[i]], y[rows, i, o], y[rows, i, o], g[rows, i, o], ALU.mult)]

    def normed(i, half):
        h8, o = slice(8 * half, 8 * half + 8), slice(512 * half, 512 * (half + 1))
        per = lambda ap: ap.rearrange("p (h v) -> p h v", h=8)
        std = stat[:, i, 16 + 8 * half:24 + 8 * half]
        yi = y[:, i, o]
        st["summed"] = t = dve.do([y_sq[i]], lambda e: e.tensor_reduce(std, per(ysq[:, o]), AX, ALU.add))
        t = act.act([t], std, std, ACT.Sqrt, scale=1.0 / 64, bias=par[:, C_EPS + 2:C_EPS + 3])
        yield
        t = dve.recip([t], std, std)
        t = dve.tt([t, y_made[i][half]], per(yi), per(yi), std.unsqueeze(2).to_broadcast([P, 8, 64]), ALU.mult)
        out_made[i][half] = t
        yield

    turned_back = [[None, None], [None, None]]

    def bases(i, half):
        bank = B[6 - 2 * i + half]
        turned_back[i][half] = bank, pe.mm([gb_made[i], bank.free], *[
            (bank[:, P * f:P * (f + 1)], bv[:, i, P * (4 * half + f):P * (4 * half + f + 1)], ident[:, :], f == 0, False) for f in range(4)])
        yield

    def outs(i, half):
        b, t = turned_back[i][half]
        t = pe.mm([out_made[i][half], t], *[
            (b[:, P * f:P * (f + 1)], y[:, i, P * (4 * half + f):P * (4 * half + f + 1)], ident[:, :], False, True) for f in range(4)])
        yield
        src = b[:, :].rearrange("p (j t) -> p j t", j=4)
        hi, lo = (o[:, 4 * half:4 * half + 4, P * i:P * (i + 1)] for o in (o_hi, o_lo))
        ta = act.act([t, bkT_made, G_made], hi, src)
        tb = dve.tt([ta], lo, src, hi.bitcast(F32), ALU.subtract)
        b.free = [ta, tb]
        for f in range(4):
            o_ready[4 * half + f] += [ta, tb]
        yield

    hs = lambda half: range(8 * half, 8 * half + 8)
    U_made = [[[], []] for _ in range(4)]
    ry = lambda c, half: B[2 * (c % 2) + half]

    def values(c):
        for half in range(2):
            b = ry(c, half)
            st["av", c, half] = pe.mm([G_made[c], V_made[c], b.free], *[
                (b[r_, 64 * (n % 8):64 * (n % 8) + 64], Gm[c][vr(c), n, r_], UV[vr(c), c, 64 * n:64 * n + 64], n % 8 == 0, c == 0)
                for n in hs(half) for r_ in [slice(0, P) if n % 8 == 0 else ur(c)]])
            yield

    inverse = chained(pairs_of_tokens(), invert())
    part = layer(S, [("rw_r", 0)], product("r"), evac_r(0), B[0:4], steps=8)
    side = prepare(3)
    for i, _ in enumerate(part):
        if i in (1, 3):
            next(side)
    S.ahead(S.find(("rw_r", 3)).index + 1)
    mixing = mix("g", [beta, kappa])
    beside(layer(S, [("rw_r", 1)], product("r"), evac_r(1), B[0:4], steps=8), (inverse, 0, 1), (mixing, 0, 1))
    for n in range(2, 4):
        beside(layer(S, [("rw_r", n)], product("r"), evac_r(n), B[0:4], steps=8), (inverse, 0, 0.5))
    K.turn += -K.turn % 4
    bonus_steps = bonuses()
    beside(layer_across(S, [("rw_v0", 0), ("rw_v0", 1)], product("v"), evac_v(0), B[0:4]), (inverse, 0, 2), (bonus_steps, 0, 1))
    drain(bonus_steps)
    t_bonus = st["bonus"]
    centered = center()
    more = chained(products(0, rho, pool), turned(0, t_TT))
    levels = lower()
    beside(layer_across(S, [("rw_v1", 0), ("rw_v1", 1)], product("v"), evac_v(1), B[0:4]), (inverse, 0, 4), (more, 0, 1), (centered, 6, 1), (levels, 6, 1))
    t_v = last()
    t_ln = [K.load(o[:, :], K.ins["rw_ln"][n:n + 1, :].to_broadcast([P, D]), after=t_v, queue=act) for n, o in enumerate((lnw, lnb))]
    ring.pop()
    first = chained(values(0), products(1, st["rk"], dve))
    beside(layer(S, ["g1"], product("g"), evac_gl, B[7:8], steps=8), (levels, 0, 1), (centered, 0, 1), (more, 1, 1), (first, 3, 1))
    t_g1 = last()
    ring.append(B[7])
    t_SB = pool.fill([st["rk"], rho, t_g1], SB[:, :, :], 0.0)
    drain(levels, centered, more)

    R0_free, SB_made = [t_W], [t_SB, t_SB]
    second_made = chained(turned(1, t_TT), scale(1))
    gates = gate()
    filler = {(0, 0): ((first, 9), (gates, 1)), (0, 1): ((gates, 1),), (0, 2): ((second_made, 3),), (0, 3): ((values(1), 2),)}

    def fill(c, place):
        for gen, n in filler.get((c, place), ()):
            for _ in range(n):
                next(gen, None)

    for c in range(4):
        i = c // 2
        R0_made, S_read = [], []
        for half in range(2):
            b = ry(c, half)
            t = st["av", c, half]
            if c:
                t = pe.mm([SB_made[half], scaled[c], t], *[(b[:, P * f:P * (f + 1)], ar[:, 4 * half + f, P * c:P * (c + 1)], SB[:, 4 * half + f, :], False, False) for f in range(4)])
                S_read.append(t)
            o = R0[ur(c), 512 * half:512 * (half + 1)]
            R0_made.append(act.act([t, R0_free], o, b[ur(c), :]) if half else dve.copy([t, R0_free], o, b[ur(c), :]))
        if c and c < 3:
            for half in range(2):
                v = SB[:, 4 * half:4 * half + 4, :]
                SB_made[half] = [pool.tt([S_read[half]], v, v, PL[:, 4 * half:4 * half + 4, c - 1:c].to_broadcast([P, 4, P]), ALU.mult)]
        fill(c, 0)
        for half in range(2):
            b = ry(c, half)
            t = pe.mm([R0_made[half], TT_made[i]], *[
                (b[ur(c), 64 * (n % 8):64 * (n % 8) + 64], TT[ur(c), 16 * i + n, :], R0[ur(c), 64 * n:64 * n + 64], n % 8 == 0, True) for n in hs(half)])
            o = UV[ur(c), c, 512 * half:512 * (half + 1)]
            U_made[c][half] = act.act([t, raw_done], o, b[ur(c), :]) if half else dve.copy([t, raw_done], o, b[ur(c), :])
        R0_free = U_made[c]
        fill(c, 1)
        if c < 3:
            for half in range(2):
                b = B[4 + half]
                t = pe.mm([U_made[c][half], bkT_made[c][half], V_made[c], b.free], *[
                    (b[:, P * f:P * (f + 1)], bkT[c][:, 4 * half + f, :], UV[:, c, P * (4 * half + f):P * (4 * half + f + 1)], f == 0, True) for f in range(4)])
                made = []
                for e in range(2):
                    r_ = slice(64 * e, 64 * e + 64)
                    o = SB[r_, 4 * half:4 * half + 4, r_]
                    f = b[r_, :].rearrange("p (j k) -> p j k", j=4)[:, :, r_]
                    made.append(dve.tt([t, SB_made[half]], o, f, o, ALU.add) if c else dve.copy([t, SB_made[half]], o, f))
                b.free = SB_made[half] = made
        fill(c, 2)
        if c < 3:
            S.ahead(S.find(("rw_o", c)).index + 1)
        for half in range(2):
            b, o = ry(c, half), slice(512 * half, 512 * (half + 1))
            t = pe.mm([U_made[c][half], R0_made[half]], *[
                (b[vr(c), 64 * (n % 8):64 * (n % 8) + 64], Gm[c][r_, n, vr(c)], UV[r_, c, 64 * n:64 * n + 64], False, True)
                for n in hs(half) for r_ in [ur(c) if n % 8 == 0 else slice(0, P)]])
            if c < 3:
                b.free = t = act.act([t, t_W], y[vr(c), i, o], b[vr(c), :])
                y_made[i][half] = [y_made[i][half], t]
            else:
                st["y", half] = t
        if c == 0:
            two, three = products(2, t_g1, dve), products(3, t, dve)
            filler[1, 0] = filler[1, 1] = ((gates, 1),)
            filler[1, 2] = (two, 5), (scale(2), 1)
        if c == 1:
            filler[1, 3] = (turned(2, st["g2"]), 2), (values(2), 2)
            filler[2, 0] = filler[2, 1] = ((three, 2),)
            filler[2, 2] = (three, 1), (scale(3), 1)
            filler[2, 3] = (values(3), 2),
        fill(c, 3)
        if c == 1:
            for half in range(2):
                weighed(0, half, [])
            filler[2, 0] += ((normed(0, 0), 2),)
            filler[2, 1] += ((normed(0, 1), 2),)
        if c == 2:
            for half in range(2):
                weighed(1, half, st["summed"])
            filler[3, 0] = ((chained(bases(0, 0), bases(0, 1)), 2),)
            back = [[outs(i, half) for half in range(2)] for i in range(2)]
            filler[3, 1] = (back[0][0], 1), (back[0][1], 1)
            filler[3, 3] = ((chained(bases(1, 0), bases(1, 1)), 2),)
    rows, after = vr(3), [[], []]
    for half in range(2):
        for n, eng in ((half, act), (1 - half, dve)):
            b, o = ry(3, n), slice(512 * n, 512 * (n + 1))
            if eng is act:
                t = act.act([st["y", n], after[n]], ysq[rows, o], b[rows, :], ACT.Square)
                y_sq[1].append(t)
            else:
                t = dve.tt([st["y", n], after[n], gw_made[1]], y[rows, 1, o], b[rows, :], g[rows, 1, o], ALU.mult)
                y_made[1][n] = [y_made[1][n], t]
            after[n] = b.free = [after[n], t]
    for _ in zip(normed(1, 0), normed(1, 1)):
        pass
    for half in range(2):
        drain(back[0][half], back[1][half])

    x_ready = [None] * 8

    def evac_out(pairno, bank, done):
        o = x[:, 2 * pairno:2 * pairno + 2, :]
        t = dve.tt([done], o, halves(bank[:, :]), o, ALU.add)
        x_ready[2 * pairno] = x_ready[2 * pairno + 1] = t
        out(pairno, x, [t], o_ready)
        return [t]

    S.lead = HIS
    drain(layer(S, [("rw_o", i) for i in range(4)], (o_hi, o_lo, o_ready), evac_out, B[0:4]))
    return x, x_ready, o_ready


def tile_cols(v):
    v = np.asarray(v).reshape(-1)
    return v.reshape(-1, P).T


def pack(i):
    f = np.float32
    z = lambda r, c: np.zeros((r, c), f)
    mats = {
        "ada": i["w_ada"][0].T,
        "w_in": i["w_in"][0],
        "w_dt": np.concatenate([i["w_in"][0][:, 6144:6176], z(D, 96)], axis=1),
        "w_sc_out": i["w_sc_out"][0],
        "w_ssd_out": i["w_ssd_out"][0],
        "w_o": i["w_o"][0],
        "w_router": i["router_w"][0].reshape(4, 2, P, 64).transpose(0, 2, 1, 3).reshape(512, P),
        "hy_in": i["hy_w_in_2"][0],
        "w_f": np.concatenate([i["hy_w_in_2"][0][:, 2048:2056], z(D, 120)], axis=1),
        "pool_w": i["hy_pool_w_2"][0].reshape(512, P),
        "hy_out": i["hy_w_out_2"][0],
        "rw_w1": np.concatenate([i["rw_w1_2"][0], z(D, 64)], axis=1),
        "rw_w2": np.concatenate([i["rw_w2_2"][0], z(64, D)], axis=0),
        "rw_a1": np.concatenate([i["rw_a1_2"][0], z(D, 64)], axis=1),
        "rw_a2": np.concatenate([i["rw_a2_2"][0], z(64, D)], axis=0),
        "rw_g1": np.concatenate([i["rw_g1_2"][0], z(D, 96)], axis=1),
        "rw_g2": np.concatenate([i["rw_g2_2"][0], z(96, D)], axis=0),
        "rw_k": i["rw_w_k_2"][0],
        "rw_r": i["rw_w_r_2"][0],
        "rw_v": i["rw_w_v_2"][0],
        "rw_o": i["rw_w_o_2"][0],
        "sh_gate": i["sh_gate"][0],
        "sh_up": i["sh_up"][0],
        "sh_down": i["sh_down"][0],
    }
    for n in range(2):
        mats[f"ffn_gate{n}"], mats[f"ffn_up{n}"], mats[f"ffn_down{n}"] = i["ffn_w_gate_2"][n], i["ffn_w_up_2"][n], i["ffn_w_down_2"][n]
    slots = plan()
    slots = [x for x in slots if x[0][0] != "expert"]
    wts = np.empty(sum(len(t) for _, t, _ in slots) * P * P, f)
    at = 0
    for _, tiles, _ in slots:
        n = len(tiles)
        out = wts[at:at + n * P * P].reshape(P, n, P)
        for t, (m, r, c) in enumerate(tiles):
            out[:, t, :] = mats[m][r:r + P, c:c + P]
        at += n * P * P
    experts = np.empty((N_EXPERTS, 3, P, SLOT), f)
    for e in range(N_EXPERTS):
        up = np.concatenate([i["w_gate"][0][e], i["w_up"][0][e]], axis=1)
        experts[e, 0:2] = up.reshape(2, 4, P, 512).transpose(0, 2, 1, 3).reshape(2, P, SLOT)
        experts[e, 2] = i["w_down"][0][e].reshape(2, P, D).transpose(1, 0, 2).reshape(P, SLOT)
    cols = {
        "b_ada": i["b_ada"],
        "ssd_conv_w": i["ssd_conv_w"][0],
        "ssd_conv_b": i["ssd_conv_b"],
        "ssd_D": np.repeat(i["ssd_D"][0], 64),
        "ssd_norm_w": i["ssd_norm_w"],
        "sc_conv_w": i["sc_conv_w"][0],
        "ln1_g": i["ln1_g"],
        "ln1_b": i["ln1_b"],
        "ln2_g": i["ln2_g"],
        "ln2_b": i["ln2_b"],
        "mix_norm": i["mix_norm_2"],
        "ffn_norm": i["ffn_norm_2"],
        "dt_bias": np.concatenate([i["ssd_dt_bias"][0], np.zeros(96, f)]),
        "A_log": np.concatenate([i["ssd_A_log"][0], np.zeros(96, f)]),
        "eps": np.repeat(np.array([1e-5, 1e-6, 64e-5, 1e-12], f), P),
    }
    cols["q_gain"] = np.tile(i["hy_q_gain_2"][0], 2)
    cols["k_gain"] = np.tile(i["hy_k_gain_2"][0], 2)
    cols["qk_eps"] = np.concatenate([np.full(8, 64e-6, f), np.full(120, 1e-6, f)])
    cols["f_bias"] = np.concatenate([i["hy_f_bias_2"][0], np.zeros(120, f)])
    cols["pool_scale"] = i["hy_pool_scale_2"]
    for n in ("mu", "w0", "a0", "k_k", "k_a", "r_k"):
        cols[f"rw_{n}"] = i[f"rw_{n}_2"]
    con = constants()
    con["router_bias"] = np.broadcast_to(i["router_bias"], (P, 64))
    par = np.concatenate([tile_cols(cols[n]) for n, _ in PARAMS] + [con[n] for n in STAY + LATE], axis=1).astype(f)
    xT = np.ascontiguousarray(i["x"][0].T).reshape(8, P, T).transpose(1, 0, 2).reshape(P, 8 * T)
    return {
        "xT": np.ascontiguousarray(xT),
        "c": np.ascontiguousarray(i["c"]),
        "wts": wts,
        "experts": experts,
        "rw_ln": np.stack([i["rw_ln_w_2"][0], i["rw_ln_b_2"][0]]),
        "par": np.ascontiguousarray(par),
        "cst": np.ascontiguousarray(np.concatenate([con[n] for n in CONST], axis=1).astype(f)),
    }


def setup(K):
    con = constants()
    K.c = {}
    K.ccol = {}
    at = 0
    for n in CONST:
        K.ccol[n] = (at, con[n].shape[1])
        at += con[n].shape[1]
    K.cst = lambda n: K.ins["cst"][:, K.ccol[n][0]:K.ccol[n][0] + K.ccol[n][1]]
    n = NPAR + sum(con[n].shape[1] for n in STAY)
    K.par = K.buf("par", 0, [P, n + sum(LATE_COLS.values())])
    K.t_par = K.load(K.par[:, 0:n], K.ins["par"][:, 0:n])
    K.t_cst = [K.t_par]
    at = NPAR
    for n in STAY:
        K.c[n] = K.par[:, at:at + con[n].shape[1]]
        at += con[n].shape[1]
    for n in LATE:
        K.c[n] = K.par[:, at:at + LATE_COLS[n]]
        at += LATE_COLS[n]
    assert at * 4 <= 8 * 1024
    K.acc = K.buf("acc", 9, [P, 48])
    K.mod = K.buf("mod", 9.25, [P, 48])
    K.small = K.buf("small", 9.5, [P, 64])
    K.mod_ready = [None] * 48
    K.nroot = 0
    K.ada_last = []


def setup_late(K):
    n = NPAR + sum(K.c[m].shape[1] for m in STAY)
    K.t_late = K.load(K.par[:, n:], K.ins["par"][:, n:], queue=K.act)


def program(nc, ins, out):
    with ExitStack() as ctx:
        K = Core(nc, ctx, ins)
        S = Stream(K, plan(), ins["wts"], ins["experts"])
        x, ready, after, norm = moe(K, S, *first_block(K, S), fox_norm(K))
        first, mix, second = ffn_norm(K, 0), rwkv_norm(K), ffn_norm(K, 1)
        x, ready = fox(K, S, x, ready, after, norm, first.pair)
        x, ready = ffn(K, S, 0, x, ready, first, lambda n, x, t: mix.pair(n, x, t, eng=K.dve if n == 3 else K.pool))
        x, ready, after = rwkv(K, S, x, ready, mix, second.pair)

        def store(i, x, ready):
            o = out.rearrange("p (j t) -> p j t", j=8)[:, 2 * i:2 * i + 2, :]
            K.final.append(K.load(o, x[:, 2 * i:2 * i + 2, :], after=ready))

        ffn(K, S, 1, x, ready, second, store, after)
        K.run()


def kernel(**inputs):
    import concourse.bacc as _bacc
    from concourse.bass_utils import run_bass_kernel_spmd as _run

    nc = _bacc.Bacc("TRN2", target_bir_lowering=False, num_devices=1)
    arrays, args = {}, {}
    for name, a in pack({n: np.asarray(v) for n, v in inputs.items()}).items():
        arrays["in_" + name] = a
        args[name] = nc.dram_tensor("in_" + name, a.shape, mybir.dt.from_np(a.dtype), kind="ExternalInput").ap()
    out = nc.dram_tensor("out", (P, 8 * T), F32, kind="ExternalOutput").ap()
    program(nc, args, out)
    r = _run(nc, [arrays], core_ids=[0])
    got = r.results[0]["out"].reshape(P, 8, T)
    return np.ascontiguousarray(got.transpose(2, 1, 0)).reshape(1, T, D)
```

```python
from contextlib import ExitStack

import numpy as np

import concourse.bass as bass
from concourse import mybir
from concourse.alu_op_type import AluOpType as ALU

ACT = mybir.ActivationFunctionType
F32 = mybir.dt.float32
F32R = mybir.dt.float32r
BF16 = mybir.dt.bfloat16
I32 = mybir.dt.int32
AX = mybir.AxisListType.X

P = 128
T = 256
D = 1024
ALPHA = 2.0 ** 0.25
TILE = 128
SLOT = 16 * TILE
RING = 7
NARROW = 4
RING_KB = 10
HI_KB = RING_KB + 8 * RING
HIS = 3
AREA = HI_KB + 8 * HIS
N_EXPERTS = 64
FIXED = 5
MORE = (68, 76, 84, 92, 8, 48)


class Count:

    def __init__(self, name, sem):
        self.name, self.sem, self.count = name, sem, 0


class Branch:
    def __init__(self, flag, limit, after):
        self.flag, self.limit, self.after, self.items, self.adds = flag, limit, after, [], 0


class Queue:

    def __init__(self, name, core):
        self.main = Count(name, core.sem("s_" + name))
        self.side = Count(name + "_if", core.sem("s_" + name + "_if"))
        self.items, self.open = [], []
        self.flags = None

    def into(self):
        return self.open[-1].items if self.open else self.items

    def do(self, after, emit):
        count = self.side if self.open else self.main
        for b in self.open:
            b.adds += 1
        count.count += 1
        self.into().append((tuple(flat(after)), emit, count, 1))
        return (count, count.count)

    def dma(self, after, load, out, in_):
        load.count += 16
        self.into().append((tuple(flat(after)), lambda e: e.dma_start(out, in_), load, 16))
        return (load, load.count)

    def load_flags(self, after, row):
        self.flags = (tuple(flat(after)), row)
        self.items.append(("flags",))

    def branch(self, flag, limit, after=()):
        b = Branch(flag, limit, tuple(flat(after)))
        self.into().append(b)
        self.open.append(b)

    def close(self):
        self.open.pop()

    def run(self, eng):
        self.emit(eng, self.items, {})

    def emit(self, eng, items, seen):
        def wait(after):
            for count, value in after:
                if seen.get(count.name, 0) < value:
                    eng.wait_ge(count.sem, value)
                    seen[count.name] = value

        for item in items:
            if isinstance(item, Branch):
                with eng.If_cmp(self.regs[item.flag], item.limit, "IS_GT"):
                    self.emit(eng, item.items, dict(seen))
                with eng.Else():
                    for count, value in item.after:
                        eng.wait_ge(count.sem, value)
                    eng.sem_inc(self.side.sem, item.adds)
            elif item[0] == "flags":
                after, row = self.flags
                n = row.shape[1]
                self.regs = [eng.alloc_register(f"{self.main.name}_flag{i}") for i in range(n)]
                wait(after)
                eng.reg_load(self.regs, row)
            else:
                after, emit, count, add = item
                wait(after)
                emit(eng).then_inc(count.sem, add)

    def act(self, after, out, in_, func=ACT.Copy, **kw):
        return self.do(after, lambda e: e.activation(out, in_, func, **kw))

    def tt(self, after, out, a, b, op):
        return self.do(after, lambda e: e.tensor_tensor(out, a, b, op=op))

    def ts(self, after, out, a, s1, op0, s2=None, op1=ALU.bypass, **kw):
        return self.do(after, lambda e: e.tensor_scalar(out, a, s1, s2, op0=op0, op1=op1, **kw))

    def stt(self, after, out, a, s, b, op0, op1):
        return self.do(after, lambda e: e.scalar_tensor_tensor(out, a, s, b, op0=op0, op1=op1))

    def copy(self, after, out, a):
        return self.do(after, lambda e: e.tensor_copy(out, a))

    def recip(self, after, out, a):
        return self.do(after, lambda e: e.reciprocal(out, a))

    def fill(self, after, out, value):
        return self.do(after, lambda e: e.memset(out, value))

    def mm(self, after, *calls):

        def emit(e):
            for out, lhsT, rhs, start, stop in calls:
                ins = e.matmul(out, lhsT, rhs, start=start, stop=stop, skip_group_check=True)
            return ins

        return self.do(after, emit)

    def tr(self, after, ident, *calls):

        def emit(e):
            for out, in_ in calls:
                n = in_.shape[0]
                ins = e.transpose(out, in_, ident[0:n, 0:n])
            return ins

        return self.do(after, emit)


def flat(x):
    if isinstance(x, tuple) and len(x) == 2 and isinstance(x[1], int):
        yield x
        return
    for y in x or ():
        yield from flat(y)


class Bank:

    def __init__(self, t):
        self.t, self.free = t, []

    def __getitem__(self, k):
        return self.t[k]


class Slot:
    def __init__(self, index, key, tiles, split):
        self.index, self.key, self.tiles, self.split = index, key, tiles, split
        self.done = []


class Core:
    def __init__(self, nc, ctx, ins):
        self.nc, self.ctx, self.ins = nc, ctx, ins
        self.arena = ctx.enter_context(nc.sbuf_tensor("arena", [P, 53200], F32))
        self.base = 16512
        self.pe = Queue("pe", self)
        self.act = Queue("act", self)
        self.dve = Queue("dve", self)
        self.pool = Queue("pool", self)
        self.sp = []
        self.actdma = []
        self.banks = [Bank(ctx.enter_context(nc.psum_tensor(f"ps{i}", [P, 512], F32))) for i in range(8)]
        self.nload = 0
        self.final = []
        self.turn = 0

    def sem(self, name):
        return self.ctx.enter_context(self.nc.semaphore(name))

    def buf(self, name, kb, shape, dt=F32):
        n = 1
        for s in shape[1:]:
            n *= s
        assert kb * 1024 + n * (2 if dt == BF16 else 4) <= 212800, (name, kb)
        return self.nc.alloc_sbuf_tensor_at(name, list(shape), dt, offset=self.base + int(kb * 1024))

    def load(self, out, in_, after=(), queue=None):
        self.nload += 1
        load = Count(f"ld{self.nload}", self.sem(f"ld{self.nload}"))
        if queue:
            return queue.dma(after, load, out, in_)
        load.count = 16
        self.sp.append((list(flat(after)), lambda e: e.dma_start(out, in_).then_inc(load.sem, 16)))
        return (load, 16)

    def run(self):
        with self.nc.Block() as block:

            @block.sync
            def _(eng):
                seen = {}
                for after, emit in self.sp:
                    for queue, count in flat(after() if callable(after) else after):
                        if seen.get(queue.name, 0) < count:
                            eng.wait_ge(queue.sem, count)
                            seen[queue.name] = count
                    emit(eng)
                for queue, count in self.final:
                    eng.wait_ge(queue.sem, count)

            @block.tensor
            def _(eng):
                self.pe.run(eng)

            @block.scalar
            def _(eng):
                self.act.run(eng)

            @block.vector
            def _(eng):
                self.dve.run(eng)

            @block.gpsimd
            def _(eng):
                self.pool.run(eng)


class Stream:

    def __init__(self, core, plan, wts, experts):
        self.core, self.experts = core, experts
        self.order, self.order_ready, self.regs = None, [], None
        self.lo_engines = (core.dve,)
        self.lead, self.late = HIS, 0
        self.slots = [Slot(i, *p) for i, p in enumerate(plan)]
        self.next = self.nready = self.issued = 0
        at = [RING_KB + 8 * i for i in range(RING)] + [AREA + k for k in MORE] + [HI_KB + 8 * i for i in range(HIS)]
        self.raw = [core.buf(f"wraw{i}", kb, [P, SLOT]) for i, kb in enumerate(at)]
        self.lo = [core.buf(f"wlo{i}", kb, [P, SLOT], F32R) for i, kb in enumerate(at[:RING])]
        self.hi = [core.buf(f"whi{i}", HI_KB + 8 * i, [P, SLOT], F32R) for i in range(HIS)]
        self.before = [()] * len(at)
        sems = [Count(f"ring{i}", core.sem(f"ring{i}")) for i in range(len(at))]
        user = [None] * len(at)
        hi_user = [None] * HIS
        at = turn = wide = nsplit = 0
        narrow = False
        for s in self.slots:
            s.n = len(s.tiles) * TILE
            if s.key[0] == "expert":
                order = [*range(RING, RING + 4), *[(turn + i) % RING for i in range(RING)], *range(RING + 6, RING + 9),
                         RING + 4, RING + 5]
                s.place = order[wide % len(order)]
                wide += 1
            else:
                n = NARROW if narrow or s.key == "wa1" else RING
                narrow = n == NARROW
                s.place = turn % n
                turn += 1
            h = s.place - RING - len(MORE)
            if s.split:
                h = nsplit % HIS
                nsplit += 1
                s.hi, s.hi_prev, hi_user[h] = self.hi[h], hi_user[h], s
            load = sems[s.place]
            load.count += 16
            s.landed = (load, load.count)
            s.prev, user[s.place] = user[s.place], s
            if s.place >= RING + len(MORE):
                s.prev, hi_user[h] = hi_user[h], s
            s.raw = self.raw[s.place]
            if s.key[0] != "expert":
                s.src = wts[at:at + P * s.n].rearrange("(p n) -> p n", p=P)
                at += P * s.n
        self.total = at
        self.user = user

    def find(self, key):
        return next(s for s in self.slots if s.key == key)

    def issue(self, upto):
        while self.issued < min(upto, len(self.slots)):
            s = self.slots[self.issued]
            free = lambda s=s: s.prev.done if s.prev else self.before[s.place]
            if s.key[0] == "expert":
                self.issue_expert(s, free)
            else:
                self.core.sp.append((free, lambda e, s=s: e.dma_start(s.raw[:, 0:s.n], s.src).then_inc(s.landed[0].sem, 16)))
            self.issued += 1

    def issue_expert(self, s, free):
        _, place, part, group = s.key

        def fixed(e):
            e.dma_start(s.raw[:, :], self.experts[place, part]).then_inc(s.landed[0].sem, 16)

        def sorted_(e):
            if not self.regs:
                self.regs = [e.alloc_register(f"expert{i}") for i in range(4)]
            if part == 0 and place == group[0]:
                regs = self.regs[0:len(group)]
                e.reg_load(regs, self.order[:, place:place + len(group)])
                self.which = [e.snap(r, min_val=0, max_val=N_EXPERTS - 1) for r in regs]
            src = self.experts[bass.ds(self.which[place - group[0]], 1), part, :, :].rearrange("o p n -> (o p) n")
            e.dma_start(s.raw[:, :], src).then_inc(s.landed[0].sem, 16)

        if place < FIXED:
            self.core.sp.append((free, fixed))
        else:
            waits = lambda: [free(), self.order_ready]
            self.core.sp.append((waits, sorted_))

    def split(self, s, engine=None):
        core, last = self.core, s.hi_prev
        engine = engine or self.lo_engines[s.index % len(self.lo_engines)]
        s.lo = self.lo[s.place]
        a = core.act.act([s.landed, last.done if last else []], s.hi[:, 0:s.n], s.raw[:, 0:s.n])
        b = engine.tt([a], s.lo[:, 0:s.n], s.raw[:, 0:s.n], s.hi[:, 0:s.n].bitcast(F32), ALU.subtract)
        s.ready = [a, b]

    def take(self, key):
        s = self.slots[self.next]
        assert s.key == key, (s.key, key)
        self.next += 1
        self.issue(s.index + len(self.raw))
        self.look(s, self.lead - self.late)
        return s

    def look(self, s, n):
        upto, left = s.index, n - (not s.split)
        while upto < min(s.index + n + 2, len(self.slots)) and left >= self.slots[upto].split:
            left -= self.slots[upto].split
            upto += 1
        self.ahead(upto, None, s)

    def ahead(self, upto, engine=None, now=None):
        while self.nready < min(upto, len(self.slots)):
            f = self.slots[self.nready]
            if f.split and now and not now.split and now.key[0] == "expert":
                break
            self.nready += 1
            if f.split:
                self.split(f, engine)
            else:
                f.ready = [f.landed]



FIXED_PAIRS = [(0, 1), (2, 3)]
SOLOS = [(p,) for p in range(4, 12)]
PAIRS = [(p, p + 1) for p in range(12, 32, 2)]
QUADS = [tuple(range(p, p + 4)) for p in range(32, 64, 4)]
FLAGS = FIXED_PAIRS + SOLOS + PAIRS + QUADS
KINDS = dict(f=iter(FIXED_PAIRS), s=iter(SOLOS), p=iter(PAIRS), q=iter(QUADS))
GROUPS = [next(KINDS[k]) for k in "ffqsqsqsqpqsqssqsqsppppppppp"]
ROUNDS = {1: 2, 2: 4, 4: 3}

PARAMS = []


def param(name, n):
    at = sum(k for _, k in PARAMS)
    PARAMS.append((name, n))
    return at


C_BADA = param("b_ada", 48)
C_CONVW = param("ssd_conv_w", 128)
C_CONVB = param("ssd_conv_b", 32)
C_D = param("ssd_D", 16)
C_NORM = param("ssd_norm_w", 16)
C_SCW = param("sc_conv_w", 24)
C_LN1G = param("ln1_g", 8)
C_LN1B = param("ln1_b", 8)
C_LN2G = param("ln2_g", 8)
C_LN2B = param("ln2_b", 8)
C_MIX = param("mix_norm", 16)
C_FFN = param("ffn_norm", 16)
C_DTB = param("dt_bias", 1)
C_ALOG = param("A_log", 1)
C_EPS = param("eps", 4)
C_QG = param("q_gain", 1)
C_KG = param("k_gain", 1)
C_QKE = param("qk_eps", 1)
C_FB = param("f_bias", 1)
C_PSC = param("pool_scale", 4)
C_MU = param("rw_mu", 48)
C_W0 = param("rw_w0", 8)
C_A0 = param("rw_a0", 8)
C_KK = param("rw_k_k", 8)
C_KA = param("rw_k_a", 8)
C_RK = param("rw_r_k", 8)
NPAR = sum(k for _, k in PARAMS)


def plan():
    out = []

    def add(key, tiles, split=True):
        out.append((key, tiles, split))

    def pair(key, mat, m0, nk=8, split=True):
        add(key, [(mat, P * k, m0 + P * m) for k in range(nk) for m in range(2)], split)

    def rows(key, *r0):
        add(key, [("ada", r, P * q) for r in r0 for q in range(8)], False)

    for j in range(8):
        rows(("ada", j), 1024 + P * j, P * j)
        add(("sc_ch", j), [("w_in", P * j, m0 + P * m) for m0 in (7200, 8224) for m in range(8)])
    add("dt", [("w_dt", P * k, 0) for k in range(8)])
    for i in range(4):
        pair(("B", i), "w_in", 4096 + 256 * i)
    for i in range(4):
        pair(("C", i), "w_in", 5120 + 256 * i)
    for i in range(8):
        pair(("xs", i), "w_in", 2048 + 256 * i)
    spare = [[2048 + 256 * j, 2048 + 256 * j + P] for j in range(4)]
    spare += [[4096 + P * j, 3072 + P * j] for j in range(8)]
    spare += [[5120 + 256 * j, 5120 + 256 * j + P] for j in range(4)]
    for what, mat, m0 in (("sc_b", "w_in", 6176), ("sc_out", "w_sc_out", 0), ("gb", "w_in", 10272)):
        for i in range(4):
            pair((what, i), mat, m0 + 256 * i)
            j = {"sc_b": -4, "sc_out": 0, "gb": 4}[what] + i
            if j > 1:
                rows(("ada", 6 + j), *spare[j - 2])
    pair(("ga", 0), "w_in", 9248)
    rows(("ada", 14), *spare[6])
    for i in range(8):
        pair(("z", i), "w_in", 256 * i)
        if i < 5:
            rows(("ada", 15 + i), *spare[7 + i])
    for i in range(1, 4):
        pair(("ga", i), "w_in", 9248 + 256 * i)
    for i in range(8):
        add(("ssd_out", i), [("w_ssd_out", P * k, P * m) for k in range(8 * (i % 2), 8 * (i % 2) + 8) for m in (i - i % 2, i - i % 2 + 1)])
        if i % 2:
            rows(("ada", 20 + i // 2), *spare[12 + i // 2])
    for i in range(4):
        pair(("w_o", i), "w_o", 256 * i)
    add("router", [("w_router", P * k, 0) for k in range(4)], False)
    pair("sh_gate", "sh_gate", 0)
    pair("sh_up", "sh_up", 0)
    add("sh_down", [("sh_down", P * k, P * m) for m in range(8) for k in range(2)])
    for group in GROUPS:
        for half in range(2):
            for p in group:
                add(("expert", p, half, group), range(16), False)
        for p in group:
            add(("expert", p, 2, group), range(16), False)

    def across(key, mat, m0, split=True):
        for half in range(2):
            add((key, half), [(mat, P * k, m0 + P * m) for k in range(4 * half, 4 * half + 4) for m in range(4)], split)

    def ffn(n):
        for m in range(22):
            add(("gate_up", n, m), [(f"{w}{n}", P * k, P * m) for k in range(8) for w in ("ffn_gate", "ffn_up")])
        tiles = [(f"ffn_down{n}", P * k, P * m) for m in range(8) for k in range(22)]
        for i in range(11):
            add(("down", n, i), tiles[16 * i:16 * i + 16])

    pair(("q", 0), "hy_in", 0)
    add("hy_f", [("w_f", P * k, 0) for k in range(8)])
    pair(("q", 1), "hy_in", 256)
    for i in range(2):
        pair(("k", i), "hy_in", 512 + 256 * i)
    across("v", "hy_in", 1024)
    pair(("og", 0), "hy_in", 1536)
    across("u", "hy_in", 2056)
    pair(("og", 1), "hy_in", 1792)
    add("pool", [("pool_w", P * g, 0) for g in range(4)])
    for i, k0 in enumerate((4, 6, 0, 2)):
        add(("hy_out", i), [("hy_out", P * k, P * m) for m in range(8) for k in (k0, k0 + 1)])
    ffn(0)
    add("wa1", [(f"rw_{x}1", P * k, 0) for x in "wa" for k in range(8)], False)
    add("wa2", [(f"rw_{x}2", 0, P * m) for x in "wa" for m in range(8)], False)
    for i in range(4):
        pair(("rw_k", i), "rw_k", 256 * i, split=False)
    for i in range(4):
        pair(("rw_r", i), "rw_r", 256 * i)
    across("rw_v0", "rw_v", 0, False)
    across("rw_v1", "rw_v", 512, False)
    pair("g1", "rw_g1", 0, split=False)
    add("g2", [("rw_g2", P * k, P * m) for k in range(2) for m in range(8)], False)
    for i in range(4):
        pair(("rw_o", i), "rw_o", 256 * i)
    ffn(1)
    return out


def constants():
    c = {}
    c["ident"] = np.eye(P)
    c["mean"] = np.full((P, P), 1.0 / D)
    k = np.arange(P)
    tri = (k[:, None] <= k[None, :]) * 1.0
    c["iota"] = np.broadcast_to(np.arange(1.0, 257), (P, 256))
    for n in ROUNDS:
        w = P // n
        c[f"slot{n}"] = k[:, None] % w + w * np.arange(ROUNDS[n])[None, :] + 1.0
        c[f"of{n}"] = np.tile(k[:, None] // w == np.arange(n)[None, :], 2) * 1.0
    e = np.arange(N_EXPERTS)
    bump = np.maximum(FIXED - e, 0) * 1000.0
    c["bump"] = np.broadcast_to(bump, (P, N_EXPERTS))
    c["own"] = np.stack([np.tile(bump, 2), np.tile(e, 2)], axis=1)
    c["upto"] = (e[None, :] <= (k % N_EXPERTS)[:, None]) * 1.0
    g = np.arange(8)
    c["before"] = np.broadcast_to((g[None, :] < g[:, None]).reshape(1, 64), (P, 64)) * 1.0
    c["tri"] = tri
    n = np.arange(8)
    c["heads"] = np.concatenate([((2 * i + k[:, None] // 64) == np.arange(16)[None, :]) * (1.0 if i < 4 else 1.0 / 64) for i in n], axis=1)
    c["neg"] = np.concatenate([np.zeros((P, P)), (k[None, :] > k[:, None]) * -1e30], axis=1)
    s, t = np.arange(T)[:, None], np.arange(T)[None, :]
    bands = []
    for w in (2, 4, 8, 16):
        b = ((s <= t) & (s > t - w)) / np.minimum(t + 1, w) - (s == t)
        bands += [b[0:P], b[P:, P:]]
    c["band"] = np.concatenate(bands, axis=1)
    c["sum16"] = np.concatenate([(2 * i + k[:, None] // 64) == np.arange(16)[None, :] for i in n], axis=1) * 1.0
    s, t = k[:, None] % 64, np.arange(64)[None, :]
    c["chunk"] = np.concatenate([s <= t, s < t, s < t, s <= t], axis=1) * 1.0
    c["mask"] = np.concatenate([tri, np.ones((P, P)), tri], axis=1)
    return c


STAY = ["mean", "ident"]
LATE_COLS = dict(iota=256, slot1=2, of1=2, slot2=4, of2=4, slot4=3, of4=8, before=64, tri=P, router_bias=64, bump=64, own=2, upto=64)
LATE = list(LATE_COLS)
CONST = ["mask", "heads", "neg", "band", "sum16", "chunk"]


def layer(S, keys, x, evac, banks, nk=8, steps=2, half=None):
    K = S.core
    hi, lo, ready = x
    mts = {}
    mine = {}
    for key in keys:
        tiles = list(enumerate(S.find(key).tiles))
        n = len(tiles) // 2
        mine[key] = tiles if half is None else tiles[n * half:n * (half + 1)]
        for _, (mat, _, m0) in mine[key]:
            mts.setdefault((mat, m0), len(mts))
    for key in keys:
        s = S.find(key) if half else S.take(key)
        nt = len(mine[key])
        for n, (t, (mat, k0, m0)) in enumerate(mine[key]):
            mt, k = mts[mat, m0], k0 // P
            pairno, odd = divmod(mt, 2)
            first, last = k == 0 and odd == 0, k == nk - 1
            if first:
                bank = banks[K.turn % len(banks)]
                K.turn += 1
            after = [s.ready if n == 0 else [], bank.free if first else [], ready[k]]
            o = bank[:, T * odd:T * (odd + 1)]
            w = slice(TILE * t, TILE * (t + 1))
            if s.split:
                tok = K.pe.mm(after, (o, s.hi[:, w], hi[:, k, :], first, False), (o, s.hi[:, w], lo[:, k, :], False, False),
                              (o, s.lo[:, w], hi[:, k, :], False, last))
            else:
                tok = K.pe.mm(after, (o, s.raw[:, w], hi[:, k, :], first, last))
            if n == nt - 1:
                s.done.append(tok)
            if last and (odd == 1 or mt == len(mts) - 1):
                bank.free = evac(pairno, bank, tok)
            if S.late and n == nt // 4:
                S.look(s, S.lead)
            if (n + 1) % max(1, nt // steps) == 0:
                yield


def weave(main, side, per, jobs=()):
    jobs = iter(jobs)
    for _ in main:
        for _ in range(per):
            next(side, None)
        for job in jobs:
            job()
            break
    return side


def every(n, gen):
    for _ in gen:
        for _ in range(n - 1):
            yield
        yield


def chained(*gens):
    for gen in gens:
        yield from gen


def drain(*gens):
    for gen in gens:
        for _ in gen:
            pass


def halves(ap):
    return ap.rearrange("p (i t) -> p i t", i=2)


def split_x(K, xh, xl, k, x32, after, eng=None):
    a = K.act.act(after, xh[:, k, :], x32)
    b = (eng or K.dve).tt([a], xl[:, k, :], x32, xh[:, k, :].bitcast(F32), ALU.subtract)
    return [a, b]


class InverseRoot:

    def __init__(self, K, bank, eps):
        self.K, self.bank, self.eps = K, bank, eps
        self.cols = K.buf(f"root{K.nroot}", 8 + K.nroot / 32, [P, 2])[:, :]
        K.nroot += 1
        self.early = K.act.act([K.t_par], self.cols[:, 0:1], K.par[:, C_EPS:C_EPS + 1], ACT.Sqrt)

    def add(self, ready, tile, first, last):
        b = self.bank
        self.done = self.K.pe.mm([ready, b.free if first else []], *[
            (b[:, i:i + 1], tile[:, P * i:P * (i + 1)], self.K.c["mean"][:, 0:1], first and i == 0, last) for i in range(2)])

    def squares(self, x, ready, sq, free):
        for j in range(8):
            t = self.K.act.act([ready[j], free], sq[:, j, :], x[:, j, :], ACT.Square)
            self.add(t, sq[:, j, :], j == 0, j == 7)

    def columns(self):
        K, b = self.K, self.bank
        t = K.act.act([self.done, self.early], self.cols, b[:, 0:2], ACT.Sqrt, bias=K.par[:, C_EPS + self.eps:C_EPS + self.eps + 1])
        b.free = [t]
        return K.dve.recip([t], self.cols, self.cols)

    def row(self, t):
        K, b = self.K, self.bank
        t = K.pe.mm([t, b.free], *[(b[:, P * i:P * (i + 1)], self.cols[:, i:i + 1].to_broadcast([P, P]), K.c["ident"][:, :], i == 0, True) for i in range(2)])
        return b[:, 0:T], t


def layer_norm(K, src, ready, sq, bm, bv, sq_free, out, dst=None, mean=None, gain=None):
    dst = dst or src
    made = []
    if mean:
        for j in range(8):
            made.append(K.dve.stt([ready[j], mean[2]], dst[:, j, :], src[:, j, :], mean[0], mean[1], ALU.subtract, ALU.subtract))
    else:
        for j in range(8):
            if gain:
                tg = K.pe.mm([ready[j], K.t_cst, gain[2].free if j == 0 else []], (gain[2][:, 0:T], K.par[:, gain[0] + j:gain[0] + j + 1].to_broadcast([P, P]),
                                                              src[:, j, :], j == 0, j == 7))
            t = K.pe.mm([ready[j], bm.free if j == 0 else [], K.t_cst],
                        (bm[:, 0:T], K.c["mean"][:, :], src[:, j, :], j == 0, j == 7))
        for j in range(8):
            made.append(K.dve.tt([t], dst[:, j, :], src[:, j, :], bm[:, 0:T], ALU.subtract))
        bm.free = [made]
    if gain:
        _, gmean, bg, tile, spare = gain
        a = K.dve.ts([t, gmean[1]], spare, bm[:, 0:T], gmean[0], ALU.mult)
        a = K.dve.stt([a, tg], tile, bg[:, 0:T], 1.0 / D, spare, ALU.mult, ALU.subtract)
        bm.free, bg.free = [made, a], [a]
    root = InverseRoot(K, bv, 0)
    root.squares(dst, made, sq, sq_free)
    r, t = root.row(root.columns())
    late = []
    for j in range(8):
        late.append((j, K.dve.tt([t], dst[:, j, :], dst[:, j, :], r, ALU.mult)))
        if j == 3 and gain:
            tg = K.dve.tt([a, t], tile, tile, r, ALU.mult)
        if j > 1:
            out(*late[j - 2])
    bv.free = [late[7][1]]
    out(*late[6])
    out(*late[7])
    return tg if gain else t


def modulation(K, S, i, share=False):
    s = S.take(("ada", i))
    sums, late = [], []
    for h in range(2):
        j = s.tiles[8 * h][1] // P
        w, a = s.raw[:, D * h:D * (h + 1)], K.acc[:, j:j + 1]
        if share and h:
            t = K.pool.tt([s.ready, K.t_csil, K.prod_free, K.prod_also], K.prod[:, :], w, K.csil[:, :], ALU.mult)
            late.append((j, a, t, K.prod))
        else:
            t = K.dve.do([s.ready, K.t_csil, K.ada_last],
                         lambda e, w=w, a=a: e.tensor_tensor_reduce(K.scr[:, :], w, K.csil[:, :], 1.0, 0.0, ALU.mult, ALU.add, a))
            K.ada_last = [t]
            sums.append((j, t))
        s.done.append(t)
        yield
    for j, a, t, o in late:
        t = K.act.act([t], o[:, :], o[:, :], accum_out=a)
        K.prod_free = [t]
        sums.append((j, t))
    yield
    for j, t in sums:
        plus = 1.0 if j // 8 in (1, 4) else 0.0
        K.mod_ready[j] = K.dve.stt([t, K.t_par], K.mod[:, j:j + 1], K.acc[:, j:j + 1], plus, K.par[:, C_BADA + j:C_BADA + j + 1], ALU.add, ALU.add)


def first_block(K, S):
    pe, act, dve, pool = K.pe, K.act, K.dve, K.pool
    B = K.banks
    A = AREA

    h_hi = K.buf("h_hi", A, [P, 8, T], F32R)
    h_lo = K.buf("h_lo", A + 8, [P, 8, T], F32R)
    xs = K.buf("xs", A + 16, [P, 16, T])
    Bm = K.buf("Bm", A + 32, [P, 8, T])
    Cm = K.buf("Cm", A + 40, [P, 8, T])
    s_hi = K.buf("s_hi", A + 48, [P, 8, T], F32R)
    s_lo = K.buf("s_lo", A + 56, [P, 8, T], F32R)
    K.csil = csil = K.buf("csil", A + 64, [P, D])
    xT = K.buf("xT", A + 68, [P, 2, 2, T])
    CBm = K.buf("CBm", A + 72, [P, 2, 384])
    E = K.buf("E", A + 75, [P, 2, 2, 384])
    sc = K.buf("sc", A + 81, [P, 2, 2, 384])
    mask = K.buf("mask", A + 87, [P, 384])
    dtT = K.buf("dtT", A + 88.5, [P, 2, 32])
    AcsT = K.buf("AcsT", A + 88.75, [P, 2, 32])
    dt = K.buf("dt", A + 89, [32, T])
    dA = K.buf("dA", A + 90, [32, T])
    Acs = K.buf("Acs", A + 91, [32, T])
    tmp = K.buf("tmp", A + 92, [P, 4, T])
    K.scr = K.buf("scr", A + 115, [P, D], BF16)
    yb = ch = K.buf("yb", A + 100, [P, 8, T])
    gate = K.buf("gate", A + 108, [P, 2, 2, T])

    xf = K.buf("xf", A + 16, [P, 8, T])
    sq = K.buf("sq", A + 24, [P, 8, T])
    K.prod = K.buf("prod", A + 96, [P, D])
    K.prod_free, K.prod_also = [], []

    t_x = K.load(xf[:, :, :], K.ins["xT"].rearrange("p (j t) -> p j t", t=T))
    setup(K)
    par, t_par, ident = K.par, K.t_par, K.c["ident"]
    K.t_csil = K.load(csil[:, :], K.ins["c"].to_broadcast([P, D]))
    S.issue(1)
    t_mask = K.load(mask[:, :], K.cst("mask"), queue=act)
    K.t_csil = act.act([K.t_csil], csil[:, :], csil[:, :], ACT.Silu)

    t = dve.tt([t_x], sq[:, 0:4, :], xf[:, 0:4, :], xf[:, 4:8, :], ALU.add)
    t = dve.tt([t], sq[:, 4:6, :], sq[:, 0:2, :], sq[:, 2:4, :], ALU.add)
    t = t_sum = pe.mm([t, K.t_cst], *[(B[0][:, 0:T], K.c["mean"][:, :], sq[:, 4 + i, :], i == 0, i == 1) for i in range(2)])
    made = [dve.tt([t], xf[:, j, :], xf[:, j, :], B[0][:, 0:T], ALU.subtract) for j in range(8)]
    mods = [modulation(K, S, j, True) for j in range(8)]
    S.lead = 1
    root = InverseRoot(K, B[7], 0)
    root.squares(xf, made, sq, [t_sum])
    next(mods[0])
    next(mods[0])
    t = root.columns()
    next(mods[0])
    r, t = root.row(t)
    rs = K.buf("rs", A + 92, [P, T])
    drain(mods[0])
    t_r = B[7].free = [dve.copy([t], rs[:, :], r)]

    h_ready = []
    for j in range(8):
        x = xf[:, j, :]
        t = dve.tt([t_r], x, x, rs[:, :], ALU.mult)
        t = dve.ts([t, K.mod_ready[8 + j], K.mod_ready[j]], x, x, K.mod[:, 8 + j:9 + j], ALU.mult, K.mod[:, j:j + 1], ALU.add)
        a = dve.copy([t], h_hi[:, j, :], x)
        h_ready.append([a, dve.tt([a], h_lo[:, j, :], x, h_hi[:, j, :].bitcast(F32), ALU.subtract)])
        s = S.take(("sc_ch", j))
        if j < 7:
            drain(mods[j + 1])
        else:
            S.lead, S.late = HIS, 1
            S.ahead(S.find(("B", 0)).index + 1)
        tiles = [(B[m // 2][:, T * (m % 2):T * (m % 2 + 1)], slice(TILE * m, TILE * (m + 1))) for m in range(16)]
        for m, (o, w) in enumerate(tiles):
            first = j == 0 and m % 2 == 0
            pe.mm([s.ready[0], h_ready[j], made if m == 0 else t_r if m == 14 else []],
                  (o, s.hi[:, w], h_hi[:, j, :], first, False), (o, s.hi[:, w], h_lo[:, j, :], False, False))
        done = [pe.mm([s.ready], (o, s.lo[:, w], h_hi[:, j, :], False, j == 7)) for o, w in tiles]
        s.done.append(done[15])
    h = (h_hi, h_lo, h_ready)

    for i in range(4):
        B[i].free = [act.act([done[2 * i + 1], K.prod_free], ch[:, 2 * i:2 * i + 2, :], halves(B[i][:, :]))]
    ch_made = []
    for i in range(4):
        o, b = ch[:, 2 * i:2 * i + 2, :], B[4 + i]
        b.free = [dve.tt([done[9 + 2 * i], B[i].free], o, halves(b[:, :]), o, ALU.mult)]
        ch_made.append(b.free)

    t_dt = []
    dt_raw = []

    def evac_dt(_, bank, done):
        t = act.act([done, t_par], dt[:, :], bank[0:32, 0:T], ACT.Identity, bias=par[0:32, C_DTB:C_DTB + 1])
        dt_raw.append(t)
        return [t]

    def steps_dt():
        d = dt[:, :]
        u, p, z, z2 = (tmp[0:32, i, :] for i in range(4))
        t = dve.stt([dt_raw], u, d, -1.0, d, ALU.mult, ALU.min)
        t = act.act([t], u, u, ACT.Exp)
        ta = act.act([t_par], K.small[0:32, 0:1], par[0:32, C_ALOG:C_ALOG + 1], ACT.Exp)
        yield
        t = dve.ts([t], z, u, 2.0, ALU.add)
        t = dve.recip([t], z, z)
        t = dve.tt([t], z, z, u, ALU.mult)
        t = dve.tt([t], z2, z, z, ALU.mult)
        yield
        t = dve.ts([t], p, z2, 2.0 / 17, ALU.mult)
        for c in (15, 13, 11, 9, 7, 5, 3):
            t = dve.stt([t], p, p, 2.0 / c, z2, ALU.add, ALU.mult)
            if c in (11, 3):
                yield
        t = dve.stt([t], p, p, 2.0, z, ALU.add, ALU.mult)
        t = dve.stt([t], d, d, 0.0, p, ALU.max, ALU.add)
        t1 = dve.ts([t, ta], dA[:, :], d, K.small[0:32, 0:1], ALU.mult, -1.0, ALU.mult)
        t2 = dve.fill([t], z2, 0.0)
        t3 = dve.do([t1, t2], lambda e: e.tensor_tensor_scan(Acs[:, :], dA[:, :], z2, 0.0, ALU.add, ALU.add))
        yield
        yield
        b = B[7]
        tt = pe.tr([t3, K.t_cst, b.free], ident,
                   *[(b[:, 32 * i:32 * (i + 1)], d[:, P * i:P * (i + 1)]) for i in range(2)],
                   *[(b[:, 64 + 32 * i:96 + 32 * i], Acs[:, P * i:P * (i + 1)]) for i in range(2)])
        t4 = dve.copy([tt], dtT[:, :, :], b[:, 0:64].rearrange("p (i h) -> p i h", i=2))
        t5 = dve.copy([tt], AcsT[:, :, :], b[:, 64:128].rearrange("p (i h) -> p i h", i=2))
        b.free = [t4, t5]
        t_dt.append([t3, t4, t5])
        yield

    dense = [B[0], B[1], B[2]]
    drain(layer(S, ["dt"], h, evac_dt, dense, steps=1))

    late = []

    def silu_late():
        for made, o, t in late:
            made.append(act.act([t], o, o, ACT.Silu))
        late.clear()

    def conv(dst, tile0, made):
        def evac(pairno, bank, done):
            t, js = [], (2 * pairno, 2 * pairno + 1)
            src = [bank[:, T * i:T * (i + 1)] for i in range(2)]
            for i, j in enumerate(js):
                f = tile0 + j
                t.append(act.act([done, t_par], dst[:, j, :], src[i], ACT.Identity, bias=par[:, C_CONVB + f:C_CONVB + f + 1],
                                 scale=par[:, C_CONVW + 96 + f:C_CONVW + 97 + f]))
            silu_late()
            for n in range(1, 4):
                for i, j in enumerate(js):
                    k = C_CONVW + 32 * (3 - n) + tile0 + j
                    o = dst[:, j, n:T]
                    t[i] = dve.stt([t] if n == 1 else [t[i]], o, src[i][:, 0:T - n], par[:, k:k + 1], o, ALU.mult, ALU.add)
            late.extend((made, dst[:, j, :], t[i]) for i, j in enumerate(js))
            return t
        return evac

    B_made, C_made, xs_made = [], [], []
    side = weave(layer(S, [("B", i) for i in range(4)], h, conv(Bm, 16, B_made), dense, steps=1), steps_dt(), 1)
    weave(layer(S, [("C", i) for i in range(4)], h, conv(Cm, 24, C_made), dense, steps=1), side, 1)
    drain(side)
    drain(layer(S, [("xs", i) for i in range(8)], h, conv(xs, 0, xs_made), dense))
    silu_late()

    y_made = [None] * 16

    def ssd():
        bT, bC, bR = B[3], B[4], [B[5], B[6]]
        xT_made, xT_free, CB_made, CB_free = {}, {}, {}, {}
        E_free, sc_free = {}, {}

        def group(g):
            q = g % 2
            tt = pe.tr([bT.free, xs_made[2 * g], xs_made[2 * g + 1], K.t_cst], ident,
                       *[(bT[:, T * i + P * f:T * i + P * (f + 1)], xs[:, 2 * g + f, P * i:P * (i + 1)])
                         for i in range(2) for f in range(2)])
            tc = pe.mm([bC.free, B_made[g], C_made[g]],
                       (bC[:, 0:T], Bm[:, g, 0:P], Cm[:, g, :], True, True),
                       (bC[:, T:384], Bm[:, g, P:T], Cm[:, g, P:T], False, True))
            t = dve.tt([tt, t_dt, xT_free.get(g - 2)], xT[:, q, :, :].rearrange("p i (h d) -> p i h d", h=4),
                       bT[:, :].rearrange("p (i h d) -> p i h d", i=2, h=4),
                       dtT[:, :, 4 * g:4 * g + 4].unsqueeze(3).to_broadcast([P, 2, 4, 64]), ALU.mult)
            bT.free = [t]
            xT_made[g] = [t, tt]
            t = dve.tt([tc, t_mask, CB_free.get(g - 2)], CBm[:, q, :], bC[:, 0:384], mask[:, :], ALU.mult)
            bC.free = [t]
            CB_made[g] = [t]

        def decay(n):
            r, h0, bank = n % 2, 2 * n, bR[n % 2]
            tr = pe.mm([bank.free, t_dt], *[(bank[:, T * j:T * (j + 1)], ident[0:32, h0 + j:h0 + j + 1].to_broadcast([32, P]),
                                             Acs[:, :], j == 0, True) for j in range(2)])
            te = []
            for j in range(2):
                te.append(act.act([tr, E_free.get(n - 2)], E[:, r, j, 0:T], bank[:, T * j:T * (j + 1)], ACT.Relu, scale=-1.0,
                                  bias=AcsT[:, 0, h0 + j:h0 + j + 1]))
                te.append(act.act([tr, E_free.get(n - 2)], E[:, r, j, T:384], bank[:, T * j + P:T * (j + 1)], ACT.Relu,
                                  scale=-1.0, bias=AcsT[:, 1, h0 + j:h0 + j + 1]))
            bank.free = te
            E_made[n] = act.act([te], E[:, r, :, :], E[:, r, :, :], ACT.Exp, scale=-1.0)

        def score(n):
            r, g = n % 2, n // 2
            t = dve.tt([E_made[n], CB_made[g], sc_free.get(n - 2)], sc[:, r, :, :], E[:, r, :, :],
                       CBm[:, g % 2, :].unsqueeze(1).to_broadcast([P, 2, 384]), ALU.mult)
            E_free[n] = [t]
            CB_free.setdefault(g, []).append(t)
            sc_made[n] = [t]

        def output(n):
            r, g, i = n % 2, n // 2, n % 2
            bY = (B[7], B[1])[r]
            calls = []
            for st in range(2):
                for j in range(2):
                    o = bY[64 * j:64 * (j + 1), 0:T] if st == 0 else bY[64 * j:64 * (j + 1), P:T]
                    w_ = xT[:, g % 2, st, P * i + 64 * j:P * i + 64 * (j + 1)]
                    calls.append((o, w_, sc[:, r, j, 0:T] if st == 0 else sc[:, r, j, T:384], st == 0, st == 1))
            ty = pe.mm([bY.free, sc_made[n], xT_made[g]], *calls)
            sc_free[n] = [ty]
            xT_free.setdefault(g, []).append(ty)
            t = dve.stt([ty, xT_made[g]], xs[:, n, :], xs[:, n, :], par[:, C_D + n:C_D + n + 1], bY[:, 0:T], ALU.mult, ALU.add)
            bY.free = [t]
            y_made[n] = t

        E_made, sc_made = {}, {}
        group(0)
        yield
        decay(0)
        yield
        for n in range(16):
            if n + 1 < 16:
                decay(n + 1)
            score(n)
            yield
            if n:
                output(n - 1)
                yield
            if n % 2 == 0 and n + 2 < 16:
                group(n // 2 + 1)
                yield
        output(15)
        yield

    side = ssd()

    u_ready, u_made = [], []
    st = dict(tmp_free=[t_dt])

    def conv3(f):
        if f < 8:
            o, i = tmp[:, f % 2, :], f // 2
            a = dve.ts([ch_made[i], st["tmp_free"]], o, ch[:, f, :], par[:, C_SCW + 16 + f:C_SCW + 17 + f], ALU.mult)
            for k in (1, 2):
                w = C_SCW + 8 * (2 - k) + f
                a = dve.stt([a], o[:, k:T], ch[:, f, 0:T - k], par[:, w:w + 1], o[:, k:T], ALU.mult, ALU.add)
            u_made.append(a)

    def evac_b(i):
        def evac(_, bank, done):
            a = dve.tt([done, u_made, st["tmp_free"]], tmp[:, 2:4, :], halves(bank[:, :]), tmp[:, 0:2, :], ALU.mult)
            for n in range(2):
                u_ready.append(split_x(K, s_hi, s_lo, 2 * i + n, tmp[:, 2 + n, :], [a], pool))
            st["tmp_free"] = u_ready[-2:]
            return [a]
        return evac

    def jobs(n, later=0, share=True):
        last, m = st["mod"], modulation(K, S, n, share)
        st["mod"] = m
        yield lambda: next(last, None)
        for _ in range(later):
            yield lambda: None
        yield lambda: next(m)
        yield lambda: (next(m), drain(last))

    st["mod"] = iter(())
    dense = [B[0], B[2]]
    conv3(0)
    conv3(1)
    for i in range(4):
        weave(layer(S, [("sc_b", i)], h, evac_b(i), dense, steps=4), side, 1)
        conv3(2 * i + 2)
        conv3(2 * i + 3)

    yb_made = [None] * 8

    def evac_sc(i):
        def evac(_, bank, done):
            yb_made[2 * i] = yb_made[2 * i + 1] = t = act.act([done, u_made], yb[:, 2 * i:2 * i + 2, :], halves(bank[:, :]))
            return [t]
        return evac

    for i in range(4):
        weave(layer(S, [("sc_out", i)], (s_hi, s_lo, u_ready), evac_sc(i), dense, steps=4), side, 1, jobs(6 + i) if i > 1 else ())

    ga = K.buf("ga", A + 48, [P, 8, T])
    ga_made = [None] * 8
    gate_free = [[], []]

    def evac_gb(i):
        def evac(_, bank, done):
            q = i % 2
            t = act.act([done, gate_free[q]], gate[:, q, :, :], halves(bank[:, :]), ACT.Tanh, scale=0.5)
            t2 = pool.ts([t], gate[:, q, :, :], gate[:, q, :, :], 0.5, ALU.mult, 0.5, ALU.add)
            o = yb[:, 2 * i:2 * i + 2, :]
            t2 = pool.tt([t2, yb_made[2 * i]], o, o, gate[:, q, :, :], ALU.mult)
            yb_made[2 * i] = yb_made[2 * i + 1] = t2
            gate_free[q] = [t2]
            return [t]
        return evac

    def evac_ga(i):
        def evac(_, bank, done):
            o = ga[:, 2 * i:2 * i + 2, :]
            t = act.act([done, yb_made], o, halves(bank[:, :]), ACT.Tanh, scale=0.5)
            t2 = pool.ts([t], o, o, 0.5, ALU.mult, 0.5, ALU.add)
            ga_made[2 * i] = ga_made[2 * i + 1] = t2
            return [t]
        return evac

    for i in range(4):
        weave(layer(S, [("gb", i)], h, evac_gb(i), dense, steps=4), side, 1, jobs(10 + i))
    weave(layer(S, [("ga", 0)], h, evac_ga(0), dense, steps=4), side, 1, jobs(14))
    drain(side)

    tz = K.buf("tz", A + 32, [P, 2, 2, T])
    sqz = K.buf("sqz", A + 36, [P, 2, 2, T])
    yn = K.buf("yn", A + 40, [P, 2, T])
    r8 = K.buf("r8", A + 42, [P, 8, 2])
    K.prod, K.prod_also = K.buf("prod2", A + 44, [P, D]), y_made
    y_hi = K.buf("y_hi", A + 68, [P, 16, T], F32R)
    y_lo = K.buf("y_lo", A + 84, [P, 16, T], F32R)
    tz_free, sq_free, sq_made, g_made, r_made = [[y_made], [y_made]], [[y_made], [y_made]], {}, [], {}
    ms, rb = [B[3], B[6]], [B[4], B[5]]
    y_ready = []
    yn_free = [[y_made, K.prod_free], [y_made]]

    def evac_z(g):
        def evac(_, bank, done):
            q, y = g % 2, xs[:, 2 * g:2 * g + 2, :]
            t = act.act([done, tz_free[q]], tz[:, q, :, :], halves(bank[:, :]), ACT.Silu)
            t2 = dve.tt([t, y_made], y, y, tz[:, q, :, :], ALU.mult)
            tz_free[q] = [t2]
            g_made.append(t2)
            sq_made[g] = act.act([t2, sq_free[q]], sqz[:, q, :, :], y, ACT.Square)
            return [t]
        return evac

    def mean_square(g):
        if g < 0:
            return
        q, b, n = g % 2, ms[g // 4], g % 4
        sq_free[q] = st["ms"] = pe.mm([sq_made[g], b.free if n == 0 else []],
                                      *[(b[:, 2 * n + i:2 * n + i + 1], sqz[:, q, f, P * i:P * (i + 1)], K.c["mean"][:, 0:1], n + i + f == 0, True)
                                        for i in range(2) for f in range(2)])

    def roots(n):
        o, b = r8[:, 4 * n:4 * n + 4, :], ms[n]
        t = act.act([st["ms"], y_made], o, b[:, 0:8].rearrange("p (g i) -> p g i", i=2), ACT.Sqrt, scale=4.0, bias=par[:, C_EPS:C_EPS + 1])
        b.free = [t]
        t = dve.recip([t], o, o)
        for g in range(4):
            r_made[4 * n + g] = t

    def norm_y(groups):
        def lo(f, i, a):
            yn_free[i] = [a, dve.tt([a], y_lo[:, f, :], yn[:, i, :], y_hi[:, f, :].bitcast(F32), ALU.subtract)]
            y_ready.append(yn_free[i])

        late = None
        for g in groups:
            if g % 2 == 0:
                b = rb[g // 2 % 2]
                t_b = pe.mm([r_made[g], b.free], *[(b[:, T * j + P * i:T * j + P * (i + 1)], r8[:, g + j, i:i + 1].to_broadcast([P, P]), ident[:, :],
                                                   i + j == 0, True) for j in range(2) for i in range(2)])
                made = []
            for i in range(2):
                f = 2 * g + i
                t = dve.stt([t_b, g_made[g], yn_free[i]], yn[:, i, :], xs[:, f, :], par[:, C_NORM + f:C_NORM + f + 1],
                            b[:, T * (g % 2):T * (g % 2 + 1)], ALU.mult, ALU.mult)
                made.append(t)
                if late:
                    lo(*late)
                late = (f, i, act.act([t], y_hi[:, f, :], yn[:, i, :]))
            b.free = made
            yield
        lo(*late)

    side = iter(())
    for g in range(8):
        if g < 5:
            more = jobs(15 + g)
        else:
            more = [lambda: roots(0), lambda: (next(st["mod"]), drain(st["mod"]))] if g == 5 else []
        if g == 6:
            side = every(2, norm_y(range(4)))
        weave(layer(S, [("z", g)], h, evac_z(g), dense, steps=4), side, 1, [lambda: mean_square(g - 2), *more])
    weave(layer(S, [("ga", 1)], h, evac_ga(1), dense, steps=4), side, 1,
          [lambda: mean_square(6), lambda: None, lambda: (mean_square(7), roots(1))])
    drain(side)
    side = chained(iter((0, 0)), norm_y(range(4, 8)))
    for i in (2, 3):
        weave(layer(S, [("ga", i)], h, evac_ga(i), dense, steps=4), side, 1)
    drain(side)

    m_hi = K.buf("m_hi", A, [P, 8, T], F32R)
    m_lo = K.buf("m_lo", A + 8, [P, 8, T], F32R)
    m_ready = []

    def evac_ssd(pairno):
        def evac(_, bank, done):
            out = []
            for i in range(2):
                j = 2 * pairno + i
                t = dve.tt([done, ga_made[j]], ga[:, j, :], bank[:, T * i:T * (i + 1)], ga[:, j, :], ALU.mult)
                out.append(t)
                t = dve.tt([t, yb_made[j]], ga[:, j, :], ga[:, j, :], yb[:, j, :], ALU.add)
                m_ready.append(split_x(K, m_hi, m_lo, j, ga[:, j, :], [t], pool))
            return out
        return evac

    xa = K.buf("xa", A + 16, [P, 8, T])
    v = K.buf("v", A + 24, [P, 8, T])
    sq1 = K.buf("sq1", A + 32, [P, 8, T])
    x1 = K.buf("x1", A + 40, [P, 8, T])
    setup_late(K)
    t_xa = K.load(xa[:, :, :], K.ins["xT"].rearrange("p (j t) -> p j t", t=T), after=[y_ready], queue=act)
    for i in range(4):
        weave(layer(S, [("ssd_out", 2 * i), ("ssd_out", 2 * i + 1)], (y_hi, y_lo, y_ready), evac_ssd(i), dense, nk=16), (), 0, jobs(20 + i, 1, False))
    drain(st["mod"])
    t_xa = act.act([t_xa], xa[:, :, :], xa[:, :, :], ACT.Copy, scale=ALPHA)

    v_ready = []

    def evac_o(pairno, bank, done):
        for i in range(2):
            j = 2 * pairno + i
            v_ready.append(dve.stt([done, t_xa, K.mod_ready[16 + j]], v[:, j, :], bank[:, T * i:T * (i + 1)],
                                   K.mod[:, 16 + j:17 + j], xa[:, j, :], ALU.mult, ALU.add))
        return v_ready[-2:]

    gains, scale = par[:, C_LN1G:C_LN1G + 8], K.mod[:, 32:40]
    w_sq = K.buf("ln_wsq", A + 61, [P, 8, 2])
    w_v = K.buf("ln_wv", A + 61.125, [P, 8, 3])
    b0 = K.buf("ln_b0", A + 61.25, [P, 8])
    bs = K.buf("ln_bs", A + 61.3125, [P, 8])
    two8 = K.buf("ln_two8", A + 61.375, [P, 2, 8])
    ln_mean, ln_two = K.small[:, 16:18], K.small[:, 18:20]
    ln = dict(w_sq=w_sq, w_v=w_v, bs=bs, mean=ln_mean, two=ln_two)

    def prepare_mean():
        b = B[6]
        t = pe.mm([b.free], (b[:, 0:16], K.c["mean"][:, :], par[:, C_LN1G:C_LN1G + 16], True, True))
        b.free = st["ln"] = [dve.do([t], lambda e: e.tensor_reduce(ln_mean, b[:, 0:16].rearrange("p (n j) -> p n j", n=2), AX, ALU.add))]
        t = dve.ts([st["ln"]], b0[:, :], par[:, C_LN1B:C_LN1B + 8], ln_mean[:, 1:2], ALU.subtract)
        t1 = dve.tt([t], two8[:, 0, :], b0[:, :], b0[:, :], ALU.mult)
        t2 = dve.tt([t], two8[:, 1, :], b0[:, :], gains, ALU.mult)
        st["ln"] = [t1, t2, dve.fill([], w_sq[:, :, 0], 1.0 / D), dve.stt([], w_sq[:, :, 1], gains, 1.0 / D, gains, ALU.mult, ALU.mult),
                    dve.fill([], w_v[:, :, 0], 1.0 / D), dve.ts([], w_v[:, :, 1], gains, 1.0 / D, ALU.mult),
                    dve.ts([t2], w_v[:, :, 2], two8[:, 1, :], 1.0 / D, ALU.mult), dve.tt([t, K.mod_ready[32:40]], bs[:, :], b0[:, :], scale, ALU.mult)]

    def prepare_two():
        b = B[7]
        t = pe.mm([st["ln"], b.free], (b[:, 0:16], K.c["mean"][:, :], two8[:, :, :].rearrange("p n j -> p (n j)"), True, True))
        t = dve.do([t], lambda e: e.tensor_reduce(ln_two, b[:, 0:16].rearrange("p (n j) -> p n j", n=2), AX, ALU.add))
        b.free = [t]
        ln["ready"] = [st["ln"], dve.ts([t], ln_two[:, 0:1], ln_two[:, 0:1], 1e-5, ALU.add)]

    bm, bv = B[4], B[5]
    for i in range(4):
        drain(layer(S, [("w_o", i)], (m_hi, m_lo, m_ready), lambda _, b, d, i=i: evac_o(i, b, d), dense))
        if i == 0:
            prepare_mean()
        if i == 1:
            prepare_two()
        for j in range(max(0, 2 * i - 2), 2 * i if i < 3 else 8):
            t_m = pe.mm([v_ready[j], bm.free if j == 0 else []], (bm[:, 0:T], K.c["mean"][:, :], v[:, j, :], j == 0, j == 7))
            t_v = pe.mm([ln["ready"], bv.free if j == 0 else []],
                        *[(bv[:, 3 * n:3 * n + 3], v[:, j, P * n:P * (n + 1)], w_v[:, j, :], j + n == 0, j == 7) for n in range(2)])
    for i in range(RING, RING + 4):
        S.before[i] = m_ready
    S.late = 0
    return v, t_m, t_v, ln


def moe(K, S, v, t_m, t_v, ln, norm):
    pe, act, dve = K.pe, K.act, K.dve
    B, A, R = K.banks, AREA, AREA + 56
    par, ident = K.par, K.c["ident"]
    iota = K.c["iota"]

    h2 = K.buf("h2", A, [P, 8, T])
    h2_hi = K.buf("h2_hi", A + 8, [P, 8, T], F32R)
    h2_lo = K.buf("h2_lo", A + 48, [P, 8, T], F32R)
    sq2 = K.buf("sq2", A + 32, [P, 8, T])
    x1 = K.buf("x1", A + 40, [P, 8, T])
    n_hi = K.buf("n_hi", A + 16, [P, 2, D], F32R)
    n_lo = K.buf("n_lo", A + 32, [P, 2, D], F32R)
    hs = K.buf("hs", A + 112, [P, 2, T])
    hs_hi = K.buf("hs_hi", A + 65, [P, 2, T], F32R)
    hs_lo = K.buf("hs_lo", A + 115, [P, 2, T], F32R)

    vc = K.buf("ln_vc", A + 61.4375, [P, 2, 4])
    sc = K.buf("ln_sc", A + 61.5, [P, 2, 4])
    roots = K.buf("ln_roots", A + 61.5625, [P, 2, 4])
    q = K.buf("ln_q", A + 32, [P, 8, T])
    balpha = K.buf("ln_balpha", A + 67, [P, 8])
    bm, bv, bs, bn, b1, brr = B[4], B[5], B[6], B[7], B[1], B[3]
    mean, nm, ngb = (vc[:, :, n] for n in range(3))
    var, gg, w = (sc[:, :, n] for n in range(3))
    r, r1, rr = (roots[:, :, n] for n in range(3))

    def row(b, t, col):
        return pe.mm([t, b.free], *[(b[:, P * i:P * (i + 1)], col[:, i:i + 1].to_broadcast([P, P]), ident[:, :], i == 0, True) for i in range(2)])

    t_d = []
    for j in range(8):
        t_d.append(dve.tt([t_m], v[:, j, :], v[:, j, :], bm[:, 0:T], ALU.subtract))
        if j == 0:
            a = dve.copy([t_v], vc[:, :, 0:3], bv[:, 0:6].rearrange("p (i n) -> p i n", i=2))
            bv.free = [a]
        if j in (1, 2):
            o = vc[:, :, j]
            a = dve.stt([a], o, mean, (ln["mean"][:, 0:1], ln["two"][:, 1:2])[j - 1], o, ALU.mult, ALU.subtract)
            if j == 1:
                t_nm = a
    bm.free = [t_d]
    t_gb = a
    for j in range(8):
        t = act.act([t_d[j]], sq2[:, j, :], v[:, j, :], ACT.Square)
        t = pe.mm([t, bs.free if j == 0 else []],
                  *[(bs[:, 2 * i:2 * i + 2], sq2[:, j, P * i:P * (i + 1)], ln["w_sq"][:, j, :], j + i == 0, j == 7) for i in range(2)])
        if j == 3:
            t_nm = row(bn, t_nm, nm)
    t_sq = t
    e_made = []

    def some_e(n):
        for j in range(len(e_made), n):
            e_made.append(dve.stt([t_nm, t_d[j]], h2[:, j, :], v[:, j, :], par[:, C_LN1G + j:C_LN1G + j + 1], bn[:, 0:T], ALU.mult, ALU.add))

    t_alpha = dve.ts([], balpha[:, :], par[:, C_LN1B:C_LN1B + 8], ALPHA, ALU.mult)
    some_e(4)
    a = dve.copy([t_sq], sc[:, :, 0:2], bs[:, 0:4].rearrange("p (i n) -> p i n", i=2))
    bs.free = [a]
    t_r = act.act([a], r, var, ACT.Sqrt, bias=par[:, C_EPS:C_EPS + 1])
    t = dve.tt([t_gb], w, nm, nm, ALU.mult)
    a = dve.tt([a, t], gg, gg, w, ALU.subtract)
    some_e(6)
    t_r = dve.recip([t_r], r, r)
    a = dve.tt([a, t_r], gg, gg, r, ALU.mult)
    a = dve.stt([a], gg, ngb, -2.0, gg, ALU.mult, ALU.add)
    a = dve.tt([a], gg, gg, r, ALU.mult)
    a = act.act([a], r1, gg, ACT.Sqrt, bias=ln["two"][:, 0:1])
    early = act.act([t_r], K.small[:, 20:21], ln["two"][:, 0:1], ACT.Sigmoid)
    some_e(8)
    bn.free = e_made
    a = dve.recip([a], r1, r1)
    t_rr = dve.tt([a], rr, r, r1, ALU.mult)
    t_r1 = row(b1, a, r1)
    t_rr = row(brr, t_rr, rr)

    h2_ready, h2_split = [], []
    for j in range(8):
        t = act.act([t_r1, t_sq], q[:, j, :], b1[:, 0:T], ACT.Identity, scale=ln["bs"][:, j:j + 1], bias=K.mod[:, 24 + j:25 + j])
        a = dve.stt([t_rr], h2[:, j, :], h2[:, j, :], K.mod[:, 32 + j:33 + j], brr[:, 0:T], ALU.mult, ALU.mult)
        h2_ready.append(dve.tt([a, t], h2[:, j, :], h2[:, j, :], q[:, j, :], ALU.add))
    b1.free, brr.free = [t], [a]
    for j in range(8):
        h2_split.append(split_x(K, h2_hi, h2_lo, j, h2[:, j, :], [h2_ready[j]]))

    s = S.take("router")
    b = B[7]
    for k in range(8):
        w = s.raw[:, P * (k // 2) + 64 * (k % 2):P * (k // 2) + 64 * (k % 2) + 64]
        t = pe.mm([s.ready, h2_ready[k], b.free if k == 0 else []],
                  *[(b[:, 64 * i:64 * (i + 1)], h2[:, k, P * i:P * (i + 1)], w, k == 0 and i == 0, k == 7) for i in range(2)])
    s.done.append(t)
    sig = K.buf("sig", R, [P, 2, 64])
    bi = K.buf("bi", R + 0.5, [P, 2, 64])
    bm = K.buf("bm", R + 1, [P, 2, 64])
    mr = K.buf("mr", R + 1.5, [P, 2, 64])
    g8 = K.buf("g8", R + 2, [P, 16, 8])
    gt = K.buf("gt", R + 2.5, [P, 16, 8])
    eq = K.buf("eq", R + 3, [P, 16, 8])
    gs = K.buf("gs", R + 3.5, [P, 16])
    cnt = K.buf("cnt", R + 3.5625, [P, 16])
    mx = K.buf("mx", R + 3.625, [P, 2, 8])
    gsum = K.buf("gsum", R + 3.6875, [P, 2])
    M = K.buf("M", R + 4, [P, 2, 64], BF16)
    tri = K.buf("tri", R + 4.25, [P, P], BF16)
    ones = K.buf("ones", R + 4.5, [P, P], BF16)
    one_of = K.buf("one_of", R + 4.75, [64, 64], BF16)
    G = K.buf("G", R + 5, [P, 2, 64])
    Gs = K.buf("Gs", R + 5.5, [P, 2, 2, 64], F32R)
    rm = K.buf("rm", R + 6.5, [P, 2, 64])
    rmT = K.buf("rmT", R + 7, [64, T], BF16)
    flags = K.buf("flags", R + 7.5, [1, len(GROUPS)], I32)
    gc = K.buf("gc", R + 7.625, [P, 2])
    junk = K.buf("junk", R + 7.6875, [P, 8])
    order = K.buf("order", R + 7.75, [1, N_EXPERTS], I32)
    rmU = K.buf("rmU", R + 1.5, [P, 2, 64])
    kb = K.buf("kb", R + 2, [64, 64])
    tie = K.buf("tie", R + 2.25, [64, 64])
    Pi = K.buf("Pi", R + 2.5, [64, 64])
    Pib = K.buf("Pib", R + 2.75, [64, 64], BF16)
    rmTu = K.buf("rmTu", R + 3, [64, T], BF16)
    kc = K.buf("kc", R + 3.75, [64, 2])
    cb = K.buf("cb", R + 3.875, [64, 2], BF16)
    GT = K.buf("GT", R, [64, T])

    t_sig = act.act([t], sig[:, :, :], halves(b[:, 0:P]), ACT.Sigmoid)
    b.free = [t_sig]
    t = dve.copy([K.t_late], tri[:, :], K.c["tri"])
    t_bf = [t, dve.fill([], ones[:, :], 1.0), dve.copy([K.t_cst], one_of[:, :], ident[0:64, 0:64])]

    bias = K.c["router_bias"]
    t = dve.tt([t_sig, K.t_late], bi[:, :, :], sig[:, :, :], bias.unsqueeze(1).to_broadcast([P, 2, 64]), ALU.add)
    t = [dve.do([t], lambda e, i=i, g=g: e.max(out=g8[:, 8 * i + g, :], in_=bi[:, i, 8 * g:8 * g + 8]))
         for i in range(2) for g in range(8)]
    t = dve.tt([t], gs[:, :], g8[:, :, 0], g8[:, :, 1], ALU.add)
    one = gs[:, :].unsqueeze(2).to_broadcast([P, 16, 8])
    for i in range(2):
        a = slice(8 * i, 8 * i + 8)
        other = gs[:, a].unsqueeze(1).to_broadcast([P, 8, 8])
        one = gs[:, a].unsqueeze(2).to_broadcast([P, 8, 8])
        t1 = dve.tt([t], eq[:, a, :], other, one, ALU.is_equal)
        t2 = dve.tt([t], gt[:, a, :], other, one, ALU.is_gt)
        t1 = dve.tt([t1], eq[:, a, :], eq[:, a, :], K.c["before"].rearrange("p (g h) -> p g h", g=8), ALU.mult)
        t3 = dve.tt([t1, t2], gt[:, a, :], gt[:, a, :], eq[:, a, :], ALU.add)
        t3 = dve.do([t3], lambda e, a=a: e.tensor_reduce(cnt[:, a], gt[:, a, :], AX, ALU.add))
        t3 = dve.ts([t3], cnt[:, a], cnt[:, a], 4.0, ALU.is_ge, -1e30, ALU.mult)
        c = cnt[:, a].unsqueeze(2).to_broadcast([P, 8, 8])
        t3 = dve.tt([t3], bm[:, i, :].rearrange("p (g h) -> p g h", g=8), bi[:, i, :].rearrange("p (g h) -> p g h", g=8), c, ALU.add)
        t3 = dve.do([t3], lambda e, i=i: e.max(out=mx[:, i, :], in_=bm[:, i, :]))
        t3 = dve.do([t3], lambda e, i=i: e.match_replace(out=mr[:, i, :], in_to_replace=mx[:, i, :], in_values=bm[:, i, :], imm_value=-2e30))
        t_M = dve.tt([t3], M[:, i, :], mr[:, i, :], bm[:, i, :], ALU.is_lt)

    two = [B[5], B[6]]
    hs_ready = []
    st = {}

    def evac_gate(_, bank, done):
        st["g"] = act.act([done], hs[:, :, :], halves(bank[:, :]), ACT.Silu)
        return [st["g"]]

    def evac_up(_, bank, done):
        t = dve.tt([done, st["g"]], hs[:, :, :], halves(bank[:, :]), hs[:, :, :], ALU.mult)
        for i in range(2):
            hs_ready.append(split_x(K, hs_hi, hs_lo, i, hs[:, i, :], [t]))
        return [t]

    n_made = []
    for i in range(2):
        for q in range(2):
            b = B[2 * i + q]
            t = pe.tr([b.free, h2_ready], ident, *[(b[:, P * f:P * (f + 1)], h2[:, 4 * q + f, P * i:P * (i + 1)]) for f in range(4)])
            o = slice(512 * q, 512 * (q + 1))
            t1 = act.act([t], n_hi[:, i, o], b[:, :])
            t2 = dve.tt([t1], n_lo[:, i, o], b[:, :], n_hi[:, i, o].bitcast(F32), ALU.subtract)
            b.free = [t2]
            n_made.append(t2)

    drain(layer(S, ["sh_gate"], (h2_hi, h2_lo, h2_split), evac_gate, two))
    drain(layer(S, ["sh_up"], (h2_hi, h2_lo, h2_split), evac_up, two))
    S.before[RING + 4] = S.before[RING + 5] = [hs_ready]

    Pm = K.buf("Pm", A + 108, [P, 2, 2, P], F32R)
    PT = [K.buf("PT", A + 110, [P, 2, T], F32R)[:, q, :] for q in range(2)] + [K.buf("PT2", A + 64, [P, T], F32R)[:, :]]
    xg = K.buf("xg", A + 100, [P, 2, 8, P])
    sg = K.buf("sg", A + 112, [P, T])
    hm = K.buf("hm", A + 113, [P, T])
    hmT = K.buf("hmT", A + 114, [P, 2, P])
    y_hi = K.buf("ye_hi", A + 24, [P, 2, D], F32R)
    y_lo = K.buf("ye_lo", A, [P, 2, D], F32R)
    acc = B[0:4]
    free = {"xg0": [], "xg1": [], "sg": [hs_ready], "hm": [hs_ready]}
    made = {}

    def onehot(g, j, q):
        n = len(g)
        w = P // n
        made["P"] = dve.tt([made["rm"], K.t_late, free.get(f"P{q}")], Pm[:, q, :, :].rearrange("p i (e s) -> p i e s", e=n),
                           made["places"][:, :, g[0]:g[0] + n].unsqueeze(3).to_broadcast([P, 2, n, w]),
                           iota[:, w * j:w * (j + 1)].unsqueeze(1).unsqueeze(1).to_broadcast([P, 2, n, w]), ALU.is_equal)

    def gather(q):
        out = []
        for half in range(2):
            b = B[5 + half]
            t = pe.mm([made["P"], n_made, b.free, free[f"xg{q}"]],
                      *[(b[:, P * f:P * (f + 1)], n[:, i, 512 * half + P * f:512 * half + P * (f + 1)], Pm[:, q, i, :],
                         f == 0 and i == 0 and n is n_hi, False) for f in range(4) for i in range(2) for n in (n_hi, n_lo)])
            o, src = xg[:, q, 4 * half:4 * half + 4, :], b[:, :].rearrange("p (f s) -> p f s", f=4)
            out.append(act.act([t], o, src) if half == 0 else dve.copy([t], o, src))
            b.free = [out[-1]]
        made[f"xg{q}"] = out

    def places(g, j, q, z):
        n = len(g)
        w = P // n
        b = B[7]
        t = pe.mm([b.free, t_rm, made["P"], t_G, t_bf],
                  *[(b[w * e:w * (e + 1), 0:T], one_of[:, g[e]:g[e] + 1].to_broadcast([64, w]), rmT[:, :], True, True) for e in range(n)],
                  *[(b[:, T:T + 2 * n], Pm[:, q, i, :], Gs[:, i, :, g[0]:g[0] + n], False, i == 1) for i in range(2)])
        free[f"P{q}"] = [t]
        a = dve.ts([t, K.t_late, free.get(f"PT{z}")], PT[z], b[:, 0:T], K.c[f"slot{n}"][:, j:j + 1], ALU.is_equal)
        c = dve.do([t, free.get(f"gc{q}"), free.get("junk")],
                   lambda e: e.tensor_tensor_reduce(junk[:, 0:2 * n], b[:, T:T + 2 * n], K.c[f"of{n}"], 1.0, 0.0, ALU.mult, ALU.add,
                                                    gc[:, q:q + 1]))
        free["junk"] = [c]
        b.free = [a, c]
        made[f"PT{z}"], made[f"gc{q}"] = a, c

    def up(b, q, ws):
        n = len(ws) // 2
        w = P // n
        for half in range(2):
            calls = []
            for k in range(4 * half, 4 * half + 4):
                for e in range(n):
                    calls.append((b[w * e:w * (e + 1), :], xg[:, q, k, w * e:w * (e + 1)],
                                  ws[n * half + e].raw[:, 512 * (k % 4):512 * (k % 4 + 1)], k == 0, k == 7))
            mine = ws[n * half:n * (half + 1)]
            t = pe.mm([b.free if half == 0 else [], made[f"xg{q}"], [s.ready for s in mine]], *calls)
            for s in mine:
                s.done.append(t)
        free[f"xg{q}"] = [t]
        made["up"] = t

    def middle(b, q):
        t = act.act([made["up"], free.get("sg")], sg[:, :], b[:, 0:T], ACT.Silu)
        t = dve.stt([t, made[f"gc{q}"], free.get("hm")], hm[:, :], sg[:, :], gc[:, q:q + 1], b[:, T:2 * T], ALU.mult, ALU.mult)
        b.free = free["sg"] = free[f"gc{q}"] = [t]
        made["hm"] = t

    def turn(b):
        t = pe.tr([b.free, made["hm"]], ident, *[(b[:, P * k:P * (k + 1)], hm[:, P * k:P * (k + 1)]) for k in range(2)])
        free["hm"] = [t]
        t = act.act([t, free.get("hmT")], hmT[:, :, :], b[:, 0:T].rearrange("p (k s) -> p k s", k=2))
        b.free = [t]
        made["hmT"] = t

    def down(q, ws):
        out, w = [], P // len(ws)
        for n in range(2):
            b, o = B[5 + n], slice(512 * n, 512 * (n + 1))
            t = pe.mm([b.free, made["hmT"], [s.ready for s in ws]],
                      *[(b[w * e:w * (e + 1), :], hmT[:, k, w * e:w * (e + 1)], s.raw[:, D * k + 512 * n:D * k + 512 * (n + 1)],
                         k == 0, k == 1) for k in range(2) for e, s in enumerate(ws)])
            a = act.act([t, free[f"y{q}"]], y_hi[:, q, o], b[:, :])
            a = dve.tt([a], y_lo[:, q, o], b[:, :], y_hi[:, q, o].bitcast(F32), ALU.subtract)
            b.free = [a]
            out.append(a)
        for s in ws:
            s.done.append(t)
        free["hmT"] = [t]
        made[f"y{q}"] = out

    def combine(q, z):
        calls = []
        for m in range(8):
            o = acc[m // 2][:, T * (m % 2):T * (m % 2 + 1)]
            for y in (y_hi, y_lo):
                calls.append((o, y[:, q, P * m:P * (m + 1)], PT[z], False, False))
        t = pe.mm([made[f"y{q}"], made[f"PT{z}"]], *calls)
        free[f"y{q}"] = free[f"PT{z}"] = [t]
        made["acc"] = t

    t = dve.tt([t_M], G[:, :, :], sig[:, :, :], M[:, :, :], ALU.mult)
    t = dve.do([t], lambda e: e.tensor_reduce(gsum[:, :], G[:, :, :], AX, ALU.add))
    t = dve.recip([t], gsum[:, :], gsum[:, :])
    t_G = [dve.ts([t], G[:, i, :], G[:, i, :], gsum[:, i:i + 1], ALU.mult, 2.5, ALU.mult) for i in range(2)]

    bc, bq, bg, bu = B[7], B[6], B[4], B[5]
    t = pe.mm([bc.free, t_bf, t_M], (bc[:, 0:64], tri[:, :], M[:, 0, :], True, True),
              (bc[:, 64:P], ones[:, :], M[:, 0, :], False, False), (bc[:, 64:P], tri[:, :], M[:, 1, :], False, True),
              *[(bc[0:64, P:P + 64], ones[:, 0:64], M[:, i, :], False, i == 1) for i in range(2)],
              *[(bc[0:64, P + 64:P + 65], M[:, i, :], ones[:, 0:1], False, i == 1) for i in range(2)])
    t_row = row(bq, t_r, r)
    t_G = pe.tr([bg.free, t_G], ident, *[(bg[0:64, P * i:P * (i + 1)], G[:, i, :]) for i in range(2)])
    s = S.take("sh_down")
    for n, (_, k0, m0) in enumerate(s.tiles):
        m, k = m0 // P, k0 // P
        o = B[m // 2][:, T * (m % 2):T * (m % 2 + 1)]
        wh, wl = s.hi[:, P * n:P * (n + 1)], s.lo[:, P * n:P * (n + 1)]
        first = k == 0 and m % 2 == 0
        t_acc = pe.mm([s.ready, hs_ready[k], B[m // 2].free if first else []],
                      (o, wh, hs_hi[:, k, :], first, False), (o, wh, hs_lo[:, k, :], False, False),
                      (o, wl, hs_hi[:, k, :], False, False))
    s.done.append(t_acc)

    own = K.c["own"]
    t_rm = dve.tt([t], rmU[:, :, :], halves(bc[:, 0:P]), M[:, :, :], ALU.mult)
    made["rm"], made["places"] = t_rm, rmU
    onehot(GROUPS[0], 0, 0)
    t1 = dve.tt([t], kb[:, :], bc[0:64, P:P + 64], K.c["bump"][0:64, :], ALU.add)
    t2 = dve.tt([t], kc[:, 0:1], bc[0:64, P + 64:P + 65], own[0:64, 0:1], ALU.add)
    t3 = dve.copy([t], cb[:, 0:1], bc[0:64, P + 64:P + 65])
    t4 = dve.copy([K.t_late], cb[:, 1:2], own[0:64, 1:2])
    bc.free = [t1, t2, t3, t_rm]
    t1 = dve.stt([t1, t2], tie[:, :], kb[:, :], kc[:, 0:1], K.c["upto"][0:64, :], ALU.is_equal, ALU.mult)
    t1 = dve.stt([t1], kb[:, :], kb[:, :], kc[:, 0:1], tie[:, :], ALU.is_gt, ALU.add)
    t1 = dve.do([t1], lambda e: e.tensor_reduce(kc[:, 1:2], kb[:, :], AX, ALU.add))
    t_Pi = dve.ts([t1, K.t_late], Pi[:, :], iota[0:64, 0:64], kc[:, 1:2], ALU.is_equal)
    t_Pib = dve.copy([t_Pi], Pib[:, :], Pi[:, :])
    t_G = bg.free = [dve.copy([t_G], GT[:, :], bg[0:64, 0:T])]
    t_x1 = []
    for j in range(8):
        a = dve.stt([t_row], x1[:, j, :], v[:, j, :], par[:, C_LN1G + j:C_LN1G + j + 1], bq[:, 0:T], ALU.mult, ALU.mult)
        t_x1.append(act.act([a, t_alpha], x1[:, j, :], x1[:, j, :], ACT.Identity, bias=balpha[:, j:j + 1], scale=ALPHA))
    bq.free = [a]
    free["y0"] = free["y1"] = [n_made, h2_split, t_x1]

    t = pe.mm([bc.free, t_Pib, t3, t4], (bc[0:1, 0:64], cb[:, 1:2], Pib[:, :], True, True), (bc[0:1, 64:P], cb[:, 0:1], Pib[:, :], False, True))
    t1 = dve.copy([t], order[:, :], bc[0:1, 0:64])
    S.order, S.order_ready = order, [t1]
    t2 = dve.copy([t], K.small[0:1, 0:64], bc[0:1, 64:P])
    bc.free = [t1, t2]
    t = pe.tr([bu.free, t_rm], ident, *[(bu[0:64, P * i:P * (i + 1)], rmU[:, i, :]) for i in range(2)])
    t_rm = bu.free = [dve.copy([t], rmTu[:, :], bu[0:64, 0:T])]
    t = pe.mm([t_G, t_Pi], *[(bg[:, 64 * i:64 * (i + 1)], GT[:, P * i:P * (i + 1)], Pi[:, :], i == 0, True) for i in range(2)])
    t = dve.copy([t], Gs[:, :, 0, :], halves(bg[:, 0:P]))
    t_G = dve.tt([t], Gs[:, :, 1, :], halves(bg[:, 0:P]), Gs[:, :, 0, :].bitcast(F32), ALU.subtract)
    bg.free = [t_G]
    t1 = [dve.do([t2], lambda e, f=f, n=n, o=o: e.tensor_reduce(flags[:, o], K.small[0:1, f].rearrange("p (g e) -> p g e", e=n), AX, ALU.max))
          for f, n, o in ((slice(0, 4), 2, slice(0, 2)), (slice(4, 12), 1, slice(2, 10)), (slice(12, 32), 2, slice(10, 20)),
                          (slice(32, 64), 4, slice(20, 28)))]
    gather(0)
    t = pe.mm([bc.free, t_Pib, t_rm], *[(bc[:, 64 * i:64 * (i + 1)], rmTu[:, P * i:P * (i + 1)], Pib[:, :], i == 0, True) for i in range(2)],
              (bc[0:64, P:P + T], Pib[:, :], rmTu[:, :], False, True))
    a = dve.copy([t], rm[:, :, :], halves(bc[:, 0:P]))
    t2 = dve.copy([t], rmT[:, :], bc[0:64, P:P + T])
    bc.free = t_rm = [a, t2]
    made["rm"], made["places"] = t_rm, rm
    wu = [S.take(("expert", p, half, GROUPS[0])) for half in range(2) for p in GROUPS[0]]
    up(B[4], 0, wu)
    for q in (pe, act, dve):
        q.load_flags(t1, flags[:, :])
    places(GROUPS[0], 0, 0, 0)
    for i, g in enumerate(GROUPS):
        q, r = i % 2, 1 - i % 2
        then = GROUPS[i + 1] if i + 1 < len(GROUPS) else None
        if i:
            wu = [S.take(("expert", p, half, g)) for half in range(2) for p in g]
            up(B[4], q, wu)
        if then:
            onehot(then, 0, r)
        middle(B[4], q)
        if i:
            combine(r, r)
        turn(B[7])
        if then:
            gather(r)
            places(then, 0, r, r)
        wd = [S.take(("expert", p, 2, g)) for p in g]
        down(q, wd)
        flag = FLAGS.index(g)
        before = dict(free), [list(flat(b.free)) for b in B]
        for j in range(1, ROUNDS[len(g)]):
            for queue in (pe, act, dve):
                queue.branch(flag, P // len(g) * j, made["acc"] if j > 1 else [])
            onehot(g, j, q)
            gather(q)
            places(g, j, q, 2)
            up(B[7], q, wu)
            middle(B[7], q)
            turn(B[5])
            down(r, wd)
            combine(r, 2)
        for j in range(1, ROUNDS[len(g)]):
            for queue in (pe, act, dve):
                queue.close()
        for k, tokens in before[0].items():
            free[k] = list(dict.fromkeys(flat([free[k], tokens])))
        for b, tokens in zip(B, before[1]):
            b.free = list(dict.fromkeys(flat([b.free, tokens])))
    combine(1, 1)

    v3 = K.buf("v3", A + 16, [P, 8, T])
    sq3 = K.buf("sq3", A + 32, [P, 8, T])
    x2 = K.buf("x2", A + 40, [P, 8, T])
    v_ready, x2_ready = [], []
    for j in range(8):
        v_ready.append(dve.stt([made["acc"], t_x1, K.mod_ready[40 + j]], v3[:, j, :], acc[j // 2][:, T * (j % 2):T * (j % 2 + 1)],
                               K.mod[:, 40 + j:41 + j], x1[:, j, :], ALU.mult, ALU.add))
        acc[j // 2].free = [v_ready[-1]]

    def out_x2(j, t):
        x2_ready.append(act.act([t], x2[:, j, :], v3[:, j, :], ACT.Identity, bias=par[:, C_LN2B + j:C_LN2B + j + 1],
                                scale=par[:, C_LN2G + j:C_LN2G + j + 1]))
        if j % 2:
            norm.pair(j // 2, x2, x2_ready[j - 1:], after)

    after = [made["acc"]] + [s.done for s in S.user[RING:]]
    S.ahead(S.next + HIS, K.pool)
    layer_norm(K, v3, v_ready, sq3, B[4], B[5], [made["acc"]], out_x2)
    return x2, x2_ready, after, norm


def layer_across(S, keys, x, evac, banks):
    K = S.core
    hi, lo, ready = x
    mine = [banks[(K.turn + i) % len(banks)] for i in range(2)]
    K.turn += 2
    for n, key in enumerate(keys):
        s = S.take(key)
        for q in range(4):
            k = 4 * n + q
            w = slice(512 * q, 512 * (q + 1))
            first, last = k == 0, k == 4 * len(keys) - 1
            for i in range(2):
                b, t = mine[i], slice(P * i, P * (i + 1))
                after = [s.ready, ready[k], b.free if first else []]
                if s.split:
                    tok = K.pe.mm(after, (b[:, :], hi[:, k, t], s.hi[:, w], first, False), (b[:, :], lo[:, k, t], s.hi[:, w], False, False),
                                  (b[:, :], hi[:, k, t], s.lo[:, w], False, last))
                else:
                    tok = K.pe.mm(after, (b[:, :], hi[:, k, t], s.raw[:, w], first, last))
                if q == 3 and i == 1:
                    s.done.append(tok)
                if last:
                    b.free = evac(i, b, tok)
            yield


class Rms:

    def __init__(self, K, total, sq, r=None, gain=None, hi=None, lo=None):
        self.K, self.total, self.sq, self.r, self.gain, self.hi, self.lo = K, total, sq, r, gain, hi, lo
        self.ready = [None] * 8
        self.done = []

    def pair(self, n, x, ready, after=(), eng=None):
        K = self.K
        for j in (2 * n, 2 * n + 1):
            if self.hi is None:
                break
            c = K.par[:, self.gain + j:self.gain + j + 1]
            a = K.act.act([ready, after], self.hi[:, j, :], x[:, j, :], ACT.Copy, scale=c)
            b = K.dve.stt([a], self.lo[:, j, :], x[:, j, :], c, self.hi[:, j, :].bitcast(F32), ALU.mult, ALU.subtract)
            self.ready[j] = [a, b]
        eng = eng or K.pool
        o = x[:, 2 * n:2 * n + 2, :]
        t = eng.tt([ready, after, self.done], self.sq if n else self.total, o, o, ALU.mult)
        if n and eng is K.pool:
            t = eng.tt([t], self.total, self.total, self.sq, ALU.add)
        self.done = [t] if eng is K.pool else [self.done, t]

    def sums(self):
        o = self.total[:, 0, :]
        self.done = [self.K.pool.tt(self.done, o, o, self.total[:, 1, :], ALU.add)]

    def finish(self, bank, parts):
        root = InverseRoot(self.K, bank, 1)
        for n, p in enumerate(parts):
            root.add(self.done, p, n == 0, n == len(parts) - 1)
        t = root.columns()
        return root.row(t), (root.cols, t)

    def keep(self, bank):
        (row, t), cols = self.finish(bank, [self.total[:, 0, :]])
        t = self.K.act.act([t], self.r, row)
        bank.free = [t]
        return t, cols


def log1p_exp(dve, act, u, p, z, z2, t):
    t = act.act([t], u, u, ACT.Exp)
    t = dve.ts([t], z, u, 2.0, ALU.add)
    t = dve.recip([t], z, z)
    yield
    t = dve.tt([t], z, z, u, ALU.mult)
    t = dve.tt([t], z2, z, z, ALU.mult)
    t = dve.ts([t], p, z2, 2.0 / 17, ALU.mult)
    for c in (15, 13, 11, 9, 7, 5, 3):
        t = dve.stt([t], p, p, 2.0 / c, z2, ALU.add, ALU.mult)
    t = dve.stt([t], p, p, 2.0, z, ALU.add, ALU.mult)
    yield t


def fox_norm(K):
    A = AREA
    spare = K.buf("f_spare", A + 48, [P, 2, 2, T])
    return Rms(K, spare[:, 0, :, :], spare[:, 1, :, :], K.buf("f_r", A + 56, [P, T])[:, :], C_MIX,
               K.buf("f_hi", A, [P, 8, T], F32R), K.buf("f_lo", A + 8, [P, 8, T], F32R))


def fox(K, S, x2, x2_ready, after, norm, out):
    pe, act, dve, pool = K.pe, K.act, K.dve, K.pool
    B, A = K.banks, AREA
    par, ident = K.par, K.c["ident"]
    dense = B[0:5]

    q = K.buf("q", A + 16, [P, 8, T])
    sq = K.buf("f_sq", A + 24, [P, 8, T])
    v = K.buf("f_v", A + 32, [P, 2, 512])
    u = K.buf("f_u", A + 36, [P, 2, 512])
    og = K.buf("og", A + 57, [P, 4, T])
    r16 = K.buf("r16", A + 61, [16, T])
    c = K.buf("f_c", A + 62, [8, T])
    nc = K.buf("f_nc", A + 63, [8, T])
    f = K.buf("f_f", A + 64, [8, 5, T])
    cT = K.buf("f_cT", A + 69, [P, 2, 8])
    small = K.buf("f_small", A + 69.25, [P, 8, 6])
    lg = K.buf("lg", A + 70, [P, 2, 2, 384])
    at = K.buf("at", A + 76, [P, 2, T])
    heads = K.buf("heads", A + 78, [P, P])
    neg = K.buf("neg", A + 78.5, [P, 256])
    band = K.buf("band", A + 79.5, [P, 4, 384])
    pl = K.buf("pl", A + 86, [P, 4, T])
    pl_hi = K.buf("pl_hi", A + 90, [P, 4, T], F32R)
    pl_lo = K.buf("pl_lo", A + 94, [P, 4, T], F32R)
    cat_hi = K.buf("cat_hi", A + 98, [P, 8, T], F32R)
    cat_lo = K.buf("cat_lo", A + 106, [P, 8, T], F32R)
    pT = K.buf("pT", A + 114, [P, 2, 384])

    t_heads = K.load(heads[:, :], K.cst("heads"), after=after, queue=act)
    t_neg = K.load(neg[:, :], K.cst("neg"), after=after, queue=act)
    t_band = K.load(band[:, :, :], K.cst("band").rearrange("p (g t) -> p g t", g=4), after=after, queue=act)
    h = (norm.hi, norm.lo, norm.ready)
    st = {}
    r = norm.r
    twice = r.unsqueeze(1).to_broadcast([P, 2, T])
    waiting = []

    def later(evac):
        def f(n, bank, done):
            free = []
            todo = lambda: free.extend(evac(n, bank, done))
            if waiting is None:
                todo()
            else:
                waiting.append(todo)
            return free
        return f

    def evac_f(_, bank, done):
        t = dve.tt([done, st["r"]], f[:, 0, :], bank[0:8, 0:T], r[0:8, :], ALU.mult)
        st["f"] = act.act([t], f[:, 0, :], f[:, 0, :], ACT.Identity, bias=par[0:8, C_FB:C_FB + 1])
        return [t]

    def steps_c():
        x, w, p, z, z2 = (f[:, i, :] for i in range(5))
        t = dve.stt([st["f"]], w, x, -1.0, x, ALU.mult, ALU.min)
        for t in log1p_exp(dve, act, w, p, z, z2, t):
            yield
        t = dve.stt([t], w, x, 0.0, p, ALU.min, ALU.subtract)
        t = dve.do([t, dve.fill([], z2, 0.0)], lambda e: e.tensor_tensor_scan(c[:, :], w, z2, 0.0, ALU.add, ALU.add))
        t2 = dve.ts([t], nc[:, :], c[:, :], -1.0, ALU.mult)
        for _ in range(4):
            yield
        b = B[7]
        tt = pe.tr([t, b.free], ident, *[(b[:, 8 * i:8 * (i + 1)], c[:, P * i:P * (i + 1)]) for i in range(2)])
        t3 = dve.copy([tt], cT[:, :, :], b[:, 0:16].rearrange("p (i h) -> p i h", i=2))
        b.free = [t3]
        st["c"] = [t2, t3]
        yield

    q_made = [None] * 8
    sq_made = [None] * 8

    def evac_qk(half):
        def evac(pairno, bank, done):
            j = 4 * half + 2 * pairno
            t = dve.tt([done, st["r"]], q[:, j:j + 2, :], halves(bank[:, :]), twice, ALU.mult)
            q_made[j] = q_made[j + 1] = t
            sq_made[j] = sq_made[j + 1] = pool.tt([t], sq[:, j:j + 2, :], q[:, j:j + 2, :], q[:, j:j + 2, :], ALU.mult)
            return [t]
        return evac

    def rms():
        nonlocal waiting
        norm.sums()
        st["r"], (st["cols"], st["rT"]) = norm.keep(B[7])
        todo, waiting = waiting, None
        for t in todo:
            t()

    drain(layer(S, [("q", 0)], h, later(evac_qk(0)), dense), layer(S, ["hy_f"], h, later(evac_f), dense, steps=1))
    rms()
    evac = evac_qk(0)
    side = steps_c()
    side = weave(layer(S, [("q", 1)], h, lambda n, b, d: evac(1, b, d), dense), side, 1)
    side = weave(layer(S, [("k", 0), ("k", 1)], h, evac_qk(1), dense), side, 1)

    def qk_norm():
        b = B[6]
        for n in range(8):
            t = pe.mm([sq_made[n], t_heads, b.free if n == 0 else []], (b[0:16, 0:T], heads[:, 16 * n:16 * n + 16], sq[:, n, :], n == 0, n == 7))
        yield
        t = act.act([t], r16[:, :], b[0:16, 0:T], ACT.Sqrt, bias=par[0:16, C_QKE:C_QKE + 1])
        b.free = [t]
        t_r = dve.recip([t], r16[:, :], r16[:, :])
        yield
        for j in range(4):
            b = B[6 + j % 2]
            t = pe.mm([t_r, b.free], *[(b[64 * e:64 * (e + 1), T * m:T * (m + 1)],
                                        ident[0:16, 2 * (j + 4 * m) + e:2 * (j + 4 * m) + e + 1].to_broadcast([16, 64]), r16[:, :], m == 0, True)
                                       for m in range(2) for e in range(2)])
            out = []
            for m in range(2):
                n = j + 4 * m
                col = (C_QG, C_KG)[m]
                out.append(dve.stt([t, q_made[n]], q[:, n, :], q[:, n, :], par[:, col:col + 1], b[:, T * m:T * (m + 1)], ALU.mult, ALU.mult))
                q_made[n] = out[-1]
            b.free = out
            yield

    v_made, og_made, cat_ready = [None] * 2, [None] * 4, [None] * 8
    lg_free, pT_free, at_free = {}, [], [[], []]

    def attention():
        spans = ((0, P, 0), (P, 384, 1))
        p_made = {}

        def scores(j):
            calls = [[], []]
            for a, z, i in spans:
                for e in range(2):
                    n = 64 * e
                    calls[e].append((B[3 + e][:, a:z], q[n:n + 64, j, P * i:P * (i + 1)], q[n:n + 64, 4 + j, 0:z - a], a == 0, False))
            more = [[(B[3 + e][:, a:z], ident[0:8, 2 * j + e:2 * j + e + 1].to_broadcast([8, P]), nc[:, 0:z - a], False, True)
                     for a, z, i in spans] for e in range(2)]
            inter = [x for ab in zip(*calls) for x in ab]
            t = pe.mm([q_made[j], q_made[4 + j], st["c"], B[3].free, B[4].free], *inter, *more[0], *more[1])
            for e in range(2):
                h_, l = 2 * j + e, lg[:, j % 2, e, :]
                m = small[:, h_, :]
                made = []
                for a, z, i in spans:
                    made.append(dve.stt([t, st["c"], t_neg, lg_free.get((j - 2, e))], l[:, a:z], B[3 + e][:, a:z], cT[:, i, h_:h_ + 1],
                                        neg[:, 256 - (z - a):256], ALU.add, ALU.add))
                B[3 + e].free = made
                sums = []
                for a, z, i in spans:
                    t2 = dve.do([made[i]], lambda e_, l=l, a=a, z=z, i=i, m=m: e_.tensor_reduce(m[:, i:i + 1], l[:, a:z], AX, ALU.max, negate=True))
                    sums.append(act.act([t2], l[:, a:z], l[:, a:z], ACT.Exp, bias=m[:, i:i + 1], accum_out=m[:, 2 + i:3 + i]))
                t2 = dve.recip([sums], m[:, 4:6], m[:, 2:4])
                p_made[j, e] = [dve.ts([t2], l[:, a:z], l[:, a:z], m[:, 4 + i:5 + i], ALU.mult) for a, z, i in spans]

        def turn(j):
            for e in range(2):
                b = B[5 + e]
                t = pe.tr([p_made[j, e], b.free], ident, *[(b[:, P * n:P * (n + 1)], lg[:, j % 2, e, P * n:P * (n + 1)]) for n in range(3)])
                lg_free[j, e] = [t]
                t = act.act([t, pT_free], pT[:, e, :], b[:, 0:384])
                b.free = [t]
                p_made[j, e] = [t]

        def values(j):
            b = B[5]
            t = pe.mm([p_made[j, 0], p_made[j, 1], v_made, b.free],
                      *[(b[64 * e:64 * (e + 1), P * i:T], v[:, i, P * j + 64 * e:P * j + 64 * (e + 1)], pT[:, e, T * i:(T, 384)[i]], i == 0, i == 1)
                        for i in range(2) for e in range(2)])
            pT_free[:] = [t]
            m = j % 2
            t = dve.tt([t, og_made[j], at_free[m]], at[:, m, :], b[:, 0:T], og[:, j, :], ALU.mult)
            b.free = [t]
            cat_ready[j] = at_free[m] = split_x(K, cat_hi, cat_lo, j, at[:, m, :], [t])

        scores(0)
        yield
        scores(1)
        yield
        for j in range(4):
            turn(j)
            yield
            values(j)
            if j < 2:
                scores(j + 2)
            yield

    def evac_v(i, bank, done):
        v_made[i] = act.act([done, st["rT"]], v[:, i, :], bank[:, :], ACT.Copy, scale=st["cols"][:, i:i + 1])
        return [v_made[i]]

    u_made = [None] * 2

    def evac_u(i, bank, done):
        u_made[i] = act.act([done, st["rT"]], u[:, i, :], bank[:, :], ACT.Copy, scale=st["cols"][:, i:i + 1])
        return [u_made[i]]

    def evac_og(pairno, bank, done):
        o = og[:, 2 * pairno:2 * pairno + 2, :]
        t = dve.tt([done, st["r"]], o, halves(bank[:, :]), twice, ALU.mult)
        a = act.act([t], o, o, ACT.Tanh, scale=0.5)
        og_made[2 * pairno] = og_made[2 * pairno + 1] = pool.ts([a], o, o, 0.5, ALU.mult, 0.5, ALU.add)
        return [t]

    norm_qk = chained(side, qk_norm())
    weave(layer_across(S, [("v", 0), ("v", 1)], h, evac_v, dense), norm_qk, 1)
    drain(norm_qk)

    pl_ready = []

    def pooled():
        for g in range(4):
            b = dense[K.turn % 3]
            K.turn += 1
            t = pe.mm([u_made, t_band, b.free], (b[:, 0:T], u[:, 0, P * g:P * (g + 1)], band[:, g, 0:T], True, False),
                      (b[:, P:T], u[:, 1, P * g:P * (g + 1)], band[:, g, T:384], False, True))
            t = act.act([t], pl[:, g, :], b[:, 0:T])
            b.free = [t]
            pl_ready.append(split_x(K, pl_hi, pl_lo, g, pl[:, g, :], [t]))
            if g % 2:
                yield

    def mixed():
        s = S.take("pool")
        for g in range(4):
            b = dense[K.turn % 3]
            K.turn += 1
            wh, wl = s.hi[:, P * g:P * (g + 1)], s.lo[:, P * g:P * (g + 1)]
            t = pe.mm([s.ready, pl_ready[g], b.free], (b[:, 0:T], wh, pl_hi[:, g, :], True, False), (b[:, 0:T], wh, pl_lo[:, g, :], False, False),
                      (b[:, 0:T], wl, pl_hi[:, g, :], False, True))
            if g == 3:
                s.done.append(t)
            t = act.act([t], pl[:, g, :], b[:, 0:T], ACT.Copy, scale=par[:, C_PSC + g:C_PSC + g + 1])
            b.free = [t]
            cat_ready[4 + g] = split_x(K, cat_hi, cat_lo, 4 + g, pl[:, g, :], [t])
        yield

    x_ready = [None] * 8
    four = [B[0], B[1], B[2], B[7]]

    def project(n):
        s = S.take(("hy_out", n))
        for t, (_, k0, m0) in enumerate(s.tiles):
            k, m = k0 // P, m0 // P
            b = four[m // 2]
            o = b[:, T * (m % 2):T * (m % 2 + 1)]
            wh, wl = s.hi[:, P * t:P * (t + 1)], s.lo[:, P * t:P * (t + 1)]
            first, last = n == 0 and t % 2 == 0 and m % 2 == 0, n == 3 and t % 2 == 1
            tok = pe.mm([s.ready if t == 0 else [], b.free if first else [], cat_ready[k]],
                        (o, wh, cat_hi[:, k, :], first, False), (o, wh, cat_lo[:, k, :], False, False), (o, wl, cat_hi[:, k, :], False, last))
            if last and m % 2:
                i = slice(m - 1, m + 1)
                e = dve.tt([tok], x2[:, i, :], halves(b[:, :]), x2[:, i, :], ALU.add)
                b.free = [e]
                x_ready[m - 1] = x_ready[m] = e
                out(m // 2, x2, [e])
            if t % 4 == 3:
                if t == 15:
                    s.done.append(tok)
                yield

    S.lo_engines = (pool,)
    side = attention()
    next(side)
    dense = B[0:3]
    fill = chained(layer(S, [("og", 0)], h, evac_og, dense, steps=4), layer_across(S, [("u", 0), ("u", 1)], h, evac_u, dense), pooled(),
                   layer(S, [("og", 1)], h, lambda _, b, d: evac_og(1, b, d), dense, steps=4), mixed(), project(0), project(1))
    for n, _ in enumerate(fill):
        if n % 3 == 2:
            next(side, None)
    drain(side)
    drain(project(2), project(3))
    S.lo_engines = (dve,)
    return x2, x_ready


def ffn_norm(K, n):
    A = AREA
    spare = K.buf(f"g{n}_spare", A + 16, [P, 2, 2, T])
    return Rms(K, spare[:, 0, :, :], spare[:, 1, :, :], K.buf(f"g{n}_r", A + 24, [P, T])[:, :], C_FFN + 8 * n,
               K.buf(f"g{n}_hi", A, [P, 8, T], F32R), K.buf(f"g{n}_lo", A + 8, [P, 8, T], F32R))


def ffn(K, S, n, x, x_ready, norm, out, after=()):
    pe, act, dve, pool = K.pe, K.act, K.dve, K.pool
    B, A = K.banks, AREA
    dense = B[0:4]
    sg = K.buf(f"g{n}_sg", A + 25, [P, 2, 2, T])
    mid = K.buf(f"g{n}_mid", A + 29, [P, 2, T])
    m_hi = K.buf(f"g{n}_mhi", A + 48, [P, 22, T], F32R)
    m_lo = K.buf(f"g{n}_mlo", A + 70, [P, 22, T], F32R)
    h = (norm.hi, norm.lo, norm.ready)
    twice = norm.r.unsqueeze(1).to_broadcast([P, 2, T])
    m_ready = []
    free, sg_free = [[], []], [[], []]
    st = {}
    waiting = []
    K.turn += (3 - K.turn) % 4

    late, last = [], []

    def rest():
        for m, t in last:
            free[m % 2] = split_x(K, m_hi, m_lo, m, mid[:, m % 2, :], [t, after], pool)
            m_ready.append(free[m % 2])
        last.clear()
        for m, t in late:
            q = m % 2
            a = act.act([t], sg[:, q, 0, :], sg[:, q, 0, :], ACT.Silu)
            last.append((m, dve.tt([a, free[q]], mid[:, q, :], sg[:, q, 1, :], sg[:, q, 0, :], ALU.mult)))
            sg_free[q] = [last[-1][1]]
        late.clear()

    def evac(m, bank, done):
        rest()
        t = dve.tt([done, st["r"], sg_free[m % 2], after], sg[:, m % 2, :, :], halves(bank[:, :]), twice, ALU.mult)
        late.append((m, t))
        return [t]

    def later(m):
        def f(_, bank, done):
            if m > 1:
                return evac(m, bank, done)
            free = []
            waiting.append(lambda: free.extend(evac(m, bank, done)))
            return free
        return f

    for m in range(22):
        drain(layer(S, [("gate_up", n, m)], h, later(m), dense))
        if m == 1:
            norm.sums()
            st["r"], _ = norm.keep(B[7])
            for t in waiting:
                t()
    rest()
    rest()

    def evac_down(pairno, bank, done):
        o = x[:, 2 * pairno:2 * pairno + 2, :]
        t = dve.tt([done], o, halves(bank[:, :]), o, ALU.add)
        ready[2 * pairno] = ready[2 * pairno + 1] = t
        out(pairno, x, [t])
        return [t]

    ready = [None] * 8
    drain(layer(S, [("down", n, i) for i in range(11)], (m_hi, m_lo, m_ready), evac_down, dense, nk=22))
    return x, ready


def rwkv_norm(K):
    spare = K.buf("r_spare", AREA + 32, [P, 2, 2, T])
    return Rms(K, spare[:, 0, :, :], spare[:, 1, :, :])


def rwkv(K, S, x, x_ready, norm, out):
    pe, act, dve, pool = K.pe, K.act, K.dve, K.pool
    B, A, Q = K.banks, AREA, RING_KB + 8 * NARROW
    par, ident = K.par, K.c["ident"]
    dense = B[0:4]

    h = K.buf("r_h", A, [P, 8, T])
    xx = K.buf("r_xx", A + 8, [P, 8, T])
    mixes = {c: K.buf(f"mix_{c}", kb, [P, 8, T]) for c, kb in dict(w=A + 48, a=A + 56, k=Q + 16, r=A + 16, v=A + 24, g=A + 48).items()}
    mix_hi = {c: K.buf(f"hi_{c}", kb, [P, 8, T], F32R) for c, kb in dict(r=A + 56).items()}
    mix_lo = {c: K.buf(f"lo_{c}", kb, [P, 8, T], F32R) for c, kb in dict(r=A + 16).items()}
    ar = K.buf("ar", A + 64, [P, 8, 512])
    bk = K.buf("bk", A + 80, [P, 8, 512])
    sig = K.buf("r_sig", A + 72, [P, 8, T])
    lora = K.buf("lora", A + 104.25, [P, 2, T])
    sum16 = K.buf("sum16", A + 116, [P, P])
    cmask = K.buf("cmask", A + 116.5, [P, 256])
    cols = K.buf("r_cols", A + 117.5, [P, 8])
    Pt = K.buf("Pt", A + 96, [P, 8, 260])
    kkn = [K.buf(f"kkn{i}", kb, [P, 2 * T]) for i, kb in enumerate((A + 108.25, A + 38))]
    sq = K.buf("r_sq", A + 34, [P, 2, T])
    tmp = [[K.buf(f"r_tmp{i}{q}", kb + 2 * q, [P, 2 * T]) for q in range(2)] for i, kb in enumerate((A + 48, A + 112))]
    inv = K.buf("r_inv", A + 36, [P, 2, 16])
    going = K.buf("r_going", A + 110.25, [P, T])
    k_raw = K.buf("k_raw", Q, [P, 8, T])
    iP = K.buf("iP", Q + 8, [P, 8, T])
    PL = K.buf("PL", A + 117.53125, [P, 8, 4])

    def both(buf, j, n, which):
        ap = buf[:, j:j + n, :]
        return bass.AP(tensor=ap.tensor, offset=ap.offset + 64 * which, ap=[list(ap.ap[0]), [256, 2 * n], [64 if which else 192, 2], [1, 64]])

    quads = lambda ap: ap.rearrange("p (i q t) -> p i q t", q=2, t=64)
    flat2 = lambda buf, j: buf[:, j:j + 2, :].rearrange("p j t -> p (j t)")

    t_sum = K.load(sum16[:, :], K.cst("sum16"), after=x_ready, queue=act)
    t_mask = K.load(cmask[:, :], K.cst("chunk"), after=x_ready, queue=act)
    t_going = pool.fill([x_ready], going[:, :], 1.0)
    t_going = pool.fill([t_going], going[:, 0:T:64], 0.0)
    t_one = pool.fill([x_ready], Pt[:, :, :].rearrange("p j (c t) -> p j c t", c=4)[:, :, :, 0], 1.0)
    t_omka = pool.ts([K.t_par], cols[:, :], par[:, C_KA:C_KA + 8], -1.0, ALU.mult, 1.0, ALU.add)
    (rr, t_r), _ = norm.finish(B[7], [norm.total[:, 0, :], norm.total[:, 1, :], norm.sq[:, 0, :], norm.sq[:, 1, :]])
    h_made, xx_made = [None] * 8, [None] * 8
    mixed = {c: [None] * 8 for c in "rwkvag"}

    def shift(n):
        pair = slice(2 * n, 2 * n + 2)
        for j in (2 * n, 2 * n + 1):
            m = C_MIX + 8 + j
            h_made[j] = dve.stt([t_r], h[:, j, :], x[:, j, :], par[:, m:m + 1], rr, ALU.mult, ALU.mult)
        a = pool.ts([h_made[pair]], xx[:, pair, 0:1], h[:, pair, 0:1], -1.0, ALU.mult)
        b = (pool if n else dve).tt([h_made[pair]], xx[:, pair, 1:T], h[:, pair, 0:T - 1], h[:, pair, 1:T], ALU.subtract)
        xx_made[2 * n] = xx_made[2 * n + 1] = [a, b]

    def mix(c, after=()):
        for n in range(4):
            for j in (2 * n, 2 * n + 1):
                m = C_MU + 8 * "rwkvag".index(c) + j
                mixed[c][j] = dve.stt([h_made[j], xx_made[j], after], mixes[c][:, j, :], xx[:, j, :], par[:, m:m + 1], h[:, j, :], ALU.mult, ALU.add)
            yield

    def halve(c, after=()):
        pairs = [slice(2 * n, 2 * n + 2) for n in range(4)]
        made = [act.act([mixed[c][pair], after], mix_hi[c][:, pair, :], mixes[c][:, pair, :]) for pair in pairs]
        for pair, a in zip(pairs, made):
            b = dve.tt([a], mix_lo[c][:, pair, :], mixes[c][:, pair, :], mix_hi[c][:, pair, :].bitcast(F32), ALU.subtract)
            mixed[c][pair] = [[a, b]] * 2
            yield

    def product(c):
        return (mix_hi[c], mix_lo[c], mixed[c]) if c in mix_hi else (mixes[c], None, mixed[c])

    first = mix("w")
    shift(0)
    for n in range(4):
        if n < 3:
            shift(n + 1)
        next(first)
    B[7].free = [h_made]
    drain(mix("a"), mix("k"))
    st = {}
    S.lead = 1

    def last():
        return [S.slots[S.next - 1].done]

    low_made = {}
    sig_made, a_made = [None] * 8, [None] * 8

    def evac_lora(n, func):
        def evac(_, bank, done):
            low_made[n] = act.act([done], lora[:, n, :], bank[:, 0:T], func)
            return [low_made[n]]
        return evac

    def evac_sig(dst, col, made):
        def evac(pairno, bank, done):
            for i in range(2):
                j = 2 * pairno + i
                made[j] = act.act([done], dst(j), quads(bank[:, T * i:T * (i + 1)]), ACT.Sigmoid, bias=par[:, col + j:col + j + 1])
            return [made[2 * pairno], made[2 * pairno + 1]]
        return evac

    drain(layer(S, ["wa1"], product("w"), evac_lora(0, ACT.Tanh), dense, steps=1, half=0))
    drain(layer(S, ["wa1"], product("a"), evac_lora(1, ACT.Copy), dense, steps=1, half=1))
    t_low1 = last()
    drain(layer(S, ["wa2"], (lora, None, [low_made[0]]), evac_sig(lambda j: quads(sig[:, j, :]), C_W0, sig_made), dense, nk=1, steps=1, half=0))
    drain(layer(S, ["wa2"], (lora[:, 1:2, :], None, [low_made[1]]), evac_sig(lambda j: both(bk, j, 1, 1), C_A0, a_made), dense, nk=1, steps=1, half=1))
    t_low2 = last()

    cdec = float(np.exp(-0.5))
    alpha, beta, kappa, rho, P_made, iP_made, PL_made = ([None] * 4 for _ in range(7))
    steps_of = Pt[:, :, :].rearrange("p j (c t) -> p j c t", c=4)
    logs = [dve.do([sig_made[j], t_going], lambda e, j=j: e.tensor_tensor_scan(
        sig[:, j, :], going[:, :], sig[:, j, :], 0.0, ALU.mult, ALU.add)) for j in range(8)]
    drain(mix("r"))
    for n in range(4):
        pair = slice(2 * n, 2 * n + 2)
        decay = Pt[:, pair, :].rearrange("p j (i q t) -> p (j i) q t", i=2, q=2)
        P_made[n] = tp = act.act([logs[pair], t_one], decay[:, :, :, 1:65], quads(flat2(sig, 2 * n)), ACT.Exp, scale=-cdec)
        ti = act.act([logs[pair]], flat2(iP, 2 * n), flat2(sig, 2 * n), ACT.Exp, scale=cdec)
        iP_made[n] = [tp, ti]
        PL_made[n] = pool.copy([tp], PL[:, pair, :], steps_of[:, pair, :, 64])

    drain(halve("r", t_low1), mix("v"))

    k_made, sq_free = [None] * 8, [t_r]

    def evac_k(n):
        def evac(_, bank, done):
            nonlocal sq_free
            j = 2 * n
            t = act.act([done], k_raw[:, j:j + 2, :], halves(bank[:, :]))
            k_made[j] = k_made[j + 1] = t
            made = [act.act([done, sq_free], sq[:, i, :], bank[:, T * i:T * (i + 1)], ACT.Square, scale=par[:, C_KK + j + i:C_KK + j + i + 1]) for i in range(2)]
            st["sq", n] = made
            sq_free = []
            return [t, made]
        return evac

    def root(n):
        nonlocal sq_free
        ss, o = B[4 + n % 2], inv[:, :, 4 * n:4 * n + 4]
        t = pe.mm([st["sq", n], t_sum, ss.free], *[
            (ss[:, 4 * i + 2 * m:4 * i + 2 * m + 2], sq[:, m, P * i:P * (i + 1)], sum16[:, 18 * (2 * n + m):18 * (2 * n + m) + 2], i + m == 0, True)
            for m in range(2) for i in range(2)])
        sq_free = [t]
        ss.free = t = act.act([t], o, ss[:, 0:8].rearrange("p (i h) -> p i h", i=2), ACT.Sqrt)
        t = dve.ts([t], o, o, 1e-12, ALU.max)
        return dve.recip([t], o, o)

    kkn_free, tmp_free = [[], []], [[], []]

    def prepare(n):
        t_inv = st["inv"] = root(n)
        j, q = 2 * n, n % 2
        decay = Pt[:, j:j + 2, :].rearrange("p j (i q t) -> p (j i) q t", i=2, q=2)
        inverse = quads(flat2(iP, j))
        tk, tb = tmp[q][0][:, :], tmp[q][1][:, :]
        tka = []
        for i in range(2):
            o, c = slice(T * i, T * (i + 1)), j + i
            tka.append(act.act([a_made[c], t_omka, t_low1, tmp_free[q]], quads(tk[:, o]), both(bk, c, 1, 1), ACT.Identity,
                               scale=par[:, C_KA + c:C_KA + c + 1], bias=cols[:, c:c + 1]))
        t = dve.tt([tka, k_made[j]], tk, tk, flat2(k_raw, j), ALU.mult)
        kappa[n] = dve.tt([t, iP_made[n]], both(bk, j, 2, 0), quads(tk), inverse, ALU.mult)
        yield
        b = B[6 + q]
        t = pe.mm([t_inv, b.free], *[
            (b[64 * e:64 * (e + 1), T * m + P * i:T * m + P * (i + 1)],
             inv[:, i, 2 * (j + m) + e:2 * (j + m) + e + 1].to_broadcast([P, 64]), ident[:, :], m + i == 0, True)
            for m in range(2) for i in range(2) for e in range(2)])
        kk = []
        for i in range(2):
            o, c = slice(T * i, T * (i + 1)), j + i
            kk.append(dve.stt([t, k_made[c], kkn_free[q]], kkn[q][:, o], k_raw[:, c, :], par[:, C_KK + c:C_KK + c + 1], b[:, o], ALU.mult, ALU.mult))
        b.free = kk
        t = dve.tt([kk, a_made[j:j + 2], tmp_free[q]], quads(tb), quads(kkn[q][:, :]), both(bk, j, 2, 1), ALU.mult)
        alpha[n] = dve.stt([kk, iP_made], both(ar, j, 2, 1), quads(kkn[q][:, :]), -1.0, decay[:, :, :, 0:64], ALU.mult, ALU.mult)
        beta[n] = dve.tt([t, iP_made[n], tka], both(bk, j, 2, 1), quads(tb), inverse, ALU.mult)
        kkn_free[q] = [alpha[n], t]
        tmp_free[q] = [kappa[n], beta[n]]
        yield

    drain(layer(S, [("rw_k", 0)], product("k"), evac_k(0), dense))
    for n in range(3):
        part = layer(S, [("rw_k", n + 1)], product("k"), evac_k(n + 1), dense, steps=8)
        side = prepare(n)
        for i, _ in enumerate(part):
            if i in (1, 3):
                next(side)
            if i == 4:
                S.ahead(S.find(("rw_r", n)).index + 1)
    t_k = last()

    def evac_r(n):
        def evac(_, bank, done):
            decay = Pt[:, 2 * n:2 * n + 2, :].rearrange("p j (i q t) -> p (j i) q t", i=2, q=2)
            rho[n] = dve.tt([done, iP_made], both(ar, 2 * n, 2, 0), quads(bank[:, :]), decay[:, :, :, 1:65], ALU.mult)
            return [rho[n]]
        return evac

    ur = lambda c: slice(64 * (1 - c % 2), 64 * (2 - c % 2))
    vr = lambda c: slice(64 * (c % 2), 64 * (c % 2) + 64)
    UV = K.buf("UV", A + 96, [P, 4, D])
    bv = K.buf("bv", A, [P, 2, D])
    g = K.buf("r_g", A + 8, [P, 2, D])
    stat = K.buf("stat", 10 - 0.25, [P, 2, 32])
    bonus = K.buf("bonus", A + 117.65625, [P, 2, 16])
    V_made = [[[], []] for _ in range(4)]
    bv_made, g_made = [[[], []], [[], []]], [[], []]
    raw_done = [rho, alpha, P_made]
    held = []

    def evac_v(n):
        def evac(i, bank, done):
            held.append((i, n, bank, done))
            return []
        return evac

    def center():
        per = lambda ap: ap.rearrange("p (h v) -> p h v", h=8)
        for i, n, bank, done in held:
            o, mean = slice(512 * n, 512 * (n + 1)), stat[:, i, 8 * n:8 * n + 8]
            t = dve.do([done, bank.free], lambda e, mean=mean, bank=bank: e.tensor_reduce(mean, per(bank[:, :]), AX, ALU.add))
            made = []
            for c in (2 * i, 2 * i + 1):
                V_made[c][n] = dve.stt([t, raw_done], per(UV[vr(c), c, o]), mean[vr(c)].unsqueeze(2).to_broadcast([64, 8, 64]), -1.0 / 64,
                                       per(bank[vr(c), :]), ALU.mult, ALU.add)
                made.append(V_made[c][n])
            t = dve.tt([done, mixed["g"], t_bonus], per(bv[:, i, o]), per(bank[:, :]), bonus[:, i, 8 * n:8 * n + 8].unsqueeze(2).to_broadcast([P, 8, 64]), ALU.mult)
            bv_made[i][n] = t
            bank.free = [made, t]
            yield

    LT = K.buf("LT", A + 32, [P, 2, 16, 64])
    Zb = K.buf("Zb", A + 112, [P, 32, 32])
    Tm = K.buf("Tm", Q + 12, [P, 32, 32])
    prod = K.buf("r_prod", Q + 8, [P, 1024])
    TT = K.buf("TT", Q, [P, 32, 64])
    T11 = K.buf("T11", Q + 8, [P, 32, 32])
    strict = cmask[:, 64:128]
    lt_made = []
    every, upper, second = slice(0, P), [slice(0, 32), slice(64, 96)], [slice(32, 64), slice(96, P)]
    t_TT = []

    def turn(after, out, out_dims, in_, in_dims, rows):
        return dve.do(after, lambda e: e.transpose(out.rearrange(out_dims)[rows], in_.rearrange(in_dims)[rows]))

    def pairs_of_tokens():
        for i in range(2):
            for e in range(2):
                b, r_, calls = B[4 + 2 * i + e], slice(64 * e, 64 * e + 64), []
                for j in range(8):
                    for q in range(2):
                        o = 128 * (2 * i + q) + 64 * (1 - q)
                        calls.append((b[ur(q), 64 * j:64 * (j + 1)], bk[r_, j, o:o + 64], ar[r_, j, o:o + 64], j == 0, True))
                t = pe.mm([alpha, beta, b.free], *calls)
                yield
                t = dve.tt([t, t_mask], LT[:, i, e::2, :], b[:, :].rearrange("p (h t) -> p h t", h=8),
                           strict.unsqueeze(1).to_broadcast([P, 8, 64]), ALU.mult)
                b.free = [t]
                lt_made.append(t)
        t = [pool.fill([beta, kappa], Tm[:, :, :], 0.0)]
        st["unit"] = t = [pool.fill(t, Tm[:, :, :].rearrange("p i c -> p (i c)")[:, 0:1024:33], 1.0)]
        st["zero"] = [pool.fill(t, TT[:, :, 0:32], 0.0)]
        yield
        t = []
        for rows in (every, *second):
            half = 32 * (rows is not every)
            t = turn([lt_made, kappa, t], Zb[:, :, :], "p s t -> p t s", LT[:, :, :, half:half + 32], "p i h t -> p t (i h)", rows)
        st["Z"] = t
        yield

    def invert():
        t = [st["unit"], st["Z"]]
        for j in range(31):
            m, n = 31 - j, j + 1
            o = prod[:, 0:m * n].rearrange("p (i c) -> p i c", i=m)
            t = dve.tt(t, o, Zb[:, j, n:32].unsqueeze(2).to_broadcast([P, m, n]), Tm[:, j, 0:n].unsqueeze(1).to_broadcast([P, m, n]), ALU.mult)
            t = dve.tt([t], Tm[:, n:32, 0:n], Tm[:, n:32, 0:n], o, ALU.add)
            yield
        t11 = turn([t], T11[:, :, :], "p h s -> p s h", Tm[:, :, :], "p m s -> p s m", every)
        t = [t11, st["zero"]]
        for rows in (every, *upper):
            half = 32 * (rows is every)
            t = turn([t], TT[:, :, half:half + 32], "p h t -> p t h", Tm[:, :, :], "p t s -> p t s", rows)
        t_TT.extend([t11, t])

    rk_in = [K.buf(f"rk{n}", A + 16 + 2 * n, [P, 2 * T])[:, :] for n in range(2)]

    def bonuses():
        v = sum16[:, :].rearrange("p (j h) -> p j h", j=8)
        t_rk = pool.tt([st["inv"]], v, v, par[:, C_RK:C_RK + 8].unsqueeze(2).to_broadcast([P, 8, 16]), ALU.mult)
        b = B[7]
        t = []
        for half in range(2):
            made = [pool.tt([rho, kappa, beta, t], quads(rk_in[n % 2]), both(ar, 2 * n, 2, 0), both(bk, 2 * n, 2, 0), ALU.mult)
                    for n in (2 * half, 2 * half + 1)]
            yield
            t = pe.mm([made, t_rk, b.free if half == 0 else []], *[
                (b[:, 16 * i:16 * (i + 1)], rk_in[n][:, T * f + P * i:T * f + P * (i + 1)], sum16[:, 16 * (4 * half + 2 * n + f):16 * (4 * half + 2 * n + f) + 16],
                 half + n + f + i == 0, half + n + f == 3) for n in range(2) for f in range(2) for i in range(2)])
            yield
        st["rk"] = [t]
        st["bonus"] = act.act([t], bonus[:, :, :], b[:, 0:32].rearrange("p (i h) -> p i h", i=2))
        b.free = [st["bonus"]]

    def beside(main, *sides):
        for i, _ in enumerate(main):
            for side, start, per in sides:
                for _ in range(int(per * (i + 1 - start)) - int(per * (i - start)) if i >= start else 0):
                    next(side, None)

    Gm = [K.buf(f"Gm{c}", (A + 56, A + 16, A + 48, A + 56)[c], [P, 16, P]) for c in range(4)]
    G_made = [[], [], [], []]
    ring = B[6:8]

    def spot():
        K.turn += 1
        return ring[K.turn % len(ring)]

    def products(c, after, eng):
        m = cmask[:, P * (c % 2):P * (c % 2 + 1)]
        for n in range(4):
            b, calls = spot(), []
            e, h0 = n % 2, n // 2 * 8 + n % 2
            r_ = slice(64 * e, 64 * e + 64)
            for f in range(4):
                j = n // 2 * 4 + f
                calls.append((b[:, P * f:P * (f + 1)], bk[r_, j, P * c:P * (c + 1)], ar[r_, j, P * c:P * (c + 1)], f == 0, True))
            t = pe.mm([rho, kappa, b.free], *calls)
            o, f = Gm[c][:, h0:h0 + 7:2, :], b[:, :].rearrange("p (h t) -> p h t", h=4)
            if eng is pool:
                b.free = t = act.act([t, after], o, f)
                f = o
            t = eng.tt([t, after], o, f, m.unsqueeze(1).to_broadcast([P, 4, P]), ALU.mult)
            if eng is dve:
                b.free = [t]
            G_made[c].append(t)
            yield

    bkT = [K.buf(f"bkT{c}", kb, [P, 8, P]) for c, kb in enumerate((A + 112, Q + 12, Q + 16))]
    bkT_made = [[], [], []]

    def turned(c, after):
        for n in range(2):
            b = spot()
            t = pe.tr([beta, kappa, b.free], ident, *[(b[:, P * f:P * (f + 1)], bk[:, 4 * n + f, P * c:P * (c + 1)]) for f in range(4)])
            t = act.act([t, after], bkT[c][:, 4 * n:4 * n + 4, :], b[:, :].rearrange("p (j k) -> p j k", j=4))
            b.free = [t]
            bkT_made[c].append(t)
            yield

    scaled = [[], [], [], []]

    def scale(c):
        o = ar[:, :, P * c:P * (c + 1)]
        scaled[c] = [dve.tt([G_made[c], lt_made, st["rk"], PL_made], o, o, PL[:, :, c - 1:c].to_broadcast([P, 8, P]), ALU.mult)]
        yield

    R0 = K.buf("R0", Q + 8, [P, D])
    SB = K.buf("SB", Q + 20, [P, 8, P])
    up = lambda q: upper[1 - q]
    low = lambda q: second[1 - q]
    TT_made = [[], []]
    t_W = []

    def lower():
        t11 = [None] * 2
        for i in range(2):
            b = B[4 + i]
            t = pe.mm([t_TT[0], lt_made, b.free], *[(b[low(q), 32 * n:32 * n + 32], LT[up(q), i, n, 32:64], T11[up(q), 16 * i + n, :], n == 0, True)
                                                    for n in range(16) for q in range(2)])
            made = []
            for q in range(2):
                o, f = T11[low(q), 16 * i:16 * i + 16, :], b[low(q), :].rearrange("p (h c) -> p h c", h=16)
                made.append(dve.copy([t, made], o, f) if q else act.act([t], o, f))
            b.free = t11[i] = made
            yield
        for i in range(2):
            b = B[4 + i]
            t = pe.mm([t11[i], t_TT[0:2], b.free], *[(b[up(q), 32 * n:32 * n + 32], T11[low(q), 16 * i + n, :], TT[low(q), 16 * i + n, 32:64], n == 0, True)
                                                      for n in range(16) for q in range(2)])
            made = []
            for q in range(2):
                o, f = TT[up(q), 16 * i:16 * i + 16, 32:64], b[up(q), :].rearrange("p (h c) -> p h c", h=16)
                made.append(dve.copy([t, made], o, f) if q else act.act([t], o, f))
            b.free = made
            TT_made[i] = [t_TT, made]
            t_W[:] = [t]
            yield

    gl = K.buf("r_gl", Q + 16, [P, 2, T])
    lnw, lnb = (K.buf(n, A + 24 + kb, [P, D]) for n, kb in (("lnw", 0), ("lnb", 4)))
    gl_made = []

    def evac_gl(_, bank, done):
        gl_made.append(act.act([done, rho], gl[:, :, :], halves(bank[:, :]), ACT.Sigmoid))
        return gl_made[-1:]

    gw_made, gb_made = [None] * 2, [None] * 2

    def gate():
        s = S.take("g2")
        for i in range(2):
            for n in range(2):
                bank = spot()
                t, calls = slice(P * i, P * (i + 1)), []
                for k in range(2):
                    w = slice(D * k + 512 * n, D * k + 512 * (n + 1))
                    calls.append((bank[:, :], gl[:, k, t], s.raw[:, w], k == 0, k == 1))
                t = pe.mm([s.ready, gl_made, bank.free], *calls)
                bank.free = [act.act([t, mixed["g"]], g[:, i, 512 * n:512 * (n + 1)], bank[:, :])]
                g_made[i].append(bank.free)
                if n == 0:
                    yield
            t1 = pool.tt([t_ln, bv_made[i]], bv[:, i, :], bv[:, i, :], lnb[:, :], ALU.add)
            gb_made[i] = pool.tt([t1, g_made[i]], bv[:, i, :], bv[:, i, :], g[:, i, :], ALU.mult)
            gw_made[i] = pool.tt([gb_made[i], t_ln], g[:, i, :], g[:, i, :], lnw[:, :], ALU.mult)
            if i:
                s.done.append(t)
                st["g2"] = [t]
            yield

    y = K.buf("r_y", A + 32, [P, 2, D])
    ysq = K.buf("ysq", A + 112, [P, D])
    o_hi = K.buf("o_hi", A + 80, [P, 8, T], F32R)
    o_lo = K.buf("o_lo", A + 88, [P, 8, T], F32R)
    out_made, o_ready = [[None, None], [None, None]], [[] for _ in range(8)]
    y_made, y_sq = [[None, None], [None, None]], [[], []]

    def weighed(i, half, after):
        o = slice(512 * half, 512 * (half + 1))
        rows = slice(0, P) if i == 0 else vr(2)
        y_sq[i].append(act.act([y_made[i][half], after], ysq[rows, o], y[rows, i, o], ACT.Square))
        y_made[i][half] = [pool.tt([y_made[i][half], gw_made[i], y_sq[i]], y[rows, i, o], y[rows, i, o], g[rows, i, o], ALU.mult)]

    def normed(i, half):
        h8, o = slice(8 * half, 8 * half + 8), slice(512 * half, 512 * (half + 1))
        per = lambda ap: ap.rearrange("p (h v) -> p h v", h=8)
        std = stat[:, i, 16 + 8 * half:24 + 8 * half]
        yi = y[:, i, o]
        st["summed"] = t = dve.do([y_sq[i]], lambda e: e.tensor_reduce(std, per(ysq[:, o]), AX, ALU.add))
        t = act.act([t], std, std, ACT.Sqrt, scale=1.0 / 64, bias=par[:, C_EPS + 2:C_EPS + 3])
        yield
        t = dve.recip([t], std, std)
        t = dve.tt([t, y_made[i][half]], per(yi), per(yi), std.unsqueeze(2).to_broadcast([P, 8, 64]), ALU.mult)
        out_made[i][half] = t
        yield

    turned_back = [[None, None], [None, None]]

    def bases(i, half):
        bank = B[6 - 2 * i + half]
        turned_back[i][half] = bank, pe.mm([gb_made[i], bank.free], *[
            (bank[:, P * f:P * (f + 1)], bv[:, i, P * (4 * half + f):P * (4 * half + f + 1)], ident[:, :], f == 0, False) for f in range(4)])
        yield

    def outs(i, half):
        b, t = turned_back[i][half]
        t = pe.mm([out_made[i][half], t], *[
            (b[:, P * f:P * (f + 1)], y[:, i, P * (4 * half + f):P * (4 * half + f + 1)], ident[:, :], False, True) for f in range(4)])
        yield
        src = b[:, :].rearrange("p (j t) -> p j t", j=4)
        hi, lo = (o[:, 4 * half:4 * half + 4, P * i:P * (i + 1)] for o in (o_hi, o_lo))
        ta = act.act([t, bkT_made, G_made], hi, src)
        tb = dve.tt([ta], lo, src, hi.bitcast(F32), ALU.subtract)
        b.free = [ta, tb]
        for f in range(4):
            o_ready[4 * half + f] += [ta, tb]
        yield

    hs = lambda half: range(8 * half, 8 * half + 8)
    U_made = [[[], []] for _ in range(4)]
    ry = lambda c, half: B[2 * (c % 2) + half]

    def values(c):
        for half in range(2):
            b = ry(c, half)
            st["av", c, half] = pe.mm([G_made[c], V_made[c], b.free], *[
                (b[r_, 64 * (n % 8):64 * (n % 8) + 64], Gm[c][vr(c), n, r_], UV[vr(c), c, 64 * n:64 * n + 64], n % 8 == 0, c == 0)
                for n in hs(half) for r_ in [slice(0, P) if n % 8 == 0 else ur(c)]])
            yield

    inverse = chained(pairs_of_tokens(), invert())
    part = layer(S, [("rw_r", 0)], product("r"), evac_r(0), B[0:4], steps=8)
    side = prepare(3)
    for i, _ in enumerate(part):
        if i in (1, 3):
            next(side)
    S.ahead(S.find(("rw_r", 3)).index + 1)
    mixing = mix("g", [beta, kappa])
    beside(layer(S, [("rw_r", 1)], product("r"), evac_r(1), B[0:4], steps=8), (inverse, 0, 1), (mixing, 0, 1))
    for n in range(2, 4):
        beside(layer(S, [("rw_r", n)], product("r"), evac_r(n), B[0:4], steps=8), (inverse, 0, 0.5))
    K.turn += -K.turn % 4
    bonus_steps = bonuses()
    beside(layer_across(S, [("rw_v0", 0), ("rw_v0", 1)], product("v"), evac_v(0), B[0:4]), (inverse, 0, 2), (bonus_steps, 0, 1))
    drain(bonus_steps)
    t_bonus = st["bonus"]
    centered = center()
    more = chained(products(0, rho, pool), turned(0, t_TT))
    levels = lower()
    beside(layer_across(S, [("rw_v1", 0), ("rw_v1", 1)], product("v"), evac_v(1), B[0:4]), (inverse, 0, 4), (more, 0, 1), (centered, 6, 1), (levels, 6, 1))
    t_v = last()
    t_ln = [K.load(o[:, :], K.ins["rw_ln"][n:n + 1, :].to_broadcast([P, D]), after=t_v, queue=act) for n, o in enumerate((lnw, lnb))]
    ring.pop()
    first = chained(values(0), products(1, st["rk"], dve))
    beside(layer(S, ["g1"], product("g"), evac_gl, B[7:8], steps=8), (levels, 0, 1), (centered, 0, 1), (more, 1, 1), (first, 3, 1))
    t_g1 = last()
    ring.append(B[7])
    t_SB = pool.fill([st["rk"], rho, t_g1], SB[:, :, :], 0.0)
    drain(levels, centered, more)

    R0_free, SB_made = [t_W], [t_SB, t_SB]
    second_made = chained(turned(1, t_TT), scale(1))
    gates = gate()
    filler = {(0, 0): ((first, 9), (gates, 1)), (0, 1): ((gates, 1),), (0, 2): ((second_made, 3),), (0, 3): ((values(1), 2),)}

    def fill(c, place):
        for gen, n in filler.get((c, place), ()):
            for _ in range(n):
                next(gen, None)

    for c in range(4):
        i = c // 2
        R0_made, S_read = [], []
        for half in range(2):
            b = ry(c, half)
            t = st["av", c, half]
            if c:
                t = pe.mm([SB_made[half], scaled[c], t], *[(b[:, P * f:P * (f + 1)], ar[:, 4 * half + f, P * c:P * (c + 1)], SB[:, 4 * half + f, :], False, False) for f in range(4)])
                S_read.append(t)
            o = R0[ur(c), 512 * half:512 * (half + 1)]
            R0_made.append(act.act([t, R0_free], o, b[ur(c), :]) if half else dve.copy([t, R0_free], o, b[ur(c), :]))
        if c and c < 3:
            for half in range(2):
                v = SB[:, 4 * half:4 * half + 4, :]
                SB_made[half] = [pool.tt([S_read[half]], v, v, PL[:, 4 * half:4 * half + 4, c - 1:c].to_broadcast([P, 4, P]), ALU.mult)]
        fill(c, 0)
        for half in range(2):
            b = ry(c, half)
            t = pe.mm([R0_made[half], TT_made[i]], *[
                (b[ur(c), 64 * (n % 8):64 * (n % 8) + 64], TT[ur(c), 16 * i + n, :], R0[ur(c), 64 * n:64 * n + 64], n % 8 == 0, True) for n in hs(half)])
            o = UV[ur(c), c, 512 * half:512 * (half + 1)]
            U_made[c][half] = act.act([t, raw_done], o, b[ur(c), :]) if half else dve.copy([t, raw_done], o, b[ur(c), :])
        R0_free = U_made[c]
        fill(c, 1)
        if c < 3:
            for half in range(2):
                b = B[4 + half]
                t = pe.mm([U_made[c][half], bkT_made[c][half], V_made[c], b.free], *[
                    (b[:, P * f:P * (f + 1)], bkT[c][:, 4 * half + f, :], UV[:, c, P * (4 * half + f):P * (4 * half + f + 1)], f == 0, True) for f in range(4)])
                made = []
                for e in range(2):
                    r_ = slice(64 * e, 64 * e + 64)
                    o = SB[r_, 4 * half:4 * half + 4, r_]
                    f = b[r_, :].rearrange("p (j k) -> p j k", j=4)[:, :, r_]
                    made.append(dve.tt([t, SB_made[half]], o, f, o, ALU.add) if c else dve.copy([t, SB_made[half]], o, f))
                b.free = SB_made[half] = made
        fill(c, 2)
        if c < 3:
            S.ahead(S.find(("rw_o", c)).index + 1)
        for half in range(2):
            b, o = ry(c, half), slice(512 * half, 512 * (half + 1))
            t = pe.mm([U_made[c][half], R0_made[half]], *[
                (b[vr(c), 64 * (n % 8):64 * (n % 8) + 64], Gm[c][r_, n, vr(c)], UV[r_, c, 64 * n:64 * n + 64], False, True)
                for n in hs(half) for r_ in [ur(c) if n % 8 == 0 else slice(0, P)]])
            if c < 3:
                b.free = t = act.act([t, t_W], y[vr(c), i, o], b[vr(c), :])
                y_made[i][half] = [y_made[i][half], t]
            else:
                st["y", half] = t
        if c == 0:
            two, three = products(2, t_g1, dve), products(3, t, dve)
            filler[1, 0] = filler[1, 1] = ((gates, 1),)
            filler[1, 2] = (two, 5), (scale(2), 1)
        if c == 1:
            filler[1, 3] = (turned(2, st["g2"]), 2), (values(2), 2)
            filler[2, 0] = filler[2, 1] = ((three, 2),)
            filler[2, 2] = (three, 1), (scale(3), 1)
            filler[2, 3] = (values(3), 2),
        fill(c, 3)
        if c == 1:
            for half in range(2):
                weighed(0, half, [])
            filler[2, 0] += ((normed(0, 0), 2),)
            filler[2, 1] += ((normed(0, 1), 2),)
        if c == 2:
            for half in range(2):
                weighed(1, half, st["summed"])
            filler[3, 0] = ((chained(bases(0, 0), bases(0, 1)), 2),)
            back = [[outs(i, half) for half in range(2)] for i in range(2)]
            filler[3, 1] = (back[0][0], 1), (back[0][1], 1)
            filler[3, 3] = ((chained(bases(1, 0), bases(1, 1)), 2),)
    rows, after = vr(3), [[], []]
    for half in range(2):
        for n, eng in ((half, act), (1 - half, dve)):
            b, o = ry(3, n), slice(512 * n, 512 * (n + 1))
            if eng is act:
                t = act.act([st["y", n], after[n]], ysq[rows, o], b[rows, :], ACT.Square)
                y_sq[1].append(t)
            else:
                t = dve.tt([st["y", n], after[n], gw_made[1]], y[rows, 1, o], b[rows, :], g[rows, 1, o], ALU.mult)
                y_made[1][n] = [y_made[1][n], t]
            after[n] = b.free = [after[n], t]
    for _ in zip(normed(1, 0), normed(1, 1)):
        pass
    for half in range(2):
        drain(back[0][half], back[1][half])

    x_ready = [None] * 8

    def evac_out(pairno, bank, done):
        o = x[:, 2 * pairno:2 * pairno + 2, :]
        t = dve.tt([done], o, halves(bank[:, :]), o, ALU.add)
        x_ready[2 * pairno] = x_ready[2 * pairno + 1] = t
        out(pairno, x, [t], o_ready)
        return [t]

    S.lead = HIS
    drain(layer(S, [("rw_o", i) for i in range(4)], (o_hi, o_lo, o_ready), evac_out, B[0:4]))
    return x, x_ready, o_ready


def tile_cols(v):
    v = np.asarray(v).reshape(-1)
    return v.reshape(-1, P).T


def pack(i):
    f = np.float32
    z = lambda r, c: np.zeros((r, c), f)
    mats = {
        "ada": i["w_ada"][0].T,
        "w_in": i["w_in"][0],
        "w_dt": np.concatenate([i["w_in"][0][:, 6144:6176], z(D, 96)], axis=1),
        "w_sc_out": i["w_sc_out"][0],
        "w_ssd_out": i["w_ssd_out"][0],
        "w_o": i["w_o"][0],
        "w_router": i["router_w"][0].reshape(4, 2, P, 64).transpose(0, 2, 1, 3).reshape(512, P),
        "hy_in": i["hy_w_in_2"][0],
        "w_f": np.concatenate([i["hy_w_in_2"][0][:, 2048:2056], z(D, 120)], axis=1),
        "pool_w": i["hy_pool_w_2"][0].reshape(512, P),
        "hy_out": i["hy_w_out_2"][0],
        "rw_w1": np.concatenate([i["rw_w1_2"][0], z(D, 64)], axis=1),
        "rw_w2": np.concatenate([i["rw_w2_2"][0], z(64, D)], axis=0),
        "rw_a1": np.concatenate([i["rw_a1_2"][0], z(D, 64)], axis=1),
        "rw_a2": np.concatenate([i["rw_a2_2"][0], z(64, D)], axis=0),
        "rw_g1": np.concatenate([i["rw_g1_2"][0], z(D, 96)], axis=1),
        "rw_g2": np.concatenate([i["rw_g2_2"][0], z(96, D)], axis=0),
        "rw_k": i["rw_w_k_2"][0],
        "rw_r": i["rw_w_r_2"][0],
        "rw_v": i["rw_w_v_2"][0],
        "rw_o": i["rw_w_o_2"][0],
        "sh_gate": i["sh_gate"][0],
        "sh_up": i["sh_up"][0],
        "sh_down": i["sh_down"][0],
    }
    for n in range(2):
        mats[f"ffn_gate{n}"], mats[f"ffn_up{n}"], mats[f"ffn_down{n}"] = i["ffn_w_gate_2"][n], i["ffn_w_up_2"][n], i["ffn_w_down_2"][n]
    slots = plan()
    slots = [x for x in slots if x[0][0] != "expert"]
    wts = np.empty(sum(len(t) for _, t, _ in slots) * P * P, f)
    at = 0
    for _, tiles, _ in slots:
        n = len(tiles)
        out = wts[at:at + n * P * P].reshape(P, n, P)
        for t, (m, r, c) in enumerate(tiles):
            out[:, t, :] = mats[m][r:r + P, c:c + P]
        at += n * P * P
    experts = np.empty((N_EXPERTS, 3, P, SLOT), f)
    for e in range(N_EXPERTS):
        up = np.concatenate([i["w_gate"][0][e], i["w_up"][0][e]], axis=1)
        experts[e, 0:2] = up.reshape(2, 4, P, 512).transpose(0, 2, 1, 3).reshape(2, P, SLOT)
        experts[e, 2] = i["w_down"][0][e].reshape(2, P, D).transpose(1, 0, 2).reshape(P, SLOT)
    cols = {
        "b_ada": i["b_ada"],
        "ssd_conv_w": i["ssd_conv_w"][0],
        "ssd_conv_b": i["ssd_conv_b"],
        "ssd_D": np.repeat(i["ssd_D"][0], 64),
        "ssd_norm_w": i["ssd_norm_w"],
        "sc_conv_w": i["sc_conv_w"][0],
        "ln1_g": i["ln1_g"],
        "ln1_b": i["ln1_b"],
        "ln2_g": i["ln2_g"],
        "ln2_b": i["ln2_b"],
        "mix_norm": i["mix_norm_2"],
        "ffn_norm": i["ffn_norm_2"],
        "dt_bias": np.concatenate([i["ssd_dt_bias"][0], np.zeros(96, f)]),
        "A_log": np.concatenate([i["ssd_A_log"][0], np.zeros(96, f)]),
        "eps": np.repeat(np.array([1e-5, 1e-6, 64e-5, 1e-12], f), P),
    }
    cols["q_gain"] = np.tile(i["hy_q_gain_2"][0], 2)
    cols["k_gain"] = np.tile(i["hy_k_gain_2"][0], 2)
    cols["qk_eps"] = np.concatenate([np.full(8, 64e-6, f), np.full(120, 1e-6, f)])
    cols["f_bias"] = np.concatenate([i["hy_f_bias_2"][0], np.zeros(120, f)])
    cols["pool_scale"] = i["hy_pool_scale_2"]
    for n in ("mu", "w0", "a0", "k_k", "k_a", "r_k"):
        cols[f"rw_{n}"] = i[f"rw_{n}_2"]
    con = constants()
    con["router_bias"] = np.broadcast_to(i["router_bias"], (P, 64))
    par = np.concatenate([tile_cols(cols[n]) for n, _ in PARAMS] + [con[n] for n in STAY + LATE], axis=1).astype(f)
    xT = np.ascontiguousarray(i["x"][0].T).reshape(8, P, T).transpose(1, 0, 2).reshape(P, 8 * T)
    return {
        "xT": np.ascontiguousarray(xT),
        "c": np.ascontiguousarray(i["c"]),
        "wts": wts,
        "experts": experts,
        "rw_ln": np.stack([i["rw_ln_w_2"][0], i["rw_ln_b_2"][0]]),
        "par": np.ascontiguousarray(par),
        "cst": np.ascontiguousarray(np.concatenate([con[n] for n in CONST], axis=1).astype(f)),
    }


def setup(K):
    con = constants()
    K.c = {}
    K.ccol = {}
    at = 0
    for n in CONST:
        K.ccol[n] = (at, con[n].shape[1])
        at += con[n].shape[1]
    K.cst = lambda n: K.ins["cst"][:, K.ccol[n][0]:K.ccol[n][0] + K.ccol[n][1]]
    n = NPAR + sum(con[n].shape[1] for n in STAY)
    K.par = K.buf("par", 0, [P, n + sum(LATE_COLS.values())])
    K.t_par = K.load(K.par[:, 0:n], K.ins["par"][:, 0:n])
    K.t_cst = [K.t_par]
    at = NPAR
    for n in STAY:
        K.c[n] = K.par[:, at:at + con[n].shape[1]]
        at += con[n].shape[1]
    for n in LATE:
        K.c[n] = K.par[:, at:at + LATE_COLS[n]]
        at += LATE_COLS[n]
    assert at * 4 <= 8 * 1024
    K.acc = K.buf("acc", 9, [P, 48])
    K.mod = K.buf("mod", 9.25, [P, 48])
    K.small = K.buf("small", 9.5, [P, 64])
    K.mod_ready = [None] * 48
    K.nroot = 0
    K.ada_last = []


def setup_late(K):
    n = NPAR + sum(K.c[m].shape[1] for m in STAY)
    K.t_late = K.load(K.par[:, n:], K.ins["par"][:, n:], queue=K.act)


def program(nc, ins, out):
    with ExitStack() as ctx:
        K = Core(nc, ctx, ins)
        S = Stream(K, plan(), ins["wts"], ins["experts"])
        x, ready, after, norm = moe(K, S, *first_block(K, S), fox_norm(K))
        first, mix, second = ffn_norm(K, 0), rwkv_norm(K), ffn_norm(K, 1)
        x, ready = fox(K, S, x, ready, after, norm, first.pair)
        x, ready = ffn(K, S, 0, x, ready, first, lambda n, x, t: mix.pair(n, x, t, eng=K.dve if n == 3 else K.pool))
        x, ready, after = rwkv(K, S, x, ready, mix, second.pair)

        def store(i, x, ready):
            o = out.rearrange("p (j t) -> p j t", j=8)[:, 2 * i:2 * i + 2, :]
            K.final.append(K.load(o, x[:, 2 * i:2 * i + 2, :], after=ready))

        ffn(K, S, 1, x, ready, second, store, after)
        K.run()


def kernel(**inputs):
    import concourse.bacc as _bacc
    from concourse.bass_utils import run_bass_kernel_spmd as _run

    nc = _bacc.Bacc("TRN2", target_bir_lowering=False, num_devices=1)
    arrays, args = {}, {}
    for name, a in pack({n: np.asarray(v) for n, v in inputs.items()}).items():
        arrays["in_" + name] = a
        args[name] = nc.dram_tensor("in_" + name, a.shape, mybir.dt.from_np(a.dtype), kind="ExternalInput").ap()
    out = nc.dram_tensor("out", (P, 8 * T), F32, kind="ExternalOutput").ap()
    program(nc, args, out)
    r = _run(nc, [arrays], core_ids=[0])
    got = r.results[0]["out"].reshape(P, 8, T)
    return np.ascontiguousarray(got.transpose(2, 1, 0)).reshape(1, T, D)
```
